# Optimizing a Trainium2 kernel written in Bass

```python
import math
import jax, jax.numpy as jnp
from jax import lax
import numpy as np

D_MODEL = 1024
BATCH = 1
SEQ = 512
DEPTH = 2

GROUP_WIDTH = 256
MIX_WIDTH = 4 * GROUP_WIDTH
Q_BLOCK = 128
EPS = 1e-6
D_FF = 2816

A_HEADS = 4
A_HEAD_DIM = 64
IDX_HEADS = 8
IDX_DIM = 32
TOPK_MAX = 256
REL_BUCKETS = 32
REL_MAX_DIST = 128

B_HEADS = 4
B_KEY_DIM = 32
B_VAL_DIM = 64
B_GATE_RANK = 16
B_GATE_TAU = 16.0
B_CHUNK = 64

C_CHANNELS = 256
C_KERNEL = 31

D_HEADS = 4
D_Q_RANK = 256
D_KV_RANK = 128
D_NOPE = 64
D_ROPE = 32
D_V = 64
D_QK = D_NOPE + D_ROPE
ROPE_THETA = 10000.0

IN_WIDTHS = (
    A_HEADS * A_HEAD_DIM, A_HEADS * A_HEAD_DIM, A_HEADS * A_HEAD_DIM,
    IDX_HEADS * IDX_DIM, IDX_DIM, IDX_HEADS,
    B_HEADS * B_KEY_DIM, B_HEADS * B_KEY_DIM, B_HEADS * B_VAL_DIM,
    B_GATE_RANK, B_HEADS * B_VAL_DIM,
    2 * C_CHANNELS,
    D_Q_RANK, D_KV_RANK, D_ROPE,
)
IN_WIDTH = sum(IN_WIDTHS)


def rmsnorm(x, g):
    x32 = x.astype(jnp.float32)
    y = x32 * lax.rsqrt(jnp.mean(x32 * x32, axis=-1, keepdims=True) + EPS)
    return (y * g.astype(jnp.float32)).astype(x.dtype)

def swiglu(x, w_gate, w_up, w_down):
    return (jax.nn.silu(x @ w_gate) * (x @ w_up)) @ w_down

def t5_bucket(dist):
    max_exact = REL_BUCKETS // 2
    d = jnp.maximum(dist, 0)
    df = jnp.maximum(d, 1).astype(jnp.float32)
    large = max_exact + (jnp.log(df / max_exact) / math.log(REL_MAX_DIST / max_exact)
                         * (REL_BUCKETS - max_exact)).astype(jnp.int32)
    large = jnp.minimum(large, REL_BUCKETS - 1)
    return jnp.where(d < max_exact, d, large)

def rope(x, pos):
    half = x.shape[-1] // 2
    freqs = ROPE_THETA ** (-jnp.arange(half, dtype=jnp.float32) / half)
    ang = pos.astype(jnp.float32)[:, None] * freqs[None, :]
    cos = jnp.cos(ang)[:, None, :]
    sin = jnp.sin(ang)[:, None, :]
    x32 = x.astype(jnp.float32)
    x1, x2 = x32[..., :half], x32[..., half:]
    return jnp.concatenate([x1 * cos - x2 * sin, x2 * cos + x1 * sin], axis=-1).astype(x.dtype)

def dsa_mixer(q, k, v, iq, ik, iw, g_q, g_k, rel_bias):
    bsz, L = q.shape[0], q.shape[1]
    topk = min(TOPK_MAX, L // 4)
    q = rmsnorm(q, g_q)
    k = rmsnorm(k, g_k)
    scale = A_HEAD_DIM ** -0.5
    idx_scale = IDX_DIM ** -0.5
    w = iw.astype(jnp.float32) * (IDX_HEADS ** -0.5)
    key_pos = jnp.arange(L)

    def block(i):
        t0 = i * Q_BLOCK
        qb = lax.dynamic_slice_in_dim(q, t0, Q_BLOCK, axis=1)
        iqb = lax.dynamic_slice_in_dim(iq, t0, Q_BLOCK, axis=1)
        wb = lax.dynamic_slice_in_dim(w, t0, Q_BLOCK, axis=1)
        qpos = t0 + jnp.arange(Q_BLOCK)
        causal = key_pos[None, :] <= qpos[:, None]
        s = jax.nn.relu(jnp.einsum('bthd,bsd->bths', iqb, ik).astype(jnp.float32) * idx_scale)
        score = jnp.einsum('bths,bth->bts', s, wb)
        score = jnp.where(causal[None], score, -jnp.inf)
        _, sel = lax.top_k(score, topk)
        ks = jax.vmap(lambda kb, ib: kb[ib])(k, sel)
        vs = jax.vmap(lambda vb, ib: vb[ib])(v, sel)
        valid = sel <= qpos[None, :, None]
        bias = rel_bias[t5_bucket(qpos[None, :, None] - sel)]
        logits = (jnp.einsum('bthd,btkhd->bthk', qb, ks).astype(jnp.float32) * scale
                  + jnp.swapaxes(bias, 2, 3).astype(jnp.float32))
        logits = jnp.where(valid[:, :, None, :], logits, -jnp.inf)
        p = jax.nn.softmax(logits, axis=-1)
        return jnp.einsum('bthk,btkhd->bthd', p.astype(v.dtype), vs)

    out = lax.map(block, jnp.arange(L // Q_BLOCK))
    return jnp.moveaxis(out, 0, 1).reshape(bsz, L, A_HEADS * A_HEAD_DIM)

def gla_mixer(q, k, v, g_lat, r, w_gate_up, b_gate, g_out):
    bsz, L = q.shape[0], q.shape[1]
    f32 = jnp.float32
    log_a = jax.nn.log_sigmoid((g_lat @ w_gate_up + b_gate).astype(f32)) / B_GATE_TAU
    log_a = log_a.reshape(bsz, L, B_HEADS, B_KEY_DIM)
    qf = q.astype(f32) * (B_KEY_DIM ** -0.5)
    kf = k.astype(f32)
    vf = v.astype(f32)
    n = L // B_CHUNK

    def to_chunks(t):
        return jnp.moveaxis(t.reshape(bsz, n, B_CHUNK, t.shape[2], t.shape[3]), 1, 0)

    tri = jnp.tril(jnp.ones((B_CHUNK, B_CHUNK), dtype=bool))

    def step(S, inp):
        qc, kc, vc, gc = inp
        b = jnp.cumsum(gc, axis=1)
        o_inter = jnp.einsum('bchk,bhkv->bchv', qc * jnp.exp(b), S)
        diff = b[:, :, None] - b[:, None, :]
        decay = jnp.exp(jnp.where(tri[None, :, :, None, None], diff, -jnp.inf))
        A = jnp.einsum('bihk,bjhk,bijhk->bhij', qc, kc, decay)
        o_intra = jnp.einsum('bhij,bjhv->bihv', A, vc)
        b_last = b[:, -1]
        k_dec = kc * jnp.exp(b_last[:, None] - b)
        S = jnp.exp(b_last)[..., None] * S + jnp.einsum('bchk,bchv->bhkv', k_dec, vc)
        return S, o_inter + o_intra

    S0 = jnp.zeros((bsz, B_HEADS, B_KEY_DIM, B_VAL_DIM), f32)
    _, o = lax.scan(step, S0, (to_chunks(qf), to_chunks(kf), to_chunks(vf), to_chunks(log_a)))
    o = jnp.moveaxis(o, 0, 1).reshape(bsz, L, B_HEADS, B_VAL_DIM)
    o = rmsnorm(o, g_out).reshape(bsz, L, B_HEADS * B_VAL_DIM)
    return (o * jax.nn.silu(r.astype(f32))).astype(q.dtype)

def conv_mixer(u, w_dw, b_dw, g_norm):
    a, gate = jnp.split(u, 2, axis=-1)
    h = a * jax.nn.sigmoid(gate)
    h = lax.conv_general_dilated(h, w_dw.astype(h.dtype), window_strides=(1,),
                                 padding=[(C_KERNEL - 1, 0)],
                                 dimension_numbers=('NWC', 'WIO', 'NWC'),
                                 feature_group_count=C_CHANNELS) + b_dw
    return jax.nn.silu(rmsnorm(h, g_norm))

def mla_mixer(c_q, c_kv, k_pe, g_qa, w_uq, g_kva, w_ukv, g_q, g_k, pos):
    bsz, L = c_q.shape[0], c_q.shape[1]
    q = (rmsnorm(c_q, g_qa) @ w_uq).reshape(bsz, L, D_HEADS, D_QK)
    kv = (rmsnorm(c_kv, g_kva) @ w_ukv).reshape(bsz, L, D_HEADS, D_NOPE + D_V)
    k_nope, v = kv[..., :D_NOPE], kv[..., D_NOPE:]
    k = jnp.concatenate([k_nope, jnp.broadcast_to(k_pe[:, :, None, :], (bsz, L, D_HEADS, D_ROPE))], axis=-1)
    q = rmsnorm(q, g_q)
    k = rmsnorm(k, g_k)
    q = jnp.concatenate([q[..., :D_NOPE], rope(q[..., D_NOPE:], pos)], axis=-1)
    k = jnp.concatenate([k[..., :D_NOPE], rope(k[..., D_NOPE:], pos)], axis=-1)
    scale = D_QK ** -0.5
    key_pos = jnp.arange(L)

    def block(i):
        t0 = i * Q_BLOCK
        qb = lax.dynamic_slice_in_dim(q, t0, Q_BLOCK, axis=1)
        qpos = t0 + jnp.arange(Q_BLOCK)
        causal = key_pos[None, :] <= qpos[:, None]
        logits = jnp.einsum('bthd,bshd->bhts', qb, k).astype(jnp.float32) * scale
        logits = jnp.where(causal[None, None], logits, -jnp.inf)
        p = jax.nn.softmax(logits, axis=-1)
        return jnp.einsum('bhts,bshd->bthd', p.astype(v.dtype), v)

    out = lax.map(block, jnp.arange(L // Q_BLOCK))
    return jnp.moveaxis(out, 0, 1).reshape(bsz, L, D_HEADS * D_V)

def hybrid_layer(x, ffn1_norm, ffn1_gate, ffn1_up, ffn1_down, mix_norm, w_in,
                 a_q_norm, a_k_norm, rel_bias, b_gate_up, b_gate_bias, b_out_norm,
                 c_dw_w, c_dw_b, c_norm, d_qa_norm, d_uq, d_kva_norm, d_ukv, d_q_norm, d_k_norm,
                 w_out, ffn2_norm, ffn2_gate, ffn2_up, ffn2_down, pos):
    bsz, L = x.shape[0], x.shape[1]
    x = x + 0.5 * swiglu(rmsnorm(x, ffn1_norm), ffn1_gate, ffn1_up, ffn1_down)

    z = rmsnorm(x, mix_norm) @ w_in
    (aq, ak, av, iq, ik, iw, bq, bk, bv, bg, br, cu, dcq, dckv, dkpe) = jnp.split(
        z, np.cumsum(IN_WIDTHS)[:-1].tolist(), axis=-1)

    y_a = dsa_mixer(aq.reshape(bsz, L, A_HEADS, A_HEAD_DIM), ak.reshape(bsz, L, A_HEADS, A_HEAD_DIM),
                    av.reshape(bsz, L, A_HEADS, A_HEAD_DIM), iq.reshape(bsz, L, IDX_HEADS, IDX_DIM),
                    ik, iw, a_q_norm, a_k_norm, rel_bias)
    y_b = gla_mixer(bq.reshape(bsz, L, B_HEADS, B_KEY_DIM), bk.reshape(bsz, L, B_HEADS, B_KEY_DIM),
                    bv.reshape(bsz, L, B_HEADS, B_VAL_DIM), bg, br, b_gate_up, b_gate_bias, b_out_norm)
    y_c = conv_mixer(cu, c_dw_w, c_dw_b, c_norm)
    y_d = mla_mixer(dcq, dckv, dkpe, d_qa_norm, d_uq, d_kva_norm, d_ukv, d_q_norm, d_k_norm, pos)

    y = jnp.concatenate([y_a, y_b.astype(x.dtype), y_c.astype(x.dtype), y_d], axis=-1) @ w_out
    x = x + y

    x = x + 0.5 * swiglu(rmsnorm(x, ffn2_norm), ffn2_gate, ffn2_up, ffn2_down)
    return x

def first_inputs(seed: int = 0) -> dict:
    key = jax.random.key(seed)
    ks = iter(jax.random.split(key, 40))
    f32 = jnp.float32

    def w(shape, fan_in):
        return jax.random.normal(next(ks), shape, f32) * (fan_in ** -0.5)

    def gain(shape):
        return 1.0 + 0.05 * jax.random.normal(next(ks), shape, f32)

    def small(shape, s):
        return s * jax.random.normal(next(ks), shape, f32)

    Ld = DEPTH
    return {
        "x": jax.random.normal(next(ks), (BATCH, SEQ, D_MODEL), f32),
        "ffn1_norm": gain((Ld, D_MODEL)),
        "ffn1_gate": w((Ld, D_MODEL, D_FF), D_MODEL),
        "ffn1_up": w((Ld, D_MODEL, D_FF), D_MODEL),
        "ffn1_down": w((Ld, D_FF, D_MODEL), D_FF),
        "mix_norm": gain((Ld, D_MODEL)),
        "w_in": w((Ld, D_MODEL, IN_WIDTH), D_MODEL),
        "a_q_norm": gain((Ld, A_HEAD_DIM)),
        "a_k_norm": gain((Ld, A_HEAD_DIM)),
        "rel_bias": small((REL_BUCKETS, A_HEADS), 0.2),
        "b_gate_up": w((Ld, B_GATE_RANK, B_HEADS * B_KEY_DIM), B_GATE_RANK),
        "b_gate_bias": small((Ld, B_HEADS * B_KEY_DIM), 0.1),
        "b_out_norm": gain((Ld, B_VAL_DIM)),
        "c_dw_w": w((Ld, C_KERNEL, 1, C_CHANNELS), C_KERNEL),
        "c_dw_b": small((Ld, C_CHANNELS), 0.02),
        "c_norm": gain((Ld, C_CHANNELS)),
        "d_qa_norm": gain((Ld, D_Q_RANK)),
        "d_uq": w((Ld, D_Q_RANK, D_HEADS * D_QK), D_Q_RANK),
        "d_kva_norm": gain((Ld, D_KV_RANK)),
        "d_ukv": w((Ld, D_KV_RANK, D_HEADS * (D_NOPE + D_V)), D_KV_RANK),
        "d_q_norm": gain((Ld, D_QK)),
        "d_k_norm": gain((Ld, D_QK)),
        "w_out": w((Ld, MIX_WIDTH, D_MODEL), MIX_WIDTH),
        "ffn2_norm": gain((Ld, D_MODEL)),
        "ffn2_gate": w((Ld, D_MODEL, D_FF), D_MODEL),
        "ffn2_up": w((Ld, D_MODEL, D_FF), D_MODEL),
        "ffn2_down": w((Ld, D_FF, D_MODEL), D_FF),
    }

def first_block(x, ffn1_norm, ffn1_gate, ffn1_up, ffn1_down, mix_norm, w_in, a_q_norm, a_k_norm,
              rel_bias, b_gate_up, b_gate_bias, b_out_norm, c_dw_w, c_dw_b, c_norm,
              d_qa_norm, d_uq, d_kva_norm, d_ukv, d_q_norm, d_k_norm, w_out,
              ffn2_norm, ffn2_gate, ffn2_up, ffn2_down):
    pos = jnp.arange(x.shape[1])
    for l in range(DEPTH):
        x = hybrid_layer(x, ffn1_norm[l], ffn1_gate[l], ffn1_up[l], ffn1_down[l], mix_norm[l], w_in[l],
                         a_q_norm[l], a_k_norm[l], rel_bias, b_gate_up[l], b_gate_bias[l], b_out_norm[l],
                         c_dw_w[l], c_dw_b[l], c_norm[l], d_qa_norm[l], d_uq[l], d_kva_norm[l], d_ukv[l],
                         d_q_norm[l], d_k_norm[l], w_out[l], ffn2_norm[l], ffn2_gate[l], ffn2_up[l],
                         ffn2_down[l], pos)
    return x


N_EVEN = (DEPTH + 1) // 2
N_ODD = DEPTH // 2
HEAD_DIM = 64
ATT_HEADS = D_MODEL // (2 * HEAD_DIM)
ATT_WIDTH = ATT_HEADS * HEAD_DIM
ROPE_DIM = HEAD_DIM // 4
ROPE_THETA_2 = 500000.0
DILATED_BRANCHES = ((128, 1), (512, 4), (2048, 16))
ATT_BLOCK = 128
NEG_INF = -1e30
SSM_WIDTH = D_MODEL - ATT_WIDTH
SSM_GROUP = 16
SSM_GROUPS = SSM_WIDTH // SSM_GROUP
SSM_STATE = 64
EVEN_IN = 3 * ATT_WIDTH + SSM_WIDTH
LRU_WIDTH = D_MODEL
LRU_BLOCKS = 4
LRU_BLOCK_DIM = LRU_WIDTH // LRU_BLOCKS
CONV_WIDTH = 4
RG_C = 8.0
FFN_HIDDEN = -(-8 * D_MODEL // (3 * 256)) * 256
NORM_EPS = 1e-6


def rms_norm(x, g):
    x32 = x.astype(jnp.float32)
    y = x32 * lax.rsqrt(jnp.mean(x32 * x32, axis=-1, keepdims=True) + NORM_EPS) * g.astype(jnp.float32)
    return y.astype(x.dtype)

def swiglu_2(x, w_gate, w_up, w_down):
    return (jax.nn.silu(x @ w_gate) * (x @ w_up)) @ w_down

def _linear_combine(e1, e2):
    a1, b1 = e1
    a2, b2 = e2
    return a1 * a2, a2 * b1 + b2

def partial_rope(t, positions):
    half = ROPE_DIM // 2
    inv_freq = ROPE_THETA_2 ** (-(jnp.arange(half, dtype=jnp.float32) * 2.0 / ROPE_DIM))
    ang = positions.astype(jnp.float32)[..., None] * inv_freq
    cos = jnp.cos(ang)[:, :, None, :]
    sin = jnp.sin(ang)[:, :, None, :]
    t1 = t[..., :half]
    t2 = t[..., half:ROPE_DIM]
    return jnp.concatenate([t1 * cos - t2 * sin, t2 * cos + t1 * sin, t[..., ROPE_DIM:]], axis=-1)

def _dilated_branch(q, k, v, window, dilation):
    b, s, h, c = q.shape
    L = s // dilation
    nb = -(-L // ATT_BLOCK)
    Lp = nb * ATT_BLOCK
    span = window // dilation

    def strided(t):
        t = t.reshape(b, L, dilation, h, c).transpose(0, 2, 1, 3, 4)
        return jnp.pad(t, ((0, 0), (0, 0), (0, Lp - L), (0, 0), (0, 0)))

    def band(t):
        t = jnp.pad(strided(t), ((0, 0), (0, 0), (ATT_BLOCK, 0), (0, 0), (0, 0)))
        t = t.reshape(b, dilation, nb + 1, ATT_BLOCK, h, c)
        return jnp.concatenate([t[:, :, :-1], t[:, :, 1:]], axis=3)

    qb = strided(q).reshape(b, dilation, nb, ATT_BLOCK, h, c)
    kb = band(k)
    vb = band(v)
    scores = jnp.einsum('brnqhc,brnkhc->brnhqk', qb, kb)
    qi = jnp.arange(ATT_BLOCK)[:, None] + ATT_BLOCK
    ki = jnp.arange(2 * ATT_BLOCK)[None, :]
    dist = qi - ki
    kpos = jnp.arange(nb)[:, None, None] * ATT_BLOCK + ki[None] - ATT_BLOCK
    mask = ((dist >= 0) & (dist <= span))[None] & (kpos >= 0)
    scores = jnp.where(mask[None, None, :, None], scores, NEG_INF)
    m = jnp.max(scores, axis=-1)
    p = jnp.exp(scores - m[..., None])
    l = jnp.sum(p, axis=-1)
    acc = jnp.einsum('brnhqk,brnkhc->brnqhc', p, vb)

    def unstride(t):
        t = t.reshape((b, dilation, Lp) + t.shape[4:])[:, :, :L]
        t = jnp.moveaxis(t, 1, 2)
        return t.reshape((b, s) + t.shape[3:])

    m = jnp.moveaxis(m, -1, 3)
    l = jnp.moveaxis(l, -1, 3)
    return unstride(acc), unstride(m), unstride(l)

def dilated_attention(q, k, v):
    outs = [_dilated_branch(q, k, v, w, d) for (w, d) in DILATED_BRANCHES]
    acc_all = jnp.stack([o[0] for o in outs])
    m_all = jnp.stack([o[1] for o in outs])
    l_all = jnp.stack([o[2] for o in outs])
    wts = jnp.exp(m_all - jnp.max(m_all, axis=0, keepdims=True))
    num = jnp.einsum('ibsh,ibshc->bshc', wts, acc_all)
    den = jnp.sum(wts * l_all, axis=0)
    return num / den[..., None]

def s5_mixer(u, a_re, a_im, log_dt, b_re, b_im, c_re, c_im, d_skip, w_glu):
    b, s, _ = u.shape
    u = u.reshape(b, s, SSM_GROUPS, SSM_GROUP)
    f32 = jnp.float32
    A = lax.complex(a_re.astype(f32), a_im.astype(f32))
    dt = jnp.exp(log_dt.astype(f32))[:, None]
    a_bar = jnp.exp(A * dt)
    b_bar = ((a_bar - 1.0) / A)[..., None] * lax.complex(b_re.astype(f32), b_im.astype(f32))
    bu = jnp.einsum('gpc,bsgc->bsgp', b_bar, u.astype(jnp.complex64))
    a_seq = jnp.broadcast_to(a_bar, (s,) + a_bar.shape)
    h = jax.vmap(lambda bu_b: lax.associative_scan(_linear_combine, (a_seq, bu_b), axis=0)[1])(bu)
    c_mat = lax.complex(c_re.astype(f32), c_im.astype(f32))
    y = jnp.einsum('gcp,bsgp->bsgc', c_mat, h).real + d_skip.astype(f32) * u
    y = jax.nn.gelu(y.reshape(b, s, SSM_WIDTH))
    return y * jax.nn.sigmoid(y @ w_glu.astype(f32))

def rglru_mixer(xb, conv_w, conv_b, w_r, b_r, w_i, b_i, lam):
    b, s, r = xb.shape
    f32 = jnp.float32
    xc = lax.conv_general_dilated(xb, conv_w.astype(f32)[:, None, :], window_strides=(1,),
                                  padding=[(CONV_WIDTH - 1, 0)],
                                  dimension_numbers=('NWC', 'WIO', 'NWC'),
                                  feature_group_count=r) + conv_b.astype(f32)
    xh = xc.reshape(b, s, LRU_BLOCKS, LRU_BLOCK_DIM)
    gate_r = jax.nn.sigmoid(jnp.einsum('bshi,hij->bshj', xh, w_r.astype(f32)).reshape(b, s, r) + b_r.astype(f32))
    gate_i = jax.nn.sigmoid(jnp.einsum('bshi,hij->bshj', xh, w_i.astype(f32)).reshape(b, s, r) + b_i.astype(f32))
    log_a = -RG_C * gate_r * jax.nn.softplus(-lam.astype(f32))
    a = jnp.exp(log_a)
    mult = jnp.sqrt(-jnp.expm1(2.0 * log_a))
    _, h = lax.associative_scan(_linear_combine, (a, mult * (gate_i * xc)), axis=1)
    return h

def even_mixer(xn, positions, w_in, w_out, a_re, a_im, log_dt, b_re, b_im, c_re, c_im, d_skip, w_glu):
    b, s, _ = xn.shape
    z = (xn @ w_in).astype(jnp.float32)
    q = z[..., :ATT_WIDTH].reshape(b, s, ATT_HEADS, HEAD_DIM)
    k = z[..., ATT_WIDTH:2 * ATT_WIDTH].reshape(b, s, ATT_HEADS, HEAD_DIM)
    v = z[..., 2 * ATT_WIDTH:3 * ATT_WIDTH].reshape(b, s, ATT_HEADS, HEAD_DIM)
    u = z[..., 3 * ATT_WIDTH:]
    q = partial_rope(q, positions) * (HEAD_DIM ** -0.5)
    k = partial_rope(k, positions)
    att = dilated_attention(q, k, v).reshape(b, s, ATT_WIDTH)
    ssm = s5_mixer(u, a_re, a_im, log_dt, b_re, b_im, c_re, c_im, d_skip, w_glu)
    y = jnp.concatenate([att, ssm], axis=-1).astype(w_out.dtype)
    return (y @ w_out).astype(xn.dtype)

def odd_mixer(xn, w_in, w_out, conv_w, conv_b, w_r, b_r, w_i, b_i, lam):
    z = (xn @ w_in).astype(jnp.float32)
    h = rglru_mixer(z[..., :LRU_WIDTH], conv_w, conv_b, w_r, b_r, w_i, b_i, lam)
    y = (h * jax.nn.gelu(z[..., LRU_WIDTH:])).astype(w_out.dtype)
    return (y @ w_out).astype(xn.dtype)

def second_inputs(seed: int = 0) -> dict:
    key = jax.random.key(seed)
    ks = iter(jax.random.split(key, 32))
    f32 = jnp.float32

    def nrm(shape, scale):
        return jax.random.normal(next(ks), shape, f32) * scale

    G, P, NC, BD = SSM_GROUPS, SSM_STATE, SSM_GROUP, LRU_BLOCK_DIM
    x = nrm((BATCH, SEQ, D_MODEL), 1.0)
    offset = jax.random.randint(next(ks), (BATCH, 1), 0, SEQ, dtype=jnp.int32)
    positions = offset + jnp.arange(SEQ, dtype=jnp.int32)[None, :]
    norm_mix_pre = 1.0 + nrm((DEPTH, D_MODEL), 0.05)
    norm_mix_post = 1.0 + nrm((DEPTH, D_MODEL), 0.05)
    norm_ffn_pre = 1.0 + nrm((DEPTH, D_MODEL), 0.05)
    norm_ffn_post = 1.0 + nrm((DEPTH, D_MODEL), 0.05)
    ev_w_in = nrm((N_EVEN, D_MODEL, EVEN_IN), D_MODEL ** -0.5)
    ev_w_out = nrm((N_EVEN, D_MODEL, D_MODEL), D_MODEL ** -0.5)
    s5_a_re = -0.5 * jnp.exp(nrm((N_EVEN, G, P), 0.02))
    s5_a_im = jnp.pi * jnp.arange(P, dtype=f32) + nrm((N_EVEN, G, P), 0.02)
    s5_log_dt = jax.random.uniform(next(ks), (N_EVEN, G), f32, math.log(1e-3), math.log(1e-1))
    s5_b_re = nrm((N_EVEN, G, P, NC), (2 * NC) ** -0.5)
    s5_b_im = nrm((N_EVEN, G, P, NC), (2 * NC) ** -0.5)
    s5_c_re = nrm((N_EVEN, G, NC, P), (2 * P) ** -0.5)
    s5_c_im = nrm((N_EVEN, G, NC, P), (2 * P) ** -0.5)
    s5_d = nrm((N_EVEN, G, NC), 1.0)
    s5_w_glu = nrm((N_EVEN, SSM_WIDTH, SSM_WIDTH), SSM_WIDTH ** -0.5)
    od_w_in = nrm((N_ODD, D_MODEL, 2 * LRU_WIDTH), D_MODEL ** -0.5)
    od_w_out = nrm((N_ODD, LRU_WIDTH, D_MODEL), LRU_WIDTH ** -0.5)
    rg_conv_w = nrm((N_ODD, CONV_WIDTH, LRU_WIDTH), CONV_WIDTH ** -0.5)
    rg_conv_b = nrm((N_ODD, LRU_WIDTH), 0.01)
    rg_w_r = nrm((N_ODD, LRU_BLOCKS, BD, BD), BD ** -0.5)
    rg_b_r = nrm((N_ODD, LRU_WIDTH), 0.01)
    rg_w_i = nrm((N_ODD, LRU_BLOCKS, BD, BD), BD ** -0.5)
    rg_b_i = nrm((N_ODD, LRU_WIDTH), 0.01)
    a0 = jax.random.uniform(next(ks), (N_ODD, LRU_WIDTH), f32, 0.9, 0.999)
    sig = a0 ** (1.0 / RG_C)
    rg_lam = jnp.log(sig) - jnp.log1p(-sig)
    ffn_w_gate = nrm((DEPTH, D_MODEL, FFN_HIDDEN), D_MODEL ** -0.5)
    ffn_w_up = nrm((DEPTH, D_MODEL, FFN_HIDDEN), D_MODEL ** -0.5)
    ffn_w_down = nrm((DEPTH, FFN_HIDDEN, D_MODEL), FFN_HIDDEN ** -0.5)
    return {'x': x, 'positions': positions,
            'norm_mix_pre': norm_mix_pre, 'norm_mix_post': norm_mix_post,
            'norm_ffn_pre': norm_ffn_pre, 'norm_ffn_post': norm_ffn_post,
            'ev_w_in': ev_w_in, 'ev_w_out': ev_w_out,
            's5_a_re': s5_a_re, 's5_a_im': s5_a_im, 's5_log_dt': s5_log_dt,
            's5_b_re': s5_b_re, 's5_b_im': s5_b_im, 's5_c_re': s5_c_re, 's5_c_im': s5_c_im,
            's5_d': s5_d, 's5_w_glu': s5_w_glu,
            'od_w_in': od_w_in, 'od_w_out': od_w_out,
            'rg_conv_w': rg_conv_w, 'rg_conv_b': rg_conv_b,
            'rg_w_r': rg_w_r, 'rg_b_r': rg_b_r, 'rg_w_i': rg_w_i, 'rg_b_i': rg_b_i, 'rg_lam': rg_lam,
            'ffn_w_gate': ffn_w_gate, 'ffn_w_up': ffn_w_up, 'ffn_w_down': ffn_w_down}

def second_block(x, positions, norm_mix_pre, norm_mix_post, norm_ffn_pre, norm_ffn_post,
              ev_w_in, ev_w_out, s5_a_re, s5_a_im, s5_log_dt, s5_b_re, s5_b_im, s5_c_re, s5_c_im,
              s5_d, s5_w_glu, od_w_in, od_w_out, rg_conv_w, rg_conv_b, rg_w_r, rg_b_r, rg_w_i, rg_b_i,
              rg_lam, ffn_w_gate, ffn_w_up, ffn_w_down):
    for layer in range(DEPTH):
        hn = rms_norm(x, norm_mix_pre[layer])
        if layer % 2 == 0:
            e = layer // 2
            mix = even_mixer(hn, positions, ev_w_in[e], ev_w_out[e], s5_a_re[e], s5_a_im[e],
                             s5_log_dt[e], s5_b_re[e], s5_b_im[e], s5_c_re[e], s5_c_im[e],
                             s5_d[e], s5_w_glu[e])
        else:
            o = layer // 2
            mix = odd_mixer(hn, od_w_in[o], od_w_out[o], rg_conv_w[o], rg_conv_b[o],
                            rg_w_r[o], rg_b_r[o], rg_w_i[o], rg_b_i[o], rg_lam[o])
        x = x + rms_norm(mix, norm_mix_post[layer])
        hn = rms_norm(x, norm_ffn_pre[layer])
        ff = swiglu_2(hn, ffn_w_gate[layer], ffn_w_up[layer], ffn_w_down[layer])
        x = x + rms_norm(ff, norm_ffn_post[layer])
    return x


def setup_inputs(seed=0):
    out = dict(first_inputs(seed))
    for name, value in second_inputs(seed + 1).items():
        if name != "x":
            out[name + "_2"] = value
    return out


def reference(
    x, ffn1_norm, ffn1_gate, ffn1_up, ffn1_down, mix_norm, w_in, a_q_norm, a_k_norm, rel_bias,
    b_gate_up, b_gate_bias, b_out_norm, c_dw_w, c_dw_b, c_norm, d_qa_norm, d_uq, d_kva_norm,
    d_ukv, d_q_norm, d_k_norm, w_out, ffn2_norm, ffn2_gate, ffn2_up, ffn2_down, positions_2,
    norm_mix_pre_2, norm_mix_post_2, norm_ffn_pre_2, norm_ffn_post_2, ev_w_in_2, ev_w_out_2,
    s5_a_re_2, s5_a_im_2, s5_log_dt_2, s5_b_re_2, s5_b_im_2, s5_c_re_2, s5_c_im_2, s5_d_2,
    s5_w_glu_2, od_w_in_2, od_w_out_2, rg_conv_w_2, rg_conv_b_2, rg_w_r_2, rg_b_r_2, rg_w_i_2,
    rg_b_i_2, rg_lam_2, ffn_w_gate_2, ffn_w_up_2, ffn_w_down_2,
):
    x = first_block(
        x, ffn1_norm, ffn1_gate, ffn1_up, ffn1_down, mix_norm, w_in, a_q_norm, a_k_norm,
        rel_bias, b_gate_up, b_gate_bias, b_out_norm, c_dw_w, c_dw_b, c_norm, d_qa_norm, d_uq,
        d_kva_norm, d_ukv, d_q_norm, d_k_norm, w_out, ffn2_norm, ffn2_gate, ffn2_up, ffn2_down,
    )
    return second_block(
        x, positions_2, norm_mix_pre_2, norm_mix_post_2, norm_ffn_pre_2, norm_ffn_post_2,
        ev_w_in_2, ev_w_out_2, s5_a_re_2, s5_a_im_2, s5_log_dt_2, s5_b_re_2, s5_b_im_2,
        s5_c_re_2, s5_c_im_2, s5_d_2, s5_w_glu_2, od_w_in_2, od_w_out_2, rg_conv_w_2,
        rg_conv_b_2, rg_w_r_2, rg_b_r_2, rg_w_i_2, rg_b_i_2, rg_lam_2, ffn_w_gate_2, ffn_w_up_2,
        ffn_w_down_2,
    )


_drawn_inputs = setup_inputs


def setup_inputs(seed=0):
    import zlib

    import numpy as np

    out = dict(_drawn_inputs(seed))
    spreads = {}
    factors = {'a_q_norm': 6.361,
     'a_k_norm': 6.045,
     'd_qa_norm': 6.422,
     'd_kva_norm': 2.993,
     'd_q_norm': 6.984,
     'd_k_norm': 7.126,
     's5_a_re_2': 200.0,
     'rg_conv_b_2': 4.158,
     'rg_b_r_2': 64.0,
     'rg_b_i_2': 42.476,
     's5_a_im_2': 56.68,
     's5_log_dt_2': 60.368,
     's5_b_re_2': 64.0,
     's5_b_im_2': 64.0,
     's5_c_re_2': 64.0,
     's5_c_im_2': 64.0}
    for name, (base, spread) in spreads.items():
        noise = np.random.default_rng([zlib.crc32(name.encode()), seed]).standard_normal(out[name].shape)
        drawn = base * np.exp(spread * noise) if base else spread * noise
        out[name] = __import__('jax').numpy.asarray(drawn.astype(out[name].dtype))
    for name, factor in factors.items():
        out[name] = (out[name] * factor).astype(out[name].dtype)
    return out
```

```python
import math
from itertools import count

import numpy as np

import concourse.bass as bass
from concourse import mybir
from contextlib import ExitStack

F32 = mybir.dt.float32
I32 = mybir.dt.int32
ALU = mybir.AluOpType
ACT = mybir.ActivationFunctionType
AX = mybir.AxisListType

P = 128
SEQ = 512
TB = SEQ // P
D = 1024
KD = D // P
FF = 2816
NF = FF // P
DEPTH = 2
NEG = -1e30
SENTINEL = -3e38
EPS = 1e-6
TOPK = min(256, SEQ // 4)
A_HEADS, A_DIM = 4, 64
IDX_HEADS, IDX_DIM = 8, 32
B_HEADS, B_KEY, B_VAL, B_CHUNK, B_RANK = 4, 32, 64, 64, 16
NCH = SEQ // B_CHUNK
TAPS = 31
D_HEADS, D_NOPE, D_ROPE, D_V = 4, 64, 32, 64
D_QK = D_NOPE + D_ROPE
E_HEADS, E_DIM, E_ROPE = 8, 64, 16
SSM_G, SSM_P, SSM_C = 32, 64, 16
NST = SSM_G * SSM_P // P
LRU_TAPS = 4
BIAS_N = 640

_w = dict(aq=256, ak=256, av=256, iq=256, ik=32, iw=8, bq=128, bk=128, bv=256, bg=16, br=256,
          ca=256, cg=256, dcq=256, dckv=128, dkpe=32)
WCOL, _at = {}, 0
for _n, _c in _w.items():
    WCOL[_n] = _at
    _at += _c



def shape_constants():
    f = np.float32
    out = {}
    p = np.arange(P)
    out["ident"] = np.eye(P, dtype=f)
    out["blk64"] = ((p[:, None] // 64) == (p[None] // 64)).astype(f) / f(64)
    out["mean1024"] = np.full((P, P), 1 / 1024, f)
    out["mean256"] = np.full((P, P), 1 / 256, f)
    out["mean128"] = np.full((P, P), 1 / 128, f)
    m96 = np.zeros((P, D_QK), f)
    m96[:D_QK] = f(1) / f(D_QK)
    out["mean96"] = m96
    half = D_ROPE // 2
    r96 = np.zeros((P, D_QK), f)
    for i in range(half):
        r96[D_NOPE + half + i, D_NOPE + i] = -1
        r96[D_NOPE + i, D_NOPE + half + i] = 1
    out["rot96"] = r96
    eh = E_ROPE // 2
    r128 = np.zeros((P, P), f)
    for b in range(0, P, E_DIM):
        for i in range(eh):
            r128[b + eh + i, b + i] = -1
            r128[b + i, b + eh + i] = 1
    out["rot128"] = r128
    out["causal"] = np.where(p[None] > p[:, None], f(NEG), f(0)).astype(f)
    out["tri"] = (p[:, None] % B_CHUNK <= np.arange(B_CHUNK)[None]).astype(f)
    out["headblk"] = (p[:, None] // B_KEY == np.arange(B_HEADS * B_VAL)[None] // B_VAL).astype(f)
    dist = p[:, None] - (np.arange(SEQ)[None] - (SEQ - P))
    n = (((dist >= 0) & (dist <= 128)).astype(int) + ((dist >= 0) & (dist % 4 == 0)) + ((dist >= 0) & (dist % 16 == 0)))
    out["lnmult"] = np.where(n > 0, np.log(np.maximum(n, 1)), NEG).astype(f)
    t = np.arange(SEQ, dtype=f)
    fr = (f(10000.0) ** (-np.arange(half, dtype=f) / f(half))).astype(f)
    ang = (t[None] * fr[:, None]).astype(f)
    c96, s96 = np.zeros((P, SEQ), f), np.zeros((P, SEQ), f)
    c96[:D_NOPE] = 1
    for o in (D_NOPE, D_NOPE + half):
        c96[o:o + half], s96[o:o + half] = np.cos(ang), np.sin(ang)
    out["cos96"], out["sin96"] = c96, s96
    cm = np.ones((P, SEQ), f)
    cm[:, ::B_CHUNK] = 0
    out["chunkmask"] = cm
    out["iota"] = np.broadcast_to(t, (P, SEQ)).copy()
    out["headcol"] = (p[:, None] // B_KEY == np.arange(B_HEADS)[None]).astype(f)
    inv = (f(500000.0) ** (-(np.arange(eh, dtype=f) * f(2.0) / f(E_ROPE)))).astype(f)
    out["freq"] = np.where(p % E_DIM < E_ROPE, inv[(p % E_DIM) % eh], 0).astype(f)[:, None]
    out["eps"] = np.full((P, 1), EPS, f)
    out["halfpi"] = np.full((P, 1), math.pi / 2, f)
    hot = np.zeros((P, BIAS_N), f)
    for x in range(BIAS_N):
        d = SEQ - 1 - x
        if d < 0:
            hot[32, x] = 1
        elif d < 16:
            hot[d, x] = 1
        else:
            hot[min(16 + int(f(np.log(f(d) / f(16)) / f(math.log(128 / 16)) * f(16))), 31), x] = 1
    out["half16"] = (p[:, None] // SSM_P == np.arange(2 * SSM_C)[None] // SSM_C).astype(f)
    out["flip"] = np.eye(P, dtype=f)[::-1].copy()
    out["onehot"] = hot
    return out


CONST_COLS, _at = {}, 0
for _n, _v in shape_constants().items():
    CONST_COLS[_n] = (_at, _v.shape[1])
    _at += _v.shape[1]
CONST_W = _at
PRO_W = BIAS_N + P

ROWS1 = [("ffn1_norm", 2 * KD), ("mix_norm", 2 * KD), ("ffn2_norm", 2 * KD),
         ("norm_mix_pre_2", 2 * KD), ("norm_mix_post_2", 2 * KD), ("norm_ffn_pre_2", 2 * KD),
         ("norm_ffn_post_2", 2 * KD)]
LAYER_ROWS = [("a_q_norm", 1), ("a_k_norm", 1), ("b_gate_bias", 1), ("b_out_norm", 1), ("c_dw_b", 2), ("c_norm", 2),
              ("d_qa_norm", 2), ("d_kva_norm", 1), ("d_q_norm", 1), ("d_k_norm", 1)]
ROWS2 = [("s5_d_2", 4), ("rg_conv_b_2", 8), ("rg_b_r_2", 8), ("rg_b_i_2", 8), ("rg_lam_2", 8),
         ("rg_conv_w_2", 8 * LRU_TAPS)]


def row_starts(rows):
    out, at = {}, 0
    for n, c in rows:
        out[n] = at
        at += c
    return out, at


R1, NR1 = row_starts(ROWS1)
RL, NRL = row_starts(LAYER_ROWS)
R2, NR2 = row_starts([("layers", DEPTH * NRL)] + ROWS2)
NR3 = DEPTH * TAPS * 2

Z_BLOCKS = [
    [("iq0", 0, "feat"), ("iq1", 128, "feat")],
    [("ik", 0, "feat"), ("iw", 128, "iw"), ("bg", 136, "bg")],
    [("aq0", 0, "feat"), ("aq1", 128, "feat")],
    [("ak0", 0, "feat"), ("ak1", 128, "feat")],
    [("br0", 0, "feat"), ("br1", 128, "feat")],
    [("cg0", 0, "feat"), ("cg1", 128, "feat")],
    [("ca0", 0, "feat"), ("ca1", 128, "feat")],
    [("dcq0", 0, "feat"), ("dcq1", 128, "feat")],
    [("dckv", 0, "feat"), ("dkpe", 128, "kpe")],
    [("bq", 0, "feat"), ("bk", 128, "feat")],
    [("bv01", 0, "tok"), ("bv23", 1, "tok")],
    [("av01", 0, "tok"), ("av23", 1, "tok")],
]
Z_SRC = [("iq", 256), None, ("aq", 256), ("ak", 256), ("br", 256), ("cg", 256), ("ca", 256), ("dcq", 256),
         ("dckv", 160), ("bq", 256), ("bv", 256), ("av", 256)]
IDX_UNITS = [(tb, h) for tb in (3, 2, 1) for h in range(IDX_HEADS)]
Z_SEQ = []
_left = list(IDX_UNITS)
for _b, _chunks in enumerate(Z_BLOCKS):
    for _c, (_label, _col, _kind) in enumerate(_chunks):
        Z_SEQ.append(("z", _b, _c, _label, _col, _kind, _c == len(_chunks) - 1))
        if _b >= 2:
            for _ in range(2):
                if _left:
                    Z_SEQ.append(("idx",) + _left.pop(0))
assert not _left
Z_POS = {t[3]: n for n, t in enumerate(Z_SEQ) if t[0] == "z"}
NZ = len(Z_SEQ)
NIDX = len(IDX_UNITS)

E_BLOCKS = [("u", 1536), ("u", 1792), ("q", 0), ("q", 256), ("k", 512), ("k", 768), ("v", 1024), ("v", 1280)]
E_SEQ = []
_bu = _yy = 0
for _b, (_n, _c) in enumerate(E_BLOCKS):
    for _c in range(2):
        E_SEQ.append(("z", _b, _c, _n, 2 * (_b % 2) + _c))
        if len(E_SEQ) == 6:
            E_SEQ.append(("prep",))
        if _b >= 3:
            if _bu < NST:
                E_SEQ.append(("bu", _bu))
                _bu += 1
            if _bu >= 4:
                E_SEQ.append(("yy", _yy))
                _yy += 1
while _yy < NST:
    if _bu < NST:
        E_SEQ.append(("bu", _bu))
        _bu += 1
    E_SEQ.append(("yy", _yy))
    _yy += 1
E_Z = [t for t in E_SEQ if t[0] == "z"]
MAGIC = float(1.5 * 2 ** 23)

U_FFN = [2] * NF
U_Z = [6 if s is None else 1 for s in Z_SRC]
U_OUT = [1] * 4
U_LAYER = U_FFN + U_Z + U_OUT + U_FFN
U_EVEN = [1] * len(E_BLOCKS) + [1] * 2 + U_OUT + U_FFN
U_ODD = [1] * 8 + [1] * 2 + U_OUT + U_FFN
USE_EVEN = DEPTH * len(U_LAYER)
USE_ODD = USE_EVEN + len(U_EVEN)
DMA_EVEN = [DEPTH * sum(U_LAYER[_s::2]) for _s in range(2)]
DMA_ODD = [DMA_EVEN[_s] + sum(U_EVEN[_s::2]) for _s in range(2)]
X1 = (1 + 3 * DEPTH) * KD

IDX_POS = [n for n, t in enumerate(Z_SEQ) if t[0] == "idx"]
N_ROW_DMAS = len(ROWS1) + DEPTH * (len(LAYER_ROWS) + 3) + len(ROWS2) + 1 + 2


class Sem:

    def __init__(self, h, per, start):
        self.h, self.per, self.start = h, per, start

    def by(self, layer, k):
        return self.start + layer * self.per + k


class Eng:

    def __init__(self, e):
        self.e, self.l = e, 0


def program(nc, I, out):
    ctx = ExitStack()
    with ctx:
        def sb(name, shape, dt=F32):
            return ctx.enter_context(nc.sbuf_tensor(name, shape, dt))

        def sem(name, per=0, start=0):
            return Sem(ctx.enter_context(nc.semaphore(name)), per, start)

        x = sb("x", [P, KD, SEQ])
        xn = sb("xn", [P, KD, SEQ])
        y = xn
        wring = sb("wring", [P, 2, KD, 256])
        wdown = sb("wdown", [P, 2, NF, P])
        cst = sb("cst", [P, CONST_W - PRO_W])
        bias = sb("bias", [P, A_HEADS, SEQ])
        rows = sb("rows", [P, 4, P])
        col1 = sb("col1", [P, NR1])
        col2 = sb("col2", [P, NR2])
        col3 = sb("col3", [P, NR3])
        cur = sb("cur", [P, NRL])
        cur_dw = sb("cur_dw", [P, TAPS * 2])
        relb = sb("relb", [64, A_HEADS])
        hpad = sb("hpad", [P, 2, TAPS - 1 + SEQ])
        att_diag = sb("att_diag", [P, TB, B_HEADS, P])
        diag = sb("diag", [P, 8, P])
        small = sb("small", [P, 64])
        arena = sb("arena", [P, 46, SEQ])
        w_uq = arena[:, 43:45, 0:384]
        w_ukv = arena[:, 45, :]
        gup = sb("gup", [B_RANK, P])
        pb = [ctx.enter_context(nc.psum_tensor(f"bank{i}", [P, SEQ], F32)) for i in range(8)]
        wscr = wdown[:, :, :, :].rearrange("p a j c -> p (a j c)").rearrange("p (t c) -> p t c", c=SEQ)
        bias_dram = nc.dram_tensor("bias_by_distance", [A_HEADS, BIAS_N], F32, kind="Internal")

        def C(name):
            a, w = CONST_COLS[name]
            if a >= CONST_W - PRO_W:
                a -= CONST_W - PRO_W
                return arena[:, 12:14, :].rearrange("p t c -> p (t c)")[:, a:a + w]
            return cst[:, a:a + w]

        def T(n):
            return arena[:, n, :]

        def W(n):
            return wscr[:, n, :]

        ident = C("ident")
        hT = arena
        SQ, RT = 22, 30
        sg = arena[:, 31:33, :]
        t_iq, t_ik, t_aq, t_ak, t_av = [0, 1], 2, [3, 4], [5, 6], 7
        t_bq, t_bk, t_bv, t_br, t_ca, t_cg = 9, 10, 11, [13, 14], [15, 16], [17, 18]
        t_dcq, t_dckv, t_kpe, t_dv, t_dq, t_dk = [19, 20], 21, 22, 23, [25, 26, 27, 28], [29, 30, 31, 32]
        t_gl = 38
        t_zsq = [25, 26, 27, 28, 29, 30, 31]
        t_zr = [32, 36, 37, 39, 40, 41]
        t_hc, t_csq, t_cr = [15, 16], [17, 18], 19
        t_hraw, t_hsq, t_hr, t_hn = [0, 1], [2, 36], [37, 39], [40, 41]
        t_ab, t_qe, t_kdt, t_um = 42, 38, 42, 9
        t_o, t_osq, t_or = [10, 20], [17, 18], [2, 36]
        t_bm = [0, 1, 40]
        t_score = 33
        sc_at = {3: 0, 2: 512, 1: 896}
        scores = arena[:, 33:36, :].rearrange("p t c -> p (t c)")

        w_mn, w_la, w_e1, w_e1n, w_e2 = 9, 10, 4, 5, 6
        idx_r = [0, 1, 2, 3]
        kdm = [W(7), W(8), W(9), W(10)]

        def Sst(c):
            return wscr[:, (c - 1) // 2, ((c - 1) % 2) * 256:((c - 1) % 2) * 256 + 256]

        def p_buf(u):
            return W(4 + u % 3)

        def pt_buf(u):
            return W(7 + u % 2)

        def score(tb):
            return scores[:, sc_at[tb]:sc_at[tb] + (tb + 1) * P]

        wA = small[:, 0:32]
        m8 = small[:, 32:40]
        nmax, psum_, rsum = small[:, 40:44], small[:, 44:48], small[:, 48:52]
        glast = small[:, 52:60]

        e_q, e_k, e_v, e_u, e_cos, e_sin = 0, 4, 8, 12, 16, 17
        e_tmp = [18, 19, 20, 21]
        e_bst, e_cst, e_btr, e_bti, e_ere, e_eim = 38, 39, 41, 42, 43, 44
        e_cre, e_crn, e_cin = 45, 38, 20
        e_pos = 45
        s5_n, s5_d, s5_d2 = [T(22), T(23)], [T(24), T(25)], [T(26), T(27)]
        s5_sin, s5_cos = [T(28), T(29), T(30)], [T(31), T(32), T(33)]
        s5_a = [[T(34), T(35), T(36), T(37)], [W(0), W(1), W(2), W(3)], [W(9), W(10), T(18), T(19)]]
        s5col = sb("s5col", [P, 20, NST])
        (c_are, c_aim, c_ldt, c_dt, c_ard, c_th, c_r, c_fr, c_n, c_sin, c_cos, c_nre, c_nim, c_den, c_fre, c_fim,
         c_t1, c_t2, c_f2) = [s5col[:, i, :] for i in range(19)]
        ldt = sb("ldt", [64, 2])
        spc = sb("spc", [P, 8, KD])
        PAR_E, SP_STEPS, e_glu = 31, 19, 28
        RB, RT2 = 30, 38
        xpad = arena[:, 0:9, :].rearrange("p t c -> p (t c)")[:, 0:KD * (LRU_TAPS - 1 + SEQ)].rearrange(
            "p (k c) -> p k c", k=KD)
        o_xc, o_r, o_i, o_gel = 9, 17, 25, 33

        consts_in = sem("consts_in")
        rows_in = sem("rows_in")
        rows_zero = sem("rows_zero")
        x_in = sem("x_in")
        pro_ps = sem("pro_ps")
        cols_sb = sem("cols_sb")
        relb_in = sem("relb_in")
        relb_neg = sem("relb_neg")
        bvec_ps = sem("bvec_ps")
        bvec_sb = sem("bvec_sb")
        bvec_out = sem("bvec_out")
        bias_in = sem("bias_in")
        bias_ps = sem("bias_ps")
        bias_sb = sem("bias_sb")
        zeros_set = sem("zeros_set")
        x_ready = sem("x_ready", 24)
        sq_done = sem("sq_done", 24)
        norm_ps = sem("norm_ps", 3)
        norm_ln = sem("norm_ln", 3)
        norm_r = sem("norm_r", 3)
        xn_ready = sem("xn_ready", 24)
        w_in_sem = [sem("w_loaded0", 16 * sum(U_LAYER[0::2])), sem("w_loaded1", 16 * sum(U_LAYER[1::2]))]
        w_used = sem("w_used", len(U_LAYER), 2)
        gate_ps = sem("gate_ps", 2 * NF)
        sg_ready = sem("sg_ready", 2 * NF, 2)
        h_ready = sem("h_ready", 2 * NF, 2)
        wd_in = [sem("wd_loaded0", 16 * 8), sem("wd_loaded1", 16 * 8)]
        wd_used = sem("wd_used", 2 * KD, 2)
        z_ps = sem("z_ps", sum(len(b) - 1 for b in Z_BLOCKS))
        idx_ps = sem("idx_ps", NIDX)
        z_sb = sem("z_sb", NZ)
        zsq = sem("zsq", 7)
        idx_acc = sem("idx_acc", NIDX)
        idx_mask = sem("idx_mask", 3)
        top_max = sem("top_max", 3 * TOPK // 8)
        top_rep = sem("top_rep", 3 * TOPK // 8)
        top_done = sem("top_done", 3)
        cur_ready = sem("cur_ready", 3)
        cur_cp = sem("cur_cp", 1)
        smallw_in = sem("smallw_in", 16 * 3)
        hp_ready = sem("hp_ready", 2)
        diag_ready = sem("diag_ready", TAPS * 2)
        diag_used = sem("diag_used", TAPS * 2)
        conv_sb = sem("conv_sb", 2)
        conv_sq = sem("conv_sq", 2)
        mn_ps = sem("mn_ps", 7)
        mn_ln = sem("mn_ln", 7)
        mn_r = sem("mn_r", 7)
        mn_x = sem("mn_x", 9)
        y_conv = sem("y_conv", 2)
        gate_log_ps = sem("gate_log_ps", 1)
        g_abs = sem("g_abs", 4)
        g_min = sem("g_min", 1)
        g_b = sem("g_b", 6)
        g_exp = sem("g_exp", 5)
        b_qk = sem("b_qk", 3)
        b_kd = sem("b_kd", 1 + B_HEADS)
        kt_ps = sem("kt_ps", 1)
        kt_sb = sem("kt_sb", 1)
        u_ps = sem("u_ps", NCH - 1)
        u_msk = sem("u_msk", NCH - 1)
        s_ready = sem("s_ready", NCH - 1)
        at_ps = sem("at_ps", TB)
        at_sb = sem("at_sb", 2 * TB)
        o_ps = sem("o_ps", 2)
        o_sq = sem("o_sq", 2)
        on_ps = sem("on_ps", 2)
        on_ln = sem("on_ln", 2)
        on_r = sem("on_r", 2)
        o_n = sem("o_n", 2)
        y_b = sem("y_b", 2)
        dv_ps = sem("dv_ps", 2)
        dv_sb = sem("dv_sb", 2)
        dh_ps = sem("dh_ps", 8)
        dh_sq = sem("dh_sq", 8)
        dn_ps = sem("dn_ps", 8)
        dn_ln = sem("dn_ln", 8)
        dn_r = sem("dn_r", 8)
        dn_x = sem("dn_x", 8)
        dr_ps = sem("dr_ps", 8)
        dr_s = sem("dr_s", 8)
        dr_c = sem("dr_c", 8)
        dh_ready = sem("dh_ready", 8)
        att_bm = sem("att_bm", 12)
        att_s = sem("att_s", 32)
        att_max = sem("att_max", 32)
        att_exp = sem("att_exp", 32)
        att_rs = sem("att_rs", 32)
        att_p = sem("att_p", 32)
        att_t = sem("att_t", 32)
        att_pt = sem("att_pt", 32)
        att_o = sem("att_o", 32)
        y_att = sem("y_att", 4)
        out_ps = sem("out_ps", 4)
        s5_in = sem("s5_in")
        ldt_in = sem("ldt_in")
        ldt_row = sem("ldt_row")
        tab = sem("tab")
        tab_sin = sem("tab_sin")
        par = sem("par")
        par_act = sem("par_act")
        bc_ps = sem("bc_ps")
        bt_sb = sem("bt_sb")
        cb_sb = sem("cb_sb")
        ez_ps = sem("ez_ps")
        ez_sb = sem("ez_sb")
        s5_rnd = sem("s5_rnd")
        s5_frac = sem("s5_frac")
        s5_wrap = sem("s5_wrap")
        s5_quart = sem("s5_quart")
        s5_trig = sem("s5_trig")
        bu_ps = sem("bu_ps")
        s5_rot = sem("s5_rot")
        s5_x = sem("s5_x")
        s5_g = sem("s5_g")
        s5_p = sem("s5_p")
        s5_q = sem("s5_q")
        yy_ps = sem("yy_ps")
        s5_y = sem("s5_y")
        s5_gelu = sem("s5_gelu")
        rot_ps = sem("rot_ps")
        rot_s = sem("rot_s")
        rot_c = sem("rot_c")
        rot_ready = sem("rot_ready")
        glu_ps = sem("glu_ps")
        glu_sb = sem("glu_sb")
        y_ssm = sem("y_ssm")
        eo_ps = sem("eo_ps")
        r_ready = sem("r_ready")
        rsq = sem("rsq")
        rn_ps = sem("rn_ps")
        rn_ln = sem("rn_ln")
        rn_r = sem("rn_r")
        r_n = sem("r_n")
        pad_zero = sem("pad_zero")
        oz_ps = sem("oz_ps")
        oz_sb = sem("oz_sb")
        cv = sem("cv")
        og_ps = sem("og_ps")
        og_sb = sem("og_sb")
        sp_step = sem("sp_step")
        sp_exp = sem("sp_exp")
        o_th = sem("o_th")
        o_a = sem("o_a")
        o_a2 = sem("o_a2")
        o_q = sem("o_q")
        o_sqrt = sem("o_sqrt")
        o_gx = sem("o_gx")
        o_b = sem("o_b")
        o_h = sem("o_h")
        y_lru = sem("y_lru")
        fin_ps = sem("fin_ps")
        fin_sb = sem("fin_sb")
        fin_out = sem("fin_out")

        D_UNITS = [("D", h, tb) for h in range(D_HEADS) for tb in range(TB)]
        A_UNITS = [("A", h, tb) for h in range(A_HEADS) for tb in range(TB)]
        HYB_UNITS = D_UNITS + A_UNITS
        BM = [u for u, (m, h, tb) in enumerate(HYB_UNITS) if m == "A" and tb > 0]

        block = ctx.enter_context(nc.Block())

        def sp_ffn(sp, use0, inc0, f, gate, up, down):
            g = gate.rearrange("(k p) n -> p k n", p=P)
            u = up.rearrange("(k p) n -> p k n", p=P)
            d = down.rearrange("(j p) n -> p j n", p=P)
            with sp.e.Fori(0, NF // 2) as i:
                for c in range(2):
                    sp.e.wait_ge(w_used.h, w_used.start + use0 + 2 * i + (c - 1))
                    for s, w in enumerate((g, u)):
                        sp.e.dma_start(wring[:, c, :, s * P:(s + 1) * P],
                                       w[:, :, bass.ds(i * 2 * P + c * P, P)]).then_inc(w_in_sem[c].h, 16)
            with sp.e.Fori(0, KD // 2) as i:
                for c in range(2):
                    sp.e.wait_ge(wd_used.h, wd_used.start + f * KD + 2 * i + (c - 1))
                    sp.e.dma_start(wdown[:, c, :, :],
                                   d[:, :, bass.ds(i * 2 * P + c * P, P)]).then_inc(wd_in[c].h, 16)

        @block.sync
        def _(e):
            sp = Eng(e)
            e.sem_inc(w_used.h, w_used.start)
            e.sem_inc(wd_used.h, wd_used.start)
            e.dma_start(cst[:, :], I["consts"][:, 0:CONST_W - PRO_W]).then_inc(consts_in.h, 16)
            e.dma_start(arena[:, 12:14, :].rearrange("p t c -> p (t c)")[:, 0:PRO_W],
                        I["consts"][:, CONST_W - PRO_W:]).then_inc(relb_in.h, 16)
            e.dma_start(relb[0:32, :], I["rel_bias"]).then_inc(relb_in.h, 16)
            for tb in range(TB):
                e.dma_start(arena[:, 2 * tb:2 * tb + 2, :],
                            I["x"][0, tb * P:(tb + 1) * P, :].rearrange("p (a c) -> p a c", a=2)).then_inc(x_in.h, 16)
            for l in range(DEPTH):
                sp.l = l
                u0 = l * len(U_LAYER)
                sp_ffn(sp, u0, None, l * 2, I["ffn1_gate"][l], I["ffn1_up"][l], I["ffn1_down"][l])
                e.dma_start(w_uq, I["d_uq"][l].rearrange("(k p) n -> p k n", p=P)).then_inc(smallw_in.h, 16)
                e.dma_start(w_ukv, I["d_ukv"][l]).then_inc(smallw_in.h, 16)
                e.dma_start(gup[:, :], I["b_gate_up"][l]).then_inc(smallw_in.h, 16)
                win = I["w_in"][l].rearrange("(k p) n -> p k n", p=P)
                wout = I["w_out"][l].rearrange("(k p) n -> p k n", p=P)
                for b, src in enumerate(Z_SRC):
                    s = b % 2
                    sp.e.wait_ge(w_used.h, w_used.by(sp.l, NF + b - 1))
                    if src:
                        a, n = WCOL[src[0]], src[1]
                        e.dma_start(wring[:, s, :, 0:n], win[:, :, a:a + n]).then_inc(w_in_sem[s].h, 16)
                    else:
                        for r in range(4):
                            e.dma_start(wring[:, s, :, r * IDX_DIM:(r + 1) * IDX_DIM],
                                        win[:, :, WCOL["ik"]:WCOL["ik"] + IDX_DIM]).then_inc(w_in_sem[s].h, 16)
                        e.dma_start(wring[:, s, :, 128:136],
                                    win[:, :, WCOL["iw"]:WCOL["iw"] + IDX_HEADS]).then_inc(w_in_sem[s].h, 16)
                        e.dma_start(wring[:, s, :, 136:152],
                                    win[:, :, WCOL["bg"]:WCOL["bg"] + B_RANK]).then_inc(w_in_sem[s].h, 16)
                for b in range(4):
                    sp.e.wait_ge(w_used.h, w_used.by(sp.l, NF + len(U_Z) + b - 1))
                    e.dma_start(wring[:, b % 2, :, :], wout[:, :, b * 256:(b + 1) * 256]).then_inc(w_in_sem[b % 2].h, 16)
                sp_ffn(sp, u0 + NF + len(U_Z) + 4, None, l * 2 + 1, I["ffn2_gate"][l], I["ffn2_up"][l],
                       I["ffn2_down"][l])
            sp.l = DEPTH
            for q, n in enumerate(("s5_b_re_2", "s5_b_im_2")):
                e.dma_start(T(e_bst)[:, q * 256:(q + 1) * 256].rearrange("p (j c) -> p j c", c=SSM_C),
                            I[n][0].rearrange("(j q) p c -> (q p) j c", q=2)).then_inc(s5_in.h, 16)
            for q, n in enumerate(("s5_c_re_2", "s5_c_im_2")):
                cd = T(e_cst + q).rearrange("p (t d s) -> p t d s", t=4, d=2)
                src = I[n][0].rearrange("(t g) c s -> (g c) t s", t=4)
                for d in range(2):
                    e.dma_start(cd[:, :, d, :], src).then_inc(s5_in.h, 16)
            e.dma_start(T(e_pos).bitcast(I32), bass.AP(I["positions_2"].tensor, 0, [[0, P], [1, SEQ]])).then_inc(s5_in.h, 16)
            win = I["ev_w_in_2"][0].rearrange("(k p) n -> p k n", p=P)
            use = [0]

            def load(dst, src):
                n = USE_EVEN + use[0]
                sp.e.wait_ge(w_used.h, w_used.start + n - 1)
                e.dma_start(dst(wring[:, n % 2]), src).then_inc(w_in_sem[n % 2].h, 16)
                use[0] += 1
            for n, a in E_BLOCKS:
                load(lambda w: w, win[:, :, a:a + 256])
            for b in range(2):
                load(lambda w: w[:, 0:4, :], I["s5_w_glu_2"][0].rearrange("(k p) n -> p k n", p=P)[:, :, b * 256:(b + 1) * 256])
            for b in range(4):
                load(lambda w: w, I["ev_w_out_2"][0].rearrange("(k p) n -> p k n", p=P)[:, :, b * 256:(b + 1) * 256])
            sp_ffn(sp, USE_EVEN + use[0], None, 2 * DEPTH, I["ffn_w_gate_2"][0], I["ffn_w_up_2"][0], I["ffn_w_down_2"][0])
            use[0] += NF
            win = I["od_w_in_2"][0].rearrange("(k p) n -> p k n", p=P)
            for b in range(8):
                load(lambda w: w, win[:, :, b * 256:(b + 1) * 256])
            for n in ("rg_w_r_2", "rg_w_i_2"):
                load(lambda w: w, I[n][0].rearrange("b (k p) n -> p (b k) n", p=P))
            for b in range(4):
                load(lambda w: w, I["od_w_out_2"][0].rearrange("(k p) n -> p k n", p=P)[:, :, b * 256:(b + 1) * 256])
            sp_ffn(sp, USE_EVEN + use[0], None, 2 * DEPTH + 1, I["ffn_w_gate_2"][1], I["ffn_w_up_2"][1], I["ffn_w_down_2"][1])
            for tb in range(TB):
                sp.e.wait_ge(fin_sb.h, 2 * tb + 2)
                e.dma_start(out[0, tb * P:(tb + 1) * P, :].rearrange("p (a c) -> p a c", a=2),
                            arena[:, 2 * tb:2 * tb + 2, :]).then_inc(fin_out.h, 16)
            sp.e.wait_ge(fin_out.h, 16 * TB)

        def pe_norm(pe, n):
            for k in range(KD):
                pe.e.wait_ge(sq_done.h, n * KD + (k + 1))
                mm = nc.tensor.matmul(pb[6][:, :], C("mean1024"), T(SQ + k), start=(k == 0), stop=(k == KD - 1))
            mm.then_inc(norm_ps.h, 1)

        def pe_ffn(pe, f, incs, xs, xb):
            with pe.e.Fori(0, NF // 2) as i:
                for c in range(2):
                    n = f * NF + 2 * i + c
                    pe.e.wait_ge(w_in_sem[c].h, (incs[c] + 2 * (i + 1)) * 16)
                    pe.e.wait_ge(sg_ready.h, sg_ready.start + n - 1)
                    for k in range(KD):
                        mm = nc.tensor.matmul(pb[c][:, :], wring[:, c, k, 0:P], xn[:, k, :],
                                              start=(k == 0), stop=(k == KD - 1))
                    mm.then_inc(gate_ps.h, 1)
                    pe.e.wait_ge(h_ready.h, h_ready.start + n - 1)
                    for k in range(KD):
                        mm = nc.tensor.matmul(pb[2 + c][:, :], wring[:, c, k, P:2 * P], xn[:, k, :],
                                              start=(k == 0), stop=(k == KD - 1))
                    mm.then_inc(w_used.h, 1)
            pe.e.wait_ge(h_ready.h, h_ready.start + (f + 1) * NF)
            with pe.e.Fori(0, KD // 2) as i:
                for c in range(2):
                    pe.e.wait_ge(wd_in[c].h, (f * (KD // 2) + i + 1) * 16)
                    pe.e.wait_ge(xs.h, xb + 2 * i + (c - 1))
                    for j in range(NF):
                        mm = nc.tensor.matmul(pb[4 + c][:, :], wdown[:, c, j, :], hT[:, j, :],
                                              start=(j == 0), stop=(j == NF - 1))
                    mm.then_inc(wd_used.h, 1)

        def pe_z(pe):
            used = [sum(U_FFN[0::2]), sum(U_FFN[1::2])]
            nz = ni = 0
            for n, t in enumerate(Z_SEQ):
                bank = pb[n % 4]
                if n >= 4:
                    pe.e.wait_ge(z_sb.h, z_sb.by(pe.l, n - 3))
                if t[0] == "idx":
                    _, tb, h = t
                    if ni == 0:
                        pe.e.wait_ge(z_sb.h, z_sb.by(pe.l, Z_POS["ik"] + 1))
                    r = 32 * (h % 4)
                    N = (tb + 1) * P
                    nc.tensor.matmul(bank[:, 0:N], T(t_iq[h // 4])[r:r + 32, tb * P:(tb + 1) * P],
                                     T(t_ik)[r:r + 32, 0:N], start=True, stop=True).then_inc(idx_ps.h, 1)
                    ni += 1
                    continue
                _, b, c, label, col, kind, last = t
                s = b % 2
                if c == 0:
                    used[s] += U_Z[b]
                    pe.e.wait_ge(w_in_sem[s].h, w_in_sem[s].by(pe.l, 16 * used[s]))
                w = wring[:, s, :, :]
                if kind == "feat":
                    for k in range(KD):
                        mm = nc.tensor.matmul(bank[:, :], w[:, k, col:col + P], xn[:, k, :],
                                              start=(k == 0), stop=(k == KD - 1))
                elif kind == "bg":
                    for k in range(KD):
                        mm = nc.tensor.matmul(bank[0:B_RANK, :], w[:, k, col:col + B_RANK], xn[:, k, :],
                                              start=(k == 0), stop=(k == KD - 1))
                elif kind == "kpe":
                    for k in range(KD):
                        mm = nc.tensor.matmul(bank[64:96, :], w[:, k, col:col + D_ROPE], xn[:, k, :],
                                              start=(k == 0), stop=(k == KD - 1))
                elif kind == "iw":
                    for tb in range(TB):
                        for k in range(KD):
                            mm = nc.tensor.matmul(bank[:, 8 * tb:8 * tb + 8], xn[:, k, tb * P:(tb + 1) * P],
                                                  w[:, k, col:col + IDX_HEADS], start=(k == 0), stop=(k == KD - 1))
                else:
                    for q in range(2):
                        tb = 2 * col + q
                        for k in range(KD):
                            mm = nc.tensor.matmul(bank[:, q * 256:(q + 1) * 256], xn[:, k, tb * P:(tb + 1) * P],
                                                  w[:, k, :], start=(k == 0), stop=(k == KD - 1))
                mm.then_inc((w_used if last else z_ps).h, 1)

        def pe_mixers(pe):
            pe.e.wait_ge(z_sb.h, z_sb.by(pe.l, NZ))
            pe.e.wait_ge(smallw_in.h, smallw_in.by(pe.l, 16 * 3))
            nc.tensor.matmul(pb[0][:, :], gup[:, :], T(t_gl)[0:B_RANK, :], start=True, stop=True).then_inc(gate_log_ps.h, 1)
            for i in range(4):
                pe.e.wait_ge(zsq.h, zsq.by(pe.l, i + 1))
                if i >= 3:
                    pe.e.wait_ge(mn_ln.h, mn_ln.by(pe.l, i - 2))
                nc.tensor.matmul(pb[1 + i % 3][:, :], C("blk64"), T(t_zsq[i]), start=True, stop=True).then_inc(mn_ps.h, 1)
            pe.e.wait_ge(zsq.h, zsq.by(pe.l, 6))
            pe.e.wait_ge(mn_ln.h, mn_ln.by(pe.l, 2))
            nc.tensor.matmul(pb[2][:, :], C("mean256"), T(t_zsq[4]), start=True, stop=False)
            nc.tensor.matmul(pb[2][:, :], C("mean256"), T(t_zsq[5]), start=False, stop=True).then_inc(mn_ps.h, 1)
            pe.e.wait_ge(zsq.h, zsq.by(pe.l, 7))
            pe.e.wait_ge(mn_ln.h, mn_ln.by(pe.l, 3))
            nc.tensor.matmul(pb[3][:, :], C("mean128"), T(t_zsq[6]), start=True, stop=True).then_inc(mn_ps.h, 1)
            for ct in range(2):
                pe.e.wait_ge(hp_ready.h, hp_ready.by(pe.l, ct + 1))
                for j in range(TAPS):
                    n = ct * TAPS + j
                    pe.e.wait_ge(diag_ready.h, diag_ready.by(pe.l, n + 1))
                    nc.tensor.matmul(pb[4 + ct][:, :], diag[:, n % 8, :], hpad[:, ct, j:j + SEQ],
                                     start=(j == 0), stop=(j == TAPS - 1)).then_inc(diag_used.h, 1)
            pe.e.wait_ge(mn_x.h, mn_x.by(pe.l, 7))
            for q in range(2):
                for r in range(2):
                    tb = 2 * q + r
                    mm = nc.tensor.matmul(pb[6 + q][:, r * 256:(r + 1) * 256], T(t_dckv)[:, tb * P:(tb + 1) * P],
                                          w_ukv.rearrange("p (h t) -> p h t", h=D_HEADS)[:, :, D_NOPE:],
                                          start=True, stop=True)
                mm.then_inc(dv_ps.h, 1)
            for i in range(8 + 2):
                if i < 8:
                    raw = pb[i % 2]
                    if i == 1:
                        pe.e.wait_ge(mn_ln.h, mn_ln.by(pe.l, 6))
                    if i >= 2:
                        pe.e.wait_ge(dh_sq.h, dh_sq.by(pe.l, i - 1))
                    h = i % 4
                    if i < 4:
                        for k in range(2):
                            mm = nc.tensor.matmul(raw[0:D_QK, :], w_uq[:, k, h * D_QK:(h + 1) * D_QK], T(t_dcq[k]),
                                                  start=(k == 0), stop=(k == 1))
                    else:
                        nc.tensor.matmul(raw[0:D_NOPE, :], w_ukv[:, h * P:h * P + D_NOPE], T(t_dckv), start=True, stop=True)
                        mm = nc.tensor.matmul(raw[64:96, :], ident[64:96, 64:96], T(t_kpe)[64:96, :], start=True, stop=True)
                    mm.then_inc(dh_ps.h, 1)
                if 1 <= i < 9:
                    u = i - 1
                    pe.e.wait_ge(dh_sq.h, dh_sq.by(pe.l, u + 1))
                    if u >= 1:
                        pe.e.wait_ge(dn_ln.h, dn_ln.by(pe.l, u))
                    nc.tensor.matmul(pb[2][0:D_QK, :], C("mean96")[0:D_QK, :], T(t_hsq[u % 2])[0:D_QK, :],
                                     start=True, stop=True).then_inc(dn_ps.h, 1)
                if i >= 2:
                    u = i - 2
                    pe.e.wait_ge(dn_x.h, dn_x.by(pe.l, u + 1))
                    if u >= 1:
                        pe.e.wait_ge(dr_s.h, dr_s.by(pe.l, u))
                    nc.tensor.matmul(pb[3][0:D_QK, :], C("rot96")[0:D_QK, :], T(t_hn[u % 2])[0:D_QK, :],
                                     start=True, stop=True).then_inc(dr_ps.h, 1)
            pe.e.wait_ge(conv_sq.h, conv_sq.by(pe.l, 2))
            pe.e.wait_ge(dv_sb.h, dv_sb.by(pe.l, 1))
            nc.tensor.matmul(pb[6][:, :], C("mean256"), T(t_csq[0]), start=True, stop=False)
            nc.tensor.matmul(pb[6][:, :], C("mean256"), T(t_csq[1]), start=False, stop=True).then_inc(mn_ps.h, 1)
            pe.e.wait_ge(b_qk.h, b_qk.by(pe.l, 3))
            pe.e.wait_ge(dv_sb.h, dv_sb.by(pe.l, 2))
            for tb in range(TB):
                mm = nc.tensor.transpose(pb[7][:, tb * P:(tb + 1) * P], W(w_e2)[:, tb * P:(tb + 1) * P], ident)
            mm.then_inc(kt_ps.h, 1)
            pe.e.wait_ge(kt_sb.h, kt_sb.by(pe.l, 1))
            pe.e.wait_ge(dn_ln.h, dn_ln.by(pe.l, 8))
            pe.e.wait_ge(dr_s.h, dr_s.by(pe.l, 8))
            bv = arena[:, t_bv:t_bv + 2, :].rearrange("p t c -> p (t c)").rearrange("p (b c) -> p b c", b=TB)
            for c in range(NCH - 1):
                r = 64 * (c % 2)
                if c >= 2:
                    pe.e.wait_ge(u_msk.h, u_msk.by(pe.l, c - 1))
                nc.tensor.matmul(pb[2 + c % 2][:, 0:256], T(t_kdt)[r:r + 64, (c // 2) * P:(c // 2 + 1) * P],
                                 bv[r:r + 64, c // 2, :], start=True, stop=True).then_inc(u_ps.h, 1)
            pe.e.wait_ge(b_kd.h, b_kd.by(pe.l, 1 + B_HEADS))
            pe.e.wait_ge(conv_sb.h, conv_sb.by(pe.l, 2))
            for tb in range(TB):
                bank = pb[4 + tb % 2]
                if tb >= 2:
                    pe.e.wait_ge(at_sb.h, at_sb.by(pe.l, 2 * (tb - 1)))
                for h in range(B_HEADS):
                    mm = nc.tensor.matmul(bank[:, h * P:(h + 1) * P], kdm[h][:, tb * P:(tb + 1) * P],
                                          W(w_e1)[:, tb * P:(tb + 1) * P], start=True, stop=True)
                mm.then_inc(at_ps.h, 1)
            pe.e.wait_ge(at_sb.h, at_sb.by(pe.l, 2 * TB))
            pe.e.wait_ge(s_ready.h, s_ready.by(pe.l, NCH - 1))
            pe.e.wait_ge(dh_sq.h, dh_sq.by(pe.l, 8))
            for pr in range(2):
                o = pb[pr]
                for c in range(NCH):
                    cols = slice(c * B_CHUNK, (c + 1) * B_CHUNK)
                    half = slice(c % 2 * B_CHUNK, (c % 2 + 1) * B_CHUNK)
                    for q in range(2):
                        h = 2 * pr + q
                        mm = nc.tensor.matmul(o[64 * q:64 * q + 64, cols], bv[:, c // 2, h * B_VAL:(h + 1) * B_VAL],
                                              att_diag[:, c // 2, h, half], start=True, stop=(c == 0),
                                              skip_group_check=True)
                    if c:
                        mm = nc.tensor.matmul(o[:, cols], Sst(c)[:, pr * P:(pr + 1) * P], T(t_qe)[:, cols],
                                              start=False, stop=True, skip_group_check=True)
                mm.then_inc(o_ps.h, 1)
            for pr in range(2):
                pe.e.wait_ge(o_sq.h, o_sq.by(pe.l, pr + 1))
                pe.e.wait_ge(u_msk.h, u_msk.by(pe.l, NCH - 1))
                nc.tensor.matmul(pb[2 + pr][:, :], C("blk64"), T(t_osq[pr]), start=True, stop=True).then_inc(on_ps.h, 1)

        def pe_attention(pe, units, ops):
            U = len(units)
            for i in range(U + 3):
                if i < U:
                    ops["ready"](pe, i)
                    m, h, tb = units[i]
                    if i >= 4:
                        pe.e.wait_ge(att_exp.h, att_exp.by(pe.l, i - 3))
                    s = pb[(0, 1, 4, 5)[i % 4]]
                    N = (tb + 1) * P
                    q, k = ops["qk"](m, h)
                    msk, lo = ops["mask"](m, h, tb, i)
                    if lo:
                        nc.tensor.matmul(s[:, 0:lo], q[:, tb * P:N], k[:, 0:lo], start=True, stop=True)
                    nc.tensor.matmul(s[:, lo:N], q[:, tb * P:N], k[:, lo:N], start=True, stop=False)
                    nc.tensor.matmul(s[:, lo:N], ident, msk, start=False, stop=True).then_inc(att_s.h, 1)
                if 2 <= i < U + 2:
                    u = i - 2
                    pe.e.wait_ge(att_p.h, att_p.by(pe.l, u + 1))
                    if u >= 2:
                        pe.e.wait_ge(att_pt.h, att_pt.by(pe.l, u - 1))
                    for b in range(units[u][2] + 1):
                        mm = nc.tensor.transpose(pb[2 + u % 2][:, b * P:(b + 1) * P],
                                                 p_buf(u)[:, b * P:(b + 1) * P], ident)
                    mm.then_inc(att_t.h, 1)
                if i >= 3:
                    u = i - 3
                    m, h, tb = units[u]
                    pe.e.wait_ge(att_pt.h, att_pt.by(pe.l, u + 1))
                    if u % 8 == 0 and u >= 16:
                        pe.e.wait_ge(y_att.h, y_att.by(pe.l, u // 8 - 1))
                    o = pb[6 + (u // 8) % 2][64 * (h % 2):64 * (h % 2) + 64, tb * P:(tb + 1) * P]
                    for b in range(tb + 1):
                        mm = nc.tensor.matmul(o, ops["v"](m, h, b), pt_buf(u)[:, b * P:(b + 1) * P],
                                              start=(b == 0), stop=(b == tb))
                    mm.then_inc(att_o.h, 1)

        def hyb_qk(m, h):
            if m == "D":
                return T(t_dq[h])[0:D_QK, :], T(t_dk[h])[0:D_QK, :]
            r = 64 * (h % 2)
            return T(t_aq[h // 2])[r:r + 64, :], T(t_ak[h // 2])[r:r + 64, :]

        def hyb_mask(m, h, tb, u):
            if m == "D":
                return C("causal"), tb * P
            if tb == 0:
                return bias[:, h, SEQ - P:SEQ], 0
            return T(t_bm[BM.index(u) % 3])[:, 0:(tb + 1) * P], 0

        def hyb_v(m, h, b):
            t = t_dv if m == "D" else t_av
            v = arena[:, t:t + 2, :].rearrange("p t c -> p (t c)").rearrange("p (b c) -> p b c", b=TB)
            return v[:, b, h * 64:(h + 1) * 64]

        def hyb_ready(eng, u):
            if u == 0:
                eng.e.wait_ge(on_ln.h, on_ln.by(eng.l, 2))
                eng.e.wait_ge(y_conv.h, y_conv.by(eng.l, 2))
                eng.e.wait_ge(kt_sb.h, kt_sb.by(eng.l, 1))
                eng.e.wait_ge(at_sb.h, at_sb.by(eng.l, 2 * TB))
            m, h, tb = HYB_UNITS[u]
            if m == "D" and tb == 0:
                eng.e.wait_ge(dh_ready.h, dh_ready.by(eng.l, 5 + h))
            if m == "A" and h == 0 and tb == 0:
                eng.e.wait_ge(mn_x.h, mn_x.by(eng.l, 4))
                eng.e.wait_ge(bias_sb.h, A_HEADS)
            if u in BM:
                eng.e.wait_ge(att_bm.h, att_bm.by(eng.l, BM.index(u) + 1))

        HYB = dict(qk=hyb_qk, mask=hyb_mask, v=hyb_v, ready=hyb_ready)

        def pe_out(pe, used, ready):
            ready(pe)
            for b in range(4):
                s = b % 2
                pe.e.wait_ge(w_in_sem[s].h, w_in_sem[s].by(pe.l, 16 * (used[s] + b // 2 + 1)))
                for c in range(2):
                    dc = 2 * b + c
                    if dc >= 2:
                        pe.e.wait_ge(x_ready.h, x_ready.by(pe.l, 16 + dc - 1))
                    for k in range(KD):
                        mm = nc.tensor.matmul(pb[c][:, :], wring[:, s, k, c * P:(c + 1) * P], y[:, k, :],
                                              start=(k == 0), stop=(k == KD - 1))
                    mm.then_inc((w_used if c else out_ps).h, 1)

        E_UNITS = [("E", h, tb) for h in range(E_HEADS) for tb in range(TB)]
        e_vv = arena[:, e_v:e_v + 4, :]

        def even_qk(m, h):
            r = 64 * (h % 2)
            return T(e_q + h // 2)[r:r + 64, :], T(e_k + h // 2)[r:r + 64, :]

        def even_ready(eng, u):
            if u == 0:
                eng.e.wait_ge(glu_sb.h, 4)
            m, h, tb = E_UNITS[u]
            if tb == 0 and h % 2 == 0:
                eng.e.wait_ge(rot_ready.h, 2 * (h // 2) + 2)
            if u == 0:
                eng.e.wait_ge(ez_sb.h, len(E_Z))

        EVEN = dict(qk=even_qk, mask=lambda m, h, tb, u: (C("lnmult")[:, SEQ - (tb + 1) * P:], 0),
                    v=lambda m, h, b: e_vv[:, b, h * E_DIM:(h + 1) * E_DIM], ready=even_ready)

        def pe_even(pe):
            inc = list(DMA_EVEN)
            nz = 0
            for t in E_SEQ:
                if t[0] == "z":
                    _, b, c, n, i = t
                    s = b % 2
                    bank = pb[nz % 2]
                    if c == 0:
                        inc[s] += 1
                        pe.e.wait_ge(w_in_sem[s].h, 16 * inc[s])
                    if nz >= 2:
                        pe.e.wait_ge(ez_sb.h, nz - 1)
                    w = wring[:, s, :, :]
                    if n == "v":
                        for q in range(2):
                            tb = 2 * c + q
                            for k in range(KD):
                                mm = nc.tensor.matmul(bank[:, q * 256:(q + 1) * 256], xn[:, k, tb * P:(tb + 1) * P],
                                                      w[:, k, :], start=(k == 0), stop=(k == KD - 1))
                    else:
                        for k in range(KD):
                            mm = nc.tensor.matmul(bank[:, :], w[:, k, c * P:(c + 1) * P], xn[:, k, :],
                                                  start=(k == 0), stop=(k == KD - 1))
                    mm.then_inc((w_used if c else ez_ps).h, 1)
                    nz += 1
                elif t[0] == "prep":
                    pe.e.wait_ge(par.h, PAR_E)
                    pe.e.wait_ge(s5_in.h, 16 * 7)
                    for q, src in enumerate((e_ere, e_eim, e_cst, e_cst + 1)):
                        for i in range(4):
                            mm = nc.tensor.transpose(pb[2 + q][:, i * P:(i + 1) * P], T(src)[:, i * P:(i + 1) * P], ident)
                        mm.then_inc(bc_ps.h, 1)
                elif t[0] == "bu":
                    j = t[1]
                    if j == 0:
                        pe.e.wait_ge(bt_sb.h, 2)
                        pe.e.wait_ge(cb_sb.h, 4)
                        pe.e.wait_ge(ez_sb.h, 4)
                    if j >= 2:
                        pe.e.wait_ge(s5_rot.h, j - 1)
                    r = slice(32 * (j % 4), 32 * (j % 4) + 32)
                    for q, bt in enumerate((e_btr, e_bti)):
                        mm = nc.tensor.matmul(pb[2 + 2 * (j % 2) + q][:, :], T(bt)[r, (j // 4) * P:(j // 4 + 1) * P],
                                              T(e_u + j // 4)[r, :], start=True, stop=True)
                    mm.then_inc(bu_ps.h, 1)
                else:
                    j = t[1]
                    pe.e.wait_ge(s5_p.h, j + 1)
                    pe.e.wait_ge(s5_q.h, j + 1)
                    if j % 4 == 0 and j >= 8:
                        pe.e.wait_ge(s5_y.h, j // 4 - 1)
                    r = slice(32 * (j % 4), 32 * (j % 4) + 32)
                    a1, p3, p2, p4 = s5_a[j % 3]
                    for q, (cm, a) in enumerate(((e_cre, a1), (e_crn, p2), (e_cin, p3), (e_cin, p4))):
                        mm = nc.tensor.matmul(pb[6 + (j // 4) % 2][r, :], T(cm)[:, j * 32:(j + 1) * 32], a,
                                              start=(q == 0), stop=(q == 3))
                    mm.then_inc(yy_ps.h, 1)
            for i in range(8):
                t = (e_q if i % 2 == 0 else e_k) + i // 2
                if i < 2:
                    pe.e.wait_ge(ez_sb.h, len(E_Z))
                else:
                    pe.e.wait_ge(rot_s.h, i - 1)
                nc.tensor.matmul(pb[i % 2][:, :], C("rot128"), T(t), start=True, stop=True).then_inc(rot_ps.h, 1)
            pe.e.wait_ge(s5_gelu.h, 4)
            for b in range(2):
                s = b % 2
                pe.e.wait_ge(w_in_sem[s].h, 16 * (inc[s] + 1))
                for c in range(2):
                    for k in range(4):
                        mm = nc.tensor.matmul(pb[2 + 2 * b + c][:, :], wring[:, s, k, c * P:(c + 1) * P], T(e_u + k),
                                              start=(k == 0), stop=(k == 3))
                    mm.then_inc((w_used if c else glu_ps).h, 1)
            pe.e.wait_ge(rot_s.h, 8)

        def pe_out2(pe, use0, inc, m, ready):
            ready(pe)
            for b in range(4):
                s = b % 2
                pe.e.wait_ge(w_in_sem[s].h, 16 * (inc[s] + b // 2 + 1))
                for c in range(2):
                    dc = 2 * b + c
                    if dc >= 2:
                        pe.e.wait_ge(r_ready.h, m * KD + dc - 1)
                    for k in range(KD):
                        mm = nc.tensor.matmul(pb[c][:, :], wring[:, s, k, c * P:(c + 1) * P], y[:, k, :],
                                              start=(k == 0), stop=(k == KD - 1))
                    mm.then_inc((w_used if c else eo_ps).h, 1)

        def even_mixed(pe):
            pe.e.wait_ge(y_att.h, 4 * DEPTH + 4)
            pe.e.wait_ge(y_ssm.h, 4)

        def odd_mixed(pe):
            pe.e.wait_ge(y_lru.h, KD)

        def pe_post(pe, m):
            for k in range(KD):
                pe.e.wait_ge(rsq.h, m * KD + k + 1)
                mm = nc.tensor.matmul(pb[7][:, :], C("mean1024"), T(SQ + k), start=(k == 0), stop=(k == KD - 1))
            mm.then_inc(rn_ps.h, 1)

        def pe_odd(pe):
            inc = list(DMA_ODD)
            for n in range(2 * KD):
                s = (n // 2) % 2
                c = n % 2
                if c == 0:
                    inc[s] += 1
                    pe.e.wait_ge(w_in_sem[s].h, 16 * inc[s])
                if n >= 4:
                    pe.e.wait_ge(oz_sb.h, n - 3)
                for k in range(KD):
                    mm = nc.tensor.matmul(pb[n % 4][:, :], wring[:, s, k, c * P:(c + 1) * P], xn[:, k, :],
                                          start=(k == 0), stop=(k == KD - 1))
                mm.then_inc((w_used if c else oz_ps).h, 1)
            for g in range(2):
                inc[g] += 1
                pe.e.wait_ge(w_in_sem[g].h, 16 * inc[g])
                for m in range(KD):
                    n = g * KD + m
                    if n < 4:
                        pe.e.wait_ge(oz_sb.h, 2 * KD - 3 + n)
                    else:
                        pe.e.wait_ge(og_sb.h, n - 3)
                    b = m // 2
                    pe.e.wait_ge(cv.h, LRU_TAPS * (2 * b + 2))
                    for k in range(2):
                        mm = nc.tensor.matmul(pb[n % 4][:, :], wring[:, g, 2 * b + k, (m % 2) * P:(m % 2 + 1) * P],
                                              T(o_xc + 2 * b + k), start=(k == 0), stop=(k == 1))
                    mm.then_inc((w_used if m == KD - 1 else og_ps).h, 1)
            pe.e.wait_ge(og_sb.h, 2 * KD)

        @block.tensor
        def _(e):
            pe = Eng(e)
            pe.e.wait_ge(consts_in.h, 16)
            pe.e.wait_ge(x_in.h, 16 * TB)
            for k in range(KD):
                if k >= 2:
                    pe.e.wait_ge(x_ready.h, k - 1)
                for tb in range(TB):
                    mm = nc.tensor.transpose(pb[k % 2][:, tb * P:(tb + 1) * P],
                                             arena[:, 2 * tb + k // 4, (k % 4) * P:(k % 4 + 1) * P], ident)
                mm.then_inc(pro_ps.h, 1)
            pe.e.wait_ge(rows_in.h, 16 * N_ROW_DMAS)
            pe.e.wait_ge(ldt_row.h, 1)
            for i in range(4):
                nc.tensor.transpose(pb[2 + i][:, 0:P], rows[:, i, :], ident).then_inc(pro_ps.h, 1)
            pe.e.wait_ge(relb_in.h, 32)
            pe.e.wait_ge(relb_neg.h, 1)
            half = BIAS_N // 2
            for q in range(2):
                nc.tensor.matmul(pb[6 + q][0:A_HEADS, 0:half], relb[0:33, :], C("onehot")[0:33, q * half:(q + 1) * half],
                                 start=True, stop=True).then_inc(bvec_ps.h, 1)
            pe.e.wait_ge(cols_sb.h, 4)
            pe.e.wait_ge(bvec_sb.h, 2)
            pe.e.wait_ge(x_ready.h, KD)
            pe.e.wait_ge(bias_in.h, 16)
            for h in range(A_HEADS):
                nc.tensor.matmul(pb[h][:, :], C("flip"), hT[:, 8 + h, :], start=True, stop=True).then_inc(bias_ps.h, 1)
            pe.e.wait_ge(bias_sb.h, A_HEADS)
            for l in range(DEPTH):
                pe.l = l
                lay = [sum(U_LAYER[0::2]), sum(U_LAYER[1::2])]
                b4 = [sum((U_FFN + U_Z + U_OUT)[s::2]) for s in range(2)]
                pe_norm(pe, l * 3)
                pe.e.wait_ge(xn_ready.h, (l * 3 + 1) * KD)
                pe_ffn(pe, l * 2, [l * lay[s] for s in range(2)], x_ready, l * 24 + 8)
                pe_norm(pe, l * 3 + 1)
                pe.e.wait_ge(xn_ready.h, (l * 3 + 2) * KD)
                pe_z(pe)
                pe_mixers(pe)
                pe_attention(pe, HYB_UNITS, HYB)

                def ready(pe):
                    pe.e.wait_ge(y_conv.h, y_conv.by(pe.l, 2))
                    pe.e.wait_ge(y_b.h, y_b.by(pe.l, 2))
                    pe.e.wait_ge(y_att.h, y_att.by(pe.l, 4))
                pe_out(pe, [sum((U_FFN + U_Z)[s::2]) for s in range(2)], ready)
                pe_norm(pe, l * 3 + 2)
                pe.e.wait_ge(xn_ready.h, (l * 3 + 3) * KD)
                pe_ffn(pe, l * 2 + 1, [l * lay[s] + b4[s] for s in range(2)], x_ready, l * 24 + 24)
            pe.l = DEPTH
            n = 3 * DEPTH
            pe_norm(pe, n)
            pe.e.wait_ge(xn_ready.h, (n + 1) * KD)
            pe_even(pe)
            pe_attention(pe, E_UNITS, EVEN)
            pe_out2(pe, USE_EVEN + len(E_BLOCKS) + 2, [DMA_EVEN[s] + sum(U_EVEN[s:len(E_BLOCKS) + 2:2]) for s in range(2)], 0,
                    even_mixed)
            pe_post(pe, 0)
            pe_norm(pe, n + 1)
            pe.e.wait_ge(xn_ready.h, (n + 2) * KD)
            pe_ffn(pe, 2 * DEPTH, [DMA_EVEN[s] + sum(U_EVEN[s:-NF:2]) for s in range(2)], r_ready, KD)
            pe_post(pe, 1)
            pe_norm(pe, n + 2)
            pe.e.wait_ge(xn_ready.h, (n + 3) * KD)
            pe_odd(pe)
            pe_out2(pe, USE_ODD + 10, [DMA_ODD[s] + sum(U_ODD[s:10:2]) for s in range(2)], 2, odd_mixed)
            pe_post(pe, 2)
            pe_norm(pe, n + 3)
            pe.e.wait_ge(xn_ready.h, (n + 4) * KD)
            pe_ffn(pe, 2 * DEPTH + 1, [DMA_ODD[s] + sum(U_ODD[s:-NF:2]) for s in range(2)], r_ready, 3 * KD)
            pe_post(pe, 3)
            pe.e.wait_ge(x_ready.h, X1 + 4 * KD)
            for tb in range(TB):
                for q in range(2):
                    n = 2 * tb + q
                    if n >= 2:
                        pe.e.wait_ge(fin_sb.h, n - 1)
                    for k in range(4):
                        mm = nc.tensor.transpose(pb[n % 2][:, k * P:(k + 1) * P], x[:, 4 * q + k, tb * P:(tb + 1) * P], ident)
                    mm.then_inc(fin_ps.h, 1)

        def act_norm(act, n):
            for k in range(KD):
                act.e.wait_ge(x_ready.h, n * KD + (k + 1))
                nc.scalar.activation(T(SQ + k), x[:, k, :], ACT.Square).then_inc(sq_done.h, 1)
            act.e.wait_ge(norm_ps.h, n + 1)
            nc.scalar.activation(T(RT), pb[6][:, :], ACT.Ln, bias=C("eps")).then_inc(norm_ln.h, 1)
            act.e.wait_ge(norm_ln.h, n + 1)
            nc.scalar.activation(T(RT), T(RT), ACT.Exp, scale=-0.5).then_inc(norm_r.h, 1)

        def act_ffn(act, f):
            with act.e.Fori(0, NF // 2) as i:
                for c in range(2):
                    n = f * NF + 2 * i + c
                    act.e.wait_ge(gate_ps.h, n + 1)
                    act.e.wait_ge(h_ready.h, h_ready.start + n - 1)
                    nc.scalar.activation(sg[:, c, :], pb[c][:, :], ACT.Silu).then_inc(sg_ready.h, 1)

        def rstd(act, src, dst, ln, r, k):
            nc.scalar.activation(dst, src, ACT.Ln, bias=C("eps")[0:dst.shape[0], :]).then_inc(ln.h, 1)
            act.e.wait_ge(ln.h, ln.by(act.l, k))
            nc.scalar.activation(dst, dst, ACT.Exp, scale=-0.5).then_inc(r.h, 1)

        def act_z(act):
            ni = nps = 0
            nused = NF
            dst = dict(iq0=0, iq1=1, ik=2, aq0=3, aq1=4, ak0=5, ak1=6, av01=7, av23=8, bq=9, bk=10, bv01=11, bv23=12,
                       br0=13, br1=14, ca0=15, ca1=16, cg0=17, cg1=18, dcq0=19, dcq1=20, dckv=21)
            for n, t in enumerate(Z_SEQ):
                bank = pb[n % 4]
                if t[0] == "idx":
                    _, tb, h = t
                    N = (tb + 1) * P
                    act.e.wait_ge(idx_ps.h, idx_ps.by(act.l, ni + 1))
                    if ni >= 4:
                        act.e.wait_ge(idx_acc.h, idx_acc.by(act.l, ni - 3))
                    nc.scalar.activation(W(idx_r[ni % 4])[:, 0:N], bank[:, 0:N], ACT.Relu).then_inc(z_sb.h, 1)
                    ni += 1
                    continue
                _, b, c, label, col, kind, last = t
                if last:
                    nused += 1
                    act.e.wait_ge(w_used.h, w_used.by(act.l, nused))
                else:
                    nps += 1
                    act.e.wait_ge(z_ps.h, z_ps.by(act.l, nps))
                if label in ("aq0", "aq1", "ak0", "ak1", "dcq0", "dcq1", "dckv"):
                    q = ("aq0", "aq1", "ak0", "ak1", "dcq0", "dcq1", "dckv").index(label)
                    nc.scalar.activation(T(t_zsq[q]), bank[:, :], ACT.Square).then_inc(zsq.h, 1)
                if kind == "iw":
                    nc.scalar.activation(wA, bank[:, 0:32], ACT.Copy,
                                         scale=float((IDX_DIM * IDX_HEADS) ** -0.5)).then_inc(z_sb.h, 1)
                elif kind == "bg":
                    nc.scalar.activation(T(t_gl)[0:B_RANK, :], bank[0:B_RANK, :], ACT.Copy).then_inc(z_sb.h, 1)
                elif kind == "kpe":
                    nc.scalar.activation(T(t_kpe)[64:96, :], bank[64:96, :], ACT.Copy).then_inc(z_sb.h, 1)
                else:
                    f = {"br": ACT.Silu, "cg": ACT.Sigmoid}.get(label[:2], ACT.Copy)
                    s = float(B_KEY ** -0.5) if label == "bq" else 1.0
                    nc.scalar.activation(T(dst[label]), bank[:, :], f, scale=s).then_inc(z_sb.h, 1)

        def act_mixers(act):
            act.e.wait_ge(gate_log_ps.h, gate_log_ps.by(act.l, 1))
            act.e.wait_ge(cur_ready.h, cur_ready.by(act.l, 3))
            gb = cur[:, RL["b_gate_bias"]:RL["b_gate_bias"] + 1]
            nc.scalar.activation(W(w_mn), pb[0][:, :], ACT.Identity, bias=gb).then_inc(g_abs.h, 1)
            nc.scalar.activation(T(t_ab), pb[0][:, :], ACT.Abs, bias=gb).then_inc(g_abs.h, 1)
            act.e.wait_ge(g_abs.h, g_abs.by(act.l, 2))
            nc.scalar.activation(T(t_ab), T(t_ab), ACT.Exp, scale=-1.0).then_inc(g_abs.h, 1)
            act.e.wait_ge(g_abs.h, g_abs.by(act.l, 3))
            nc.scalar.activation(T(t_ab), T(t_ab), ACT.Ln, bias=1.0).then_inc(g_abs.h, 1)
            bank = [1, 2, 3, 1, 2, 3]
            for i in range(6):
                act.e.wait_ge(mn_ps.h, mn_ps.by(act.l, i + 1))
                rstd(act, pb[bank[i]][:, :], T(t_zr[i]), mn_ln, mn_r, i + 1)
            g = 1.0 / 16
            act.e.wait_ge(g_b.h, g_b.by(act.l, 6))
            b16 = W(w_mn)
            nc.scalar.activation(T(t_qe), b16, ACT.Exp, scale=g).then_inc(g_exp.h, 1)
            nc.scalar.activation(W(w_e1), W(w_la), ACT.Exp, scale=g).then_inc(g_exp.h, 1)
            nc.scalar.activation(W(w_e1n), W(w_la), ACT.Exp, scale=-g).then_inc(g_exp.h, 1)
            nc.scalar.activation(W(w_e2), T(t_ab), ACT.Exp, scale=g).then_inc(g_exp.h, 1)
            nc.scalar.activation(glast[:, 0:NCH], b16.rearrange("p (c t) -> p c t", c=NCH)[:, :, B_CHUNK - 1],
                                 ACT.Exp, scale=g).then_inc(g_exp.h, 1)
            for ct in range(2):
                act.e.wait_ge(diag_used.h, diag_used.by(act.l, TAPS * (ct + 1)))
                cb = cur[:, RL["c_dw_b"] + ct:RL["c_dw_b"] + ct + 1]
                nc.scalar.activation(T(t_hc[ct]), pb[4 + ct][:, :], ACT.Identity, bias=cb).then_inc(conv_sb.h, 1)
                nc.scalar.activation(T(t_csq[ct]), pb[4 + ct][:, :], ACT.Square, bias=cb).then_inc(conv_sq.h, 1)
            for q in range(2):
                act.e.wait_ge(dv_ps.h, dv_ps.by(act.l, q + 1))
                nc.scalar.activation(T(t_dv + q), pb[6 + q][:, :], ACT.Copy).then_inc(dv_sb.h, 1)
            for i in range(8 + 1):
                if i < 8:
                    act.e.wait_ge(dh_ps.h, dh_ps.by(act.l, i + 1))
                    if i >= 2:
                        act.e.wait_ge(dn_x.h, dn_x.by(act.l, i - 1))
                    nc.scalar.activation(T(t_hraw[i % 2])[0:D_QK, :], pb[i % 2][0:D_QK, :], ACT.Copy)
                    nc.scalar.activation(T(t_hsq[i % 2])[0:D_QK, :], pb[i % 2][0:D_QK, :], ACT.Square).then_inc(dh_sq.h, 1)
                if i >= 1:
                    u = i - 1
                    act.e.wait_ge(dn_ps.h, dn_ps.by(act.l, u + 1))
                    if u >= 2:
                        act.e.wait_ge(dh_ready.h, dh_ready.by(act.l, u - 1))
                    rstd(act, pb[2][0:D_QK, :], T(t_hr[u % 2])[0:D_QK, :], dn_ln, dn_r, u + 1)
            act.e.wait_ge(mn_ps.h, mn_ps.by(act.l, 7))
            rstd(act, pb[6][:, :], T(t_cr), mn_ln, mn_r, 7)
            act.e.wait_ge(kt_ps.h, kt_ps.by(act.l, 1))
            nc.scalar.activation(T(t_kdt), pb[7][:, :], ACT.Copy).then_inc(kt_sb.h, 1)
            for pr in range(2):
                act.e.wait_ge(o_ps.h, o_ps.by(act.l, pr + 1))
                nc.scalar.activation(T(t_o[pr]), pb[pr][:, :], ACT.Copy)
                nc.scalar.activation(T(t_osq[pr]), pb[pr][:, :], ACT.Square).then_inc(o_sq.h, 1)
            for pr in range(2):
                act.e.wait_ge(on_ps.h, on_ps.by(act.l, pr + 1))
                rstd(act, pb[2 + pr][:, :], T(t_or[pr]), on_ln, on_r, pr + 1)
            act.e.wait_ge(mn_x.h, mn_x.by(act.l, 9))
            for ct in range(2):
                nc.scalar.activation(y[:, 4 + ct, :], T(t_hc[ct]), ACT.Silu).then_inc(y_conv.h, 1)

        def act_attention(act, units, ytile):
            U = len(units)
            for i in range(U + 4):
                if i < U:
                    N = (units[i][2] + 1) * P
                    act.e.wait_ge(att_max.h, att_max.by(act.l, i + 1))
                    if i >= 3:
                        act.e.wait_ge(att_t.h, att_t.by(act.l, i - 2))
                    c = i % 4
                    nc.scalar.activation(p_buf(i)[:, 0:N], pb[(0, 1, 4, 5)[i % 4]][:, 0:N], ACT.Exp,
                                         bias=nmax[:, c:c + 1], accum_out=psum_[:, c:c + 1]).then_inc(att_exp.h, 1)
                u = i - 4
                if u >= 0 and u % 8 == 7:
                    act.e.wait_ge(att_o.h, att_o.by(act.l, u + 1))
                    nc.scalar.activation(y[:, ytile(u // 8), :], pb[6 + (u // 8) % 2][:, :], ACT.Copy).then_inc(y_att.h, 1)

        TWO_PI = 6.283185

        def act_even(act):
            act.e.wait_ge(cols_sb.h, 4)
            nc.scalar.activation(c_dt, c_ldt, ACT.Exp).then_inc(par_act.h, 1)
            act.e.wait_ge(par.h, 2)
            nc.scalar.activation(c_r, c_ard, ACT.Exp).then_inc(par_act.h, 1)
            act.e.wait_ge(par.h, 6)
            nc.scalar.activation(c_sin, c_fr, ACT.Sin, scale=TWO_PI).then_inc(par_act.h, 1)
            act.e.wait_ge(par.h, 8)
            nc.scalar.activation(c_cos, c_f2, ACT.Sin, scale=TWO_PI).then_inc(par_act.h, 1)
            nz = j = ny = 0
            nu = USE_EVEN
            nps = 0

            def trig(j):
                if j >= 3:
                    act.e.wait_ge(s5_p.h, j - 2)
                    act.e.wait_ge(s5_q.h, j - 2)
                act.e.wait_ge(s5_frac.h, j + 1)
                nc.scalar.activation(s5_sin[j % 3], s5_d[j % 2], ACT.Sin, scale=TWO_PI).then_inc(s5_trig.h, 1)
                act.e.wait_ge(s5_quart.h, j + 1)
                nc.scalar.activation(s5_cos[j % 3], s5_d2[j % 2], ACT.Sin, scale=TWO_PI).then_inc(s5_trig.h, 1)
            for t in E_SEQ:
                if t[0] == "z":
                    _, b, c, n, i = t
                    if c:
                        nu += 1
                        act.e.wait_ge(w_used.h, w_used.start + nu)
                    else:
                        nps += 1
                        act.e.wait_ge(ez_ps.h, nps)
                    bank = pb[nz % 2]
                    nz += 1
                    if n == "v":
                        nc.scalar.activation(e_vv[:, 2 * c:2 * c + 2, (b % 2) * 256:(b % 2 + 1) * 256],
                                             bank[:, :].rearrange("p (q c) -> p q c", q=2), ACT.Copy).then_inc(ez_sb.h, 1)
                    else:
                        dst = T(dict(u=e_u, q=e_q, k=e_k)[n] + i)
                        nc.scalar.activation(dst, bank[:, :], ACT.Copy,
                                             scale=float(E_DIM ** -0.5) if n == "q" else 1.0).then_inc(ez_sb.h, 1)
                elif t[0] == "prep":
                    for q, dst in enumerate((e_btr, e_bti)):
                        act.e.wait_ge(bc_ps.h, q + 1)
                        nc.scalar.activation(T(dst), pb[2 + q][:, :], ACT.Copy).then_inc(bt_sb.h, 1)
                    act.e.wait_ge(tab.h, 8)
                    nc.scalar.activation(T(e_sin), T(e_tmp[3]), ACT.Sin).then_inc(tab_sin.h, 1)
                    act.e.wait_ge(tab.h, 16)
                    nc.scalar.activation(T(e_cos), T(e_tmp[3]), ACT.Sin).then_inc(tab_sin.h, 1)
                    trig(0)
                elif t[0] == "bu" and t[1] + 1 < NST:
                    trig(t[1] + 1)
            for i in range(4):
                act.e.wait_ge(s5_y.h, i + 1)
                nc.scalar.activation(T(e_u + i), T(e_u + i), ACT.Gelu_apprx_tanh).then_inc(s5_gelu.h, 1)
            nu += 1
            for c in range(4):
                if c % 2:
                    act.e.wait_ge(w_used.h, w_used.start + nu + c // 2)
                else:
                    act.e.wait_ge(glu_ps.h, c // 2 + 1)
                nc.scalar.activation(T(e_glu + c), pb[2 + c][:, :], ACT.Sigmoid).then_inc(glu_sb.h, 1)

        def act_post(act, m):
            for k in range(KD):
                act.e.wait_ge(r_ready.h, m * KD + k + 1)
                nc.scalar.activation(T(SQ + k), T(RB + k), ACT.Square).then_inc(rsq.h, 1)
            act.e.wait_ge(rn_ps.h, m + 1)
            nc.scalar.activation(T(RT2), pb[7][:, :], ACT.Ln, bias=C("eps")).then_inc(rn_ln.h, 1)
            act.e.wait_ge(rn_ln.h, m + 1)
            nc.scalar.activation(T(RT2), T(RT2), ACT.Exp, scale=-0.5).then_inc(rn_r.h, 1)

        def act_odd(act):
            act.e.wait_ge(sp_step.h, 2)
            nc.scalar.activation(spc[:, 1, :], spc[:, 0, :], ACT.Exp, scale=-1.0).then_inc(sp_exp.h, 1)
            act.e.wait_ge(pad_zero.h, 1)
            for n in range(2 * KD):
                if n % 2:
                    act.e.wait_ge(w_used.h, w_used.start + USE_ODD + n // 2 + 1)
                else:
                    act.e.wait_ge(oz_ps.h, n // 2 + 1)
                if n < KD:
                    nc.scalar.activation(xpad[:, n, LRU_TAPS - 1:], pb[n % 4][:, :], ACT.Copy).then_inc(oz_sb.h, 1)
                else:
                    nc.scalar.activation(T(o_gel + n - KD), pb[n % 4][:, :], ACT.Gelu_apprx_tanh).then_inc(oz_sb.h, 1)
            for n in range(2 * KD):
                g, m = n // KD, n % KD
                if m == KD - 1:
                    act.e.wait_ge(w_used.h, w_used.start + USE_ODD + 9 + g)
                else:
                    act.e.wait_ge(og_ps.h, g * (KD - 1) + m + 1)
                bcol = R2["rg_b_i_2" if g else "rg_b_r_2"] + m
                nc.scalar.activation(T((o_i if g else o_r) + m), pb[n % 4][:, :], ACT.Sigmoid,
                                     bias=col2[:, bcol:bcol + 1]).then_inc(og_sb.h, 1)
            act.e.wait_ge(og_sb.h, KD)
            act.e.wait_ge(sp_step.h, SP_STEPS)
            for k in range(KD):
                nc.scalar.activation(W(k), T(o_r + k), ACT.Tanh, scale=spc[:, 7, k:k + 1]).then_inc(o_th.h, 1)
            for k in range(KD):
                nc.scalar.activation(T(o_r + k), T(o_r + k), ACT.Exp, scale=spc[:, 7, k:k + 1]).then_inc(o_a.h, 1)
            for k in range(KD):
                act.e.wait_ge(o_q.h, k + 1)
                nc.scalar.activation(W(k), W(k), ACT.Sqrt, scale=-1.0).then_inc(o_sqrt.h, 1)

        @block.scalar
        def _(e):
            act = Eng(e)
            e.sem_inc(sg_ready.h, sg_ready.start)
            act.e.wait_ge(rows_zero.h, 1)
            for i, n in enumerate(R1):
                e.dma_start(rows[R1[n]:R1[n] + 2 * KD, 0, :],
                            I[n].rearrange("l (k p) -> (l k) p", p=P)).then_inc(rows_in.h, 16)
            for l in range(DEPTH):
                for n, c in LAYER_ROWS:
                    r = l * NRL + RL[n]
                    w = I[n].shape[1]
                    if w == 64:
                        for q in range(2):
                            e.dma_start(rows[r:r + 1, 1, q * 64:(q + 1) * 64], I[n][l:l + 1, :]).then_inc(rows_in.h, 16)
                    elif w == D_QK:
                        e.dma_start(rows[r:r + 1, 1, 0:w], I[n][l:l + 1, :]).then_inc(rows_in.h, 16)
                    else:
                        e.dma_start(rows[r:r + c, 1, :], I[n][l].rearrange("(k p) -> k p", p=P)).then_inc(rows_in.h, 16)
            e.dma_start(rows[R2["s5_d_2"]:R2["s5_d_2"] + 4, 1, :],
                        I["s5_d_2"][0].rearrange("(k g) c -> k (g c)", k=4)).then_inc(rows_in.h, 16)
            for n in ("rg_conv_b_2", "rg_b_r_2", "rg_b_i_2", "rg_lam_2"):
                e.dma_start(rows[R2[n]:R2[n] + 8, 1, :], I[n][0].rearrange("(k p) -> k p", p=P)).then_inc(rows_in.h, 16)
            e.dma_start(rows[R2["rg_conv_w_2"]:R2["rg_conv_w_2"] + 32, 1, :],
                        I["rg_conv_w_2"][0].rearrange("j (k p) -> (j k) p", p=P)).then_inc(rows_in.h, 16)
            e.dma_start(rows[0:NR3, 2, :],
                        I["c_dw_w"].rearrange("l j o (t p) -> (l j o t) p", p=P)).then_inc(rows_in.h, 16)
            for i, n in enumerate(("s5_a_re_2", "s5_a_im_2")):
                e.dma_start(rows[i * NST:(i + 1) * NST, 3, :], I[n][0].rearrange("(j q) p -> j (q p)", q=2)).then_inc(rows_in.h, 16)
            e.dma_start(ldt[32:32 + NST, :], I["s5_log_dt_2"][0].rearrange("(j q) -> j q", q=2)).then_inc(ldt_in.h, 16)
            act.e.wait_ge(pro_ps.h, KD + 4)
            for i, (dst, n) in enumerate(((col1, NR1), (col2, NR2), (col3, NR3), (s5col, 3 * NST))):
                dst = dst[:, 0:3, :].rearrange("p a c -> p (a c)") if dst is s5col else dst[:, :]
                nc.scalar.activation(dst, pb[2 + i][:, 0:n], ACT.Copy).then_inc(cols_sb.h, 1)
            half = BIAS_N // 2
            bv4 = hT[0:A_HEADS, 20:22, 0:half]
            act.e.wait_ge(bvec_ps.h, 2)
            for q in range(2):
                nc.scalar.activation(bv4[:, q, :], pb[6 + q][0:A_HEADS, 0:half], ACT.Copy).then_inc(bvec_sb.h, 1)
            act.e.wait_ge(bvec_sb.h, 2)
            e.dma_start(bias_dram.ap().rearrange("h (q n) -> h q n", q=2), bv4).then_inc(bvec_out.h, 16)
            act.e.wait_ge(bvec_out.h, 16)
            e.dma_start(hT[:, 8:8 + A_HEADS, :], bass.AP(bias_dram, 0, [[1, P], [BIAS_N, A_HEADS], [1, SEQ]])
                        ).then_inc(bias_in.h, 16)
            for h in range(A_HEADS):
                act.e.wait_ge(bias_ps.h, h + 1)
                nc.scalar.activation(bias[:, h, :], pb[h][:, :], ACT.Copy).then_inc(bias_sb.h, 1)
            for l in range(DEPTH):
                act.l = l
                act_norm(act, l * 3)
                act_ffn(act, l * 2)
                act_norm(act, l * 3 + 1)
                act_z(act)
                act_mixers(act)
                act_attention(act, HYB_UNITS, lambda p: (6, 7, 0, 1)[p])
                act_norm(act, l * 3 + 2)
                act_ffn(act, l * 2 + 1)
            act.l = DEPTH
            n = 3 * DEPTH
            act_norm(act, n)
            act_even(act)
            act_attention(act, E_UNITS, lambda p: p)
            act_post(act, 0)
            act_norm(act, n + 1)
            act_ffn(act, 2 * DEPTH)
            act_post(act, 1)
            act_norm(act, n + 2)
            act_odd(act)
            act_post(act, 2)
            act_norm(act, n + 3)
            act_ffn(act, 2 * DEPTH + 1)
            act_post(act, 3)
            for n in range(2 * TB):
                act.e.wait_ge(fin_ps.h, n + 1)
                nc.scalar.activation(arena[:, n, :], pb[n % 2][:, :], ACT.Copy).then_inc(fin_sb.h, 1)

        def dve_norm(dve, n, g):
            dve.e.wait_ge(norm_r.h, n + 1)
            for k in range(KD):
                nc.vector.scalar_tensor_tensor(out=xn[:, k, :], in0=x[:, k, :], scalar=g(k), in1=T(RT),
                                               op0=ALU.mult, op1=ALU.mult).then_inc(xn_ready.h, 1)

        def dve_ffn(dve, f, u0, down):
            with dve.e.Fori(0, NF // 2) as i:
                for c in range(2):
                    dve.e.wait_ge(sg_ready.h, sg_ready.start + f * NF + 2 * i + (c + 1))
                    dve.e.wait_ge(w_used.h, w_used.start + u0 + 2 * i + (c + 1))
                    nc.vector.tensor_tensor(hT[:, bass.ds(2 * i + c, 1), :].rearrange("p a c -> p (a c)"), pb[2 + c][:, :],
                                            sg[:, c, :], ALU.mult).then_inc(h_ready.h, 1)
            with dve.e.Fori(0, KD // 2) as i:
                for c in range(2):
                    dve.e.wait_ge(wd_used.h, wd_used.start + f * KD + 2 * i + (c + 1))
                    down(i, c)

        def add_half(i, c):
            xk = x[:, bass.ds(2 * i + c, 1), :].rearrange("p a c -> p (a c)")
            nc.vector.scalar_tensor_tensor(out=xk, in0=pb[4 + c][:, :], scalar=0.5, in1=xk,
                                           op0=ALU.mult, op1=ALU.add).then_inc(x_ready.h, 1)

        def dve_index(dve):
            ni = nt = 0
            for tb in (3, 2, 1):
                N = (tb + 1) * P
                for h in range(IDX_HEADS):
                    dve.e.wait_ge(z_sb.h, z_sb.by(dve.l, IDX_POS[ni] + 1))
                    w = wA[:, tb * 8 + h:tb * 8 + h + 1]
                    r = W(idx_r[ni % 4])[:, 0:N]
                    if h == 0:
                        ins = nc.vector.tensor_scalar(score(tb), r, w, None, ALU.mult)
                    else:
                        dve.e.wait_ge(idx_acc.h, idx_acc.by(dve.l, ni))
                        ins = nc.vector.scalar_tensor_tensor(out=score(tb), in0=r, scalar=w, in1=score(tb),
                                                             op0=ALU.mult, op1=ALU.add)
                    ins.then_inc(idx_acc.h, 1)
                    ni += 1
                dve.e.wait_ge(idx_acc.h, idx_acc.by(dve.l, ni))
                dg = score(tb)[:, tb * P:]
                nc.vector.tensor_tensor(dg, dg, C("causal"), ALU.add).then_inc(idx_mask.h, 1)
                dve.e.wait_ge(idx_mask.h, idx_mask.by(dve.l, 4 - tb))
                for r in range(TOPK // 8):
                    if r:
                        dve.e.wait_ge(top_rep.h, top_rep.by(dve.l, nt))
                    nc.vector.max(m8, score(tb)).then_inc(top_max.h, 1)
                    nt += 1
                    dve.e.wait_ge(top_max.h, top_max.by(dve.l, nt))
                    nc.vector.match_replace(score(tb), m8, score(tb), SENTINEL).then_inc(top_rep.h, 1)
                dve.e.wait_ge(top_rep.h, top_rep.by(dve.l, nt))
                nc.vector.tensor_scalar(score(tb), score(tb), 0.9 * SENTINEL, NEG, ALU.is_gt, ALU.mult).then_inc(top_done.h, 1)

        def dve_mixers(dve):
            dve.e.wait_ge(g_abs.h, g_abs.by(dve.l, 1))
            nc.vector.tensor_scalar(W(w_mn), W(w_mn), 0.0, None, ALU.min).then_inc(g_min.h, 1)
            dve.e.wait_ge(g_min.h, g_min.by(dve.l, 1))
            dve.e.wait_ge(g_abs.h, g_abs.by(dve.l, 4))
            nc.vector.tensor_tensor(W(w_la), W(w_mn), T(t_ab), ALU.subtract).then_inc(g_b.h, 1)
            dve.e.wait_ge(g_b.h, g_b.by(dve.l, 1))
            nc.vector.tensor_tensor_scan(W(w_mn), C("chunkmask"), W(w_la), 0.0, ALU.mult, ALU.add).then_inc(g_b.h, 1)
            dve.e.wait_ge(g_b.h, g_b.by(dve.l, 2))

            def chunks(t):
                return t.rearrange("p (c t) -> p c t", c=NCH)
            b = chunks(W(w_mn))
            mid = b[:, :, B_CHUNK // 2 - 1:B_CHUNK // 2].to_broadcast([P, NCH, B_CHUNK])
            end = b[:, :, B_CHUNK - 1:B_CHUNK].to_broadcast([P, NCH, B_CHUNK])
            nc.vector.tensor_tensor(chunks(T(t_ab)), end, b, ALU.subtract).then_inc(g_b.h, 1)
            nc.vector.tensor_tensor(chunks(W(w_la)), b, mid, ALU.subtract).then_inc(g_b.h, 1)
            dve.e.wait_ge(g_b.h, g_b.by(dve.l, 4))
            lim = 16.0 * 85.0
            nc.vector.tensor_scalar(W(w_la), W(w_la), lim, -lim, ALU.min, ALU.max).then_inc(g_b.h, 1)
            dve.e.wait_ge(g_b.h, g_b.by(dve.l, 5))
            nc.vector.tensor_scalar(T(t_ab), T(t_ab), 0.0, None, ALU.min).then_inc(g_b.h, 1)
            for i, (t, r, gc) in enumerate([(t_aq[0], 0, "a_q_norm"), (t_aq[1], 1, "a_q_norm"), (t_ak[0], 2, "a_k_norm"),
                                            (t_ak[1], 3, "a_k_norm"), (t_dcq[0], 4, "d_qa_norm"),
                                            (t_dcq[1], 4, "d_qa_norm"), (t_dckv, 5, "d_kva_norm")]):
                col = RL[gc] + (1 if i == 5 else 0)
                dve.e.wait_ge(mn_r.h, mn_r.by(dve.l, r + 1))
                nc.vector.scalar_tensor_tensor(out=T(t), in0=T(t), scalar=cur[:, col:col + 1], in1=T(t_zr[r]),
                                               op0=ALU.mult, op1=ALU.mult).then_inc(mn_x.h, 1)
            for n, (e_, t) in enumerate(((T(t_qe), t_bq), (W(w_e1), t_bq), (W(w_e2), t_bk))):
                dve.e.wait_ge(g_exp.h, g_exp.by(dve.l, (1, 2, 4)[n]))
                nc.vector.tensor_tensor(e_, e_, T(t), ALU.mult).then_inc(b_qk.h, 1)
            for i in range(8 + 1):
                if i < 8:
                    col = RL["d_q_norm" if i < 4 else "d_k_norm"]
                    dve.e.wait_ge(dn_r.h, dn_r.by(dve.l, i + 1))
                    if i >= 2:
                        dve.e.wait_ge(dr_c.h, dr_c.by(dve.l, i - 1))
                    nc.vector.scalar_tensor_tensor(out=T(t_hn[i % 2])[0:D_QK, :], in0=T(t_hraw[i % 2])[0:D_QK, :],
                                                   scalar=cur[0:D_QK, col:col + 1], in1=T(t_hr[i % 2])[0:D_QK, :],
                                                   op0=ALU.mult, op1=ALU.mult).then_inc(dn_x.h, 1)
                if i >= 1:
                    u = i - 1
                    dve.e.wait_ge(dr_ps.h, dr_ps.by(dve.l, u + 1))
                    nc.vector.tensor_tensor(T(t_hr[u % 2])[0:D_QK, :], pb[3][0:D_QK, :], C("sin96")[0:D_QK, :],
                                            ALU.mult).then_inc(dr_s.h, 1)
            dve.e.wait_ge(mn_r.h, mn_r.by(dve.l, 7))
            for ct in range(2):
                col = RL["c_norm"] + ct
                nc.vector.scalar_tensor_tensor(out=T(t_hc[ct]), in0=T(t_hc[ct]), scalar=cur[:, col:col + 1], in1=T(t_cr),
                                               op0=ALU.mult, op1=ALU.mult).then_inc(mn_x.h, 1)
            for c in range(NCH - 1):
                dve.e.wait_ge(u_ps.h, u_ps.by(dve.l, c + 1))
                um = Sst(1) if c == 0 else T(t_um)[:, (c % 2) * 256:(c % 2) * 256 + 256]
                nc.vector.tensor_tensor(um, pb[2 + c % 2][:, 0:256], C("headblk"), ALU.mult).then_inc(u_msk.h, 1)
                dve.e.wait_ge(u_msk.h, u_msk.by(dve.l, c + 1))
                if c == 0:
                    dve.e.sem_inc(s_ready.h, 1)
                    continue
                dve.e.wait_ge(s_ready.h, s_ready.by(dve.l, c))
                nc.vector.scalar_tensor_tensor(out=Sst(c + 1), in0=Sst(c), scalar=glast[:, c:c + 1], in1=um,
                                               op0=ALU.mult, op1=ALU.add).then_inc(s_ready.h, 1)
            for tb in range(TB):
                dve.e.wait_ge(at_ps.h, at_ps.by(dve.l, tb + 1))
                for q in range(2):
                    r = slice(64 * q, 64 * q + 64)
                    src = pb[4 + tb % 2][r, :].rearrange("p (h c) -> p h c", h=B_HEADS)[:, :, r]
                    tri = C("tri")[r, :].unsqueeze(1).to_broadcast([64, B_HEADS, B_CHUNK])
                    nc.vector.tensor_tensor(att_diag[r, tb, :, r], src, tri, ALU.mult).then_inc(at_sb.h, 1)
            for pr in range(2):
                col = RL["b_out_norm"]
                dve.e.wait_ge(on_r.h, on_r.by(dve.l, pr + 1))
                nc.vector.scalar_tensor_tensor(out=T(t_o[pr]), in0=T(t_o[pr]), scalar=cur[:, col:col + 1],
                                               in1=T(t_or[pr]), op0=ALU.mult, op1=ALU.mult).then_inc(o_n.h, 1)

        def dve_attention(dve, units):
            U = len(units)
            for i in range(U + 2):
                if i < U:
                    N = (units[i][2] + 1) * P
                    c = i % 4
                    dve.e.wait_ge(att_s.h, att_s.by(dve.l, i + 1))
                    nc.vector.tensor_reduce(nmax[:, c:c + 1], pb[(0, 1, 4, 5)[i % 4]][:, 0:N], AX.X, ALU.max,
                                            negate=True).then_inc(att_max.h, 1)
                if 1 <= i < U + 1:
                    u = i - 1
                    c = u % 4
                    dve.e.wait_ge(att_exp.h, att_exp.by(dve.l, u + 1))
                    if u >= 4:
                        dve.e.wait_ge(att_p.h, att_p.by(dve.l, u - 3))
                    nc.vector.reciprocal(rsum[:, c:c + 1], psum_[:, c:c + 1]).then_inc(att_rs.h, 1)
                if i >= 2:
                    u = i - 2
                    N = (units[u][2] + 1) * P
                    dve.e.wait_ge(att_t.h, att_t.by(dve.l, u + 1))
                    if u >= 2:
                        dve.e.wait_ge(att_o.h, att_o.by(dve.l, u - 1))
                    nc.vector.tensor_copy(pt_buf(u)[:, 0:N], pb[2 + u % 2][:, 0:N]).then_inc(att_pt.h, 1)

        def dve_out_add(dve):
            for dc in range(KD):
                if dc % 2:
                    dve.e.wait_ge(w_used.h, w_used.by(dve.l, NF + len(U_Z) + dc // 2 + 1))
                else:
                    dve.e.wait_ge(out_ps.h, out_ps.by(dve.l, dc // 2 + 1))
                nc.vector.tensor_tensor(x[:, dc, :], pb[dc % 2][:, :], x[:, dc, :], ALU.add).then_inc(x_ready.h, 1)

        def to_r(i, c):
            nc.vector.tensor_copy(arena[:, bass.ds(2 * i + (RB + c), 1), :].rearrange("p a c -> p (a c)"),
                                  pb[4 + c][:, :]).then_inc(r_ready.h, 1)

        def dve_out_r(dve, use0, eo0):
            for dc in range(KD):
                if dc % 2:
                    dve.e.wait_ge(w_used.h, w_used.start + use0 + dc // 2 + 1)
                else:
                    dve.e.wait_ge(eo_ps.h, eo0 + dc // 2 + 1)
                nc.vector.tensor_copy(T(RB + dc), pb[dc % 2][:, :]).then_inc(r_ready.h, 1)

        def dve_post(dve, m, g):
            dve.e.wait_ge(rn_r.h, m + 1)
            for k in range(KD):
                nc.vector.scalar_tensor_tensor(out=T(RB + k), in0=T(RB + k), scalar=g(k), in1=T(RT2),
                                               op0=ALU.mult, op1=ALU.mult).then_inc(r_n.h, 1)
            for k in range(KD):
                dve.e.wait_ge(r_n.h, m * KD + k + 1)
                nc.vector.tensor_tensor(x[:, k, :], x[:, k, :], T(RB + k), ALU.add).then_inc(x_ready.h, 1)

        C1 = 6.28125
        C2 = float(np.float32(np.round((2 * math.pi - C1) * 2 ** 21) / 2 ** 21))
        C3 = float(np.float32(2 * math.pi - C1 - C2))

        def dve_even(dve):
            V = nc.vector
            ts, tt, stt = V.tensor_scalar, V.tensor_tensor, V.scalar_tensor_tensor
            par_n = count(1)
            dve.e.wait_ge(cols_sb.h, 4)
            dve.e.wait_ge(par_act.h, 1)
            tt(c_th, c_aim, c_dt, ALU.mult).then_inc(par.h, 1)
            dve.e.wait_ge(par.h, next(par_n))
            tt(c_ard, c_are, c_dt, ALU.mult).then_inc(par.h, 1)
            dve.e.wait_ge(par.h, next(par_n))
            ts(c_t1, c_th, float(1 / (2 * math.pi)), None, ALU.mult).then_inc(par.h, 1)
            dve.e.wait_ge(par.h, next(par_n))
            ts(c_n, c_t1, MAGIC, None, ALU.add).then_inc(par.h, 1)
            dve.e.wait_ge(par.h, next(par_n))
            ts(c_n, c_n, MAGIC, None, ALU.subtract).then_inc(par.h, 1)
            dve.e.wait_ge(par.h, next(par_n))
            tt(c_fr, c_t1, c_n, ALU.subtract).then_inc(par.h, 1)
            dve.e.wait_ge(par.h, next(par_n))
            ts(c_t2, c_fr, 0.25, None, ALU.is_gt).then_inc(par.h, 1)
            dve.e.wait_ge(par.h, next(par_n))
            stt(c_f2, c_fr, 0.25, c_t2, ALU.add, ALU.subtract).then_inc(par.h, 1)
            dve.e.wait_ge(par.h, next(par_n))
            dve.e.wait_ge(par_act.h, 4)
            tt(c_nre, c_r, c_cos, ALU.mult).then_inc(par.h, 1)
            dve.e.wait_ge(par.h, next(par_n))
            ts(c_nre, c_nre, 1.0, None, ALU.subtract).then_inc(par.h, 1)
            dve.e.wait_ge(par.h, next(par_n))
            tt(c_nim, c_r, c_sin, ALU.mult).then_inc(par.h, 1)
            dve.e.wait_ge(par.h, next(par_n))
            tt(c_den, c_are, c_are, ALU.mult).then_inc(par.h, 1)
            dve.e.wait_ge(par.h, next(par_n))
            tt(c_t1, c_aim, c_aim, ALU.mult).then_inc(par.h, 1)
            dve.e.wait_ge(par.h, next(par_n))
            tt(c_den, c_den, c_t1, ALU.add).then_inc(par.h, 1)
            dve.e.wait_ge(par.h, next(par_n))
            V.reciprocal(c_den, c_den).then_inc(par.h, 1)
            dve.e.wait_ge(par.h, next(par_n))
            tt(c_t1, c_nre, c_are, ALU.mult).then_inc(par.h, 1)
            dve.e.wait_ge(par.h, next(par_n))
            tt(c_t2, c_nim, c_aim, ALU.mult).then_inc(par.h, 1)
            dve.e.wait_ge(par.h, next(par_n))
            tt(c_fre, c_t1, c_t2, ALU.add).then_inc(par.h, 1)
            dve.e.wait_ge(par.h, next(par_n))
            tt(c_fre, c_fre, c_den, ALU.mult).then_inc(par.h, 1)
            dve.e.wait_ge(par.h, next(par_n))
            tt(c_t1, c_nim, c_are, ALU.mult).then_inc(par.h, 1)
            dve.e.wait_ge(par.h, next(par_n))
            tt(c_t2, c_nre, c_aim, ALU.mult).then_inc(par.h, 1)
            dve.e.wait_ge(par.h, next(par_n))
            tt(c_fim, c_t1, c_t2, ALU.subtract).then_inc(par.h, 1)
            dve.e.wait_ge(par.h, next(par_n))
            tt(c_fim, c_fim, c_den, ALU.mult).then_inc(par.h, 1)
            dve.e.wait_ge(par.h, next(par_n))
            dve.e.wait_ge(s5_in.h, 16 * 7)
            bre, bim = [T(e_bst)[:, q * 256:(q + 1) * 256].rearrange("p (j c) -> p j c", c=SSM_C) for q in range(2)]
            sc = [T(e_tmp[1])[:, 0:256], T(e_tmp[1])[:, 256:], T(e_tmp[2])[:, 0:256], T(e_tmp[2])[:, 256:]]
            sc = [t.rearrange("p (j c) -> p j c", c=SSM_C) for t in sc]

            def wide(c):
                return c.unsqueeze(2).to_broadcast([P, NST, SSM_C])
            tt(sc[0], bre, wide(c_fre), ALU.mult).then_inc(par.h, 1)
            dve.e.wait_ge(par.h, next(par_n))
            tt(sc[1], bim, wide(c_fim), ALU.mult).then_inc(par.h, 1)
            dve.e.wait_ge(par.h, next(par_n))
            tt(sc[2], bre, wide(c_fim), ALU.mult).then_inc(par.h, 1)
            dve.e.wait_ge(par.h, next(par_n))
            tt(sc[3], bim, wide(c_fre), ALU.mult).then_inc(par.h, 1)
            dve.e.wait_ge(par.h, next(par_n))
            tt(sc[0], sc[0], sc[1], ALU.subtract).then_inc(par.h, 1)
            dve.e.wait_ge(par.h, next(par_n))
            tt(sc[2], sc[2], sc[3], ALU.add).then_inc(par.h, 1)
            dve.e.wait_ge(par.h, next(par_n))
            half = C("half16").rearrange("p (q c) -> p q c", q=2).unsqueeze(1).to_broadcast([P, NST, 2, SSM_C])
            for src, dst in ((sc[0], e_ere), (sc[2], e_eim)):
                tt(T(dst).rearrange("p (j q c) -> p j q c", j=NST, q=2),
                        src.unsqueeze(2).to_broadcast([P, NST, 2, SSM_C]), half, ALU.mult).then_inc(par.h, 1)
                dve.e.wait_ge(par.h, next(par_n))
            assert next(par_n) == PAR_E + 1
            tab_n = count(1)
            ang, rnd, red = T(e_tmp[1]), T(e_tmp[2]), T(e_tmp[3])
            for q in range(2):
                if q == 0:
                    V.tensor_copy(ang, T(e_pos).bitcast(I32)).then_inc(tab.h, 1)
                    dve.e.wait_ge(tab.h, next(tab_n))
                    ts(ang, ang, C("freq"), None, ALU.mult).then_inc(tab.h, 1)
                    dve.e.wait_ge(tab.h, next(tab_n))
                    ts(rnd, ang, float(1 / (2 * math.pi)), MAGIC, ALU.mult, ALU.add).then_inc(tab.h, 1)
                    dve.e.wait_ge(tab.h, next(tab_n))
                else:
                    ts(rnd, ang, float(1 / (2 * math.pi)), 0.25, ALU.mult, ALU.add).then_inc(tab.h, 1)
                    dve.e.wait_ge(tab.h, next(tab_n))
                    ts(rnd, rnd, MAGIC, None, ALU.add).then_inc(tab.h, 1)
                    dve.e.wait_ge(tab.h, next(tab_n))
                ts(rnd, rnd, MAGIC, None, ALU.subtract).then_inc(tab.h, 1)
                dve.e.wait_ge(tab.h, next(tab_n))
                if q:
                    dve.e.wait_ge(tab_sin.h, 1)
                stt(red, rnd, -C1, ang, ALU.mult, ALU.add).then_inc(tab.h, 1)
                dve.e.wait_ge(tab.h, next(tab_n))
                stt(red, rnd, -C2, red, ALU.mult, ALU.add).then_inc(tab.h, 1)
                dve.e.wait_ge(tab.h, next(tab_n))
                stt(red, rnd, -C3, red, ALU.mult, ALU.add).then_inc(tab.h, 1)
                dve.e.wait_ge(tab.h, next(tab_n))
                if q:
                    ts(red, red, float(np.float32(math.pi / 2)), None, ALU.add).then_inc(tab.h, 1)
                    dve.e.wait_ge(tab.h, next(tab_n))
                lim = float(np.nextafter(np.float32(math.pi), np.float32(0)))
                ts(red, red, lim, -lim, ALU.min, ALU.max).then_inc(tab.h, 1)
                dve.e.wait_ge(tab.h, next(tab_n))
            dve.e.wait_ge(tab_sin.h, 2)
            cw = C("half16").unsqueeze(1).to_broadcast([P, NST, 2 * SSM_C])

            def tiles(t):
                return t.rearrange("p (j c) -> p j c", j=NST)
            dve.e.wait_ge(bc_ps.h, 4)
            dve.e.wait_ge(bt_sb.h, 2)
            tt(tiles(T(e_cre)), tiles(pb[4][:, :]), cw, ALU.mult).then_inc(cb_sb.h, 1)
            tt(tiles(T(e_cin)), tiles(pb[5][:, :]), cw, ALU.mult).then_inc(cb_sb.h, 1)
            dve.e.wait_ge(cb_sb.h, 2)
            ts(T(e_crn), T(e_cre), -1.0, None, ALU.mult).then_inc(cb_sb.h, 1)
            ts(T(e_cin), T(e_cin), -1.0, None, ALU.mult).then_inc(cb_sb.h, 1)

            def angles(j):
                dve.e.wait_ge(s5_rnd.h, 2 * j + 2)
                if j >= 2:
                    dve.e.wait_ge(s5_trig.h, 2 * (j - 2) + 2)
                stt(s5_d[j % 2], C("iota"), c_fr[:, j:j + 1], s5_n[j % 2], ALU.mult, ALU.subtract).then_inc(s5_frac.h, 1)
                dve.e.wait_ge(s5_frac.h, j + 1)
                dve.e.wait_ge(s5_wrap.h, j + 1)
                stt(s5_d2[j % 2], s5_d[j % 2], 0.25, s5_n[j % 2], ALU.add, ALU.subtract).then_inc(s5_quart.h, 1)

            def rotate_in(j):
                a = s5_a[j % 3]
                dve.e.wait_ge(bu_ps.h, j + 1)
                dve.e.wait_ge(s5_trig.h, 2 * j + 2)
                if j >= 3:
                    dve.e.wait_ge(yy_ps.h, j - 2)
                if j == 2:
                    dve.e.wait_ge(tab_sin.h, 2)
                b = [pb[2 + 2 * (j % 2) + q][:, :] for q in range(2)]
                tt(a[0], b[0], s5_cos[j % 3], ALU.mult)
                tt(a[1], b[1], s5_sin[j % 3], ALU.mult)
                tt(a[2], b[1], s5_cos[j % 3], ALU.mult)
                tt(a[3], b[0], s5_sin[j % 3], ALU.mult).then_inc(s5_rot.h, 1)

            def scan(j):
                a = s5_a[j % 3]
                r = c_r[:, j:j + 1].to_broadcast([P, SEQ])
                dve.e.wait_ge(s5_x.h, 2 * j + 2)
                V.tensor_tensor_scan(a[1], r, a[0], 0.0, ALU.mult, ALU.add).then_inc(s5_g.h, 1)
                V.tensor_tensor_scan(a[3], r, a[2], 0.0, ALU.mult, ALU.add).then_inc(s5_g.h, 1)
                dve.e.wait_ge(s5_g.h, 2 * j + 1)
                tt(a[0], a[1], s5_cos[j % 3], ALU.mult)
                tt(a[1], a[1], s5_sin[j % 3], ALU.mult).then_inc(s5_p.h, 1)

            def skip(i):
                dve.e.wait_ge(yy_ps.h, 4 * i + 4)
                dcol = R2["s5_d_2"] + i
                stt(T(e_u + i), T(e_u + i), col2[:, dcol:dcol + 1], pb[6 + i % 2][:, :], ALU.mult, ALU.add).then_inc(s5_y.h, 1)
            angles(0)
            for j in range(NST + 1):
                if j + 1 < NST:
                    angles(j + 1)
                if j < NST:
                    rotate_in(j)
                if j >= 1:
                    scan(j - 1)
                if j >= 6 and (j - 6) % 4 == 0:
                    skip((j - 6) // 4)
            for i in range((NST - 6) // 4 + 1, 4):
                skip(i)
            for i in range(8):
                dve.e.wait_ge(rot_ps.h, i + 1)
                if i >= 2:
                    dve.e.wait_ge(rot_ready.h, i - 1)
                tt(s5_n[i % 2], pb[i % 2][:, :], T(e_sin), ALU.mult).then_inc(rot_s.h, 1)

        def dve_odd(dve):
            V = nc.vector
            ts, tt, stt = V.tensor_scalar, V.tensor_tensor, V.scalar_tensor_tensor
            V.memset(xpad[:, :, 0:LRU_TAPS - 1], 0.0).then_inc(pad_zero.h, 1)
            sp_n = count(1)
            lam = col2[:, R2["rg_lam_2"]:R2["rg_lam_2"] + KD]
            S = [spc[:, i, :] for i in range(8)]
            ts(S[2], lam, -1.0, None, ALU.mult).then_inc(sp_step.h, 1)
            dve.e.wait_ge(sp_step.h, next(sp_n))
            tt(S[0], lam, S[2], ALU.max).then_inc(sp_step.h, 1)
            dve.e.wait_ge(sp_step.h, next(sp_n))
            dve.e.wait_ge(sp_exp.h, 1)
            ts(S[3], S[1], 2.0, None, ALU.add).then_inc(sp_step.h, 1)
            dve.e.wait_ge(sp_step.h, next(sp_n))
            V.reciprocal(S[3], S[3]).then_inc(sp_step.h, 1)
            dve.e.wait_ge(sp_step.h, next(sp_n))
            tt(S[3], S[1], S[3], ALU.mult).then_inc(sp_step.h, 1)
            dve.e.wait_ge(sp_step.h, next(sp_n))
            tt(S[4], S[3], S[3], ALU.mult).then_inc(sp_step.h, 1)
            dve.e.wait_ge(sp_step.h, next(sp_n))
            ts(S[5], S[4], 1 / 19, None, ALU.mult).then_inc(sp_step.h, 1)
            dve.e.wait_ge(sp_step.h, next(sp_n))
            for o in (17, 15, 13, 11, 9, 7, 5, 3):
                stt(S[5], S[5], 1 / o, S[4], ALU.add, ALU.mult).then_inc(sp_step.h, 1)
                dve.e.wait_ge(sp_step.h, next(sp_n))
            stt(S[5], S[5], 1.0, S[3], ALU.add, ALU.mult).then_inc(sp_step.h, 1)
            dve.e.wait_ge(sp_step.h, next(sp_n))
            ts(S[2], S[2], 0.0, None, ALU.max).then_inc(sp_step.h, 1)
            dve.e.wait_ge(sp_step.h, next(sp_n))
            stt(S[6], S[5], 2.0, S[2], ALU.mult, ALU.add).then_inc(sp_step.h, 1)
            dve.e.wait_ge(sp_step.h, next(sp_n))
            ts(S[7], S[6], -8.0, None, ALU.mult).then_inc(sp_step.h, 1)
            dve.e.wait_ge(sp_step.h, next(sp_n))
            assert next(sp_n) == SP_STEPS + 1
            for k in range(KD):
                dve.e.wait_ge(oz_sb.h, k + 1)
                for j in range(LRU_TAPS):
                    w = R2["rg_conv_w_2"] + j * KD + k
                    w = col2[:, w:w + 1]
                    src = xpad[:, k, j:j + SEQ]
                    if j == 0:
                        b = R2["rg_conv_b_2"] + k
                        ins = ts(T(o_xc + k), src, w, col2[:, b:b + 1], ALU.mult, ALU.add)
                    else:
                        dve.e.wait_ge(cv.h, LRU_TAPS * k + j)
                        ins = stt(T(o_xc + k), src, w, T(o_xc + k), ALU.mult, ALU.add)
                    ins.then_inc(cv.h, 1)
            for k in range(KD):
                dve.e.wait_ge(o_a2.h, k + 1)
                stt(W(k), xpad[:, k, 0:SEQ], 1.0, W(k), ALU.add, ALU.mult).then_inc(o_q.h, 1)
            for k in range(KD):
                dve.e.wait_ge(o_gx.h, k + 1)
                dve.e.wait_ge(o_sqrt.h, k + 1)
                tt(T(o_i + k), T(o_i + k), W(k), ALU.mult).then_inc(o_b.h, 1)
                dve.e.wait_ge(o_b.h, k + 1)
                V.tensor_tensor_scan(T(o_xc + k), T(o_r + k), T(o_i + k), 0.0, ALU.mult, ALU.add).then_inc(o_h.h, 1)

        @block.vector
        def _(e):
            dve = Eng(e)
            e.sem_inc(h_ready.h, h_ready.start)
            nc.vector.memset(relb[32:64, :], NEG).then_inc(relb_neg.h, 1)
            dve.e.wait_ge(rows_zero.h, 1)
            dve.e.wait_ge(ldt_in.h, 16)
            nc.vector.tensor_copy(rows[32:32 + NST, 3, :].rearrange("j (q p) -> j q p", q=2),
                                  ldt[32:32 + NST, :].unsqueeze(2).to_broadcast([NST, 2, SSM_P])).then_inc(ldt_row.h, 1)
            for k in range(KD):
                dve.e.wait_ge(pro_ps.h, k + 1)
                nc.vector.tensor_copy(x[:, k, :], pb[k % 2][:, :]).then_inc(x_ready.h, 1)
            dve.e.wait_ge(consts_in.h, 16)
            dve.e.wait_ge(cols_sb.h, 4)
            for l in range(DEPTH):
                dve.l = l
                nc.vector.tensor_copy(cur[:, :], col2[:, bass.ds(l * NRL, NRL)]).then_inc(cur_cp.h, 1)
                nc.vector.tensor_copy(cur_dw[:, :], col3[:, bass.ds(l * TAPS * 2, TAPS * 2)]).then_inc(cur_ready.h, 1)
                dve.e.wait_ge(cur_cp.h, cur_cp.by(dve.l, 1))
                for n, s in (("a_q_norm", A_DIM ** -0.5), ("d_q_norm", D_QK ** -0.5)):
                    c = cur[:, RL[n]:RL[n] + 1]
                    nc.vector.tensor_scalar(c, c, float(s), None, ALU.mult).then_inc(cur_ready.h, 1)

                def gain(name):
                    return lambda k: col1[:, bass.ds(l * KD + (R1[name] + k), 1)]
                dve_norm(dve, l * 3, gain("ffn1_norm"))
                dve_ffn(dve, l * 2, l * len(U_LAYER), add_half)
                dve_norm(dve, l * 3 + 1, gain("mix_norm"))
                dve_index(dve)
                dve_mixers(dve)
                dve_attention(dve, HYB_UNITS)
                dve_out_add(dve)
                dve_norm(dve, l * 3 + 2, gain("ffn2_norm"))
                dve_ffn(dve, l * 2 + 1, l * len(U_LAYER) + (NF + len(U_Z) + 4), add_half)
            dve.l = DEPTH
            def gain2(name, i):
                return lambda k: col1[:, R1[name] + i * KD + k:R1[name] + i * KD + k + 1]
            n = 3 * DEPTH
            dve_norm(dve, n, gain2("norm_mix_pre_2", 0))
            dve_even(dve)
            dve_attention(dve, E_UNITS)
            dve_out_r(dve, USE_EVEN + len(E_BLOCKS) + 2, 0)
            dve_post(dve, 0, gain2("norm_mix_post_2", 0))
            dve_norm(dve, n + 1, gain2("norm_ffn_pre_2", 0))
            dve_ffn(dve, 2 * DEPTH, USE_EVEN + len(E_BLOCKS) + 6, to_r)
            dve_post(dve, 1, gain2("norm_ffn_post_2", 0))
            dve_norm(dve, n + 2, gain2("norm_mix_pre_2", 1))
            dve_odd(dve)
            dve_out_r(dve, USE_ODD + 10, 4)
            dve_post(dve, 2, gain2("norm_mix_post_2", 1))
            dve_norm(dve, n + 3, gain2("norm_ffn_pre_2", 1))
            dve_ffn(dve, 2 * DEPTH + 1, USE_ODD + 14, to_r)
            dve_post(dve, 3, gain2("norm_ffn_post_2", 1))

        def pool_mixers(pool):
            for ct in range(2):
                pool.e.wait_ge(z_sb.h, z_sb.by(pool.l, max(Z_POS[f"ca{ct}"], Z_POS[f"cg{ct}"]) + 1))
                nc.gpsimd.tensor_tensor(hpad[:, ct, TAPS - 1:], T(t_ca[ct]), T(t_cg[ct]), ALU.mult).then_inc(hp_ready.h, 1)
            pool_diag(pool, 8, TAPS * 2)
            pool.e.wait_ge(g_exp.h, g_exp.by(pool.l, 3))
            nc.gpsimd.tensor_tensor(W(w_e1n), W(w_e1n), T(t_bk), ALU.mult).then_inc(b_kd.h, 1)
            pool.e.wait_ge(b_kd.h, b_kd.by(pool.l, 1))
            pool.e.wait_ge(g_exp.h, g_exp.by(pool.l, 5))
            for h in range(B_HEADS):
                nc.gpsimd.tensor_scalar(kdm[h], W(w_e1n), C("headcol")[:, h:h + 1], None, ALU.mult).then_inc(b_kd.h, 1)
            for u in range(8):
                dst = T((t_dq + t_dk)[u])[0:D_QK, :]
                pool.e.wait_ge(dn_x.h, dn_x.by(pool.l, u + 1))
                nc.gpsimd.tensor_tensor(dst, T(t_hn[u % 2])[0:D_QK, :], C("cos96")[0:D_QK, :], ALU.mult).then_inc(dr_c.h, 1)
                pool.e.wait_ge(dr_c.h, dr_c.by(pool.l, u + 1))
                pool.e.wait_ge(dr_s.h, dr_s.by(pool.l, u + 1))
                nc.gpsimd.tensor_tensor(dst, dst, T(t_hr[u % 2])[0:D_QK, :], ALU.add).then_inc(dh_ready.h, 1)
            for pr in range(2):
                pool.e.wait_ge(o_n.h, o_n.by(pool.l, pr + 1))
                nc.gpsimd.tensor_tensor(y[:, 2 + pr, :], T(t_o[pr]), T(t_br[pr]), ALU.mult).then_inc(y_b.h, 1)

        def pool_diag(pool, a, b):
            for n in range(a, b):
                ct, j = n // TAPS, n % TAPS
                if n >= 8:
                    pool.e.wait_ge(diag_used.h, diag_used.by(pool.l, n - 7))
                nc.gpsimd.tensor_scalar(diag[:, n % 8, :], ident, cur_dw[:, 2 * j + ct:2 * j + ct + 1], None,
                                        ALU.mult).then_inc(diag_ready.h, 1)

        def pool_attention(pool, units):
            U = len(units)
            for i in range(U + 1):
                for u in ([0, 1, 2] if i == 0 else [i + 2]):
                    if u in BM and units is HYB_UNITS:
                        _, h, tb = units[u]
                        n = BM.index(u)
                        if n == 0:
                            pool.e.wait_ge(top_done.h, top_done.by(pool.l, 3))
                            pool.e.wait_ge(bias_sb.h, A_HEADS)
                        if n >= 3:
                            pool.e.wait_ge(att_s.h, att_s.by(pool.l, BM[n - 3] + 1))
                        nc.gpsimd.tensor_tensor(T(t_bm[n % 3])[:, 0:(tb + 1) * P], bias[:, h, SEQ - (tb + 1) * P:],
                                                score(tb), ALU.add).then_inc(att_bm.h, 1)
                if i >= 1:
                    u = i - 1
                    c = u % 4
                    pool.e.wait_ge(att_rs.h, att_rs.by(pool.l, u + 1))
                    p = p_buf(u)[:, 0:(units[u][2] + 1) * P]
                    nc.gpsimd.tensor_scalar(p, p, rsum[:, c:c + 1], None, ALU.mult).then_inc(att_p.h, 1)

        def pool_even(pool):
            G = nc.gpsimd
            ts, tt = G.tensor_scalar, G.tensor_tensor

            def turns(j):
                if j >= 2:
                    pool.e.wait_ge(s5_quart.h, j - 1)
                ts(s5_n[j % 2], C("iota"), c_fr[:, j:j + 1], MAGIC, ALU.mult, ALU.add).then_inc(s5_rnd.h, 1)
                pool.e.wait_ge(s5_rnd.h, 2 * j + 1)
                ts(s5_n[j % 2], s5_n[j % 2], MAGIC, None, ALU.subtract).then_inc(s5_rnd.h, 1)

            def wrap(j):
                pool.e.wait_ge(s5_frac.h, j + 1)
                ts(s5_n[j % 2], s5_d[j % 2], 0.25, None, ALU.is_gt).then_inc(s5_wrap.h, 1)

            def frame(j):
                a = s5_a[j % 3]
                pool.e.wait_ge(s5_rot.h, j + 1)
                tt(a[0], a[0], a[1], ALU.add).then_inc(s5_x.h, 1)
                tt(a[2], a[2], a[3], ALU.subtract).then_inc(s5_x.h, 1)

            def back(j):
                a = s5_a[j % 3]
                pool.e.wait_ge(s5_g.h, 2 * j + 2)
                tt(a[2], a[3], s5_sin[j % 3], ALU.mult)
                tt(a[3], a[3], s5_cos[j % 3], ALU.mult).then_inc(s5_q.h, 1)
            pool.e.wait_ge(par.h, PAR_E)
            turns(0)
            turns(1)
            wrap(0)
            for j in range(NST + 1):
                if j + 1 < NST:
                    wrap(j + 1)
                if j + 2 < NST:
                    turns(j + 2)
                if j < NST:
                    frame(j)
                if j >= 1:
                    back(j - 1)
            for i in range(8):
                t = T((e_q if i % 2 == 0 else e_k) + i // 2)
                pool.e.wait_ge(rot_ps.h, i + 1)
                tt(t, t, T(e_cos), ALU.mult).then_inc(rot_c.h, 1)
                pool.e.wait_ge(rot_c.h, i + 1)
                pool.e.wait_ge(rot_s.h, i + 1)
                tt(t, t, s5_n[i % 2], ALU.add).then_inc(rot_ready.h, 1)
            for c in range(4):
                pool.e.wait_ge(glu_sb.h, c + 1)
                tt(y[:, 4 + c, :], T(e_u + c), T(e_glu + c), ALU.mult).then_inc(y_ssm.h, 1)

        def pool_odd(pool):
            tt = nc.gpsimd.tensor_tensor
            for k in range(KD):
                pool.e.wait_ge(og_sb.h, KD + k + 1)
                pool.e.wait_ge(cv.h, LRU_TAPS * (k + 1))
                tt(T(o_i + k), T(o_i + k), T(o_xc + k), ALU.mult).then_inc(o_gx.h, 1)
            for k in range(KD):
                pool.e.wait_ge(o_a.h, k + 1)
                tt(xpad[:, k, 0:SEQ], T(o_r + k), T(o_r + k), ALU.mult).then_inc(o_a2.h, 1)
            for k in range(KD):
                pool.e.wait_ge(o_h.h, k + 1)
                tt(y[:, k, :], T(o_xc + k), T(o_gel + k), ALU.mult).then_inc(y_lru.h, 1)

        @block.gpsimd
        def _(e):
            pool = Eng(e)
            nc.gpsimd.memset(rows[:, :, :], 0.0).then_inc(rows_zero.h, 1)
            nc.gpsimd.memset(hpad[:, :, 0:TAPS - 1], 0.0)
            nc.gpsimd.memset(att_diag[:, :, :, :], 0.0).then_inc(zeros_set.h, 1)
            pool.e.wait_ge(consts_in.h, 16)
            for l in range(DEPTH):
                pool.l = l
                pool.e.wait_ge(cur_ready.h, cur_ready.by(pool.l, 3))
                pool_diag(pool, 0, 8)
                pool_mixers(pool)
                pool_attention(pool, HYB_UNITS)
            pool.l = DEPTH
            pool_even(pool)
            pool_attention(pool, E_UNITS)
            pool_odd(pool)


_NAMES = ["x", "ffn1_norm", "ffn1_gate", "ffn1_up", "ffn1_down", "mix_norm", "w_in", "a_q_norm", "a_k_norm", "rel_bias",
          "b_gate_up", "b_gate_bias", "b_out_norm", "c_dw_w", "c_dw_b", "c_norm", "d_qa_norm", "d_uq", "d_kva_norm",
          "d_ukv", "d_q_norm", "d_k_norm", "w_out", "ffn2_norm", "ffn2_gate", "ffn2_up", "ffn2_down", "positions_2",
          "norm_mix_pre_2", "norm_mix_post_2", "norm_ffn_pre_2", "norm_ffn_post_2", "ev_w_in_2", "ev_w_out_2",
          "s5_a_re_2", "s5_a_im_2", "s5_log_dt_2", "s5_b_re_2", "s5_b_im_2", "s5_c_re_2", "s5_c_im_2", "s5_d_2",
          "s5_w_glu_2", "od_w_in_2", "od_w_out_2", "rg_conv_w_2", "rg_conv_b_2", "rg_w_r_2", "rg_b_r_2", "rg_w_i_2",
          "rg_b_i_2", "rg_lam_2", "ffn_w_gate_2", "ffn_w_up_2", "ffn_w_down_2"]


def kernel(**inputs):
    import concourse.bacc as bacc
    from concourse.bass_utils import run_bass_kernel_spmd

    nc = bacc.Bacc("TRN2", target_bir_lowering=False, num_devices=1)
    arrays = {"in_" + n: np.ascontiguousarray(inputs[n]) for n in _NAMES}
    consts = shape_constants()
    arrays["in_consts"] = np.ascontiguousarray(np.concatenate(list(consts.values()), axis=1))
    I = {n[3:]: nc.dram_tensor(n, a.shape, mybir.dt.from_np(a.dtype), kind="ExternalInput").ap()
         for n, a in arrays.items()}
    out = nc.dram_tensor("out_x", (1, SEQ, D), F32, kind="ExternalOutput").ap()
    program(nc, I, out)
    r = run_bass_kernel_spmd(nc, [arrays], core_ids=[0])
    return r.results[0]["out_x"]
```

```python
import math
from itertools import count

import numpy as np

import concourse.bass as bass
from concourse import mybir
from contextlib import ExitStack

F32 = mybir.dt.float32
F32R = mybir.dt.float32r
I32 = mybir.dt.int32
ALU = mybir.AluOpType
ACT = mybir.ActivationFunctionType
AX = mybir.AxisListType

P = 128
SEQ = 512
TB = SEQ // P
D = 1024
KD = D // P
FF = 2816
NF = FF // P
DEPTH = 2
NEG = -1e30
SENTINEL = -3e38
EPS = 1e-6
TOPK = min(256, SEQ // 4)
A_HEADS, A_DIM = 4, 64
IDX_HEADS, IDX_DIM = 8, 32
B_HEADS, B_KEY, B_VAL, B_CHUNK, B_RANK = 4, 32, 64, 64, 16
NCH = SEQ // B_CHUNK
TAPS = 31
D_HEADS, D_NOPE, D_ROPE, D_V = 4, 64, 32, 64
D_QK = D_NOPE + D_ROPE
E_HEADS, E_DIM, E_ROPE = 8, 64, 16
SSM_G, SSM_P, SSM_C = 32, 64, 16
NST = SSM_G * SSM_P // P
LRU_TAPS = 4
BIAS_N = 640

_w = dict(aq=256, ak=256, av=256, iq=256, ik=32, iw=8, bq=128, bk=128, bv=256, bg=16, br=256,
          ca=256, cg=256, dcq=256, dckv=128, dkpe=32)
WCOL, _at = {}, 0
for _n, _c in _w.items():
    WCOL[_n] = _at
    _at += _c



def shape_constants():
    f = np.float32
    out = {}
    p = np.arange(P)
    out["ident"] = np.eye(P, dtype=f)
    out["blk64"] = ((p[:, None] // 64) == (p[None] // 64)).astype(f) / f(64)
    out["mean1024"] = np.full((P, P), 1 / 1024, f)
    out["mean256"] = np.full((P, P), 1 / 256, f)
    out["mean128"] = np.full((P, P), 1 / 128, f)
    m96 = np.zeros((P, D_QK), f)
    m96[:D_QK] = f(1) / f(D_QK)
    out["mean96"] = m96
    half = D_ROPE // 2
    r96 = np.zeros((P, D_QK), f)
    for i in range(half):
        r96[D_NOPE + half + i, D_NOPE + i] = -1
        r96[D_NOPE + i, D_NOPE + half + i] = 1
    out["rot96"] = r96
    eh = E_ROPE // 2
    r128 = np.zeros((P, P), f)
    for b in range(0, P, E_DIM):
        for i in range(eh):
            r128[b + eh + i, b + i] = -1
            r128[b + i, b + eh + i] = 1
    out["rot128"] = r128
    out["causal"] = np.where(p[None] > p[:, None], f(NEG), f(0)).astype(f)
    out["tri"] = (p[:, None] % B_CHUNK <= np.arange(B_CHUNK)[None]).astype(f)
    out["headblk"] = (p[:, None] // B_KEY == np.arange(B_HEADS * B_VAL)[None] // B_VAL).astype(f)
    dist = p[:, None] - (np.arange(SEQ)[None] - (SEQ - P))
    n = (((dist >= 0) & (dist <= 128)).astype(int) + ((dist >= 0) & (dist % 4 == 0)) + ((dist >= 0) & (dist % 16 == 0)))
    out["lnmult"] = np.where(n > 0, np.log(np.maximum(n, 1)), NEG).astype(f)
    t = np.arange(SEQ, dtype=f)
    fr = (f(10000.0) ** (-np.arange(half, dtype=f) / f(half))).astype(f)
    ang = (t[None] * fr[:, None]).astype(f)
    c96, s96 = np.zeros((P, SEQ), f), np.zeros((P, SEQ), f)
    c96[:D_NOPE] = 1
    for o in (D_NOPE, D_NOPE + half):
        c96[o:o + half], s96[o:o + half] = np.cos(ang), np.sin(ang)
    out["cos96"], out["sin96"] = c96, s96
    cm = np.ones((P, SEQ), f)
    cm[:, ::B_CHUNK] = 0
    out["chunkmask"] = cm
    out["iota"] = np.broadcast_to(t, (P, SEQ)).copy()
    out["headcol"] = (p[:, None] // B_KEY == np.arange(B_HEADS)[None]).astype(f)
    inv = (f(500000.0) ** (-(np.arange(eh, dtype=f) * f(2.0) / f(E_ROPE)))).astype(f)
    out["freq"] = np.where(p % E_DIM < E_ROPE, inv[(p % E_DIM) % eh], 0).astype(f)[:, None]
    out["eps"] = np.full((P, 1), EPS, f)
    out["halfpi"] = np.full((P, 1), math.pi / 2, f)
    hot = np.zeros((P, BIAS_N), f)
    for x in range(BIAS_N):
        d = SEQ - 1 - x
        if d < 0:
            hot[32, x] = 1
        elif d < 16:
            hot[d, x] = 1
        else:
            hot[min(16 + int(f(np.log(f(d) / f(16)) / f(math.log(128 / 16)) * f(16))), 31), x] = 1
    out["half16"] = (p[:, None] // SSM_P == np.arange(2 * SSM_C)[None] // SSM_C).astype(f)
    out["flip"] = np.eye(P, dtype=f)[::-1].copy()
    out["onehot"] = hot
    return out


CONST_COLS, _at = {}, 0
for _n, _v in shape_constants().items():
    CONST_COLS[_n] = (_at, _v.shape[1])
    _at += _v.shape[1]
CONST_W = _at
PRO_W = BIAS_N + P

ROWS1 = [("ffn1_norm", 2 * KD), ("mix_norm", 2 * KD), ("ffn2_norm", 2 * KD),
         ("norm_mix_pre_2", 2 * KD), ("norm_mix_post_2", 2 * KD), ("norm_ffn_pre_2", 2 * KD),
         ("norm_ffn_post_2", 2 * KD)]
LAYER_ROWS = [("a_q_norm", 1), ("a_k_norm", 1), ("b_gate_bias", 1), ("b_out_norm", 1), ("c_dw_b", 2), ("c_norm", 2),
              ("d_qa_norm", 2), ("d_kva_norm", 1), ("d_q_norm", 1), ("d_k_norm", 1)]
ROWS2 = [("s5_d_2", 4), ("rg_conv_b_2", 8), ("rg_b_r_2", 8), ("rg_b_i_2", 8), ("rg_lam_2", 8),
         ("rg_conv_w_2", 8 * LRU_TAPS)]


def row_starts(rows):
    out, at = {}, 0
    for n, c in rows:
        out[n] = at
        at += c
    return out, at


R1, NR1 = row_starts(ROWS1)
RL, NRL = row_starts(LAYER_ROWS)
R2, NR2 = row_starts([("layers", DEPTH * NRL)] + ROWS2)
NR3 = DEPTH * TAPS * 2

Z_BLOCKS = [
    [("iq0", 0, "feat"), ("iq1", 128, "feat")],
    [("ik", 0, "feat"), ("iw", 128, "iw"), ("bg", 136, "bg")],
    [("aq0", 0, "feat"), ("aq1", 128, "feat")],
    [("ak0", 0, "feat"), ("ak1", 128, "feat")],
    [("br0", 0, "feat"), ("br1", 128, "feat")],
    [("cg0", 0, "feat"), ("cg1", 128, "feat")],
    [("ca0", 0, "feat"), ("ca1", 128, "feat")],
    [("dcq0", 0, "feat"), ("dcq1", 128, "feat")],
    [("dckv", 0, "feat"), ("dkpe", 128, "kpe")],
    [("bq", 0, "feat"), ("bk", 128, "feat")],
    [("bv01", 0, "tok"), ("bv23", 1, "tok")],
    [("av01", 0, "tok"), ("av23", 1, "tok")],
]
Z_SRC = [("iq", 256), None, ("aq", 256), ("ak", 256), ("br", 256), ("cg", 256), ("ca", 256), ("dcq", 256),
         ("dckv", 160), ("bq", 256), ("bv", 256), ("av", 256)]
IDX_UNITS = [(tb, h) for tb in (3, 2, 1) for h in range(IDX_HEADS)]
Z_SEQ = []
_left = list(IDX_UNITS)
for _b, _chunks in enumerate(Z_BLOCKS):
    for _c, (_label, _col, _kind) in enumerate(_chunks):
        Z_SEQ.append(("z", _b, _c, _label, _col, _kind, _c == len(_chunks) - 1))
        if _b >= 2:
            for _ in range(2):
                if _left:
                    Z_SEQ.append(("idx",) + _left.pop(0))
assert not _left
Z_POS = {t[3]: n for n, t in enumerate(Z_SEQ) if t[0] == "z"}
NZ = len(Z_SEQ)
NIDX = len(IDX_UNITS)

E_BLOCKS = [("u", 1536), ("u", 1792), ("q", 0), ("q", 256), ("k", 512), ("k", 768), ("v", 1024), ("v", 1280)]
E_SEQ = []
_bu = _yy = 0
for _b, (_n, _c) in enumerate(E_BLOCKS):
    for _c in range(2):
        E_SEQ.append(("z", _b, _c, _n, 2 * (_b % 2) + _c))
        if len(E_SEQ) == 6:
            E_SEQ.append(("prep",))
        if _b >= 3:
            if _bu < NST:
                E_SEQ.append(("bu", _bu))
                _bu += 1
            if _bu >= 4:
                E_SEQ.append(("yy", _yy))
                _yy += 1
while _yy < NST:
    if _bu < NST:
        E_SEQ.append(("bu", _bu))
        _bu += 1
    E_SEQ.append(("yy", _yy))
    _yy += 1
E_Z = [t for t in E_SEQ if t[0] == "z"]
MAGIC = float(1.5 * 2 ** 23)

U_Z = [6 if s is None else 1 for s in Z_SRC]
U_OUT = [1] * 4
U_LAYER = U_Z + U_OUT
U_EVEN = [1] * len(E_BLOCKS) + [1] * 2 + U_OUT
U_ODD = [1] * 8 + [1] * 2 + U_OUT
USE_EVEN = DEPTH * len(U_LAYER)
USE_ODD = USE_EVEN + len(U_EVEN)
USE_END = USE_ODD + len(U_ODD)
DMA_EVEN = [DEPTH * sum(U_LAYER[_s::2]) for _s in range(2)]
DMA_ODD = [DMA_EVEN[_s] + sum(U_EVEN[_s::2]) for _s in range(2)]
UNITS = 3 * NF
SLOTS = 4
assert NF % 2 == 0 and (2 * NF) % SLOTS == 0 and KD == 8


def unit_loads(f, slot, turn):
    return 16 * (f * len(range(slot, UNITS, SLOTS)) + turn + 1)


X1 = (1 + 3 * DEPTH) * KD

IDX_POS = [n for n, t in enumerate(Z_SEQ) if t[0] == "idx"]
N_ROW_DMAS = len(ROWS1) + DEPTH * (len(LAYER_ROWS) + 3) + len(ROWS2) + 1 + 2


class Sem:

    def __init__(self, h, per, start):
        self.h, self.per, self.start = h, per, start

    def by(self, layer, k):
        return self.start + layer * self.per + k


class Eng:

    def __init__(self, e):
        self.e, self.l = e, 0


def program(nc, I, out):
    ctx = ExitStack()
    with ctx:
        at = {}

        def sb(name, shape, dt=F32):
            at[name] = -(-nc.sbuf_base // 32) * 32
            return ctx.enter_context(nc.sbuf_tensor(name, shape, dt))

        def over(name, shape, base, skip=0):
            return nc.alloc_sbuf_tensor_at(name, shape, F32R, offset=at[base] + skip)

        def sem(name, per=0, start=0):
            return Sem(ctx.enter_context(nc.semaphore(name)), per, start)

        x = sb("x", [P, KD, SEQ])
        xn = sb("xn", [P, KD, SEQ])
        y = xn
        wring = sb("wring", [P, 2, KD, 256])
        scratch = sb("scratch", [P, 11, SEQ])
        cst = sb("cst", [P, CONST_W - PRO_W])
        bias = sb("bias", [P, A_HEADS, SEQ])
        rows = sb("rows", [P, 4, P])
        col1 = sb("col1", [P, NR1])
        col2 = sb("col2", [P, NR2])
        col3 = sb("col3", [P, NR3])
        cur = sb("cur", [P, NRL])
        cur_dw = sb("cur_dw", [P, TAPS * 2])
        relb = sb("relb", [64, A_HEADS])
        hpad = sb("hpad", [P, 2, TAPS - 1 + SEQ])
        att_diag = sb("att_diag", [P, TB, B_HEADS, P])
        sb("xn_more", [P, 2, SEQ])
        small = sb("small", [P, 64])
        arena = sb("arena", [P, 46, SEQ])
        w_uq = arena[:, 43:45, 0:384]
        w_ukv = arena[:, 45, :]
        wunit = wring[:, :, :, :].rearrange("p s k c -> p (s k c)").rearrange("p (u c) -> p u c", u=SLOTS)
        w_lo = over("w_lo", [P, SLOTS, KD, P], "wring")
        w_hi = over("w_hi", [P, SLOTS, KD, P], "scratch")
        xn_lo = over("xn_lo", [P, KD, SEQ], "xn")
        xn_hi = over("xn_hi", [P, KD, SEQ], "hpad")
        h_hi = over("h_hi", [P, NF, SEQ], "arena")
        h_lo = over("h_lo", [P, NF, SEQ], "arena", NF * SEQ * 4)
        H_LO = NF
        gup = sb("gup", [B_RANK, P])
        pb = [ctx.enter_context(nc.psum_tensor(f"bank{i}", [P, SEQ], F32)) for i in range(8)]
        bias_dram = nc.dram_tensor("bias_by_distance", [A_HEADS, BIAS_N], F32, kind="Internal")

        def C(name):
            a, w = CONST_COLS[name]
            if a >= CONST_W - PRO_W:
                a -= CONST_W - PRO_W
                return arena[:, 12:14, :].rearrange("p t c -> p (t c)")[:, a:a + w]
            return cst[:, a:a + w]

        def T(n):
            return arena[:, n, :]

        def W(n):
            return scratch[:, n, :]

        ident = C("ident")
        SQ, RT = 22, 30
        sg = arena[:, 44:46, :]
        t_iq, t_ik, t_aq, t_ak, t_av = [0, 1], 2, [3, 4], [5, 6], 7
        t_bq, t_bk, t_bv, t_br, t_ca, t_cg = 9, 10, 11, [13, 14], [15, 16], [17, 18]
        t_dcq, t_dckv, t_kpe, t_dv, t_dq, t_dk = [19, 20], 21, 22, 23, [25, 26, 27, 28], [29, 30, 31, 32]
        t_gl = 38
        t_zsq = [25, 26, 27, 28, 29, 30, 31]
        t_zr = [32, 36, 37, 39, 40, 41]
        t_hc, t_csq, t_cr = [15, 16], [17, 18], 19
        t_hraw, t_hsq, t_hr, t_hn = [0, 1], [2, 36], [37, 39], [40, 41]
        t_ab, t_qe, t_kdt, t_um = 42, 38, 42, 9
        t_o, t_osq, t_or = [10, 20], [17, 18], [2, 36]
        t_bm = [0, 1, 40]
        t_score = 33
        sc_at = {3: 0, 2: 512, 1: 896}
        scores = arena[:, 33:36, :].rearrange("p t c -> p (t c)")

        w_mn, w_la, w_e1, w_e1n, w_e2 = 9, 10, 4, 5, 6
        idx_r = [0, 1, 2, 3]
        kdm = [W(7), W(8), W(9), W(10)]

        def Sst(c):
            return scratch[:, (c - 1) // 2, ((c - 1) % 2) * 256:((c - 1) % 2) * 256 + 256]

        def p_buf(u):
            return W(4 + u % 3)

        def pt_buf(u):
            return W(7 + u % 2)

        def score(tb):
            return scores[:, sc_at[tb]:sc_at[tb] + (tb + 1) * P]

        wA = small[:, 0:32]
        m8 = small[:, 32:40]
        nmax, psum_, rsum = small[:, 40:44], small[:, 44:48], small[:, 48:52]
        glast = small[:, 52:60]

        e_q, e_k, e_v, e_u, e_cos, e_sin = 0, 4, 8, 12, 16, 17
        e_tmp = [18, 19, 20, 21]
        e_bst, e_cst, e_btr, e_bti, e_ere, e_eim = 38, 39, 41, 42, 43, 44
        e_cre, e_crn, e_cin = 45, 38, 20
        e_pos = 45
        s5_n, s5_d, s5_d2 = [T(22), T(23)], [T(24), T(25)], [T(26), T(27)]
        s5_sin, s5_cos = [T(28), T(29), T(30)], [T(31), T(32), T(33)]
        s5_a = [[T(34), T(35), T(36), T(37)], [W(0), W(1), W(2), W(3)], [W(9), W(10), T(18), T(19)]]
        s5col = sb("s5col", [P, 20, NST])
        (c_are, c_aim, c_ldt, c_dt, c_ard, c_th, c_r, c_fr, c_n, c_sin, c_cos, c_nre, c_nim, c_den, c_fre, c_fim,
         c_t1, c_t2, c_f2) = [s5col[:, i, :] for i in range(19)]
        ldt = sb("ldt", [64, 2])
        spc = sb("spc", [P, 8, KD])
        PAR_E, SP_STEPS, e_glu = 31, 19, 28
        RB, RT2 = 30, 38
        xpad = arena[:, 0:9, :].rearrange("p t c -> p (t c)")[:, 0:KD * (LRU_TAPS - 1 + SEQ)].rearrange(
            "p (k c) -> p k c", k=KD)
        o_xc, o_r, o_i, o_gel = 9, 17, 25, 33

        consts_in = sem("consts_in")
        rows_in = sem("rows_in")
        rows_zero = sem("rows_zero")
        token_dma = sem("token_dma")
        pro_ps = sem("pro_ps")
        pro_sb = sem("pro_sb")
        relb_in = sem("relb_in")
        relb_neg = sem("relb_neg")
        bias_dma = sem("bias_dma")
        zeros_set = sem("zeros_set", 1)
        x_ready = sem("x_ready", 24)
        sq_done = sem("sq_done", 24)
        norm_ps = sem("norm_ps", 3)
        norm_ln = sem("norm_ln", 3)
        norm_r = sem("norm_r", 3)
        xn_ready = sem("xn_ready", 24)
        w_in_sem = [sem("w_loaded0", 16 * sum(U_LAYER[0::2])), sem("w_loaded1", 16 * sum(U_LAYER[1::2]))]
        w_used = sem("w_used", len(U_LAYER))
        u_in = [sem(f"u_loaded{q}") for q in range(SLOTS)]
        u_hi = sem("u_hi")
        u_lo = sem("u_lo")
        unit_ps = sem("unit_ps")
        xn_hi_ready = sem("xn_hi_ready")
        xn_lo_ready = sem("xn_lo_ready")
        sg_ready = sem("sg_ready", 0, 2)
        h_full = sem("h_full", 0, 2)
        h_hi_ready = sem("h_hi_ready")
        h_lo_ready = sem("h_lo_ready")
        down_ps = sem("down_ps")
        z_ps = sem("z_ps", sum(len(b) - 1 for b in Z_BLOCKS))
        idx_ps = sem("idx_ps", NIDX)
        z_sb = sem("z_sb", NZ)
        zsq = sem("zsq", 7)
        idx_acc = sem("idx_acc", NIDX)
        idx_mask = sem("idx_mask", 3)
        top_max = sem("top_max", 3 * TOPK // 8)
        top_rep = sem("top_rep", 3 * TOPK // 8)
        top_done = sem("top_done", 3)
        cur_ready = sem("cur_ready", 4)
        smallw_in = sem("smallw_in", 16 * 3)
        hp_ready = sem("hp_ready", 2)
        conv = sem("conv", TAPS * 2)
        conv_sq = sem("conv_sq", 2)
        mn_ps = sem("mn_ps", 7)
        mn_ln = sem("mn_ln", 7)
        mn_r = sem("mn_r", 7)
        mn_x = sem("mn_x", 9)
        y_conv = sem("y_conv", 2)
        gate_log_ps = sem("gate_log_ps", 1)
        g_abs = sem("g_abs", 4)
        g_min = sem("g_min", 1)
        g_b = sem("g_b", 6)
        g_exp = sem("g_exp", 5)
        b_qk = sem("b_qk", 3)
        b_kd = sem("b_kd", 1 + B_HEADS)
        kt_ps = sem("kt_ps", 1)
        kt_sb = sem("kt_sb", 1)
        u_ps = sem("u_ps", NCH - 1)
        u_msk = sem("u_msk", NCH - 1)
        s_ready = sem("s_ready", NCH - 1)
        at_ps = sem("at_ps", TB)
        at_sb = sem("at_sb", 2 * TB)
        o_ps = sem("o_ps", 2)
        o_sq = sem("o_sq", 2)
        on_ps = sem("on_ps", 2)
        on_ln = sem("on_ln", 2)
        on_r = sem("on_r", 2)
        o_n = sem("o_n", 2)
        y_b = sem("y_b", 2)
        dv_ps = sem("dv_ps", 2)
        dv_sb = sem("dv_sb", 2)
        dh_ps = sem("dh_ps", 8)
        dh_sq = sem("dh_sq", 8)
        dn_ps = sem("dn_ps", 8)
        dn_ln = sem("dn_ln", 8)
        dn_r = sem("dn_r", 8)
        dn_x = sem("dn_x", 8)
        dr_ps = sem("dr_ps", 8)
        dr_s = sem("dr_s", 8)
        dr_c = sem("dr_c", 8)
        dh_ready = sem("dh_ready", 8)
        att_bm = sem("att_bm", 12)
        att_s = sem("att_s", 32)
        att_max = sem("att_max", 32)
        att_exp = sem("att_exp", 32)
        att_rs = sem("att_rs", 32)
        att_p = sem("att_p", 32)
        att_t = sem("att_t", 32)
        att_pt = sem("att_pt", 32)
        att_o = sem("att_o", 32)
        y_att = sem("y_att", 4)
        out_ps = sem("out_ps", 4)
        s5_in = sem("s5_in")
        ldt_in = sem("ldt_in")
        ldt_row = sem("ldt_row")
        tab = sem("tab")
        tab_sin = sem("tab_sin")
        par = sem("par")
        par_act = sem("par_act")
        bc_ps = sem("bc_ps")
        bt_sb = sem("bt_sb")
        cb_sb = sem("cb_sb")
        ez_ps = sem("ez_ps")
        ez_sb = sem("ez_sb")
        s5_rnd = sem("s5_rnd")
        s5_frac = sem("s5_frac")
        s5_wrap = sem("s5_wrap")
        s5_quart = sem("s5_quart")
        s5_trig = sem("s5_trig")
        bu_ps = sem("bu_ps")
        s5_rot = sem("s5_rot")
        s5_x = sem("s5_x")
        s5_g = sem("s5_g")
        s5_p = sem("s5_p")
        s5_q = sem("s5_q")
        yy_ps = sem("yy_ps")
        s5_y = sem("s5_y")
        s5_gelu = sem("s5_gelu")
        rot_ps = sem("rot_ps")
        rot_s = sem("rot_s")
        rot_c = sem("rot_c")
        rot_ready = sem("rot_ready")
        glu_ps = sem("glu_ps")
        glu_sb = sem("glu_sb")
        y_ssm = sem("y_ssm")
        eo_ps = sem("eo_ps")
        r_ready = sem("r_ready")
        rsq = sem("rsq")
        rn_ps = sem("rn_ps")
        rn_ln = sem("rn_ln")
        rn_r = sem("rn_r")
        r_n = sem("r_n")
        pad_zero = sem("pad_zero")
        oz_ps = sem("oz_ps")
        oz_sb = sem("oz_sb")
        cv = sem("cv")
        og_ps = sem("og_ps")
        og_sb = sem("og_sb")
        sp_step = sem("sp_step")
        o_th = sem("o_th")
        o_a = sem("o_a")
        o_a2 = sem("o_a2")
        o_q = sem("o_q")
        o_sqrt = sem("o_sqrt")
        o_gx = sem("o_gx")
        o_b = sem("o_b")
        o_h = sem("o_h")
        y_lru = sem("y_lru")
        fin_ps = sem("fin_ps")
        fin_sb = sem("fin_sb")

        D_UNITS = [("D", h, tb) for h in range(D_HEADS) for tb in range(TB)]
        A_UNITS = [("A", h, tb) for h in range(A_HEADS) for tb in range(TB)]
        HYB_UNITS = D_UNITS + A_UNITS
        BM = [u for u, (m, h, tb) in enumerate(HYB_UNITS) if m == "A" and tb > 0]

        block = ctx.enter_context(nc.Block())

        def sp_ffn(sp, f, used, gate, up, down):
            gu = [w.rearrange("(k p) n -> p k n", p=P) for w in (gate, up)]
            d = down.rearrange("(j p) n -> p j n", p=P)
            u0 = f * UNITS
            for q in range(SLOTS):
                if used is None:
                    if f:
                        sp.e.wait_ge(unit_ps.h, u0)
                else:
                    sp.e.wait_ge(w_used.h, used - 1 + q // 2)
                sp.e.dma_start(wunit[:, q, :].rearrange("p (k c) -> p k c", k=KD),
                               gu[q % 2][:, :, (q // 2) * P:(q // 2 + 1) * P]).then_inc(u_in[q].h, 16)
            with sp.e.Fori(0, NF // 2 - 1) as i:
                for q in range(SLOTS):
                    sp.e.wait_ge(unit_ps.h, u0 + SLOTS * i + (q + 1))
                    sp.e.dma_start(wunit[:, q, :].rearrange("p (k c) -> p k c", k=KD),
                                   gu[q % 2][:, :, bass.ds(i * 2 * P + (2 + q // 2) * P, P)]).then_inc(u_in[q].h, 16)
            u0 += 2 * NF - SLOTS
            with sp.e.Fori(0, NF // SLOTS) as i:
                for q in range(SLOTS):
                    sp.e.wait_ge(unit_ps.h, u0 + SLOTS * i + (q + 1))
                    sp.e.dma_start(wunit[:, q, :].unsqueeze(1), d[:, bass.ds(SLOTS * i + q, 1), :]).then_inc(u_in[q].h, 16)
            for k in range(NF // SLOTS * SLOTS, NF):
                sp.e.wait_ge(unit_ps.h, u0 + k + 1)
                sp.e.dma_start(wunit[:, k % SLOTS, :], d[:, k, :]).then_inc(u_in[k % SLOTS].h, 16)

        @block.sync
        def _(e):
            sp = Eng(e)
            e.dma_start(cst[:, :], I["consts"][:, 0:CONST_W - PRO_W]).then_inc(consts_in.h, 16)
            e.dma_start(arena[:, 12:14, :].rearrange("p t c -> p (t c)")[:, 0:PRO_W],
                        I["consts"][:, CONST_W - PRO_W:]).then_inc(relb_in.h, 16)
            e.dma_start(relb[0:32, :], I["rel_bias"]).then_inc(relb_in.h, 16)
            for tb in range(TB):
                e.dma_start(arena[:, 2 * tb:2 * tb + 2, :],
                            I["x"][0, tb * P:(tb + 1) * P, :].rearrange("p (a c) -> p a c", a=2)).then_inc(token_dma.h, 16)
            for l in range(DEPTH):
                sp.l = l
                sp_ffn(sp, l * 2, None, I["ffn1_gate"][l], I["ffn1_up"][l], I["ffn1_down"][l])
                sp.e.wait_ge(unit_ps.h, (l * 2 + 1) * UNITS)
                e.dma_start(w_uq, I["d_uq"][l].rearrange("(k p) n -> p k n", p=P)).then_inc(smallw_in.h, 16)
                e.dma_start(w_ukv, I["d_ukv"][l]).then_inc(smallw_in.h, 16)
                e.dma_start(gup[:, :], I["b_gate_up"][l]).then_inc(smallw_in.h, 16)
                win = I["w_in"][l].rearrange("(k p) n -> p k n", p=P)
                wout = I["w_out"][l].rearrange("(k p) n -> p k n", p=P)
                for b, src in enumerate(Z_SRC):
                    s = b % 2
                    if b >= 2:
                        sp.e.wait_ge(w_used.h, w_used.by(sp.l, b - 1))
                    if src:
                        a, n = WCOL[src[0]], src[1]
                        e.dma_start(wring[:, s, :, 0:n], win[:, :, a:a + n]).then_inc(w_in_sem[s].h, 16)
                    else:
                        for r in range(4):
                            e.dma_start(wring[:, s, :, r * IDX_DIM:(r + 1) * IDX_DIM],
                                        win[:, :, WCOL["ik"]:WCOL["ik"] + IDX_DIM]).then_inc(w_in_sem[s].h, 16)
                        e.dma_start(wring[:, s, :, 128:136],
                                    win[:, :, WCOL["iw"]:WCOL["iw"] + IDX_HEADS]).then_inc(w_in_sem[s].h, 16)
                        e.dma_start(wring[:, s, :, 136:152],
                                    win[:, :, WCOL["bg"]:WCOL["bg"] + B_RANK]).then_inc(w_in_sem[s].h, 16)
                for b in range(4):
                    sp.e.wait_ge(w_used.h, w_used.by(sp.l, len(U_Z) + b - 1))
                    e.dma_start(wring[:, b % 2, :, :], wout[:, :, b * 256:(b + 1) * 256]).then_inc(w_in_sem[b % 2].h, 16)
                sp_ffn(sp, l * 2 + 1, (l + 1) * len(U_LAYER), I["ffn2_gate"][l], I["ffn2_up"][l],
                       I["ffn2_down"][l])
            sp.l = DEPTH
            sp.e.wait_ge(unit_ps.h, 2 * DEPTH * UNITS)
            for q, n in enumerate(("s5_b_re_2", "s5_b_im_2")):
                e.dma_start(T(e_bst)[:, q * 256:(q + 1) * 256].rearrange("p (j c) -> p j c", c=SSM_C),
                            I[n][0].rearrange("(j q) p c -> (q p) j c", q=2)).then_inc(s5_in.h, 16)
            for q, n in enumerate(("s5_c_re_2", "s5_c_im_2")):
                cd = T(e_cst + q).rearrange("p (t d s) -> p t d s", t=4, d=2)
                src = I[n][0].rearrange("(t g) c s -> (g c) t s", t=4)
                for d in range(2):
                    e.dma_start(cd[:, :, d, :], src).then_inc(s5_in.h, 16)
            e.dma_start(T(e_pos).bitcast(I32), bass.AP(I["positions_2"].tensor, 0, [[0, P], [1, SEQ]])).then_inc(s5_in.h, 16)
            win = I["ev_w_in_2"][0].rearrange("(k p) n -> p k n", p=P)
            use = [0]

            def load(dst, src):
                n = USE_EVEN + use[0]
                if n not in (USE_EVEN, USE_EVEN + 1, USE_ODD, USE_ODD + 1):
                    sp.e.wait_ge(w_used.h, n - 1)
                e.dma_start(dst(wring[:, n % 2]), src).then_inc(w_in_sem[n % 2].h, 16)
                use[0] += 1
            for n, a in E_BLOCKS:
                load(lambda w: w, win[:, :, a:a + 256])
            for b in range(2):
                load(lambda w: w[:, 0:4, :], I["s5_w_glu_2"][0].rearrange("(k p) n -> p k n", p=P)[:, :, b * 256:(b + 1) * 256])
            for b in range(4):
                load(lambda w: w, I["ev_w_out_2"][0].rearrange("(k p) n -> p k n", p=P)[:, :, b * 256:(b + 1) * 256])
            sp_ffn(sp, 2 * DEPTH, USE_ODD, I["ffn_w_gate_2"][0], I["ffn_w_up_2"][0], I["ffn_w_down_2"][0])
            sp.e.wait_ge(unit_ps.h, (2 * DEPTH + 1) * UNITS)
            win = I["od_w_in_2"][0].rearrange("(k p) n -> p k n", p=P)
            for b in range(8):
                load(lambda w: w, win[:, :, b * 256:(b + 1) * 256])
            for n in ("rg_w_r_2", "rg_w_i_2"):
                load(lambda w: w, I[n][0].rearrange("b (k p) n -> p (b k) n", p=P))
            for b in range(4):
                load(lambda w: w, I["od_w_out_2"][0].rearrange("(k p) n -> p k n", p=P)[:, :, b * 256:(b + 1) * 256])
            sp_ffn(sp, 2 * DEPTH + 1, USE_END, I["ffn_w_gate_2"][1], I["ffn_w_up_2"][1], I["ffn_w_down_2"][1])
            for tb in range(TB):
                sp.e.wait_ge(fin_sb.h, 2 * tb + 2)
                e.dma_start(out[0, tb * P:(tb + 1) * P, :].rearrange("p (a c) -> p a c", a=2),
                            arena[:, 2 * tb:2 * tb + 2, :]).then_inc(token_dma.h, 16)
            sp.e.wait_ge(token_dma.h, 2 * 16 * TB)

        def pe_norm(pe, n):
            for k in range(KD):
                pe.e.wait_ge(sq_done.h, n * KD + (k + 1))
                mm = nc.tensor.matmul(pb[6][:, :], C("mean1024"), T(SQ + k), start=(k == 0), stop=(k == KD - 1))
            mm.then_inc(norm_ps.h, 1)

        def split_product(ps, slot, t, hi, lo, start, stop):
            nc.tensor.matmul(ps, w_hi[:, slot, t, :], hi, start=start, stop=False)
            nc.tensor.matmul(ps, w_lo[:, slot, t, :], hi, start=False, stop=False)
            return nc.tensor.matmul(ps, w_hi[:, slot, t, :], lo, start=False, stop=stop)

        def down_bank(m):
            return pb[(m + 6) % 8][:, :]

        def pe_ffn(pe, f):
            u0 = f * UNITS
            with pe.e.Fori(0, NF // 2) as i:
                for c in range(2):
                    n = f * NF + 2 * i + c
                    pe.e.wait_ge(u_lo.h, u0 + SLOTS * i + (2 * c + 1))
                    pe.e.wait_ge(sg_ready.h, sg_ready.start + n - 1)
                    for k in range(KD):
                        if c == 0:
                            pe.e.wait_ge(xn_lo_ready.h, f * KD + k + 1)
                        mm = split_product(pb[c][:, :], 2 * c, k, xn_hi[:, k, :], xn_lo[:, k, :], k == 0, k == KD - 1)
                    mm.then_inc(unit_ps.h, 1)
                    pe.e.wait_ge(u_lo.h, u0 + SLOTS * i + (2 * c + 2))
                    pe.e.wait_ge(h_full.h, h_full.start + n - 1)
                    for k in range(KD):
                        mm = split_product(pb[2 + c][:, :], 2 * c + 1, k, xn_hi[:, k, :], xn_lo[:, k, :], k == 0, k == KD - 1)
                    mm.then_inc(unit_ps.h, 1)
            u0 += 2 * NF

            def down_unit(slot, hi, lo, stop):
                for m in range(KD):
                    mm = split_product(down_bank(m), slot, m, hi, lo, False, stop)
                    if stop and m < KD - 1:
                        mm.then_inc(down_ps.h, 1)
                mm.then_inc(unit_ps.h, 1)
            pe.e.wait_ge(u_lo.h, u0 + 1)
            pe.e.wait_ge(h_lo_ready.h, f * NF + 1)
            for m in (0, 1, 6, 7, 2, 4, 3, 5):
                if m in (2, 3):
                    pe.e.wait_ge(sg_ready.h, sg_ready.start + (f + 1) * NF + (m - 3))
                if m in (4, 5):
                    pe.e.wait_ge(h_full.h, h_full.start + (f + 1) * NF + (m - 5))
                mm = split_product(down_bank(m), 0, m, h_hi[:, 0, :], h_lo[:, 0, :], True, False)
            mm.then_inc(unit_ps.h, 1)
            for k in range(1, SLOTS):
                pe.e.wait_ge(u_lo.h, u0 + k + 1)
                pe.e.wait_ge(h_lo_ready.h, f * NF + k + 1)
                down_unit(k, h_hi[:, k, :], h_lo[:, k, :], False)
            with pe.e.Fori(0, NF // SLOTS - 1) as i:
                for q in range(SLOTS):
                    pe.e.wait_ge(u_lo.h, u0 + SLOTS * i + (SLOTS + q + 1))
                    pe.e.wait_ge(h_lo_ready.h, f * NF + SLOTS * i + (SLOTS + q + 1))
                    hi, lo = [t[:, bass.ds(SLOTS * i + (SLOTS + q), 1), :].rearrange("p a c -> p (a c)") for t in (h_hi, h_lo)]
                    down_unit(q, hi, lo, False)
            for k in range(NF // SLOTS * SLOTS, NF):
                pe.e.wait_ge(u_lo.h, u0 + k + 1)
                pe.e.wait_ge(h_lo_ready.h, f * NF + k + 1)
                down_unit(k % SLOTS, h_hi[:, k, :], h_lo[:, k, :], k == NF - 1)

        def pe_z(pe, norms):
            used = [0, 0]
            nz = ni = 0
            for n, t in enumerate(Z_SEQ):
                bank = pb[n % 4]
                if n >= 4:
                    pe.e.wait_ge(z_sb.h, z_sb.by(pe.l, n - 3))
                if t[0] == "idx":
                    _, tb, h = t
                    if ni == 0:
                        pe.e.wait_ge(z_sb.h, z_sb.by(pe.l, Z_POS["ik"] + 1))
                    r = 32 * (h % 4)
                    N = (tb + 1) * P
                    nc.tensor.matmul(bank[:, 0:N], T(t_iq[h // 4])[r:r + 32, tb * P:(tb + 1) * P],
                                     T(t_ik)[r:r + 32, 0:N], start=True, stop=True).then_inc(idx_ps.h, 1)
                    ni += 1
                    continue
                _, b, c, label, col, kind, last = t
                s = b % 2
                if c == 0:
                    used[s] += U_Z[b]
                    pe.e.wait_ge(w_in_sem[s].h, w_in_sem[s].by(pe.l, 16 * used[s]))
                w = wring[:, s, :, :]
                if kind == "feat":
                    for k in range(KD):
                        if n == 0:
                            pe.e.wait_ge(xn_ready.h, norms * KD + k + 1)
                        mm = nc.tensor.matmul(bank[:, :], w[:, k, col:col + P], xn[:, k, :],
                                              start=(k == 0), stop=(k == KD - 1))
                elif kind == "bg":
                    for k in range(KD):
                        mm = nc.tensor.matmul(bank[0:B_RANK, :], w[:, k, col:col + B_RANK], xn[:, k, :],
                                              start=(k == 0), stop=(k == KD - 1))
                elif kind == "kpe":
                    for k in range(KD):
                        mm = nc.tensor.matmul(bank[64:96, :], w[:, k, col:col + D_ROPE], xn[:, k, :],
                                              start=(k == 0), stop=(k == KD - 1))
                elif kind == "iw":
                    for tb in range(TB):
                        for k in range(KD):
                            mm = nc.tensor.matmul(bank[:, 8 * tb:8 * tb + 8], xn[:, k, tb * P:(tb + 1) * P],
                                                  w[:, k, col:col + IDX_HEADS], start=(k == 0), stop=(k == KD - 1))
                else:
                    for q in range(2):
                        tb = 2 * col + q
                        for k in range(KD):
                            mm = nc.tensor.matmul(bank[:, q * 256:(q + 1) * 256], xn[:, k, tb * P:(tb + 1) * P],
                                                  w[:, k, :], start=(k == 0), stop=(k == KD - 1))
                mm.then_inc((w_used if last else z_ps).h, 1)

        def pe_mixers(pe):
            pe.e.wait_ge(z_sb.h, z_sb.by(pe.l, NZ))
            pe.e.wait_ge(smallw_in.h, smallw_in.by(pe.l, 16 * 3))
            nc.tensor.matmul(pb[0][:, :], gup[:, :], T(t_gl)[0:B_RANK, :], start=True, stop=True).then_inc(gate_log_ps.h, 1)
            for i in range(4):
                pe.e.wait_ge(zsq.h, zsq.by(pe.l, i + 1))
                if i >= 3:
                    pe.e.wait_ge(mn_ln.h, mn_ln.by(pe.l, i - 2))
                nc.tensor.matmul(pb[1 + i % 3][:, :], C("blk64"), T(t_zsq[i]), start=True, stop=True).then_inc(mn_ps.h, 1)
            pe.e.wait_ge(zsq.h, zsq.by(pe.l, 6))
            pe.e.wait_ge(mn_ln.h, mn_ln.by(pe.l, 2))
            nc.tensor.matmul(pb[2][:, :], C("mean256"), T(t_zsq[4]), start=True, stop=False)
            nc.tensor.matmul(pb[2][:, :], C("mean256"), T(t_zsq[5]), start=False, stop=True).then_inc(mn_ps.h, 1)
            pe.e.wait_ge(zsq.h, zsq.by(pe.l, 7))
            pe.e.wait_ge(mn_ln.h, mn_ln.by(pe.l, 3))
            nc.tensor.matmul(pb[3][:, :], C("mean128"), T(t_zsq[6]), start=True, stop=True).then_inc(mn_ps.h, 1)
            pe.e.wait_ge(mn_x.h, mn_x.by(pe.l, 7))
            for q in range(2):
                for r in range(2):
                    tb = 2 * q + r
                    mm = nc.tensor.matmul(pb[6 + q][:, r * 256:(r + 1) * 256], T(t_dckv)[:, tb * P:(tb + 1) * P],
                                          w_ukv.rearrange("p (h t) -> p h t", h=D_HEADS)[:, :, D_NOPE:],
                                          start=True, stop=True)
                mm.then_inc(dv_ps.h, 1)
            for i in range(8 + 2):
                if i < 8:
                    raw = pb[i % 2]
                    if i == 1:
                        pe.e.wait_ge(mn_ln.h, mn_ln.by(pe.l, 6))
                    if i >= 2:
                        pe.e.wait_ge(dh_sq.h, dh_sq.by(pe.l, i - 1))
                    h = i % 4
                    if i < 4:
                        for k in range(2):
                            mm = nc.tensor.matmul(raw[0:D_QK, :], w_uq[:, k, h * D_QK:(h + 1) * D_QK], T(t_dcq[k]),
                                                  start=(k == 0), stop=(k == 1))
                    else:
                        nc.tensor.matmul(raw[0:D_NOPE, :], w_ukv[:, h * P:h * P + D_NOPE], T(t_dckv), start=True, stop=True)
                        mm = nc.tensor.matmul(raw[64:96, :], ident[64:96, 64:96], T(t_kpe)[64:96, :], start=True, stop=True)
                    mm.then_inc(dh_ps.h, 1)
                if 1 <= i < 9:
                    u = i - 1
                    pe.e.wait_ge(dh_sq.h, dh_sq.by(pe.l, u + 1))
                    if u >= 1:
                        pe.e.wait_ge(dn_ln.h, dn_ln.by(pe.l, u))
                    nc.tensor.matmul(pb[2][0:D_QK, :], C("mean96")[0:D_QK, :], T(t_hsq[u % 2])[0:D_QK, :],
                                     start=True, stop=True).then_inc(dn_ps.h, 1)
                if i >= 2:
                    u = i - 2
                    pe.e.wait_ge(dn_x.h, dn_x.by(pe.l, u + 1))
                    if u >= 1:
                        pe.e.wait_ge(dr_s.h, dr_s.by(pe.l, u))
                    nc.tensor.matmul(pb[3][0:D_QK, :], C("rot96")[0:D_QK, :], T(t_hn[u % 2])[0:D_QK, :],
                                     start=True, stop=True).then_inc(dr_ps.h, 1)
            pe.e.wait_ge(conv_sq.h, conv_sq.by(pe.l, 2))
            pe.e.wait_ge(dv_sb.h, dv_sb.by(pe.l, 1))
            nc.tensor.matmul(pb[6][:, :], C("mean256"), T(t_csq[0]), start=True, stop=False)
            nc.tensor.matmul(pb[6][:, :], C("mean256"), T(t_csq[1]), start=False, stop=True).then_inc(mn_ps.h, 1)
            pe.e.wait_ge(b_qk.h, b_qk.by(pe.l, 3))
            pe.e.wait_ge(dv_sb.h, dv_sb.by(pe.l, 2))
            for tb in range(TB):
                mm = nc.tensor.transpose(pb[7][:, tb * P:(tb + 1) * P], W(w_e2)[:, tb * P:(tb + 1) * P], ident)
            mm.then_inc(kt_ps.h, 1)
            pe.e.wait_ge(kt_sb.h, kt_sb.by(pe.l, 1))
            pe.e.wait_ge(dn_ln.h, dn_ln.by(pe.l, 8))
            pe.e.wait_ge(dr_s.h, dr_s.by(pe.l, 8))
            bv = arena[:, t_bv:t_bv + 2, :].rearrange("p t c -> p (t c)").rearrange("p (b c) -> p b c", b=TB)
            for c in range(NCH - 1):
                r = 64 * (c % 2)
                if c >= 2:
                    pe.e.wait_ge(u_msk.h, u_msk.by(pe.l, c - 1))
                nc.tensor.matmul(pb[2 + c % 2][:, 0:256], T(t_kdt)[r:r + 64, (c // 2) * P:(c // 2 + 1) * P],
                                 bv[r:r + 64, c // 2, :], start=True, stop=True).then_inc(u_ps.h, 1)
            pe.e.wait_ge(b_kd.h, b_kd.by(pe.l, 1 + B_HEADS))
            for tb in range(TB):
                bank = pb[4 + tb % 2]
                if tb >= 2:
                    pe.e.wait_ge(at_sb.h, at_sb.by(pe.l, 2 * (tb - 1)))
                for h in range(B_HEADS):
                    mm = nc.tensor.matmul(bank[:, h * P:(h + 1) * P], kdm[h][:, tb * P:(tb + 1) * P],
                                          W(w_e1)[:, tb * P:(tb + 1) * P], start=True, stop=True)
                mm.then_inc(at_ps.h, 1)
            pe.e.wait_ge(at_sb.h, at_sb.by(pe.l, 2 * TB))
            pe.e.wait_ge(s_ready.h, s_ready.by(pe.l, NCH - 1))
            pe.e.wait_ge(dh_sq.h, dh_sq.by(pe.l, 8))
            for pr in range(2):
                o = pb[pr]
                for c in range(NCH):
                    cols = slice(c * B_CHUNK, (c + 1) * B_CHUNK)
                    half = slice(c % 2 * B_CHUNK, (c % 2 + 1) * B_CHUNK)
                    for q in range(2):
                        h = 2 * pr + q
                        mm = nc.tensor.matmul(o[64 * q:64 * q + 64, cols], bv[:, c // 2, h * B_VAL:(h + 1) * B_VAL],
                                              att_diag[:, c // 2, h, half], start=True, stop=(c == 0),
                                              skip_group_check=True)
                    if c:
                        mm = nc.tensor.matmul(o[:, cols], Sst(c)[:, pr * P:(pr + 1) * P], T(t_qe)[:, cols],
                                              start=False, stop=True, skip_group_check=True)
                mm.then_inc(o_ps.h, 1)
            for pr in range(2):
                pe.e.wait_ge(o_sq.h, o_sq.by(pe.l, pr + 1))
                pe.e.wait_ge(u_msk.h, u_msk.by(pe.l, NCH - 1))
                nc.tensor.matmul(pb[2 + pr][:, :], C("blk64"), T(t_osq[pr]), start=True, stop=True).then_inc(on_ps.h, 1)

        def pe_attention(pe, units, ops):
            U = len(units)
            for i in range(U + 3):
                if i < U:
                    ops["ready"](pe, i)
                    m, h, tb = units[i]
                    if i >= 4:
                        pe.e.wait_ge(att_exp.h, att_exp.by(pe.l, i - 3))
                    s = pb[(0, 1, 4, 5)[i % 4]]
                    N = (tb + 1) * P
                    q, k = ops["qk"](m, h)
                    msk, lo = ops["mask"](m, h, tb, i)
                    if lo:
                        nc.tensor.matmul(s[:, 0:lo], q[:, tb * P:N], k[:, 0:lo], start=True, stop=True)
                    nc.tensor.matmul(s[:, lo:N], q[:, tb * P:N], k[:, lo:N], start=True, stop=False)
                    nc.tensor.matmul(s[:, lo:N], ident, msk, start=False, stop=True).then_inc(att_s.h, 1)
                if 2 <= i < U + 2:
                    u = i - 2
                    pe.e.wait_ge(att_p.h, att_p.by(pe.l, u + 1))
                    if u >= 2:
                        pe.e.wait_ge(att_pt.h, att_pt.by(pe.l, u - 1))
                    for b in range(units[u][2] + 1):
                        mm = nc.tensor.transpose(pb[2 + u % 2][:, b * P:(b + 1) * P],
                                                 p_buf(u)[:, b * P:(b + 1) * P], ident)
                    mm.then_inc(att_t.h, 1)
                if i >= 3:
                    u = i - 3
                    m, h, tb = units[u]
                    pe.e.wait_ge(att_pt.h, att_pt.by(pe.l, u + 1))
                    if u % 8 == 0 and u >= 16:
                        pe.e.wait_ge(y_att.h, y_att.by(pe.l, u // 8 - 1))
                    o = pb[6 + (u // 8) % 2][64 * (h % 2):64 * (h % 2) + 64, tb * P:(tb + 1) * P]
                    for b in range(tb + 1):
                        mm = nc.tensor.matmul(o, ops["v"](m, h, b), pt_buf(u)[:, b * P:(b + 1) * P],
                                              start=(b == 0), stop=(b == tb))
                    mm.then_inc(att_o.h, 1)

        def hyb_qk(m, h):
            if m == "D":
                return T(t_dq[h])[0:D_QK, :], T(t_dk[h])[0:D_QK, :]
            r = 64 * (h % 2)
            return T(t_aq[h // 2])[r:r + 64, :], T(t_ak[h // 2])[r:r + 64, :]

        def hyb_mask(m, h, tb, u):
            if m == "D":
                return C("causal"), tb * P
            if tb == 0:
                return bias[:, h, SEQ - P:SEQ], 0
            return T(t_bm[BM.index(u) % 3])[:, 0:(tb + 1) * P], 0

        def hyb_v(m, h, b):
            t = t_dv if m == "D" else t_av
            v = arena[:, t:t + 2, :].rearrange("p t c -> p (t c)").rearrange("p (b c) -> p b c", b=TB)
            return v[:, b, h * 64:(h + 1) * 64]

        def hyb_ready(eng, u):
            if u == 0:
                eng.e.wait_ge(on_ln.h, on_ln.by(eng.l, 2))
                eng.e.wait_ge(y_conv.h, y_conv.by(eng.l, 2))
                eng.e.wait_ge(kt_sb.h, kt_sb.by(eng.l, 1))
                eng.e.wait_ge(at_sb.h, at_sb.by(eng.l, 2 * TB))
            m, h, tb = HYB_UNITS[u]
            if m == "D" and tb == 0:
                eng.e.wait_ge(dh_ready.h, dh_ready.by(eng.l, 5 + h))
            if m == "A" and h == 0 and tb == 0:
                eng.e.wait_ge(mn_x.h, mn_x.by(eng.l, 4))
                eng.e.wait_ge(pro_sb.h, 4 + 2 + A_HEADS)
            if u in BM:
                eng.e.wait_ge(att_bm.h, att_bm.by(eng.l, BM.index(u) + 1))

        HYB = dict(qk=hyb_qk, mask=hyb_mask, v=hyb_v, ready=hyb_ready)

        def pe_out(pe, used, ready):
            ready(pe)
            for b in range(4):
                s = b % 2
                pe.e.wait_ge(w_in_sem[s].h, w_in_sem[s].by(pe.l, 16 * (used[s] + b // 2 + 1)))
                for c in range(2):
                    dc = 2 * b + c
                    if dc >= 2:
                        pe.e.wait_ge(x_ready.h, x_ready.by(pe.l, 16 + dc - 1))
                    for k in range(KD):
                        mm = nc.tensor.matmul(pb[c][:, :], wring[:, s, k, c * P:(c + 1) * P], y[:, k, :],
                                              start=(k == 0), stop=(k == KD - 1))
                    mm.then_inc((w_used if c else out_ps).h, 1)

        E_UNITS = [("E", h, tb) for h in range(E_HEADS) for tb in range(TB)]
        e_vv = arena[:, e_v:e_v + 4, :]

        def even_qk(m, h):
            r = 64 * (h % 2)
            return T(e_q + h // 2)[r:r + 64, :], T(e_k + h // 2)[r:r + 64, :]

        def even_ready(eng, u):
            if u == 0:
                eng.e.wait_ge(glu_sb.h, 4)
            m, h, tb = E_UNITS[u]
            if tb == 0 and h % 2 == 0:
                eng.e.wait_ge(rot_ready.h, 2 * (h // 2) + 2)
            if u == 0:
                eng.e.wait_ge(ez_sb.h, len(E_Z))

        EVEN = dict(qk=even_qk, mask=lambda m, h, tb, u: (C("lnmult")[:, SEQ - (tb + 1) * P:], 0),
                    v=lambda m, h, b: e_vv[:, b, h * E_DIM:(h + 1) * E_DIM], ready=even_ready)

        def pe_even(pe, norms):
            inc = list(DMA_EVEN)
            nz = 0
            for t in E_SEQ:
                if t[0] == "z":
                    _, b, c, n, i = t
                    s = b % 2
                    bank = pb[nz % 2]
                    if c == 0:
                        inc[s] += 1
                        pe.e.wait_ge(w_in_sem[s].h, 16 * inc[s])
                    if nz >= 2:
                        pe.e.wait_ge(ez_sb.h, nz - 1)
                    w = wring[:, s, :, :]
                    if n == "v":
                        for q in range(2):
                            tb = 2 * c + q
                            for k in range(KD):
                                mm = nc.tensor.matmul(bank[:, q * 256:(q + 1) * 256], xn[:, k, tb * P:(tb + 1) * P],
                                                      w[:, k, :], start=(k == 0), stop=(k == KD - 1))
                    else:
                        for k in range(KD):
                            if nz == 0:
                                pe.e.wait_ge(xn_ready.h, norms * KD + k + 1)
                            mm = nc.tensor.matmul(bank[:, :], w[:, k, c * P:(c + 1) * P], xn[:, k, :],
                                                  start=(k == 0), stop=(k == KD - 1))
                    mm.then_inc((w_used if c else ez_ps).h, 1)
                    nz += 1
                elif t[0] == "prep":
                    pe.e.wait_ge(par.h, PAR_E)
                    pe.e.wait_ge(s5_in.h, 16 * 7)
                    for q, src in enumerate((e_ere, e_eim, e_cst, e_cst + 1)):
                        for i in range(4):
                            mm = nc.tensor.transpose(pb[2 + q][:, i * P:(i + 1) * P], T(src)[:, i * P:(i + 1) * P], ident)
                        mm.then_inc(bc_ps.h, 1)
                elif t[0] == "bu":
                    j = t[1]
                    if j == 0:
                        pe.e.wait_ge(bt_sb.h, 2)
                        pe.e.wait_ge(cb_sb.h, 4)
                        pe.e.wait_ge(ez_sb.h, 4)
                    if j >= 2:
                        pe.e.wait_ge(s5_rot.h, j - 1)
                    r = slice(32 * (j % 4), 32 * (j % 4) + 32)
                    for q, bt in enumerate((e_btr, e_bti)):
                        mm = nc.tensor.matmul(pb[2 + 2 * (j % 2) + q][:, :], T(bt)[r, (j // 4) * P:(j // 4 + 1) * P],
                                              T(e_u + j // 4)[r, :], start=True, stop=True)
                    mm.then_inc(bu_ps.h, 1)
                else:
                    j = t[1]
                    pe.e.wait_ge(s5_p.h, j + 1)
                    pe.e.wait_ge(s5_q.h, j + 1)
                    if j % 4 == 0 and j >= 8:
                        pe.e.wait_ge(s5_y.h, j // 4 - 1)
                    r = slice(32 * (j % 4), 32 * (j % 4) + 32)
                    a1, p3, p2, p4 = s5_a[j % 3]
                    for q, (cm, a) in enumerate(((e_cre, a1), (e_crn, p2), (e_cin, p3), (e_cin, p4))):
                        mm = nc.tensor.matmul(pb[6 + (j // 4) % 2][r, :], T(cm)[:, j * 32:(j + 1) * 32], a,
                                              start=(q == 0), stop=(q == 3))
                    mm.then_inc(yy_ps.h, 1)
            for i in range(8):
                t = (e_q if i % 2 == 0 else e_k) + i // 2
                if i < 2:
                    pe.e.wait_ge(ez_sb.h, len(E_Z))
                else:
                    pe.e.wait_ge(rot_s.h, i - 1)
                nc.tensor.matmul(pb[i % 2][:, :], C("rot128"), T(t), start=True, stop=True).then_inc(rot_ps.h, 1)
            pe.e.wait_ge(s5_gelu.h, 4)
            for b in range(2):
                s = b % 2
                pe.e.wait_ge(w_in_sem[s].h, 16 * (inc[s] + 1))
                for c in range(2):
                    for k in range(4):
                        mm = nc.tensor.matmul(pb[2 + 2 * b + c][:, :], wring[:, s, k, c * P:(c + 1) * P], T(e_u + k),
                                              start=(k == 0), stop=(k == 3))
                    mm.then_inc((w_used if c else glu_ps).h, 1)
            pe.e.wait_ge(rot_s.h, 8)

        def pe_out2(pe, use0, inc, m, ready):
            ready(pe)
            for b in range(4):
                s = b % 2
                pe.e.wait_ge(w_in_sem[s].h, 16 * (inc[s] + b // 2 + 1))
                for c in range(2):
                    dc = 2 * b + c
                    if dc >= 2:
                        pe.e.wait_ge(r_ready.h, m * KD + dc - 1)
                    for k in range(KD):
                        mm = nc.tensor.matmul(pb[c][:, :], wring[:, s, k, c * P:(c + 1) * P], y[:, k, :],
                                              start=(k == 0), stop=(k == KD - 1))
                    mm.then_inc((w_used if c else eo_ps).h, 1)

        def even_mixed(pe):
            pe.e.wait_ge(y_att.h, 4 * DEPTH + 4)
            pe.e.wait_ge(y_ssm.h, 4)

        def odd_mixed(pe):
            pe.e.wait_ge(y_lru.h, KD)

        def pe_post(pe, m):
            for k in range(KD):
                pe.e.wait_ge(rsq.h, m * KD + k + 1)
                mm = nc.tensor.matmul(pb[6][:, :], C("mean1024"), T(SQ + k), start=(k == 0), stop=(k == KD - 1))
            mm.then_inc(rn_ps.h, 1)

        def pe_odd(pe, norms):
            inc = list(DMA_ODD)
            for n in range(2 * KD):
                s = (n // 2) % 2
                c = n % 2
                if c == 0:
                    inc[s] += 1
                    pe.e.wait_ge(w_in_sem[s].h, 16 * inc[s])
                if n >= 4:
                    pe.e.wait_ge(oz_sb.h, n - 3)
                for k in range(KD):
                    if n == 0:
                        pe.e.wait_ge(xn_ready.h, norms * KD + k + 1)
                    mm = nc.tensor.matmul(pb[n % 4][:, :], wring[:, s, k, c * P:(c + 1) * P], xn[:, k, :],
                                          start=(k == 0), stop=(k == KD - 1))
                mm.then_inc((w_used if c else oz_ps).h, 1)
            for g in range(2):
                inc[g] += 1
                pe.e.wait_ge(w_in_sem[g].h, 16 * inc[g])
                for m in range(KD):
                    n = g * KD + m
                    if n < 4:
                        pe.e.wait_ge(oz_sb.h, 2 * KD - 3 + n)
                    else:
                        pe.e.wait_ge(og_sb.h, n - 3)
                    b = m // 2
                    pe.e.wait_ge(cv.h, LRU_TAPS * (2 * b + 2))
                    for k in range(2):
                        mm = nc.tensor.matmul(pb[n % 4][:, :], wring[:, g, 2 * b + k, (m % 2) * P:(m % 2 + 1) * P],
                                              T(o_xc + 2 * b + k), start=(k == 0), stop=(k == 1))
                    mm.then_inc((w_used if m == KD - 1 else og_ps).h, 1)
            pe.e.wait_ge(og_sb.h, 2 * KD)

        @block.tensor
        def _(e):
            pe = Eng(e)
            pe.e.wait_ge(consts_in.h, 16)
            pe.e.wait_ge(token_dma.h, 16 * TB)
            for k in range(KD):
                if k >= 2:
                    pe.e.wait_ge(x_ready.h, k - 1)
                for tb in range(TB):
                    mm = nc.tensor.transpose(pb[k % 2][:, tb * P:(tb + 1) * P],
                                             arena[:, 2 * tb + k // 4, (k % 4) * P:(k % 4 + 1) * P], ident)
                mm.then_inc(pro_ps.h, 1)
            pe.e.wait_ge(rows_in.h, 16 * N_ROW_DMAS)
            pe.e.wait_ge(ldt_row.h, 1)
            for i in range(4):
                nc.tensor.transpose(pb[2 + i][:, 0:P], rows[:, i, :], ident).then_inc(pro_ps.h, 1)
            pe.e.wait_ge(relb_in.h, 32)
            pe.e.wait_ge(relb_neg.h, 1)
            half = BIAS_N // 2
            for q in range(2):
                nc.tensor.matmul(pb[6 + q][0:A_HEADS, 0:half], relb[0:33, :], C("onehot")[0:33, q * half:(q + 1) * half],
                                 start=True, stop=True).then_inc(pro_ps.h, 1)
            pe.e.wait_ge(pro_sb.h, 4)
            pe.e.wait_ge(pro_sb.h, 4 + 2)
            pe.e.wait_ge(x_ready.h, KD)
            pe.e.wait_ge(bias_dma.h, 32)
            for h in range(A_HEADS):
                nc.tensor.matmul(pb[h][:, :], C("flip"), arena[:, 8 + h, :], start=True, stop=True).then_inc(pro_ps.h, 1)
            pe.e.wait_ge(pro_sb.h, 4 + 2 + A_HEADS)
            for l in range(DEPTH):
                pe.l = l
                pe_norm(pe, l * 3)
                pe_ffn(pe, l * 2)
                pe_norm(pe, l * 3 + 1)
                pe_z(pe, l * 3 + 1)
                pe_mixers(pe)
                pe_attention(pe, HYB_UNITS, HYB)

                def ready(pe):
                    pe.e.wait_ge(y_conv.h, y_conv.by(pe.l, 2))
                    pe.e.wait_ge(y_b.h, y_b.by(pe.l, 2))
                    pe.e.wait_ge(y_att.h, y_att.by(pe.l, 4))
                pe_out(pe, [sum(U_Z[s::2]) for s in range(2)], ready)
                pe_norm(pe, l * 3 + 2)
                pe_ffn(pe, l * 2 + 1)
            pe.l = DEPTH
            n = 3 * DEPTH
            pe_norm(pe, n)
            pe_even(pe, n)
            pe_attention(pe, E_UNITS, EVEN)
            pe_out2(pe, USE_EVEN + len(E_BLOCKS) + 2, [DMA_EVEN[s] + sum(U_EVEN[s:len(E_BLOCKS) + 2:2]) for s in range(2)], 0,
                    even_mixed)
            pe_post(pe, 0)
            pe_norm(pe, n + 1)
            pe_ffn(pe, 2 * DEPTH)
            pe_post(pe, 1)
            pe_norm(pe, n + 2)
            pe_odd(pe, n + 2)
            pe_out2(pe, USE_ODD + 10, [DMA_ODD[s] + sum(U_ODD[s:10:2]) for s in range(2)], 2, odd_mixed)
            pe_post(pe, 2)
            pe_norm(pe, n + 3)
            pe_ffn(pe, 2 * DEPTH + 1)
            pe_post(pe, 3)
            pe.e.wait_ge(x_ready.h, X1 + 4 * KD)
            for tb in range(TB):
                for q in range(2):
                    n = 2 * tb + q
                    if n >= 2:
                        pe.e.wait_ge(fin_sb.h, n - 1)
                    for k in range(4):
                        mm = nc.tensor.transpose(pb[n % 2][:, k * P:(k + 1) * P], x[:, 4 * q + k, tb * P:(tb + 1) * P], ident)
                    mm.then_inc(fin_ps.h, 1)

        LN_EXP = "natural_log_exp_and_others"

        def act_norm(act, n, f=None):
            nc.scalar.preload_act_table_set(LN_EXP)
            for k in range(KD):
                act.e.wait_ge(x_ready.h, n * KD + (k + 1))
                nc.scalar.activation(T(SQ + k), x[:, k, :], ACT.Square).then_inc(sq_done.h, 1)
            if f is not None:
                for q in range(2):
                    act.e.wait_ge(u_in[q].h, unit_loads(f, q, 0))
                    split_unit(q)
            act.e.wait_ge(norm_ps.h, n + 1)
            nc.scalar.activation(T(RT), pb[6][:, :], ACT.Ln, bias=C("eps")).then_inc(norm_ln.h, 1)
            act.e.wait_ge(norm_ln.h, n + 1)
            nc.scalar.activation(T(RT), T(RT), ACT.Exp, scale=-0.5).then_inc(norm_r.h, 1)
            if f is not None:
                nc.scalar.preload_act_table(ACT.Silu)
                for k in range(KD):
                    act.e.wait_ge(xn_ready.h, n * KD + k + 1)
                    nc.scalar.activation(xn_hi[:, k, :], xn[:, k, :], ACT.Copy).then_inc(xn_hi_ready.h, 1)

        def split_unit(slot):
            nc.scalar.activation(w_hi[:, slot, :, :].rearrange("p k c -> p (k c)"), wunit[:, slot, :], ACT.Copy).then_inc(u_hi.h, 1)

        def act_ffn(act, f):
            with act.e.Fori(0, NF // 2) as i:
                for c in range(2):
                    n = f * NF + 2 * i + c
                    slots = (2, 3) if c == 0 else (0, 1)
                    act.e.wait_ge(u_in[slots[0]].h, unit_loads(f, slots[0], c) + 16 * i)
                    split_unit(slots[0])
                    act.e.wait_ge(unit_ps.h, f * UNITS + SLOTS * i + (2 * c + 1))
                    act.e.wait_ge(h_full.h, h_full.start + n - 1)
                    nc.scalar.activation(sg[:, c, :], pb[c][:, :], ACT.Silu).then_inc(sg_ready.h, 1)
                    act.e.wait_ge(u_in[slots[1]].h, unit_loads(f, slots[1], c) + 16 * i)
                    split_unit(slots[1])
                    act.e.wait_ge(h_full.h, h_full.start + n + 1)
                    nc.scalar.activation(h_hi[:, bass.ds(2 * i + c, 1), :].rearrange("p a c -> p (a c)"),
                                         arena[:, bass.ds(2 * i + (H_LO + c), 1), :].rearrange("p a c -> p (a c)"),
                                         ACT.Copy).then_inc(h_hi_ready.h, 1)
            with act.e.Fori(0, NF // SLOTS) as i:
                for q in range(SLOTS):
                    s = (q + 2) % SLOTS
                    act.e.wait_ge(u_in[s].h, unit_loads(f, s, NF // 2 + (q + 2) // SLOTS) + 16 * i)
                    split_unit(s)

        def rstd(act, src, dst, ln, r, k):
            nc.scalar.activation(dst, src, ACT.Ln, bias=C("eps")[0:dst.shape[0], :]).then_inc(ln.h, 1)
            act.e.wait_ge(ln.h, ln.by(act.l, k))
            nc.scalar.activation(dst, dst, ACT.Exp, scale=-0.5).then_inc(r.h, 1)

        def act_z(act):
            ni = nps = 0
            nused = 0
            dst = dict(iq0=0, iq1=1, ik=2, aq0=3, aq1=4, ak0=5, ak1=6, av01=7, av23=8, bq=9, bk=10, bv01=11, bv23=12,
                       br0=13, br1=14, ca0=15, ca1=16, cg0=17, cg1=18, dcq0=19, dcq1=20, dckv=21)
            for n, t in enumerate(Z_SEQ):
                bank = pb[n % 4]
                if t[0] == "idx":
                    _, tb, h = t
                    N = (tb + 1) * P
                    act.e.wait_ge(idx_ps.h, idx_ps.by(act.l, ni + 1))
                    if ni >= 4:
                        act.e.wait_ge(idx_acc.h, idx_acc.by(act.l, ni - 3))
                    nc.scalar.activation(W(idx_r[ni % 4])[:, 0:N], bank[:, 0:N], ACT.Relu).then_inc(z_sb.h, 1)
                    ni += 1
                    continue
                _, b, c, label, col, kind, last = t
                if last:
                    nused += 1
                    act.e.wait_ge(w_used.h, w_used.by(act.l, nused))
                else:
                    nps += 1
                    act.e.wait_ge(z_ps.h, z_ps.by(act.l, nps))
                if label in ("aq0", "aq1", "ak0", "ak1", "dcq0", "dcq1", "dckv"):
                    q = ("aq0", "aq1", "ak0", "ak1", "dcq0", "dcq1", "dckv").index(label)
                    nc.scalar.activation(T(t_zsq[q]), bank[:, :], ACT.Square).then_inc(zsq.h, 1)
                if kind == "iw":
                    nc.scalar.activation(wA, bank[:, 0:32], ACT.Copy,
                                         scale=float((IDX_DIM * IDX_HEADS) ** -0.5)).then_inc(z_sb.h, 1)
                elif kind == "bg":
                    nc.scalar.activation(T(t_gl)[0:B_RANK, :], bank[0:B_RANK, :], ACT.Copy).then_inc(z_sb.h, 1)
                elif kind == "kpe":
                    nc.scalar.activation(T(t_kpe)[64:96, :], bank[64:96, :], ACT.Copy).then_inc(z_sb.h, 1)
                else:
                    f = {"br": ACT.Silu, "cg": ACT.Sigmoid}.get(label[:2], ACT.Copy)
                    s = float(B_KEY ** -0.5) if label == "bq" else 1.0
                    nc.scalar.activation(T(dst[label]), bank[:, :], f, scale=s).then_inc(z_sb.h, 1)

        def act_mixers(act):
            nc.scalar.preload_act_table_set(LN_EXP)
            act.e.wait_ge(gate_log_ps.h, gate_log_ps.by(act.l, 1))
            act.e.wait_ge(cur_ready.h, cur_ready.by(act.l, 4))
            gb = cur[:, RL["b_gate_bias"]:RL["b_gate_bias"] + 1]
            nc.scalar.activation(W(w_mn), pb[0][:, :], ACT.Identity, bias=gb).then_inc(g_abs.h, 1)
            nc.scalar.activation(T(t_ab), pb[0][:, :], ACT.Abs, bias=gb).then_inc(g_abs.h, 1)
            act.e.wait_ge(g_abs.h, g_abs.by(act.l, 2))
            nc.scalar.activation(T(t_ab), T(t_ab), ACT.Exp, scale=-1.0).then_inc(g_abs.h, 1)
            act.e.wait_ge(g_abs.h, g_abs.by(act.l, 3))
            nc.scalar.activation(T(t_ab), T(t_ab), ACT.Ln, bias=1.0).then_inc(g_abs.h, 1)
            bank = [1, 2, 3, 1, 2, 3]
            for i in range(6):
                act.e.wait_ge(mn_ps.h, mn_ps.by(act.l, i + 1))
                rstd(act, pb[bank[i]][:, :], T(t_zr[i]), mn_ln, mn_r, i + 1)
            g = 1.0 / 16
            act.e.wait_ge(g_b.h, g_b.by(act.l, 6))
            b16 = W(w_mn)
            nc.scalar.activation(T(t_qe), b16, ACT.Exp, scale=g).then_inc(g_exp.h, 1)
            nc.scalar.activation(W(w_e1), W(w_la), ACT.Exp, scale=g).then_inc(g_exp.h, 1)
            nc.scalar.activation(W(w_e1n), W(w_la), ACT.Exp, scale=-g).then_inc(g_exp.h, 1)
            nc.scalar.activation(W(w_e2), T(t_ab), ACT.Exp, scale=g).then_inc(g_exp.h, 1)
            nc.scalar.activation(glast[:, 0:NCH], b16.rearrange("p (c t) -> p c t", c=NCH)[:, :, B_CHUNK - 1],
                                 ACT.Exp, scale=g).then_inc(g_exp.h, 1)
            for ct in range(2):
                act.e.wait_ge(conv.h, conv.by(act.l, 2 * TAPS - 1 + ct))
                nc.scalar.activation(T(t_csq[ct]), T(t_hc[ct]), ACT.Square).then_inc(conv_sq.h, 1)
            for q in range(2):
                act.e.wait_ge(dv_ps.h, dv_ps.by(act.l, q + 1))
                nc.scalar.activation(T(t_dv + q), pb[6 + q][:, :], ACT.Copy).then_inc(dv_sb.h, 1)
            for i in range(8 + 1):
                if i < 8:
                    act.e.wait_ge(dh_ps.h, dh_ps.by(act.l, i + 1))
                    if i >= 2:
                        act.e.wait_ge(dn_x.h, dn_x.by(act.l, i - 1))
                    nc.scalar.activation(T(t_hraw[i % 2])[0:D_QK, :], pb[i % 2][0:D_QK, :], ACT.Copy)
                    nc.scalar.activation(T(t_hsq[i % 2])[0:D_QK, :], pb[i % 2][0:D_QK, :], ACT.Square).then_inc(dh_sq.h, 1)
                if i >= 1:
                    u = i - 1
                    act.e.wait_ge(dn_ps.h, dn_ps.by(act.l, u + 1))
                    if u >= 2:
                        act.e.wait_ge(dh_ready.h, dh_ready.by(act.l, u - 1))
                    rstd(act, pb[2][0:D_QK, :], T(t_hr[u % 2])[0:D_QK, :], dn_ln, dn_r, u + 1)
            act.e.wait_ge(mn_ps.h, mn_ps.by(act.l, 7))
            rstd(act, pb[6][:, :], T(t_cr), mn_ln, mn_r, 7)
            act.e.wait_ge(kt_ps.h, kt_ps.by(act.l, 1))
            nc.scalar.activation(T(t_kdt), pb[7][:, :], ACT.Copy).then_inc(kt_sb.h, 1)
            for pr in range(2):
                act.e.wait_ge(o_ps.h, o_ps.by(act.l, pr + 1))
                nc.scalar.activation(T(t_o[pr]), pb[pr][:, :], ACT.Copy)
                nc.scalar.activation(T(t_osq[pr]), pb[pr][:, :], ACT.Square).then_inc(o_sq.h, 1)
            for pr in range(2):
                act.e.wait_ge(on_ps.h, on_ps.by(act.l, pr + 1))
                rstd(act, pb[2 + pr][:, :], T(t_or[pr]), on_ln, on_r, pr + 1)
            act.e.wait_ge(mn_x.h, mn_x.by(act.l, 9))
            for ct in range(2):
                nc.scalar.activation(y[:, 4 + ct, :], T(t_hc[ct]), ACT.Silu).then_inc(y_conv.h, 1)

        def act_attention(act, units, ytile):
            U = len(units)
            for i in range(U + 4):
                if i < U:
                    N = (units[i][2] + 1) * P
                    act.e.wait_ge(att_max.h, att_max.by(act.l, i + 1))
                    if i >= 3:
                        act.e.wait_ge(att_t.h, att_t.by(act.l, i - 2))
                    c = i % 4
                    nc.scalar.activation(p_buf(i)[:, 0:N], pb[(0, 1, 4, 5)[i % 4]][:, 0:N], ACT.Exp,
                                         bias=nmax[:, c:c + 1], accum_out=psum_[:, c:c + 1]).then_inc(att_exp.h, 1)
                u = i - 4
                if u >= 0 and u % 8 == 7:
                    act.e.wait_ge(att_o.h, att_o.by(act.l, u + 1))
                    nc.scalar.activation(y[:, ytile(u // 8), :], pb[6 + (u // 8) % 2][:, :], ACT.Copy).then_inc(y_att.h, 1)

        TWO_PI = 6.283185

        def act_even(act):
            act.e.wait_ge(pro_sb.h, 4)
            nc.scalar.activation(c_dt, c_ldt, ACT.Exp).then_inc(par_act.h, 1)
            act.e.wait_ge(par.h, 2)
            nc.scalar.activation(c_r, c_ard, ACT.Exp).then_inc(par_act.h, 1)
            act.e.wait_ge(par.h, 6)
            nc.scalar.activation(c_sin, c_fr, ACT.Sin, scale=TWO_PI).then_inc(par_act.h, 1)
            act.e.wait_ge(par.h, 8)
            nc.scalar.activation(c_cos, c_f2, ACT.Sin, scale=TWO_PI).then_inc(par_act.h, 1)
            nz = j = ny = 0
            nu = USE_EVEN
            nps = 0

            def trig(j):
                if j >= 3:
                    act.e.wait_ge(s5_p.h, j - 2)
                    act.e.wait_ge(s5_q.h, j - 2)
                act.e.wait_ge(s5_frac.h, j + 1)
                nc.scalar.activation(s5_sin[j % 3], s5_d[j % 2], ACT.Sin, scale=TWO_PI).then_inc(s5_trig.h, 1)
                act.e.wait_ge(s5_quart.h, j + 1)
                nc.scalar.activation(s5_cos[j % 3], s5_d2[j % 2], ACT.Sin, scale=TWO_PI).then_inc(s5_trig.h, 1)
            for t in E_SEQ:
                if t[0] == "z":
                    _, b, c, n, i = t
                    if c:
                        nu += 1
                        act.e.wait_ge(w_used.h, nu)
                    else:
                        nps += 1
                        act.e.wait_ge(ez_ps.h, nps)
                    bank = pb[nz % 2]
                    nz += 1
                    if n == "v":
                        nc.scalar.activation(e_vv[:, 2 * c:2 * c + 2, (b % 2) * 256:(b % 2 + 1) * 256],
                                             bank[:, :].rearrange("p (q c) -> p q c", q=2), ACT.Copy).then_inc(ez_sb.h, 1)
                    else:
                        dst = T(dict(u=e_u, q=e_q, k=e_k)[n] + i)
                        nc.scalar.activation(dst, bank[:, :], ACT.Copy,
                                             scale=float(E_DIM ** -0.5) if n == "q" else 1.0).then_inc(ez_sb.h, 1)
                elif t[0] == "prep":
                    for q, dst in enumerate((e_btr, e_bti)):
                        act.e.wait_ge(bc_ps.h, q + 1)
                        nc.scalar.activation(T(dst), pb[2 + q][:, :], ACT.Copy).then_inc(bt_sb.h, 1)
                    act.e.wait_ge(tab.h, 8)
                    nc.scalar.activation(T(e_sin), T(e_tmp[3]), ACT.Sin).then_inc(tab_sin.h, 1)
                    act.e.wait_ge(tab.h, 16)
                    nc.scalar.activation(T(e_cos), T(e_tmp[3]), ACT.Sin).then_inc(tab_sin.h, 1)
                    trig(0)
                elif t[0] == "bu" and t[1] + 1 < NST:
                    trig(t[1] + 1)
            for i in range(4):
                act.e.wait_ge(s5_y.h, i + 1)
                nc.scalar.activation(T(e_u + i), T(e_u + i), ACT.Gelu_apprx_tanh).then_inc(s5_gelu.h, 1)
            nu += 1
            for c in range(4):
                if c % 2:
                    act.e.wait_ge(w_used.h, nu + c // 2)
                else:
                    act.e.wait_ge(glu_ps.h, c // 2 + 1)
                nc.scalar.activation(T(e_glu + c), pb[2 + c][:, :], ACT.Sigmoid).then_inc(glu_sb.h, 1)

        def act_post(act, m):
            nc.scalar.preload_act_table_set(LN_EXP)
            for k in range(KD):
                act.e.wait_ge(r_ready.h, m * KD + k + 1)
                nc.scalar.activation(T(SQ + k), T(RB + k), ACT.Square).then_inc(rsq.h, 1)
            act.e.wait_ge(rn_ps.h, m + 1)
            nc.scalar.activation(T(RT2), pb[6][:, :], ACT.Ln, bias=C("eps")).then_inc(rn_ln.h, 1)
            act.e.wait_ge(rn_ln.h, m + 1)
            nc.scalar.activation(T(RT2), T(RT2), ACT.Exp, scale=-0.5).then_inc(rn_r.h, 1)

        def act_odd(act):
            act.e.wait_ge(sp_step.h, 2)
            nc.scalar.activation(spc[:, 1, :], spc[:, 0, :], ACT.Exp, scale=-1.0).then_inc(par_act.h, 1)
            act.e.wait_ge(pad_zero.h, 1)
            for n in range(2 * KD):
                if n % 2:
                    act.e.wait_ge(w_used.h, USE_ODD + n // 2 + 1)
                else:
                    act.e.wait_ge(oz_ps.h, n // 2 + 1)
                if n < KD:
                    nc.scalar.activation(xpad[:, n, LRU_TAPS - 1:], pb[n % 4][:, :], ACT.Copy).then_inc(oz_sb.h, 1)
                else:
                    nc.scalar.activation(T(o_gel + n - KD), pb[n % 4][:, :], ACT.Gelu_apprx_tanh).then_inc(oz_sb.h, 1)
            for n in range(2 * KD):
                g, m = n // KD, n % KD
                if m == KD - 1:
                    act.e.wait_ge(w_used.h, USE_ODD + 9 + g)
                else:
                    act.e.wait_ge(og_ps.h, g * (KD - 1) + m + 1)
                bcol = R2["rg_b_i_2" if g else "rg_b_r_2"] + m
                nc.scalar.activation(T((o_i if g else o_r) + m), pb[n % 4][:, :], ACT.Sigmoid,
                                     bias=col2[:, bcol:bcol + 1]).then_inc(og_sb.h, 1)
            act.e.wait_ge(og_sb.h, KD)
            act.e.wait_ge(sp_step.h, SP_STEPS)
            for k in range(KD):
                nc.scalar.activation(W(k), T(o_r + k), ACT.Tanh, scale=spc[:, 7, k:k + 1]).then_inc(o_th.h, 1)
            for k in range(KD):
                nc.scalar.activation(T(o_r + k), T(o_r + k), ACT.Exp, scale=spc[:, 7, k:k + 1]).then_inc(o_a.h, 1)
            for k in range(KD):
                act.e.wait_ge(o_q.h, k + 1)
                nc.scalar.activation(W(k), W(k), ACT.Sqrt, scale=-1.0).then_inc(o_sqrt.h, 1)

        @block.scalar
        def _(e):
            act = Eng(e)
            e.sem_inc(sg_ready.h, sg_ready.start)
            act.e.wait_ge(rows_zero.h, 1)
            for i, n in enumerate(R1):
                e.dma_start(rows[R1[n]:R1[n] + 2 * KD, 0, :],
                            I[n].rearrange("l (k p) -> (l k) p", p=P)).then_inc(rows_in.h, 16)
            for l in range(DEPTH):
                for n, c in LAYER_ROWS:
                    r = l * NRL + RL[n]
                    w = I[n].shape[1]
                    if w == 64:
                        for q in range(2):
                            e.dma_start(rows[r:r + 1, 1, q * 64:(q + 1) * 64], I[n][l:l + 1, :]).then_inc(rows_in.h, 16)
                    elif w == D_QK:
                        e.dma_start(rows[r:r + 1, 1, 0:w], I[n][l:l + 1, :]).then_inc(rows_in.h, 16)
                    else:
                        e.dma_start(rows[r:r + c, 1, :], I[n][l].rearrange("(k p) -> k p", p=P)).then_inc(rows_in.h, 16)
            e.dma_start(rows[R2["s5_d_2"]:R2["s5_d_2"] + 4, 1, :],
                        I["s5_d_2"][0].rearrange("(k g) c -> k (g c)", k=4)).then_inc(rows_in.h, 16)
            for n in ("rg_conv_b_2", "rg_b_r_2", "rg_b_i_2", "rg_lam_2"):
                e.dma_start(rows[R2[n]:R2[n] + 8, 1, :], I[n][0].rearrange("(k p) -> k p", p=P)).then_inc(rows_in.h, 16)
            e.dma_start(rows[R2["rg_conv_w_2"]:R2["rg_conv_w_2"] + 32, 1, :],
                        I["rg_conv_w_2"][0].rearrange("j (k p) -> (j k) p", p=P)).then_inc(rows_in.h, 16)
            e.dma_start(rows[0:NR3, 2, :],
                        I["c_dw_w"].rearrange("l j o (t p) -> (l j o t) p", p=P)).then_inc(rows_in.h, 16)
            for i, n in enumerate(("s5_a_re_2", "s5_a_im_2")):
                e.dma_start(rows[i * NST:(i + 1) * NST, 3, :], I[n][0].rearrange("(j q) p -> j (q p)", q=2)).then_inc(rows_in.h, 16)
            e.dma_start(ldt[32:32 + NST, :], I["s5_log_dt_2"][0].rearrange("(j q) -> j q", q=2)).then_inc(ldt_in.h, 16)
            act.e.wait_ge(pro_ps.h, KD + 4)
            for i, (dst, n) in enumerate(((col1, NR1), (col2, NR2), (col3, NR3), (s5col, 3 * NST))):
                dst = dst[:, 0:3, :].rearrange("p a c -> p (a c)") if dst is s5col else dst[:, :]
                nc.scalar.activation(dst, pb[2 + i][:, 0:n], ACT.Copy).then_inc(pro_sb.h, 1)
            half = BIAS_N // 2
            bv4 = arena[0:A_HEADS, 20:22, 0:half]
            act.e.wait_ge(pro_ps.h, KD + 4 + 2)
            for q in range(2):
                nc.scalar.activation(bv4[:, q, :], pb[6 + q][0:A_HEADS, 0:half], ACT.Copy).then_inc(pro_sb.h, 1)
            act.e.wait_ge(pro_sb.h, 4 + 2)
            e.dma_start(bias_dram.ap().rearrange("h (q n) -> h q n", q=2), bv4).then_inc(bias_dma.h, 16)
            act.e.wait_ge(bias_dma.h, 16)
            e.dma_start(arena[:, 8:8 + A_HEADS, :], bass.AP(bias_dram, 0, [[1, P], [BIAS_N, A_HEADS], [1, SEQ]])
                        ).then_inc(bias_dma.h, 16)
            for h in range(A_HEADS):
                act.e.wait_ge(pro_ps.h, KD + 4 + 2 + h + 1)
                nc.scalar.activation(bias[:, h, :], pb[h][:, :], ACT.Copy).then_inc(pro_sb.h, 1)
            for l in range(DEPTH):
                act.l = l
                act_norm(act, l * 3, l * 2)
                act_ffn(act, l * 2)
                act_norm(act, l * 3 + 1)
                act_z(act)
                act_mixers(act)
                act_attention(act, HYB_UNITS, lambda p: (6, 7, 0, 1)[p])
                act_norm(act, l * 3 + 2, l * 2 + 1)
                act_ffn(act, l * 2 + 1)
            act.l = DEPTH
            n = 3 * DEPTH
            act_norm(act, n)
            act_even(act)
            act_attention(act, E_UNITS, lambda p: p)
            act_post(act, 0)
            act_norm(act, n + 1, 2 * DEPTH)
            act_ffn(act, 2 * DEPTH)
            act_post(act, 1)
            act_norm(act, n + 2)
            act_odd(act)
            act_post(act, 2)
            act_norm(act, n + 3, 2 * DEPTH + 1)
            act_ffn(act, 2 * DEPTH + 1)
            act_post(act, 3)
            for n in range(2 * TB):
                act.e.wait_ge(fin_ps.h, n + 1)
                nc.scalar.activation(arena[:, n, :], pb[n % 2][:, :], ACT.Copy).then_inc(fin_sb.h, 1)

        def dve_norm(dve, n, g, f=None):
            if f is not None:
                for q in range(2):
                    dve.e.wait_ge(u_hi.h, f * UNITS + q + 1)
                    split_rest(q)
            dve.e.wait_ge(norm_r.h, n + 1)
            for k in range(KD):
                nc.vector.scalar_tensor_tensor(out=xn[:, k, :], in0=x[:, k, :], scalar=g(k), in1=T(RT),
                                               op0=ALU.mult, op1=ALU.mult).then_inc(xn_ready.h, 1)
                if f is not None and k >= 1:
                    dve.e.wait_ge(xn_hi_ready.h, f * KD + k)
                    nc.vector.tensor_tensor(xn_lo[:, k - 1, :], xn[:, k - 1, :], xn_hi[:, k - 1, :].bitcast(F32),
                                            ALU.subtract).then_inc(xn_lo_ready.h, 1)
            if f is not None:
                dve.e.wait_ge(xn_hi_ready.h, (f + 1) * KD)
                nc.vector.tensor_tensor(xn_lo[:, KD - 1, :], xn[:, KD - 1, :], xn_hi[:, KD - 1, :].bitcast(F32),
                                        ALU.subtract).then_inc(xn_lo_ready.h, 1)

        def split_rest(slot):
            nc.vector.tensor_tensor(w_lo[:, slot, :, :].rearrange("p k c -> p (k c)"), wunit[:, slot, :],
                                    w_hi[:, slot, :, :].rearrange("p k c -> p (k c)").bitcast(F32),
                                    ALU.subtract).then_inc(u_lo.h, 1)

        def dve_ffn(dve, f, take):
            with dve.e.Fori(0, NF // 2) as i:
                for c in range(2):
                    for q in range(2):
                        dve.e.wait_ge(u_hi.h, f * UNITS + SLOTS * i + (2 * c + q + 3))
                        split_rest((2 * c + q + 2) % SLOTS)
                    dve.e.wait_ge(sg_ready.h, sg_ready.start + f * NF + 2 * i + (c + 1))
                    dve.e.wait_ge(unit_ps.h, f * UNITS + SLOTS * i + (2 * c + 2))
                    h = arena[:, bass.ds(2 * i + (H_LO + c), 1), :].rearrange("p a c -> p (a c)")
                    nc.vector.tensor_tensor(h, pb[2 + c][:, :], sg[:, c, :], ALU.mult).then_inc(h_full.h, 1)
                    dve.e.wait_ge(h_hi_ready.h, f * NF + 2 * i + (c + 1))
                    hi, lo = [t[:, bass.ds(2 * i + c, 1), :].rearrange("p a c -> p (a c)") for t in (h_hi, h_lo)]
                    nc.vector.tensor_tensor(lo, h, hi.bitcast(F32), ALU.subtract).then_inc(h_lo_ready.h, 1)
            with dve.e.Fori(0, NF // SLOTS) as i:
                for q in range(SLOTS):
                    dve.e.wait_ge(u_hi.h, f * UNITS + 2 * NF + SLOTS * i + (q + 3))
                    split_rest((q + 2) % SLOTS)
            for m in range(KD):
                if m < KD - 1:
                    dve.e.wait_ge(down_ps.h, f * (KD - 1) + m + 1)
                else:
                    dve.e.wait_ge(unit_ps.h, (f + 1) * UNITS)
                take(m)

        def add_half(m):
            nc.vector.scalar_tensor_tensor(out=x[:, m, :], in0=down_bank(m), scalar=0.5, in1=x[:, m, :],
                                           op0=ALU.mult, op1=ALU.add).then_inc(x_ready.h, 1)

        def dve_index(dve):
            ni = nt = 0
            for tb in (3, 2, 1):
                N = (tb + 1) * P
                for h in range(IDX_HEADS):
                    dve.e.wait_ge(z_sb.h, z_sb.by(dve.l, IDX_POS[ni] + 1))
                    w = wA[:, tb * 8 + h:tb * 8 + h + 1]
                    r = W(idx_r[ni % 4])[:, 0:N]
                    if h == 0:
                        ins = nc.vector.tensor_scalar(score(tb), r, w, None, ALU.mult)
                    else:
                        dve.e.wait_ge(idx_acc.h, idx_acc.by(dve.l, ni))
                        ins = nc.vector.scalar_tensor_tensor(out=score(tb), in0=r, scalar=w, in1=score(tb),
                                                             op0=ALU.mult, op1=ALU.add)
                    ins.then_inc(idx_acc.h, 1)
                    ni += 1
                dve.e.wait_ge(idx_acc.h, idx_acc.by(dve.l, ni))
                dg = score(tb)[:, tb * P:]
                nc.vector.tensor_tensor(dg, dg, C("causal"), ALU.add).then_inc(idx_mask.h, 1)
                dve.e.wait_ge(idx_mask.h, idx_mask.by(dve.l, 4 - tb))
                for r in range(TOPK // 8):
                    if r:
                        dve.e.wait_ge(top_rep.h, top_rep.by(dve.l, nt))
                    nc.vector.max(m8, score(tb)).then_inc(top_max.h, 1)
                    nt += 1
                    dve.e.wait_ge(top_max.h, top_max.by(dve.l, nt))
                    nc.vector.match_replace(score(tb), m8, score(tb), SENTINEL).then_inc(top_rep.h, 1)
                dve.e.wait_ge(top_rep.h, top_rep.by(dve.l, nt))
                nc.vector.tensor_scalar(score(tb), score(tb), 0.9 * SENTINEL, NEG, ALU.is_gt, ALU.mult).then_inc(top_done.h, 1)

        def dve_conv(dve):
            dve.e.wait_ge(hp_ready.h, hp_ready.by(dve.l, 2))
            for n in range(2 * TAPS):
                j, ct = n // 2, n % 2
                w = cur_dw[:, n:n + 1]
                src = hpad[:, ct, j:j + SEQ]
                if j == 0:
                    b = RL["c_dw_b"] + ct
                    ins = nc.vector.tensor_scalar(T(t_hc[ct]), src, w, cur[:, b:b + 1], ALU.mult, ALU.add)
                else:
                    dve.e.wait_ge(conv.h, conv.by(dve.l, n - 1))
                    ins = nc.vector.scalar_tensor_tensor(out=T(t_hc[ct]), in0=src, scalar=w, in1=T(t_hc[ct]),
                                                         op0=ALU.mult, op1=ALU.add)
                ins.then_inc(conv.h, 1)

        def dve_mixers(dve):
            dve.e.wait_ge(g_abs.h, g_abs.by(dve.l, 1))
            nc.vector.tensor_scalar(W(w_mn), W(w_mn), 0.0, None, ALU.min).then_inc(g_min.h, 1)
            dve.e.wait_ge(g_min.h, g_min.by(dve.l, 1))
            dve.e.wait_ge(g_abs.h, g_abs.by(dve.l, 4))
            nc.vector.tensor_tensor(W(w_la), W(w_mn), T(t_ab), ALU.subtract).then_inc(g_b.h, 1)
            dve.e.wait_ge(g_b.h, g_b.by(dve.l, 1))
            nc.vector.tensor_tensor_scan(W(w_mn), C("chunkmask"), W(w_la), 0.0, ALU.mult, ALU.add).then_inc(g_b.h, 1)
            dve.e.wait_ge(g_b.h, g_b.by(dve.l, 2))

            def chunks(t):
                return t.rearrange("p (c t) -> p c t", c=NCH)
            b = chunks(W(w_mn))
            mid = b[:, :, B_CHUNK // 2 - 1:B_CHUNK // 2].to_broadcast([P, NCH, B_CHUNK])
            end = b[:, :, B_CHUNK - 1:B_CHUNK].to_broadcast([P, NCH, B_CHUNK])
            nc.vector.tensor_tensor(chunks(T(t_ab)), end, b, ALU.subtract).then_inc(g_b.h, 1)
            nc.vector.tensor_tensor(chunks(W(w_la)), b, mid, ALU.subtract).then_inc(g_b.h, 1)
            dve.e.wait_ge(g_b.h, g_b.by(dve.l, 4))
            lim = 16.0 * 85.0
            nc.vector.tensor_scalar(W(w_la), W(w_la), lim, -lim, ALU.min, ALU.max).then_inc(g_b.h, 1)
            dve.e.wait_ge(g_b.h, g_b.by(dve.l, 5))
            nc.vector.tensor_scalar(T(t_ab), T(t_ab), 0.0, None, ALU.min).then_inc(g_b.h, 1)
            for i, (t, r, gc) in enumerate([(t_aq[0], 0, "a_q_norm"), (t_aq[1], 1, "a_q_norm"), (t_ak[0], 2, "a_k_norm"),
                                            (t_ak[1], 3, "a_k_norm"), (t_dcq[0], 4, "d_qa_norm"),
                                            (t_dcq[1], 4, "d_qa_norm"), (t_dckv, 5, "d_kva_norm")]):
                col = RL[gc] + (1 if i == 5 else 0)
                dve.e.wait_ge(mn_r.h, mn_r.by(dve.l, r + 1))
                nc.vector.scalar_tensor_tensor(out=T(t), in0=T(t), scalar=cur[:, col:col + 1], in1=T(t_zr[r]),
                                               op0=ALU.mult, op1=ALU.mult).then_inc(mn_x.h, 1)
            for n, (e_, t) in enumerate(((T(t_qe), t_bq), (W(w_e1), t_bq), (W(w_e2), t_bk))):
                dve.e.wait_ge(g_exp.h, g_exp.by(dve.l, (1, 2, 4)[n]))
                nc.vector.tensor_tensor(e_, e_, T(t), ALU.mult).then_inc(b_qk.h, 1)
            for i in range(8 + 1):
                if i < 8:
                    col = RL["d_q_norm" if i < 4 else "d_k_norm"]
                    dve.e.wait_ge(dn_r.h, dn_r.by(dve.l, i + 1))
                    if i >= 2:
                        dve.e.wait_ge(dr_c.h, dr_c.by(dve.l, i - 1))
                    nc.vector.scalar_tensor_tensor(out=T(t_hn[i % 2])[0:D_QK, :], in0=T(t_hraw[i % 2])[0:D_QK, :],
                                                   scalar=cur[0:D_QK, col:col + 1], in1=T(t_hr[i % 2])[0:D_QK, :],
                                                   op0=ALU.mult, op1=ALU.mult).then_inc(dn_x.h, 1)
                if i >= 1:
                    u = i - 1
                    dve.e.wait_ge(dr_ps.h, dr_ps.by(dve.l, u + 1))
                    nc.vector.tensor_tensor(T(t_hr[u % 2])[0:D_QK, :], pb[3][0:D_QK, :], C("sin96")[0:D_QK, :],
                                            ALU.mult).then_inc(dr_s.h, 1)
            dve.e.wait_ge(mn_r.h, mn_r.by(dve.l, 7))
            for ct in range(2):
                col = RL["c_norm"] + ct
                nc.vector.scalar_tensor_tensor(out=T(t_hc[ct]), in0=T(t_hc[ct]), scalar=cur[:, col:col + 1], in1=T(t_cr),
                                               op0=ALU.mult, op1=ALU.mult).then_inc(mn_x.h, 1)
            for c in range(NCH - 1):
                dve.e.wait_ge(u_ps.h, u_ps.by(dve.l, c + 1))
                um = Sst(1) if c == 0 else T(t_um)[:, (c % 2) * 256:(c % 2) * 256 + 256]
                nc.vector.tensor_tensor(um, pb[2 + c % 2][:, 0:256], C("headblk"), ALU.mult).then_inc(u_msk.h, 1)
                dve.e.wait_ge(u_msk.h, u_msk.by(dve.l, c + 1))
                if c == 0:
                    dve.e.sem_inc(s_ready.h, 1)
                    continue
                dve.e.wait_ge(s_ready.h, s_ready.by(dve.l, c))
                nc.vector.scalar_tensor_tensor(out=Sst(c + 1), in0=Sst(c), scalar=glast[:, c:c + 1], in1=um,
                                               op0=ALU.mult, op1=ALU.add).then_inc(s_ready.h, 1)
            for tb in range(TB):
                dve.e.wait_ge(at_ps.h, at_ps.by(dve.l, tb + 1))
                for q in range(2):
                    r = slice(64 * q, 64 * q + 64)
                    src = pb[4 + tb % 2][r, :].rearrange("p (h c) -> p h c", h=B_HEADS)[:, :, r]
                    tri = C("tri")[r, :].unsqueeze(1).to_broadcast([64, B_HEADS, B_CHUNK])
                    nc.vector.tensor_tensor(att_diag[r, tb, :, r], src, tri, ALU.mult).then_inc(at_sb.h, 1)
            for pr in range(2):
                col = RL["b_out_norm"]
                dve.e.wait_ge(on_r.h, on_r.by(dve.l, pr + 1))
                nc.vector.scalar_tensor_tensor(out=T(t_o[pr]), in0=T(t_o[pr]), scalar=cur[:, col:col + 1],
                                               in1=T(t_or[pr]), op0=ALU.mult, op1=ALU.mult).then_inc(o_n.h, 1)

        def dve_attention(dve, units):
            U = len(units)
            for i in range(U + 2):
                if i < U:
                    N = (units[i][2] + 1) * P
                    c = i % 4
                    dve.e.wait_ge(att_s.h, att_s.by(dve.l, i + 1))
                    nc.vector.tensor_reduce(nmax[:, c:c + 1], pb[(0, 1, 4, 5)[i % 4]][:, 0:N], AX.X, ALU.max,
                                            negate=True).then_inc(att_max.h, 1)
                if 1 <= i < U + 1:
                    u = i - 1
                    c = u % 4
                    dve.e.wait_ge(att_exp.h, att_exp.by(dve.l, u + 1))
                    if u >= 4:
                        dve.e.wait_ge(att_p.h, att_p.by(dve.l, u - 3))
                    nc.vector.reciprocal(rsum[:, c:c + 1], psum_[:, c:c + 1]).then_inc(att_rs.h, 1)
                if i >= 2:
                    u = i - 2
                    N = (units[u][2] + 1) * P
                    dve.e.wait_ge(att_t.h, att_t.by(dve.l, u + 1))
                    if u >= 2:
                        dve.e.wait_ge(att_o.h, att_o.by(dve.l, u - 1))
                    nc.vector.tensor_copy(pt_buf(u)[:, 0:N], pb[2 + u % 2][:, 0:N]).then_inc(att_pt.h, 1)

        def dve_out_add(dve):
            for dc in range(KD):
                if dc % 2:
                    dve.e.wait_ge(w_used.h, w_used.by(dve.l, len(U_Z) + dc // 2 + 1))
                else:
                    dve.e.wait_ge(out_ps.h, out_ps.by(dve.l, dc // 2 + 1))
                nc.vector.tensor_tensor(x[:, dc, :], pb[dc % 2][:, :], x[:, dc, :], ALU.add).then_inc(x_ready.h, 1)

        def to_r(m):
            nc.vector.tensor_copy(T(RB + m), down_bank(m)).then_inc(r_ready.h, 1)

        def dve_out_r(dve, use0, eo0):
            for dc in range(KD):
                if dc % 2:
                    dve.e.wait_ge(w_used.h, use0 + dc // 2 + 1)
                else:
                    dve.e.wait_ge(eo_ps.h, eo0 + dc // 2 + 1)
                nc.vector.tensor_copy(T(RB + dc), pb[dc % 2][:, :]).then_inc(r_ready.h, 1)

        def dve_post(dve, m, g):
            dve.e.wait_ge(rn_r.h, m + 1)
            for k in range(KD):
                nc.vector.scalar_tensor_tensor(out=T(RB + k), in0=T(RB + k), scalar=g(k), in1=T(RT2),
                                               op0=ALU.mult, op1=ALU.mult).then_inc(r_n.h, 1)
            for k in range(KD):
                dve.e.wait_ge(r_n.h, m * KD + k + 1)
                nc.vector.tensor_tensor(x[:, k, :], x[:, k, :], T(RB + k), ALU.add).then_inc(x_ready.h, 1)

        C1 = 6.28125
        C2 = float(np.float32(np.round((2 * math.pi - C1) * 2 ** 21) / 2 ** 21))
        C3 = float(np.float32(2 * math.pi - C1 - C2))

        def dve_even(dve):
            V = nc.vector
            ts, tt, stt = V.tensor_scalar, V.tensor_tensor, V.scalar_tensor_tensor
            par_n = count(1)
            dve.e.wait_ge(pro_sb.h, 4)
            dve.e.wait_ge(par_act.h, 1)
            tt(c_th, c_aim, c_dt, ALU.mult).then_inc(par.h, 1)
            dve.e.wait_ge(par.h, next(par_n))
            tt(c_ard, c_are, c_dt, ALU.mult).then_inc(par.h, 1)
            dve.e.wait_ge(par.h, next(par_n))
            ts(c_t1, c_th, float(1 / (2 * math.pi)), None, ALU.mult).then_inc(par.h, 1)
            dve.e.wait_ge(par.h, next(par_n))
            ts(c_n, c_t1, MAGIC, None, ALU.add).then_inc(par.h, 1)
            dve.e.wait_ge(par.h, next(par_n))
            ts(c_n, c_n, MAGIC, None, ALU.subtract).then_inc(par.h, 1)
            dve.e.wait_ge(par.h, next(par_n))
            tt(c_fr, c_t1, c_n, ALU.subtract).then_inc(par.h, 1)
            dve.e.wait_ge(par.h, next(par_n))
            ts(c_t2, c_fr, 0.25, None, ALU.is_gt).then_inc(par.h, 1)
            dve.e.wait_ge(par.h, next(par_n))
            stt(c_f2, c_fr, 0.25, c_t2, ALU.add, ALU.subtract).then_inc(par.h, 1)
            dve.e.wait_ge(par.h, next(par_n))
            dve.e.wait_ge(par_act.h, 4)
            tt(c_nre, c_r, c_cos, ALU.mult).then_inc(par.h, 1)
            dve.e.wait_ge(par.h, next(par_n))
            ts(c_nre, c_nre, 1.0, None, ALU.subtract).then_inc(par.h, 1)
            dve.e.wait_ge(par.h, next(par_n))
            tt(c_nim, c_r, c_sin, ALU.mult).then_inc(par.h, 1)
            dve.e.wait_ge(par.h, next(par_n))
            tt(c_den, c_are, c_are, ALU.mult).then_inc(par.h, 1)
            dve.e.wait_ge(par.h, next(par_n))
            tt(c_t1, c_aim, c_aim, ALU.mult).then_inc(par.h, 1)
            dve.e.wait_ge(par.h, next(par_n))
            tt(c_den, c_den, c_t1, ALU.add).then_inc(par.h, 1)
            dve.e.wait_ge(par.h, next(par_n))
            V.reciprocal(c_den, c_den).then_inc(par.h, 1)
            dve.e.wait_ge(par.h, next(par_n))
            tt(c_t1, c_nre, c_are, ALU.mult).then_inc(par.h, 1)
            dve.e.wait_ge(par.h, next(par_n))
            tt(c_t2, c_nim, c_aim, ALU.mult).then_inc(par.h, 1)
            dve.e.wait_ge(par.h, next(par_n))
            tt(c_fre, c_t1, c_t2, ALU.add).then_inc(par.h, 1)
            dve.e.wait_ge(par.h, next(par_n))
            tt(c_fre, c_fre, c_den, ALU.mult).then_inc(par.h, 1)
            dve.e.wait_ge(par.h, next(par_n))
            tt(c_t1, c_nim, c_are, ALU.mult).then_inc(par.h, 1)
            dve.e.wait_ge(par.h, next(par_n))
            tt(c_t2, c_nre, c_aim, ALU.mult).then_inc(par.h, 1)
            dve.e.wait_ge(par.h, next(par_n))
            tt(c_fim, c_t1, c_t2, ALU.subtract).then_inc(par.h, 1)
            dve.e.wait_ge(par.h, next(par_n))
            tt(c_fim, c_fim, c_den, ALU.mult).then_inc(par.h, 1)
            dve.e.wait_ge(par.h, next(par_n))
            dve.e.wait_ge(s5_in.h, 16 * 7)
            bre, bim = [T(e_bst)[:, q * 256:(q + 1) * 256].rearrange("p (j c) -> p j c", c=SSM_C) for q in range(2)]
            sc = [T(e_tmp[1])[:, 0:256], T(e_tmp[1])[:, 256:], T(e_tmp[2])[:, 0:256], T(e_tmp[2])[:, 256:]]
            sc = [t.rearrange("p (j c) -> p j c", c=SSM_C) for t in sc]

            def wide(c):
                return c.unsqueeze(2).to_broadcast([P, NST, SSM_C])
            tt(sc[0], bre, wide(c_fre), ALU.mult).then_inc(par.h, 1)
            dve.e.wait_ge(par.h, next(par_n))
            tt(sc[1], bim, wide(c_fim), ALU.mult).then_inc(par.h, 1)
            dve.e.wait_ge(par.h, next(par_n))
            tt(sc[2], bre, wide(c_fim), ALU.mult).then_inc(par.h, 1)
            dve.e.wait_ge(par.h, next(par_n))
            tt(sc[3], bim, wide(c_fre), ALU.mult).then_inc(par.h, 1)
            dve.e.wait_ge(par.h, next(par_n))
            tt(sc[0], sc[0], sc[1], ALU.subtract).then_inc(par.h, 1)
            dve.e.wait_ge(par.h, next(par_n))
            tt(sc[2], sc[2], sc[3], ALU.add).then_inc(par.h, 1)
            dve.e.wait_ge(par.h, next(par_n))
            half = C("half16").rearrange("p (q c) -> p q c", q=2).unsqueeze(1).to_broadcast([P, NST, 2, SSM_C])
            for src, dst in ((sc[0], e_ere), (sc[2], e_eim)):
                tt(T(dst).rearrange("p (j q c) -> p j q c", j=NST, q=2),
                        src.unsqueeze(2).to_broadcast([P, NST, 2, SSM_C]), half, ALU.mult).then_inc(par.h, 1)
                dve.e.wait_ge(par.h, next(par_n))
            assert next(par_n) == PAR_E + 1
            tab_n = count(1)
            ang, rnd, red = T(e_tmp[1]), T(e_tmp[2]), T(e_tmp[3])
            for q in range(2):
                if q == 0:
                    V.tensor_copy(ang, T(e_pos).bitcast(I32)).then_inc(tab.h, 1)
                    dve.e.wait_ge(tab.h, next(tab_n))
                    ts(ang, ang, C("freq"), None, ALU.mult).then_inc(tab.h, 1)
                    dve.e.wait_ge(tab.h, next(tab_n))
                    ts(rnd, ang, float(1 / (2 * math.pi)), MAGIC, ALU.mult, ALU.add).then_inc(tab.h, 1)
                    dve.e.wait_ge(tab.h, next(tab_n))
                else:
                    ts(rnd, ang, float(1 / (2 * math.pi)), 0.25, ALU.mult, ALU.add).then_inc(tab.h, 1)
                    dve.e.wait_ge(tab.h, next(tab_n))
                    ts(rnd, rnd, MAGIC, None, ALU.add).then_inc(tab.h, 1)
                    dve.e.wait_ge(tab.h, next(tab_n))
                ts(rnd, rnd, MAGIC, None, ALU.subtract).then_inc(tab.h, 1)
                dve.e.wait_ge(tab.h, next(tab_n))
                if q:
                    dve.e.wait_ge(tab_sin.h, 1)
                stt(red, rnd, -C1, ang, ALU.mult, ALU.add).then_inc(tab.h, 1)
                dve.e.wait_ge(tab.h, next(tab_n))
                stt(red, rnd, -C2, red, ALU.mult, ALU.add).then_inc(tab.h, 1)
                dve.e.wait_ge(tab.h, next(tab_n))
                stt(red, rnd, -C3, red, ALU.mult, ALU.add).then_inc(tab.h, 1)
                dve.e.wait_ge(tab.h, next(tab_n))
                if q:
                    ts(red, red, float(np.float32(math.pi / 2)), None, ALU.add).then_inc(tab.h, 1)
                    dve.e.wait_ge(tab.h, next(tab_n))
                lim = float(np.nextafter(np.float32(math.pi), np.float32(0)))
                ts(red, red, lim, -lim, ALU.min, ALU.max).then_inc(tab.h, 1)
                dve.e.wait_ge(tab.h, next(tab_n))
            dve.e.wait_ge(tab_sin.h, 2)
            cw = C("half16").unsqueeze(1).to_broadcast([P, NST, 2 * SSM_C])

            def tiles(t):
                return t.rearrange("p (j c) -> p j c", j=NST)
            dve.e.wait_ge(bc_ps.h, 4)
            dve.e.wait_ge(bt_sb.h, 2)
            tt(tiles(T(e_cre)), tiles(pb[4][:, :]), cw, ALU.mult).then_inc(cb_sb.h, 1)
            tt(tiles(T(e_cin)), tiles(pb[5][:, :]), cw, ALU.mult).then_inc(cb_sb.h, 1)
            dve.e.wait_ge(cb_sb.h, 2)
            ts(T(e_crn), T(e_cre), -1.0, None, ALU.mult).then_inc(cb_sb.h, 1)
            ts(T(e_cin), T(e_cin), -1.0, None, ALU.mult).then_inc(cb_sb.h, 1)

            def angles(j):
                dve.e.wait_ge(s5_rnd.h, 2 * j + 2)
                if j >= 2:
                    dve.e.wait_ge(s5_trig.h, 2 * (j - 2) + 2)
                stt(s5_d[j % 2], C("iota"), c_fr[:, j:j + 1], s5_n[j % 2], ALU.mult, ALU.subtract).then_inc(s5_frac.h, 1)
                dve.e.wait_ge(s5_frac.h, j + 1)
                dve.e.wait_ge(s5_wrap.h, j + 1)
                stt(s5_d2[j % 2], s5_d[j % 2], 0.25, s5_n[j % 2], ALU.add, ALU.subtract).then_inc(s5_quart.h, 1)

            def rotate_in(j):
                a = s5_a[j % 3]
                dve.e.wait_ge(bu_ps.h, j + 1)
                dve.e.wait_ge(s5_trig.h, 2 * j + 2)
                if j >= 3:
                    dve.e.wait_ge(yy_ps.h, j - 2)
                if j == 2:
                    dve.e.wait_ge(tab_sin.h, 2)
                b = [pb[2 + 2 * (j % 2) + q][:, :] for q in range(2)]
                tt(a[0], b[0], s5_cos[j % 3], ALU.mult)
                tt(a[1], b[1], s5_sin[j % 3], ALU.mult)
                tt(a[2], b[1], s5_cos[j % 3], ALU.mult)
                tt(a[3], b[0], s5_sin[j % 3], ALU.mult).then_inc(s5_rot.h, 1)

            def scan(j):
                a = s5_a[j % 3]
                r = c_r[:, j:j + 1].to_broadcast([P, SEQ])
                dve.e.wait_ge(s5_x.h, 2 * j + 2)
                V.tensor_tensor_scan(a[1], r, a[0], 0.0, ALU.mult, ALU.add).then_inc(s5_g.h, 1)
                V.tensor_tensor_scan(a[3], r, a[2], 0.0, ALU.mult, ALU.add).then_inc(s5_g.h, 1)
                dve.e.wait_ge(s5_g.h, 2 * j + 1)
                tt(a[0], a[1], s5_cos[j % 3], ALU.mult)
                tt(a[1], a[1], s5_sin[j % 3], ALU.mult).then_inc(s5_p.h, 1)

            def skip(i):
                dve.e.wait_ge(yy_ps.h, 4 * i + 4)
                dcol = R2["s5_d_2"] + i
                stt(T(e_u + i), T(e_u + i), col2[:, dcol:dcol + 1], pb[6 + i % 2][:, :], ALU.mult, ALU.add).then_inc(s5_y.h, 1)
            angles(0)
            for j in range(NST + 1):
                if j + 1 < NST:
                    angles(j + 1)
                if j < NST:
                    rotate_in(j)
                if j >= 1:
                    scan(j - 1)
                if j >= 6 and (j - 6) % 4 == 0:
                    skip((j - 6) // 4)
            for i in range((NST - 6) // 4 + 1, 4):
                skip(i)
            for i in range(8):
                dve.e.wait_ge(rot_ps.h, i + 1)
                if i >= 2:
                    dve.e.wait_ge(rot_ready.h, i - 1)
                tt(s5_n[i % 2], pb[i % 2][:, :], T(e_sin), ALU.mult).then_inc(rot_s.h, 1)

        def dve_odd(dve):
            V = nc.vector
            ts, tt, stt = V.tensor_scalar, V.tensor_tensor, V.scalar_tensor_tensor
            V.memset(xpad[:, :, 0:LRU_TAPS - 1], 0.0).then_inc(pad_zero.h, 1)
            sp_n = count(1)
            lam = col2[:, R2["rg_lam_2"]:R2["rg_lam_2"] + KD]
            S = [spc[:, i, :] for i in range(8)]
            ts(S[2], lam, -1.0, None, ALU.mult).then_inc(sp_step.h, 1)
            dve.e.wait_ge(sp_step.h, next(sp_n))
            tt(S[0], lam, S[2], ALU.max).then_inc(sp_step.h, 1)
            dve.e.wait_ge(sp_step.h, next(sp_n))
            dve.e.wait_ge(par_act.h, 5)
            ts(S[3], S[1], 2.0, None, ALU.add).then_inc(sp_step.h, 1)
            dve.e.wait_ge(sp_step.h, next(sp_n))
            V.reciprocal(S[3], S[3]).then_inc(sp_step.h, 1)
            dve.e.wait_ge(sp_step.h, next(sp_n))
            tt(S[3], S[1], S[3], ALU.mult).then_inc(sp_step.h, 1)
            dve.e.wait_ge(sp_step.h, next(sp_n))
            tt(S[4], S[3], S[3], ALU.mult).then_inc(sp_step.h, 1)
            dve.e.wait_ge(sp_step.h, next(sp_n))
            ts(S[5], S[4], 1 / 19, None, ALU.mult).then_inc(sp_step.h, 1)
            dve.e.wait_ge(sp_step.h, next(sp_n))
            for o in (17, 15, 13, 11, 9, 7, 5, 3):
                stt(S[5], S[5], 1 / o, S[4], ALU.add, ALU.mult).then_inc(sp_step.h, 1)
                dve.e.wait_ge(sp_step.h, next(sp_n))
            stt(S[5], S[5], 1.0, S[3], ALU.add, ALU.mult).then_inc(sp_step.h, 1)
            dve.e.wait_ge(sp_step.h, next(sp_n))
            ts(S[2], S[2], 0.0, None, ALU.max).then_inc(sp_step.h, 1)
            dve.e.wait_ge(sp_step.h, next(sp_n))
            stt(S[6], S[5], 2.0, S[2], ALU.mult, ALU.add).then_inc(sp_step.h, 1)
            dve.e.wait_ge(sp_step.h, next(sp_n))
            ts(S[7], S[6], -8.0, None, ALU.mult).then_inc(sp_step.h, 1)
            dve.e.wait_ge(sp_step.h, next(sp_n))
            assert next(sp_n) == SP_STEPS + 1
            for k in range(KD):
                dve.e.wait_ge(oz_sb.h, k + 1)
                for j in range(LRU_TAPS):
                    w = R2["rg_conv_w_2"] + j * KD + k
                    w = col2[:, w:w + 1]
                    src = xpad[:, k, j:j + SEQ]
                    if j == 0:
                        b = R2["rg_conv_b_2"] + k
                        ins = ts(T(o_xc + k), src, w, col2[:, b:b + 1], ALU.mult, ALU.add)
                    else:
                        dve.e.wait_ge(cv.h, LRU_TAPS * k + j)
                        ins = stt(T(o_xc + k), src, w, T(o_xc + k), ALU.mult, ALU.add)
                    ins.then_inc(cv.h, 1)
            for k in range(KD):
                dve.e.wait_ge(o_a2.h, k + 1)
                stt(W(k), xpad[:, k, 0:SEQ], 1.0, W(k), ALU.add, ALU.mult).then_inc(o_q.h, 1)
            for k in range(KD):
                dve.e.wait_ge(o_gx.h, k + 1)
                dve.e.wait_ge(o_sqrt.h, k + 1)
                tt(T(o_i + k), T(o_i + k), W(k), ALU.mult).then_inc(o_b.h, 1)
                dve.e.wait_ge(o_b.h, k + 1)
                V.tensor_tensor_scan(T(o_xc + k), T(o_r + k), T(o_i + k), 0.0, ALU.mult, ALU.add).then_inc(o_h.h, 1)

        @block.vector
        def _(e):
            dve = Eng(e)
            e.sem_inc(h_full.h, h_full.start)
            nc.vector.memset(relb[32:64, :], NEG).then_inc(relb_neg.h, 1)
            dve.e.wait_ge(rows_zero.h, 1)
            dve.e.wait_ge(ldt_in.h, 16)
            nc.vector.tensor_copy(rows[32:32 + NST, 3, :].rearrange("j (q p) -> j q p", q=2),
                                  ldt[32:32 + NST, :].unsqueeze(2).to_broadcast([NST, 2, SSM_P])).then_inc(ldt_row.h, 1)
            for k in range(KD):
                dve.e.wait_ge(pro_ps.h, k + 1)
                nc.vector.tensor_copy(x[:, k, :], pb[k % 2][:, :]).then_inc(x_ready.h, 1)
            dve.e.wait_ge(consts_in.h, 16)
            dve.e.wait_ge(pro_sb.h, 4)
            for l in range(DEPTH):
                dve.l = l
                nc.vector.tensor_copy(cur[:, :], col2[:, bass.ds(l * NRL, NRL)]).then_inc(cur_ready.h, 1)
                nc.vector.tensor_copy(cur_dw[:, :], col3[:, bass.ds(l * TAPS * 2, TAPS * 2)]).then_inc(cur_ready.h, 1)
                dve.e.wait_ge(cur_ready.h, cur_ready.by(dve.l, 1))
                for n, s in (("a_q_norm", A_DIM ** -0.5), ("d_q_norm", D_QK ** -0.5)):
                    c = cur[:, RL[n]:RL[n] + 1]
                    nc.vector.tensor_scalar(c, c, float(s), None, ALU.mult).then_inc(cur_ready.h, 1)

                def gain(name):
                    return lambda k: col1[:, bass.ds(l * KD + (R1[name] + k), 1)]
                dve_norm(dve, l * 3, gain("ffn1_norm"), l * 2)
                dve_ffn(dve, l * 2, add_half)
                dve_norm(dve, l * 3 + 1, gain("mix_norm"))
                dve_index(dve)
                dve_conv(dve)
                dve_mixers(dve)
                dve_attention(dve, HYB_UNITS)
                dve_out_add(dve)
                dve_norm(dve, l * 3 + 2, gain("ffn2_norm"), l * 2 + 1)
                dve_ffn(dve, l * 2 + 1, add_half)
            dve.l = DEPTH
            def gain2(name, i):
                return lambda k: col1[:, R1[name] + i * KD + k:R1[name] + i * KD + k + 1]
            n = 3 * DEPTH
            dve_norm(dve, n, gain2("norm_mix_pre_2", 0))
            dve_even(dve)
            dve_attention(dve, E_UNITS)
            dve_out_r(dve, USE_EVEN + len(E_BLOCKS) + 2, 0)
            dve_post(dve, 0, gain2("norm_mix_post_2", 0))
            dve_norm(dve, n + 1, gain2("norm_ffn_pre_2", 0), 2 * DEPTH)
            dve_ffn(dve, 2 * DEPTH, to_r)
            dve_post(dve, 1, gain2("norm_ffn_post_2", 0))
            dve_norm(dve, n + 2, gain2("norm_mix_pre_2", 1))
            dve_odd(dve)
            dve_out_r(dve, USE_ODD + 10, 4)
            dve_post(dve, 2, gain2("norm_mix_post_2", 1))
            dve_norm(dve, n + 3, gain2("norm_ffn_pre_2", 1), 2 * DEPTH + 1)
            dve_ffn(dve, 2 * DEPTH + 1, to_r)
            dve_post(dve, 3, gain2("norm_ffn_post_2", 1))

        def pool_mixers(pool):
            for ct in range(2):
                pool.e.wait_ge(z_sb.h, z_sb.by(pool.l, max(Z_POS[f"ca{ct}"], Z_POS[f"cg{ct}"]) + 1))
                nc.gpsimd.tensor_tensor(hpad[:, ct, TAPS - 1:], T(t_ca[ct]), T(t_cg[ct]), ALU.mult).then_inc(hp_ready.h, 1)
            pool.e.wait_ge(g_exp.h, g_exp.by(pool.l, 3))
            nc.gpsimd.tensor_tensor(W(w_e1n), W(w_e1n), T(t_bk), ALU.mult).then_inc(b_kd.h, 1)
            pool.e.wait_ge(b_kd.h, b_kd.by(pool.l, 1))
            pool.e.wait_ge(g_exp.h, g_exp.by(pool.l, 5))
            for h in range(B_HEADS):
                nc.gpsimd.tensor_scalar(kdm[h], W(w_e1n), C("headcol")[:, h:h + 1], None, ALU.mult).then_inc(b_kd.h, 1)
            for u in range(8):
                dst = T((t_dq + t_dk)[u])[0:D_QK, :]
                pool.e.wait_ge(dn_x.h, dn_x.by(pool.l, u + 1))
                nc.gpsimd.tensor_tensor(dst, T(t_hn[u % 2])[0:D_QK, :], C("cos96")[0:D_QK, :], ALU.mult).then_inc(dr_c.h, 1)
                pool.e.wait_ge(dr_c.h, dr_c.by(pool.l, u + 1))
                pool.e.wait_ge(dr_s.h, dr_s.by(pool.l, u + 1))
                nc.gpsimd.tensor_tensor(dst, dst, T(t_hr[u % 2])[0:D_QK, :], ALU.add).then_inc(dh_ready.h, 1)
            for pr in range(2):
                pool.e.wait_ge(o_n.h, o_n.by(pool.l, pr + 1))
                nc.gpsimd.tensor_tensor(y[:, 2 + pr, :], T(t_o[pr]), T(t_br[pr]), ALU.mult).then_inc(y_b.h, 1)

        def pool_attention(pool, units):
            U = len(units)
            for i in range(U + 1):
                for u in ([0, 1, 2] if i == 0 else [i + 2]):
                    if u in BM and units is HYB_UNITS:
                        _, h, tb = units[u]
                        n = BM.index(u)
                        if n == 0:
                            pool.e.wait_ge(top_done.h, top_done.by(pool.l, 3))
                            pool.e.wait_ge(pro_sb.h, 4 + 2 + A_HEADS)
                        if n >= 3:
                            pool.e.wait_ge(att_s.h, att_s.by(pool.l, BM[n - 3] + 1))
                        nc.gpsimd.tensor_tensor(T(t_bm[n % 3])[:, 0:(tb + 1) * P], bias[:, h, SEQ - (tb + 1) * P:],
                                                score(tb), ALU.add).then_inc(att_bm.h, 1)
                if i >= 1:
                    u = i - 1
                    c = u % 4
                    pool.e.wait_ge(att_rs.h, att_rs.by(pool.l, u + 1))
                    p = p_buf(u)[:, 0:(units[u][2] + 1) * P]
                    nc.gpsimd.tensor_scalar(p, p, rsum[:, c:c + 1], None, ALU.mult).then_inc(att_p.h, 1)

        def pool_even(pool):
            G = nc.gpsimd
            ts, tt = G.tensor_scalar, G.tensor_tensor

            def turns(j):
                if j >= 2:
                    pool.e.wait_ge(s5_quart.h, j - 1)
                ts(s5_n[j % 2], C("iota"), c_fr[:, j:j + 1], MAGIC, ALU.mult, ALU.add).then_inc(s5_rnd.h, 1)
                pool.e.wait_ge(s5_rnd.h, 2 * j + 1)
                ts(s5_n[j % 2], s5_n[j % 2], MAGIC, None, ALU.subtract).then_inc(s5_rnd.h, 1)

            def wrap(j):
                pool.e.wait_ge(s5_frac.h, j + 1)
                ts(s5_n[j % 2], s5_d[j % 2], 0.25, None, ALU.is_gt).then_inc(s5_wrap.h, 1)

            def frame(j):
                a = s5_a[j % 3]
                pool.e.wait_ge(s5_rot.h, j + 1)
                tt(a[0], a[0], a[1], ALU.add).then_inc(s5_x.h, 1)
                tt(a[2], a[2], a[3], ALU.subtract).then_inc(s5_x.h, 1)

            def back(j):
                a = s5_a[j % 3]
                pool.e.wait_ge(s5_g.h, 2 * j + 2)
                tt(a[2], a[3], s5_sin[j % 3], ALU.mult)
                tt(a[3], a[3], s5_cos[j % 3], ALU.mult).then_inc(s5_q.h, 1)
            pool.e.wait_ge(par.h, PAR_E)
            turns(0)
            turns(1)
            wrap(0)
            for j in range(NST + 1):
                if j + 1 < NST:
                    wrap(j + 1)
                if j + 2 < NST:
                    turns(j + 2)
                if j < NST:
                    frame(j)
                if j >= 1:
                    back(j - 1)
            for i in range(8):
                t = T((e_q if i % 2 == 0 else e_k) + i // 2)
                pool.e.wait_ge(rot_ps.h, i + 1)
                tt(t, t, T(e_cos), ALU.mult).then_inc(rot_c.h, 1)
                pool.e.wait_ge(rot_c.h, i + 1)
                pool.e.wait_ge(rot_s.h, i + 1)
                tt(t, t, s5_n[i % 2], ALU.add).then_inc(rot_ready.h, 1)
            for c in range(4):
                pool.e.wait_ge(glu_sb.h, c + 1)
                tt(y[:, 4 + c, :], T(e_u + c), T(e_glu + c), ALU.mult).then_inc(y_ssm.h, 1)

        def pool_odd(pool):
            tt = nc.gpsimd.tensor_tensor
            for k in range(KD):
                pool.e.wait_ge(og_sb.h, KD + k + 1)
                pool.e.wait_ge(cv.h, LRU_TAPS * (k + 1))
                tt(T(o_i + k), T(o_i + k), T(o_xc + k), ALU.mult).then_inc(o_gx.h, 1)
            for k in range(KD):
                pool.e.wait_ge(o_a.h, k + 1)
                tt(xpad[:, k, 0:SEQ], T(o_r + k), T(o_r + k), ALU.mult).then_inc(o_a2.h, 1)
            for k in range(KD):
                pool.e.wait_ge(o_h.h, k + 1)
                tt(y[:, k, :], T(o_xc + k), T(o_gel + k), ALU.mult).then_inc(y_lru.h, 1)

        @block.gpsimd
        def _(e):
            pool = Eng(e)
            nc.gpsimd.memset(rows[:, :, :], 0.0).then_inc(rows_zero.h, 1)
            pool.e.wait_ge(consts_in.h, 16)
            for l in range(DEPTH):
                pool.l = l
                pool.e.wait_ge(cur_ready.h, cur_ready.by(pool.l, 4))
                pool.e.wait_ge(unit_ps.h, 2 * l * UNITS + 2 * NF)
                nc.gpsimd.memset(hpad[:, :, 0:TAPS - 1], 0.0)
                nc.gpsimd.memset(att_diag[:, :, :, :], 0.0).then_inc(zeros_set.h, 1)
                pool_mixers(pool)
                pool_attention(pool, HYB_UNITS)
            pool.l = DEPTH
            pool_even(pool)
            pool_attention(pool, E_UNITS)
            pool_odd(pool)


_NAMES = ["x", "ffn1_norm", "ffn1_gate", "ffn1_up", "ffn1_down", "mix_norm", "w_in", "a_q_norm", "a_k_norm", "rel_bias",
          "b_gate_up", "b_gate_bias", "b_out_norm", "c_dw_w", "c_dw_b", "c_norm", "d_qa_norm", "d_uq", "d_kva_norm",
          "d_ukv", "d_q_norm", "d_k_norm", "w_out", "ffn2_norm", "ffn2_gate", "ffn2_up", "ffn2_down", "positions_2",
          "norm_mix_pre_2", "norm_mix_post_2", "norm_ffn_pre_2", "norm_ffn_post_2", "ev_w_in_2", "ev_w_out_2",
          "s5_a_re_2", "s5_a_im_2", "s5_log_dt_2", "s5_b_re_2", "s5_b_im_2", "s5_c_re_2", "s5_c_im_2", "s5_d_2",
          "s5_w_glu_2", "od_w_in_2", "od_w_out_2", "rg_conv_w_2", "rg_conv_b_2", "rg_w_r_2", "rg_b_r_2", "rg_w_i_2",
          "rg_b_i_2", "rg_lam_2", "ffn_w_gate_2", "ffn_w_up_2", "ffn_w_down_2"]


def kernel(**inputs):
    import concourse.bacc as bacc
    from concourse.bass_utils import run_bass_kernel_spmd

    nc = bacc.Bacc("TRN2", target_bir_lowering=False, num_devices=1)
    arrays = {"in_" + n: np.ascontiguousarray(inputs[n]) for n in _NAMES}
    consts = shape_constants()
    arrays["in_consts"] = np.ascontiguousarray(np.concatenate(list(consts.values()), axis=1))
    I = {n[3:]: nc.dram_tensor(n, a.shape, mybir.dt.from_np(a.dtype), kind="ExternalInput").ap()
         for n, a in arrays.items()}
    out = nc.dram_tensor("out_x", (1, SEQ, D), F32, kind="ExternalOutput").ap()
    program(nc, I, out)
    r = run_bass_kernel_spmd(nc, [arrays], core_ids=[0])
    return r.results[0]["out_x"]
```

```python
import math
from itertools import count

import numpy as np

import concourse.bass as bass
from concourse import mybir
from contextlib import ExitStack

F32 = mybir.dt.float32
F32R = mybir.dt.float32r
I32 = mybir.dt.int32
ALU = mybir.AluOpType
ACT = mybir.ActivationFunctionType
AX = mybir.AxisListType

P = 128
SEQ = 512
TB = SEQ // P
D = 1024
KD = D // P
FF = 2816
NF = FF // P
DEPTH = 2
NEG = -1e30
SENTINEL = -3e38
EPS = 1e-6
TOPK = min(256, SEQ // 4)
A_HEADS, A_DIM = 4, 64
IDX_HEADS, IDX_DIM = 8, 32
B_HEADS, B_KEY, B_VAL, B_CHUNK, B_RANK = 4, 32, 64, 64, 16
NCH = SEQ // B_CHUNK
TAPS = 31
D_HEADS, D_NOPE, D_ROPE, D_V = 4, 64, 32, 64
D_QK = D_NOPE + D_ROPE
E_HEADS, E_DIM, E_ROPE = 8, 64, 16
SSM_G, SSM_P, SSM_C = 32, 64, 16
NST = SSM_G * SSM_P // P
LRU_TAPS = 4
BIAS_N = 640

_w = dict(aq=256, ak=256, av=256, iq=256, ik=32, iw=8, bq=128, bk=128, bv=256, bg=16, br=256,
          ca=256, cg=256, dcq=256, dckv=128, dkpe=32)
WCOL, _at = {}, 0
for _n, _c in _w.items():
    WCOL[_n] = _at
    _at += _c



def shape_constants():
    f = np.float32
    out = {}
    p = np.arange(P)
    out["ident"] = np.eye(P, dtype=f)
    out["blk64"] = ((p[:, None] // 64) == (p[None] // 64)).astype(f) / f(64)
    out["mean1024"] = np.full((P, P), 1 / 1024, f)
    out["mean256"] = np.full((P, P), 1 / 256, f)
    out["mean128"] = np.full((P, P), 1 / 128, f)
    m96 = np.zeros((P, D_QK), f)
    m96[:D_QK] = f(1) / f(D_QK)
    out["mean96"] = m96
    half = D_ROPE // 2
    r96 = np.zeros((P, D_QK), f)
    for i in range(half):
        r96[D_NOPE + half + i, D_NOPE + i] = -1
        r96[D_NOPE + i, D_NOPE + half + i] = 1
    out["rot96"] = r96
    eh = E_ROPE // 2
    r128 = np.zeros((P, P), f)
    for b in range(0, P, E_DIM):
        for i in range(eh):
            r128[b + eh + i, b + i] = -1
            r128[b + i, b + eh + i] = 1
    out["rot128"] = r128
    out["causal"] = np.where(p[None] > p[:, None], f(NEG), f(0)).astype(f)
    out["tri"] = (p[:, None] % B_CHUNK <= np.arange(B_CHUNK)[None]).astype(f)
    out["headblk"] = (p[:, None] // B_KEY == np.arange(B_HEADS * B_VAL)[None] // B_VAL).astype(f)
    dist = p[:, None] - (np.arange(SEQ)[None] - (SEQ - P))
    n = (((dist >= 0) & (dist <= 128)).astype(int) + ((dist >= 0) & (dist % 4 == 0)) + ((dist >= 0) & (dist % 16 == 0)))
    out["lnmult"] = np.where(n > 0, np.log(np.maximum(n, 1)), NEG).astype(f)
    t = np.arange(SEQ, dtype=f)
    fr = (f(10000.0) ** (-np.arange(half, dtype=f) / f(half))).astype(f)
    ang = (t[None] * fr[:, None]).astype(f)
    c96, s96 = np.zeros((P, SEQ), f), np.zeros((P, SEQ), f)
    c96[:D_NOPE] = 1
    for o in (D_NOPE, D_NOPE + half):
        c96[o:o + half], s96[o:o + half] = np.cos(ang), np.sin(ang)
    out["cos96"], out["sin96"] = c96, s96
    cm = np.ones((P, SEQ), f)
    cm[:, ::B_CHUNK] = 0
    out["chunkmask"] = cm
    out["iota"] = np.broadcast_to(t, (P, SEQ)).copy()
    out["headcol"] = (p[:, None] // B_KEY == np.arange(B_HEADS)[None]).astype(f)
    inv = (f(500000.0) ** (-(np.arange(eh, dtype=f) * f(2.0) / f(E_ROPE)))).astype(f)
    out["freq"] = np.where(p % E_DIM < E_ROPE, inv[(p % E_DIM) % eh], 0).astype(f)[:, None]
    out["eps"] = np.full((P, 1), EPS, f)
    out["halfpi"] = np.full((P, 1), math.pi / 2, f)
    hot = np.zeros((P, BIAS_N), f)
    for x in range(BIAS_N):
        d = SEQ - 1 - x
        if d < 0:
            hot[32, x] = 1
        elif d < 16:
            hot[d, x] = 1
        else:
            hot[min(16 + int(f(np.log(f(d) / f(16)) / f(math.log(128 / 16)) * f(16))), 31), x] = 1
    out["half16"] = (p[:, None] // SSM_P == np.arange(2 * SSM_C)[None] // SSM_C).astype(f)
    out["flip"] = np.eye(P, dtype=f)[::-1].copy()
    out["onehot"] = hot
    return out


CONST_COLS, _at = {}, 0
for _n, _v in shape_constants().items():
    CONST_COLS[_n] = (_at, _v.shape[1])
    _at += _v.shape[1]
CONST_W = _at
PRO_W = BIAS_N + P

ROWS1 = [("ffn1_norm", 2 * KD), ("mix_norm", 2 * KD), ("ffn2_norm", 2 * KD),
         ("norm_mix_pre_2", 2 * KD), ("norm_mix_post_2", 2 * KD), ("norm_ffn_pre_2", 2 * KD),
         ("norm_ffn_post_2", 2 * KD)]
LAYER_ROWS = [("a_q_norm", 1), ("a_k_norm", 1), ("b_gate_bias", 1), ("b_out_norm", 1), ("c_dw_b", 2), ("c_norm", 2),
              ("d_qa_norm", 2), ("d_kva_norm", 1), ("d_q_norm", 1), ("d_k_norm", 1)]
ROWS2 = [("s5_d_2", 4), ("rg_conv_b_2", 8), ("rg_b_r_2", 8), ("rg_b_i_2", 8), ("rg_lam_2", 8),
         ("rg_conv_w_2", 8 * LRU_TAPS)]


def row_starts(rows):
    out, at = {}, 0
    for n, c in rows:
        out[n] = at
        at += c
    return out, at


R1, NR1 = row_starts(ROWS1)
RL, NRL = row_starts(LAYER_ROWS)
R2, NR2 = row_starts([("layers", DEPTH * NRL)] + ROWS2)
NR3 = DEPTH * TAPS * 2

Z_LABELS = ["iq0", "iq1", "ik", "misc", "aq0", "aq1", "ak0", "ak1", "br0", "br1", "cg0", "cg1", "ca0", "ca1", "dcq0", "dcq1",
            "dckv", "bq", "bk"]
Z_TOK = KD // 2
NZU = len(Z_LABELS) + Z_TOK
MISC = [(0, "bg", B_RANK), (B_RANK, "bg", B_RANK), (32, "iw", IDX_HEADS), (40, "dkpe", 24), (64, "dkpe", D_ROPE),
        (96, "dkpe", D_ROPE)]
MISC_W = 64 + D_ROPE
Z_LOADS = [{"ik": P // IDX_DIM, "misc": len(MISC)}.get(_x, 1) for _x in Z_LABELS] + [2] * Z_TOK
IDX_UNITS = [(tb, h) for tb in (3, 2, 1) for h in range(IDX_HEADS)]
Z_SEQ = []
_left = list(IDX_UNITS)
for _u, _label in enumerate(Z_LABELS):
    Z_SEQ.append(("z", _u, _label))
    if _label == "aq0":
        Z_SEQ.append(("iw",))
    if _u >= 4:
        for _ in range(2):
            if _left:
                Z_SEQ.append(("idx",) + _left.pop(0))
Z_SEQ.append(("tok",))
assert not _left
Z_POS = {t[2]: n for n, t in enumerate(Z_SEQ) if t[0] == "z"}
NZ = len(Z_SEQ)
NIDX = len(IDX_UNITS)

E_BLOCKS = [("u", 1536), ("u", 1792), ("q", 0), ("q", 256), ("k", 512), ("k", 768), ("v", 1024), ("v", 1280)]
E_SEQ = []
_bu = _yy = 0
for _b, (_n, _c) in enumerate(E_BLOCKS):
    for _c in range(2):
        E_SEQ.append(("z", _b, _c, _n, 2 * (_b % 2) + _c))
        if len(E_SEQ) == 6:
            E_SEQ.append(("prep",))
        if _b >= 3:
            if _bu < NST:
                E_SEQ.append(("bu", _bu))
                _bu += 1
            if _bu >= 4:
                E_SEQ.append(("yy", _yy))
                _yy += 1
while _yy < NST:
    if _bu < NST:
        E_SEQ.append(("bu", _bu))
        _bu += 1
    E_SEQ.append(("yy", _yy))
    _yy += 1
E_Z = [t for t in E_SEQ if t[0] == "z"]
MAGIC = float(1.5 * 2 ** 23)

USE_ODD = len(E_BLOCKS) + 2
DMA_ODD = [USE_ODD // 2] * 2
SLOTS = 4
UNITS = 3 * NF
assert NF % 2 == 0 and (2 * NF) % SLOTS == 0 and KD == 8


class Stage:

    def __init__(self, before, loads, result, ffn):
        self.loads, self.result, self.is_ffn = loads, result, ffn
        self.units, self.splits, self.results, self.ffns, self.slots, self.in_turn = before

    def after(self):
        n = len(self.loads)
        return (self.units + n, self.splits + 1, self.results + self.result, self.ffns + self.is_ffn,
                [self.slots[q] + sum(self.loads[q::SLOTS]) for q in range(SLOTS)], n % SLOTS == 0)

    def loaded(self, n):
        q = n % SLOTS
        return 16 * (self.slots[q] + sum(self.loads[q:n + 1:SLOTS]))

    def free(self, q):
        return self.units - SLOTS + 1 + q if self.in_turn else self.units


STAGES, _before = {}, (0, 0, 0, 0, [0] * SLOTS, False)
for _n in [(_k, _l) for _l in range(DEPTH) for _k in ("ffn1", "in", "out", "ffn2")] + [
        ("out", "even"), ("ffn", "even"), ("in", "odd"), ("out", "odd"), ("ffn", "odd")]:
    _ffn = _n[0].startswith("ffn")
    _loads = Z_LOADS if _n[0] == "in" and _n[1] != "odd" else [1] * (UNITS if _ffn else 2 * KD if _n[0] == "in" else KD)
    STAGES[_n] = Stage(_before, _loads, _n[0] != "in", _ffn)
    _before = STAGES[_n].after()
Z_STAGES = [STAGES["in", _l] for _l in range(DEPTH)]
Y_HYB, Y_EVEN, Y_ODD = [2, 3, 4, 5, 6, 7, 0, 1], [4, 5, 6, 7, 0, 1, 2, 3], list(range(KD))
X1 = (1 + 3 * DEPTH) * KD

IDX_POS = [n for n, t in enumerate(Z_SEQ) if t[0] == "idx"]
N_ROW_DMAS = len(ROWS1) + DEPTH * (len(LAYER_ROWS) + 3) + len(ROWS2) + 1 + 2


class Sem:

    def __init__(self, h, per, start):
        self.h, self.per, self.start = h, per, start

    def by(self, layer, k):
        return self.start + layer * self.per + k


class Eng:

    def __init__(self, e):
        self.e, self.l = e, 0


def program(nc, I, out):
    ctx = ExitStack()
    with ctx:
        at = {}

        def sb(name, shape, dt=F32):
            at[name] = -(-nc.sbuf_base // 32) * 32
            return ctx.enter_context(nc.sbuf_tensor(name, shape, dt))

        def over(name, shape, base, skip=0):
            return nc.alloc_sbuf_tensor_at(name, shape, F32R, offset=at[base] + skip)

        def sem(name, per=0, start=0):
            return Sem(ctx.enter_context(nc.semaphore(name)), per, start)

        x = sb("x", [P, KD, SEQ])
        xn = sb("xn", [P, KD, SEQ])
        y = xn
        wring = sb("wring", [P, 2, KD, 256])
        scratch = sb("scratch", [P, 11, SEQ])
        cst = sb("cst", [P, CONST_W - PRO_W])
        bias = sb("bias", [P, A_HEADS, SEQ])
        rows = sb("rows", [P, 4, P])
        col1 = sb("col1", [P, NR1])
        col2 = sb("col2", [P, NR2])
        col3 = sb("col3", [P, NR3])
        cur = sb("cur", [P, NRL])
        cur_dw = sb("cur_dw", [P, TAPS * 2])
        relb = sb("relb", [64, A_HEADS])
        hpad = sb("hpad", [P, 2, TAPS - 1 + SEQ])
        att_diag = sb("att_diag", [P, TB, B_HEADS, P])
        sb("xn_more", [P, 2, SEQ])
        small = sb("small", [P, 64])
        arena = sb("arena", [P, 46, SEQ])
        w_uq = arena[:, 43:45, 0:384]
        w_ukv = arena[:, 45, :]
        Z_HI = 36
        wunit = wring[:, :, :, :].rearrange("p s k c -> p (s k c)").rearrange("p (u c) -> p u c", u=SLOTS)
        w_lo = over("w_lo", [P, SLOTS, KD, P], "wring")
        w_hi = over("w_hi", [P, SLOTS, KD, P], "scratch")
        xn_lo = over("xn_lo", [P, KD, SEQ], "xn")
        xn_hi = over("xn_hi", [P, KD, SEQ], "hpad")
        z_hi = over("z_hi", [P, KD, SEQ], "arena", Z_HI * SEQ * 4)
        h_hi = over("h_hi", [P, NF, SEQ], "arena")
        h_lo = over("h_lo", [P, NF, SEQ], "arena", NF * SEQ * 4)
        H_LO = NF
        gup = sb("gup", [B_RANK, P])
        pb = [ctx.enter_context(nc.psum_tensor(f"bank{i}", [P, SEQ], F32)) for i in range(8)]
        bias_dram = nc.dram_tensor("bias_by_distance", [A_HEADS, BIAS_N], F32, kind="Internal")

        def C(name):
            a, w = CONST_COLS[name]
            if a >= CONST_W - PRO_W:
                a -= CONST_W - PRO_W
                return arena[:, 12:14, :].rearrange("p t c -> p (t c)")[:, a:a + w]
            return cst[:, a:a + w]

        def T(n):
            return arena[:, n, :]

        def W(n):
            return scratch[:, n, :]

        ident = C("ident")
        SQ, RT = 22, 30
        sg = arena[:, 44:46, :]
        t_iq, t_ik, t_aq, t_ak, t_av = [0, 1], 2, [3, 4], [5, 6], 7
        t_bq, t_bk, t_bv, t_br, t_ca, t_cg = 9, 10, 11, [13, 14], [15, 16], [17, 18]
        t_dcq, t_dckv, t_kpe, t_dv, t_dq, t_dk = [19, 20], 21, 22, 23, [25, 26, 27, 28], [29, 30, 31, 32]
        t_gl, t_iw = 24, 45
        t_zsq = [25, 26, 27, 28, 29, 30, 31]
        t_zr = [32, 36, 37, 39, 40, 41]
        t_hc, t_csq, t_cr = [15, 16], [17, 18], 19
        t_hraw, t_hsq, t_hr, t_hn = [0, 1], [2, 36], [37, 39], [40, 41]
        t_ab, t_qe, t_kdt, t_um = 42, 38, 42, 9
        t_o, t_osq, t_or = [10, 20], [17, 18], [2, 36]
        t_bm = [0, 1, 40]
        t_score = 33
        sc_at = {3: 0, 2: 512, 1: 896}
        scores = arena[:, 33:36, :].rearrange("p t c -> p (t c)")

        w_mn, w_la, w_e1, w_e1n, w_e2 = 9, 10, 4, 5, 6
        idx_r = [W(8), W(9), W(10), T(44)]
        kdm = [W(7), W(8), W(9), W(10)]

        def Sst(c):
            return scratch[:, (c - 1) // 2, ((c - 1) % 2) * 256:((c - 1) % 2) * 256 + 256]

        def p_buf(units, u):
            return T(((11, 12, 21) if units is HYB_UNITS else (34, 35, 36))[u % 3])

        def pt_buf(units, u):
            return T(((19, 22) if units is HYB_UNITS else (37, 39))[u % 2])

        def score(tb):
            return scores[:, sc_at[tb]:sc_at[tb] + (tb + 1) * P]

        wA = small[:, 0:32]
        m8 = small[:, 32:40]
        nmax, psum_, rsum = small[:, 40:44], small[:, 44:48], small[:, 48:52]
        glast = small[:, 52:60]

        e_q, e_k, e_v, e_u, e_cos, e_sin = 0, 4, 8, 12, 16, 17
        e_tmp = [18, 19, 20, 21]
        e_bst, e_cst, e_btr, e_bti, e_ere, e_eim = 38, 39, 41, 42, 43, 44
        e_cre, e_crn, e_cin = 45, 38, 20
        e_pos = 45
        s5_n, s5_d, s5_d2 = [T(22), T(23)], [T(24), T(25)], [T(26), T(27)]
        s5_sin, s5_cos = [T(28), T(29), T(30)], [T(31), T(32), T(33)]
        s5_a = [[T(34), T(35), T(36), T(37)], [W(0), W(1), W(2), W(3)], [W(9), W(10), T(18), T(19)]]
        s5col = sb("s5col", [P, 20, NST])
        (c_are, c_aim, c_ldt, c_dt, c_ard, c_th, c_r, c_fr, c_n, c_sin, c_cos, c_nre, c_nim, c_den, c_fre, c_fim,
         c_t1, c_t2, c_f2) = [s5col[:, i, :] for i in range(19)]
        ldt = sb("ldt", [64, 2])
        spc = sb("spc", [P, 8, KD])
        PAR_E, SP_STEPS, e_glu = 31, 19, 28
        RB, RT2 = 30, 38
        xpad = arena[:, 0:9, :].rearrange("p t c -> p (t c)")[:, 0:KD * (LRU_TAPS - 1 + SEQ)].rearrange(
            "p (k c) -> p k c", k=KD)
        o_xc, o_r, o_i, o_gel = 9, 17, 25, 33
        o_fac = nc.alloc_sbuf_tensor_at("o_fac", [P, KD, SEQ], F32, offset=at["hpad"])

        consts_in = sem("consts_in")
        rows_in = sem("rows_in")
        rows_zero = sem("rows_zero")
        token_dma = sem("token_dma")
        pro_ps = sem("pro_ps")
        pro_sb = sem("pro_sb")
        relb_in = sem("relb_in")
        relb_neg = sem("relb_neg")
        bias_dma = sem("bias_dma")
        zeros_set = sem("zeros_set", 1)
        x_ready = sem("x_ready", 24)
        sq_done = sem("sq_done", 24)
        norm_ps = sem("norm_ps", 3)
        norm_ln = sem("norm_ln", 3)
        norm_r = sem("norm_r", 3)
        xn_ready = sem("xn_ready", 24)
        w_in_sem = [sem("w_loaded0"), sem("w_loaded1")]
        w_used = sem("w_used")
        u_in = [sem(f"u_loaded{q}") for q in range(SLOTS)]
        u_hi = sem("u_hi")
        u_lo = sem("u_lo")
        unit_ps = sem("unit_ps")
        xn_hi_ready = sem("xn_hi_ready")
        xn_lo_ready = sem("xn_lo_ready")
        sg_ready = sem("sg_ready", 0, 2)
        h_full = sem("h_full", 0, 2)
        h_hi_ready = sem("h_hi_ready")
        h_lo_ready = sem("h_lo_ready")
        down_ps = sem("down_ps")
        z_ps = sem("z_ps", 1)
        idx_ps = sem("idx_ps", NIDX)
        z_sb = sem("z_sb", NZ)
        zsq = sem("zsq", 7)
        idx_acc = sem("idx_acc", NIDX)
        idx_mask = sem("idx_mask", 3)
        top_max = sem("top_max", 3 * TOPK // 8)
        top_rep = sem("top_rep", 3 * TOPK // 8)
        top_done = sem("top_done", 3)
        cur_ready = sem("cur_ready", 4)
        smallw_in = sem("smallw_in", 16 * 2)
        gup_in = sem("gup_in", 16)
        hp_ready = sem("hp_ready", 2)
        conv = sem("conv", TAPS * 2)
        conv_sq = sem("conv_sq", 2)
        mn_ps = sem("mn_ps", 7)
        mn_ln = sem("mn_ln", 7)
        mn_r = sem("mn_r", 7)
        mn_x = sem("mn_x", 9)
        y_conv = sem("y_conv", 2)
        gate_log_ps = sem("gate_log_ps", 1)
        g_abs = sem("g_abs", 4)
        g_min = sem("g_min", 1)
        g_b = sem("g_b", 6)
        g_exp = sem("g_exp", 5)
        b_qk = sem("b_qk", 3)
        b_kd = sem("b_kd", 1 + B_HEADS)
        kt_ps = sem("kt_ps", 1)
        kt_sb = sem("kt_sb", 1)
        u_ps = sem("u_ps", NCH - 1)
        u_msk = sem("u_msk", NCH - 1)
        s_ready = sem("s_ready", NCH - 1)
        at_ps = sem("at_ps", TB)
        at_sb = sem("at_sb", 2 * TB)
        o_ps = sem("o_ps", 2)
        o_sq = sem("o_sq", 2)
        on_ps = sem("on_ps", 2)
        on_ln = sem("on_ln", 2)
        on_r = sem("on_r", 2)
        o_n = sem("o_n", 2)
        y_b = sem("y_b", 2)
        dv_ps = sem("dv_ps", 2)
        dv_sb = sem("dv_sb", 2)
        dh_ps = sem("dh_ps", 8)
        dh_sq = sem("dh_sq", 8)
        dn_ps = sem("dn_ps", 8)
        dn_ln = sem("dn_ln", 8)
        dn_r = sem("dn_r", 8)
        dn_x = sem("dn_x", 8)
        dr_ps = sem("dr_ps", 8)
        dr_s = sem("dr_s", 8)
        dr_c = sem("dr_c", 8)
        dh_ready = sem("dh_ready", 8)
        att_bm = sem("att_bm", 12)
        att_s = sem("att_s", 32)
        att_max = sem("att_max", 32)
        att_exp = sem("att_exp", 32)
        att_rs = sem("att_rs", 32)
        att_p = sem("att_p", 32)
        att_t = sem("att_t", 32)
        att_pt = sem("att_pt", 32)
        att_o = sem("att_o", 32)
        y_att = sem("y_att", 4)
        s5_in = sem("s5_in")
        ldt_in = sem("ldt_in")
        ldt_row = sem("ldt_row")
        tab = sem("tab")
        tab_sin = sem("tab_sin")
        par = sem("par")
        par_act = sem("par_act")
        bc_ps = sem("bc_ps")
        bt_sb = sem("bt_sb")
        cb_sb = sem("cb_sb")
        ez_ps = sem("ez_ps")
        ez_sb = sem("ez_sb")
        s5_rnd = sem("s5_rnd")
        s5_frac = sem("s5_frac")
        s5_wrap = sem("s5_wrap")
        s5_quart = sem("s5_quart")
        s5_trig = sem("s5_trig")
        bu_ps = sem("bu_ps")
        s5_rot = sem("s5_rot")
        s5_x = sem("s5_x")
        s5_g = sem("s5_g")
        s5_p = sem("s5_p")
        s5_q = sem("s5_q")
        yy_ps = sem("yy_ps")
        s5_y = sem("s5_y")
        s5_gelu = sem("s5_gelu")
        rot_ps = sem("rot_ps")
        rot_s = sem("rot_s")
        rot_c = sem("rot_c")
        rot_ready = sem("rot_ready")
        glu_ps = sem("glu_ps")
        glu_sb = sem("glu_sb")
        y_ssm = sem("y_ssm")
        r_ready = sem("r_ready")
        rsq = sem("rsq")
        rn_ps = sem("rn_ps")
        rn_ln = sem("rn_ln")
        rn_r = sem("rn_r")
        r_n = sem("r_n")
        pad_zero = sem("pad_zero")
        oz_sb = sem("oz_sb")
        cv = sem("cv")
        og_ps = sem("og_ps")
        og_sb = sem("og_sb")
        sp_step = sem("sp_step")
        o_th = sem("o_th")
        o_a = sem("o_a")
        o_a2 = sem("o_a2")
        o_q = sem("o_q")
        o_sqrt = sem("o_sqrt")
        o_gx = sem("o_gx")
        o_b = sem("o_b")
        o_h = sem("o_h")
        y_lru = sem("y_lru")
        fin_ps = sem("fin_ps")
        fin_sb = sem("fin_sb")

        D_UNITS = [("D", h, tb) for h in range(D_HEADS) for tb in range(TB)]
        A_UNITS = [("A", h, tb) for h in range(A_HEADS) for tb in range(TB)]
        HYB_UNITS = D_UNITS + A_UNITS
        BM = [u for u, (m, h, tb) in enumerate(HYB_UNITS) if m == "A" and tb > 0]

        block = ctx.enter_context(nc.Block())

        def sp_free(sp, st, q, used):
            if used is not None:
                sp.e.wait_ge(w_used.h, used - 1 + q // 2)
            elif st.units:
                sp.e.wait_ge(unit_ps.h, st.free(q))

        def sp_ffn(sp, st, gate, up, down):
            gu = [w.rearrange("(k p) n -> p k n", p=P) for w in (gate, up)]
            d = down.rearrange("(j p) n -> p j n", p=P)
            for q in range(SLOTS):
                sp_free(sp, st, q, None)
                sp.e.dma_start(wunit[:, q, :].rearrange("p (k c) -> p k c", k=KD),
                               gu[q % 2][:, :, (q // 2) * P:(q // 2 + 1) * P]).then_inc(u_in[q].h, 16)
            with sp.e.Fori(0, NF // 2 - 1) as i:
                for q in range(SLOTS):
                    sp.e.wait_ge(unit_ps.h, st.units + SLOTS * i + (q + 1))
                    sp.e.dma_start(wunit[:, q, :].rearrange("p (k c) -> p k c", k=KD),
                                   gu[q % 2][:, :, bass.ds(i * 2 * P + (2 + q // 2) * P, P)]).then_inc(u_in[q].h, 16)
            u0 = st.units + 2 * NF - SLOTS
            with sp.e.Fori(0, NF // SLOTS) as i:
                for q in range(SLOTS):
                    sp.e.wait_ge(unit_ps.h, u0 + SLOTS * i + (q + 1))
                    sp.e.dma_start(wunit[:, q, :].unsqueeze(1), d[:, bass.ds(SLOTS * i + q, 1), :]).then_inc(u_in[q].h, 16)
            for k in range(NF // SLOTS * SLOTS, NF):
                sp.e.wait_ge(unit_ps.h, u0 + k + 1)
                sp.e.dma_start(wunit[:, k % SLOTS, :], d[:, k, :]).then_inc(u_in[k % SLOTS].h, 16)

        def sp_z(sp, st, win):
            for n in range(NZU):
                if n < SLOTS:
                    sp_free(sp, st, n, None)
                else:
                    sp.e.wait_ge(unit_ps.h, st.units + n - SLOTS + 1)
                u, loaded = wunit[:, n % SLOTS, :], u_in[n % SLOTS].h
                tiles = u.rearrange("p (k c) -> p k c", k=KD)
                label = Z_LABELS[n] if n < len(Z_LABELS) else "tok"
                if label == "tok":
                    k = 2 * (n - len(Z_LABELS))
                    for q, name in enumerate(("bv", "av")):
                        sp.e.dma_start(u.rearrange("p (k c) -> p k c", k=2)[:, :, q * 256:(q + 1) * 256],
                                       win[:, k:k + 2, WCOL[name]:WCOL[name] + 256]).then_inc(loaded, 16)
                elif label == "ik":
                    for r in range(P // IDX_DIM):
                        sp.e.dma_start(tiles[:, :, r * IDX_DIM:(r + 1) * IDX_DIM],
                                       win[:, :, WCOL["ik"]:WCOL["ik"] + IDX_DIM]).then_inc(loaded, 16)
                elif label == "misc":
                    for c, name, w in MISC:
                        sp.e.dma_start(tiles[:, :, c:c + w], win[:, :, WCOL[name]:WCOL[name] + w]).then_inc(loaded, 16)
                else:
                    name, c = (label[:-1], int(label[-1])) if label[-1] in "01" else (label, 0)
                    a = WCOL[name] + c * P
                    sp.e.dma_start(tiles, win[:, :, a:a + P]).then_inc(loaded, 16)

        def sp_out(sp, st, used, w, order):
            d = w.rearrange("(j p) n -> p j n", p=P)
            for n, k in enumerate(order):
                if n < SLOTS:
                    sp_free(sp, st, n, used)
                else:
                    sp.e.wait_ge(unit_ps.h, st.units + n - SLOTS + 1)
                sp.e.dma_start(wunit[:, n % SLOTS, :], d[:, k, :]).then_inc(u_in[n % SLOTS].h, 16)

        @block.sync
        def _(e):
            sp = Eng(e)
            e.dma_start(cst[:, :], I["consts"][:, 0:CONST_W - PRO_W]).then_inc(consts_in.h, 16)
            e.dma_start(arena[:, 12:14, :].rearrange("p t c -> p (t c)")[:, 0:PRO_W],
                        I["consts"][:, CONST_W - PRO_W:]).then_inc(relb_in.h, 16)
            e.dma_start(relb[0:32, :], I["rel_bias"]).then_inc(relb_in.h, 16)
            for tb in range(TB):
                e.dma_start(arena[:, 2 * tb:2 * tb + 2, :],
                            I["x"][0, tb * P:(tb + 1) * P, :].rearrange("p (a c) -> p a c", a=2)).then_inc(token_dma.h, 16)
            for l in range(DEPTH):
                sp.l = l
                sp_ffn(sp, STAGES["ffn1", l], I["ffn1_gate"][l], I["ffn1_up"][l], I["ffn1_down"][l])
                e.dma_start(gup[:, :], I["b_gate_up"][l]).then_inc(gup_in.h, 16)
                sp_z(sp, STAGES["in", l], I["w_in"][l].rearrange("(k p) n -> p k n", p=P))
                sp.e.wait_ge(unit_ps.h, STAGES["out", l].units)
                sp.e.wait_ge(idx_acc.h, idx_acc.by(sp.l, NIDX))
                e.dma_start(w_uq, I["d_uq"][l].rearrange("(k p) n -> p k n", p=P)).then_inc(smallw_in.h, 16)
                e.dma_start(w_ukv, I["d_ukv"][l]).then_inc(smallw_in.h, 16)
                sp_out(sp, STAGES["out", l], None, I["w_out"][l], Y_HYB)
                sp_ffn(sp, STAGES["ffn2", l], I["ffn2_gate"][l], I["ffn2_up"][l],
                       I["ffn2_down"][l])
            sp.l = DEPTH
            sp.e.wait_ge(unit_ps.h, STAGES["out", "even"].units)
            for q, n in enumerate(("s5_b_re_2", "s5_b_im_2")):
                e.dma_start(T(e_bst)[:, q * 256:(q + 1) * 256].rearrange("p (j c) -> p j c", c=SSM_C),
                            I[n][0].rearrange("(j q) p c -> (q p) j c", q=2)).then_inc(s5_in.h, 16)
            for q, n in enumerate(("s5_c_re_2", "s5_c_im_2")):
                cd = T(e_cst + q).rearrange("p (t d s) -> p t d s", t=4, d=2)
                src = I[n][0].rearrange("(t g) c s -> (g c) t s", t=4)
                for d in range(2):
                    e.dma_start(cd[:, :, d, :], src).then_inc(s5_in.h, 16)
            e.dma_start(T(e_pos).bitcast(I32), bass.AP(I["positions_2"].tensor, 0, [[0, P], [1, SEQ]])).then_inc(s5_in.h, 16)
            win = I["ev_w_in_2"][0].rearrange("(k p) n -> p k n", p=P)
            glu = I["s5_w_glu_2"][0].rearrange("(k p) n -> p k n", p=P)
            for b in range(len(E_BLOCKS) + 2):
                n = b
                if b >= 2:
                    sp.e.wait_ge(w_used.h, n - 1)
                if b < len(E_BLOCKS):
                    a = E_BLOCKS[b][1]
                    e.dma_start(wring[:, n % 2], win[:, :, a:a + 256]).then_inc(w_in_sem[n % 2].h, 16)
                else:
                    a = (b - len(E_BLOCKS)) * 256
                    e.dma_start(wring[:, n % 2, 0:4, :], glu[:, :, a:a + 256]).then_inc(w_in_sem[n % 2].h, 16)
            sp_out(sp, STAGES["out", "even"], USE_ODD, I["ev_w_out_2"][0], Y_EVEN)
            sp_ffn(sp, STAGES["ffn", "even"], I["ffn_w_gate_2"][0], I["ffn_w_up_2"][0], I["ffn_w_down_2"][0])
            st = STAGES["in", "odd"]
            win = I["od_w_in_2"][0].rearrange("(k p) n -> p k n", p=P)
            for n in range(2 * KD):
                if n < SLOTS:
                    sp_free(sp, st, n, None)
                else:
                    sp.e.wait_ge(unit_ps.h, st.units + n - SLOTS + 1)
                sp.e.dma_start(wunit[:, n % SLOTS, :].rearrange("p (k c) -> p k c", k=KD),
                               win[:, :, n * P:(n + 1) * P]).then_inc(u_in[n % SLOTS].h, 16)
            for g, n in enumerate(("rg_w_r_2", "rg_w_i_2")):
                sp.e.wait_ge(unit_ps.h, st.units + 2 * KD - SLOTS + 2 * (g + 1))
                e.dma_start(wring[:, g], I[n][0].rearrange("b (k p) n -> p (b k) n", p=P)).then_inc(w_in_sem[g].h, 16)
            sp_out(sp, STAGES["out", "odd"], USE_ODD + 2, I["od_w_out_2"][0], Y_ODD)
            sp_ffn(sp, STAGES["ffn", "odd"], I["ffn_w_gate_2"][1], I["ffn_w_up_2"][1], I["ffn_w_down_2"][1])
            for tb in range(TB):
                sp.e.wait_ge(fin_sb.h, 2 * tb + 2)
                e.dma_start(out[0, tb * P:(tb + 1) * P, :].rearrange("p (a c) -> p a c", a=2),
                            arena[:, 2 * tb:2 * tb + 2, :]).then_inc(token_dma.h, 16)
            sp.e.wait_ge(token_dma.h, 2 * 16 * TB)

        def pe_norm(pe, n):
            for k in range(KD):
                pe.e.wait_ge(sq_done.h, n * KD + (k + 1))
                mm = nc.tensor.matmul(pb[6][:, :], C("mean1024"), T(SQ + k), start=(k == 0), stop=(k == KD - 1))
            mm.then_inc(norm_ps.h, 1)

        def split_product(ps, slot, t, hi, lo, start, stop, M=P):
            nc.tensor.matmul(ps, w_hi[:, slot, t, 0:M], hi, start=start, stop=False)
            nc.tensor.matmul(ps, w_lo[:, slot, t, 0:M], hi, start=False, stop=False)
            return nc.tensor.matmul(ps, w_hi[:, slot, t, 0:M], lo, start=False, stop=stop)

        def down_bank(m):
            return pb[(m + 6) % 8][:, :]

        def down_unit(slot, hi, lo, stop):
            for m in range(KD):
                mm = split_product(down_bank(m), slot, m, hi, lo, False, stop)
                if stop and m < KD - 1:
                    mm.then_inc(down_ps.h, 1)
            mm.then_inc(unit_ps.h, 1)

        def pe_ffn(pe, st):
            f, u0 = st.ffns, st.units
            with pe.e.Fori(0, NF // 2) as i:
                for c in range(2):
                    n = f * NF + 2 * i + c
                    pe.e.wait_ge(u_lo.h, u0 + SLOTS * i + (2 * c + 1))
                    pe.e.wait_ge(sg_ready.h, sg_ready.start + n - 1)
                    for k in range(KD):
                        if c == 0:
                            pe.e.wait_ge(xn_lo_ready.h, st.splits * KD + k + 1)
                        mm = split_product(pb[c][:, :], 2 * c, k, xn_hi[:, k, :], xn_lo[:, k, :], k == 0, k == KD - 1)
                    mm.then_inc(unit_ps.h, 1)
                    pe.e.wait_ge(u_lo.h, u0 + SLOTS * i + (2 * c + 2))
                    pe.e.wait_ge(h_full.h, h_full.start + n - 1)
                    for k in range(KD):
                        mm = split_product(pb[2 + c][:, :], 2 * c + 1, k, xn_hi[:, k, :], xn_lo[:, k, :], k == 0, k == KD - 1)
                    mm.then_inc(unit_ps.h, 1)
            u0 += 2 * NF
            pe.e.wait_ge(u_lo.h, u0 + 1)
            pe.e.wait_ge(h_lo_ready.h, f * NF + 1)
            for m in (0, 1, 6, 7, 2, 4, 3, 5):
                if m in (2, 3):
                    pe.e.wait_ge(sg_ready.h, sg_ready.start + (f + 1) * NF + (m - 3))
                if m in (4, 5):
                    pe.e.wait_ge(h_full.h, h_full.start + (f + 1) * NF + (m - 5))
                mm = split_product(down_bank(m), 0, m, h_hi[:, 0, :], h_lo[:, 0, :], True, False)
            mm.then_inc(unit_ps.h, 1)
            for k in range(1, SLOTS):
                pe.e.wait_ge(u_lo.h, u0 + k + 1)
                pe.e.wait_ge(h_lo_ready.h, f * NF + k + 1)
                down_unit(k, h_hi[:, k, :], h_lo[:, k, :], False)
            with pe.e.Fori(0, NF // SLOTS - 1) as i:
                for q in range(SLOTS):
                    pe.e.wait_ge(u_lo.h, u0 + SLOTS * i + (SLOTS + q + 1))
                    pe.e.wait_ge(h_lo_ready.h, f * NF + SLOTS * i + (SLOTS + q + 1))
                    hi, lo = [t[:, bass.ds(SLOTS * i + (SLOTS + q), 1), :].rearrange("p a c -> p (a c)") for t in (h_hi, h_lo)]
                    down_unit(q, hi, lo, False)
            for k in range(NF // SLOTS * SLOTS, NF):
                pe.e.wait_ge(u_lo.h, u0 + k + 1)
                pe.e.wait_ge(h_lo_ready.h, f * NF + k + 1)
                down_unit(k % SLOTS, h_hi[:, k, :], h_lo[:, k, :], k == NF - 1)

        def pe_out(pe, st, order, free):
            for n, k in enumerate(order):
                pe.e.wait_ge(u_lo.h, st.units + n + 1)
                pe.e.wait_ge(xn_lo_ready.h, st.splits * KD + n + 1)
                if n:
                    down_unit(n % SLOTS, xn_hi[:, k, :], xn_lo[:, k, :], n == KD - 1)
                else:
                    for m in (0, 2, 3, 4, 5, 6, 7, 1):
                        free(pe, m)
                        mm = split_product(down_bank(m), 0, m, xn_hi[:, k, :], xn_lo[:, k, :], True, False)
                    mm.then_inc(unit_ps.h, 1)

        def pe_z(pe, st):
            ni = 0
            for n, t in enumerate(Z_SEQ):
                bank = pb[n % 4]
                if n >= 4 and t[0] != "tok":
                    pe.e.wait_ge(z_sb.h, z_sb.by(pe.l, n - 3))
                if t[0] == "idx":
                    _, tb, h = t
                    if ni == 0:
                        pe.e.wait_ge(z_sb.h, z_sb.by(pe.l, Z_POS["ik"] + 1))
                    r = 32 * (h % 4)
                    N = (tb + 1) * P
                    nc.tensor.matmul(bank[:, 0:N], T(t_iq[h // 4])[r:r + 32, tb * P:(tb + 1) * P],
                                     T(t_ik)[r:r + 32, 0:N], start=True, stop=True).then_inc(idx_ps.h, 1)
                    ni += 1
                elif t[0] == "iw":
                    pe.e.wait_ge(z_sb.h, z_sb.by(pe.l, Z_POS["misc"] + 1))
                    r = slice(32, 32 + IDX_HEADS)
                    for tb in range(TB):
                        mm = nc.tensor.transpose(bank[:, 8 * tb:8 * tb + 8], T(t_iw)[r, tb * P:(tb + 1) * P], ident[r, r])
                    mm.then_inc(z_ps.h, 1)
                elif t[0] == "z":
                    _, u, label = t
                    M = MISC_W if label == "misc" else P
                    pe.e.wait_ge(u_lo.h, st.units + u + 1)
                    for k in range(KD):
                        if u == 0:
                            pe.e.wait_ge(xn_lo_ready.h, st.splits * KD + k + 1)
                        mm = split_product(bank[0:M, :], u % SLOTS, k, z_hi[:, k, :], xn_lo[:, k, :], k == 0, k == KD - 1, M)
                    mm.then_inc(unit_ps.h, 1)
                else:
                    for q in range(Z_TOK):
                        u = len(Z_LABELS) + q
                        pe.e.wait_ge(u_lo.h, st.units + u + 1)
                        wh, wl = [w[:, u % SLOTS, :, :].rearrange("p k c -> p (k c)").rearrange("p (k c) -> p k c", k=2)
                                  for w in (w_hi, w_lo)]
                        for r in range(2):
                            k = 2 * q + r
                            for tb in range(TB):
                                cols = slice(tb * P, (tb + 1) * P)
                                o = pb[4 + tb][:, :]
                                nc.tensor.matmul(o, z_hi[:, k, cols], wh[:, r, :], start=(k == 0), stop=False)
                                nc.tensor.matmul(o, z_hi[:, k, cols], wl[:, r, :], start=False, stop=False)
                                mm = nc.tensor.matmul(o, xn_lo[:, k, cols], wh[:, r, :], start=False, stop=(k == KD - 1))
                        mm.then_inc(unit_ps.h, 1)

        def pe_mixers(pe):
            pe.e.wait_ge(z_sb.h, z_sb.by(pe.l, NZ - 1))
            pe.e.wait_ge(gup_in.h, gup_in.by(pe.l, 16))
            nc.tensor.matmul(pb[0][:, :], gup[:, :], T(t_gl)[0:B_RANK, :], start=True, stop=True).then_inc(gate_log_ps.h, 1)
            for i in range(4):
                pe.e.wait_ge(zsq.h, zsq.by(pe.l, i + 1))
                if i >= 3:
                    pe.e.wait_ge(mn_ln.h, mn_ln.by(pe.l, i - 2))
                nc.tensor.matmul(pb[1 + i % 3][:, :], C("blk64"), T(t_zsq[i]), start=True, stop=True).then_inc(mn_ps.h, 1)
            pe.e.wait_ge(zsq.h, zsq.by(pe.l, 6))
            pe.e.wait_ge(mn_ln.h, mn_ln.by(pe.l, 2))
            nc.tensor.matmul(pb[2][:, :], C("mean256"), T(t_zsq[4]), start=True, stop=False)
            nc.tensor.matmul(pb[2][:, :], C("mean256"), T(t_zsq[5]), start=False, stop=True).then_inc(mn_ps.h, 1)
            pe.e.wait_ge(zsq.h, zsq.by(pe.l, 7))
            pe.e.wait_ge(mn_ln.h, mn_ln.by(pe.l, 3))
            nc.tensor.matmul(pb[3][:, :], C("mean128"), T(t_zsq[6]), start=True, stop=True).then_inc(mn_ps.h, 1)
            pe.e.wait_ge(z_sb.h, z_sb.by(pe.l, NZ))
            pe.e.wait_ge(smallw_in.h, smallw_in.by(pe.l, 16 * 2))
            pe.e.wait_ge(mn_x.h, mn_x.by(pe.l, 7))
            for q in range(2):
                for r in range(2):
                    tb = 2 * q + r
                    mm = nc.tensor.matmul(pb[6 + q][:, r * 256:(r + 1) * 256], T(t_dckv)[:, tb * P:(tb + 1) * P],
                                          w_ukv.rearrange("p (h t) -> p h t", h=D_HEADS)[:, :, D_NOPE:],
                                          start=True, stop=True)
                mm.then_inc(dv_ps.h, 1)
            for i in range(8 + 2):
                if i < 8:
                    raw = pb[i % 2]
                    if i == 1:
                        pe.e.wait_ge(mn_ln.h, mn_ln.by(pe.l, 6))
                    if i >= 2:
                        pe.e.wait_ge(dh_sq.h, dh_sq.by(pe.l, i - 1))
                    h = i % 4
                    if i < 4:
                        for k in range(2):
                            mm = nc.tensor.matmul(raw[0:D_QK, :], w_uq[:, k, h * D_QK:(h + 1) * D_QK], T(t_dcq[k]),
                                                  start=(k == 0), stop=(k == 1))
                    else:
                        nc.tensor.matmul(raw[0:D_NOPE, :], w_ukv[:, h * P:h * P + D_NOPE], T(t_dckv), start=True, stop=True)
                        mm = nc.tensor.matmul(raw[64:96, :], ident[64:96, 64:96], T(t_kpe)[64:96, :], start=True, stop=True)
                    mm.then_inc(dh_ps.h, 1)
                if 1 <= i < 9:
                    u = i - 1
                    pe.e.wait_ge(dh_sq.h, dh_sq.by(pe.l, u + 1))
                    if u >= 1:
                        pe.e.wait_ge(dn_ln.h, dn_ln.by(pe.l, u))
                    nc.tensor.matmul(pb[2][0:D_QK, :], C("mean96")[0:D_QK, :], T(t_hsq[u % 2])[0:D_QK, :],
                                     start=True, stop=True).then_inc(dn_ps.h, 1)
                if i >= 2:
                    u = i - 2
                    pe.e.wait_ge(dn_x.h, dn_x.by(pe.l, u + 1))
                    if u >= 1:
                        pe.e.wait_ge(dr_s.h, dr_s.by(pe.l, u))
                    nc.tensor.matmul(pb[3][0:D_QK, :], C("rot96")[0:D_QK, :], T(t_hn[u % 2])[0:D_QK, :],
                                     start=True, stop=True).then_inc(dr_ps.h, 1)
            pe.e.wait_ge(conv_sq.h, conv_sq.by(pe.l, 2))
            pe.e.wait_ge(dv_sb.h, dv_sb.by(pe.l, 1))
            nc.tensor.matmul(pb[6][:, :], C("mean256"), T(t_csq[0]), start=True, stop=False)
            nc.tensor.matmul(pb[6][:, :], C("mean256"), T(t_csq[1]), start=False, stop=True).then_inc(mn_ps.h, 1)
            pe.e.wait_ge(b_qk.h, b_qk.by(pe.l, 3))
            pe.e.wait_ge(dv_sb.h, dv_sb.by(pe.l, 2))
            for tb in range(TB):
                mm = nc.tensor.transpose(pb[7][:, tb * P:(tb + 1) * P], W(w_e2)[:, tb * P:(tb + 1) * P], ident)
            mm.then_inc(kt_ps.h, 1)
            pe.e.wait_ge(kt_sb.h, kt_sb.by(pe.l, 1))
            pe.e.wait_ge(dn_ln.h, dn_ln.by(pe.l, 8))
            pe.e.wait_ge(dr_s.h, dr_s.by(pe.l, 8))
            bv = arena[:, t_bv:t_bv + 2, :].rearrange("p t c -> p (t c)").rearrange("p (b c) -> p b c", b=TB)
            for c in range(NCH - 1):
                r = 64 * (c % 2)
                if c >= 2:
                    pe.e.wait_ge(u_msk.h, u_msk.by(pe.l, c - 1))
                nc.tensor.matmul(pb[2 + c % 2][:, 0:256], T(t_kdt)[r:r + 64, (c // 2) * P:(c // 2 + 1) * P],
                                 bv[r:r + 64, c // 2, :], start=True, stop=True).then_inc(u_ps.h, 1)
            pe.e.wait_ge(b_kd.h, b_kd.by(pe.l, 1 + B_HEADS))
            for tb in range(TB):
                bank = pb[4 + tb % 2]
                if tb >= 2:
                    pe.e.wait_ge(at_sb.h, at_sb.by(pe.l, 2 * (tb - 1)))
                for h in range(B_HEADS):
                    mm = nc.tensor.matmul(bank[:, h * P:(h + 1) * P], kdm[h][:, tb * P:(tb + 1) * P],
                                          W(w_e1)[:, tb * P:(tb + 1) * P], start=True, stop=True)
                mm.then_inc(at_ps.h, 1)
            pe.e.wait_ge(at_sb.h, at_sb.by(pe.l, 2 * TB))
            pe.e.wait_ge(s_ready.h, s_ready.by(pe.l, NCH - 1))
            pe.e.wait_ge(dh_sq.h, dh_sq.by(pe.l, 8))
            for pr in range(2):
                o = pb[pr]
                for c in range(NCH):
                    cols = slice(c * B_CHUNK, (c + 1) * B_CHUNK)
                    half = slice(c % 2 * B_CHUNK, (c % 2 + 1) * B_CHUNK)
                    for q in range(2):
                        h = 2 * pr + q
                        mm = nc.tensor.matmul(o[64 * q:64 * q + 64, cols], bv[:, c // 2, h * B_VAL:(h + 1) * B_VAL],
                                              att_diag[:, c // 2, h, half], start=True, stop=(c == 0),
                                              skip_group_check=True)
                    if c:
                        mm = nc.tensor.matmul(o[:, cols], Sst(c)[:, pr * P:(pr + 1) * P], T(t_qe)[:, cols],
                                              start=False, stop=True, skip_group_check=True)
                mm.then_inc(o_ps.h, 1)
            for pr in range(2):
                pe.e.wait_ge(o_sq.h, o_sq.by(pe.l, pr + 1))
                pe.e.wait_ge(u_msk.h, u_msk.by(pe.l, NCH - 1))
                nc.tensor.matmul(pb[2 + pr][:, :], C("blk64"), T(t_osq[pr]), start=True, stop=True).then_inc(on_ps.h, 1)

        def pe_attention(pe, units, ops):
            U = len(units)
            for i in range(U + 3):
                if i < U:
                    ops["ready"](pe, i)
                    m, h, tb = units[i]
                    if i >= 4:
                        pe.e.wait_ge(att_exp.h, att_exp.by(pe.l, i - 3))
                    s = pb[(0, 1, 4, 5)[i % 4]]
                    N = (tb + 1) * P
                    q, k = ops["qk"](m, h)
                    msk, lo = ops["mask"](m, h, tb, i)
                    if lo:
                        nc.tensor.matmul(s[:, 0:lo], q[:, tb * P:N], k[:, 0:lo], start=True, stop=True)
                    nc.tensor.matmul(s[:, lo:N], q[:, tb * P:N], k[:, lo:N], start=True, stop=False)
                    nc.tensor.matmul(s[:, lo:N], ident, msk, start=False, stop=True).then_inc(att_s.h, 1)
                if 2 <= i < U + 2:
                    u = i - 2
                    pe.e.wait_ge(att_p.h, att_p.by(pe.l, u + 1))
                    if u >= 2:
                        pe.e.wait_ge(att_pt.h, att_pt.by(pe.l, u - 1))
                    for b in range(units[u][2] + 1):
                        mm = nc.tensor.transpose(pb[2 + u % 2][:, b * P:(b + 1) * P],
                                                 p_buf(units, u)[:, b * P:(b + 1) * P], ident)
                    mm.then_inc(att_t.h, 1)
                if i >= 3:
                    u = i - 3
                    m, h, tb = units[u]
                    pe.e.wait_ge(att_pt.h, att_pt.by(pe.l, u + 1))
                    if u % 8 == 0 and u >= 16:
                        pe.e.wait_ge(y_att.h, y_att.by(pe.l, u // 8 - 1))
                    o = pb[6 + (u // 8) % 2][64 * (h % 2):64 * (h % 2) + 64, tb * P:(tb + 1) * P]
                    for b in range(tb + 1):
                        mm = nc.tensor.matmul(o, ops["v"](m, h, b), pt_buf(units, u)[:, b * P:(b + 1) * P],
                                              start=(b == 0), stop=(b == tb))
                    mm.then_inc(att_o.h, 1)

        def hyb_qk(m, h):
            if m == "D":
                return T(t_dq[h])[0:D_QK, :], T(t_dk[h])[0:D_QK, :]
            r = 64 * (h % 2)
            return T(t_aq[h // 2])[r:r + 64, :], T(t_ak[h // 2])[r:r + 64, :]

        def hyb_mask(m, h, tb, u):
            if m == "D":
                return C("causal"), tb * P
            if tb == 0:
                return bias[:, h, SEQ - P:SEQ], 0
            return T(t_bm[BM.index(u) % 3])[:, 0:(tb + 1) * P], 0

        def hyb_v(m, h, b):
            t = t_dv if m == "D" else t_av
            v = arena[:, t:t + 2, :].rearrange("p t c -> p (t c)").rearrange("p (b c) -> p b c", b=TB)
            return v[:, b, h * 64:(h + 1) * 64]

        def hyb_ready(eng, u):
            if u == 0:
                eng.e.wait_ge(on_ln.h, on_ln.by(eng.l, 2))
                eng.e.wait_ge(y_conv.h, y_conv.by(eng.l, 2))
                eng.e.wait_ge(kt_sb.h, kt_sb.by(eng.l, 1))
                eng.e.wait_ge(at_sb.h, at_sb.by(eng.l, 2 * TB))
            m, h, tb = HYB_UNITS[u]
            if m == "D" and tb == 0:
                eng.e.wait_ge(dh_ready.h, dh_ready.by(eng.l, 5 + h))
            if m == "A" and h == 0 and tb == 0:
                eng.e.wait_ge(mn_x.h, mn_x.by(eng.l, 4))
                eng.e.wait_ge(pro_sb.h, 4 + 2 + A_HEADS)
            if u in BM:
                eng.e.wait_ge(att_bm.h, att_bm.by(eng.l, BM.index(u) + 1))

        HYB = dict(qk=hyb_qk, mask=hyb_mask, v=hyb_v, ready=hyb_ready)

        def att_free(pe, m):
            if m < 2:
                pe.e.wait_ge(y_att.h, y_att.by(pe.l, 3 + m))

        E_UNITS = [("E", h, tb) for h in range(E_HEADS) for tb in range(TB)]
        e_vv = arena[:, e_v:e_v + 4, :]

        def even_qk(m, h):
            r = 64 * (h % 2)
            return T(e_q + h // 2)[r:r + 64, :], T(e_k + h // 2)[r:r + 64, :]

        def even_ready(eng, u):
            if u == 0:
                eng.e.wait_ge(glu_sb.h, 4)
            m, h, tb = E_UNITS[u]
            if tb == 0 and h % 2 == 0:
                eng.e.wait_ge(rot_ready.h, 2 * (h // 2) + 2)
            if u == 0:
                eng.e.wait_ge(ez_sb.h, len(E_Z))

        EVEN = dict(qk=even_qk, mask=lambda m, h, tb, u: (C("lnmult")[:, SEQ - (tb + 1) * P:], 0),
                    v=lambda m, h, b: e_vv[:, b, h * E_DIM:(h + 1) * E_DIM], ready=even_ready)

        def pe_even(pe, norms):
            inc = [0, 0]
            nz = 0
            for t in E_SEQ:
                if t[0] == "z":
                    _, b, c, n, i = t
                    s = b % 2
                    bank = pb[nz % 2]
                    if c == 0:
                        inc[s] += 1
                        pe.e.wait_ge(w_in_sem[s].h, 16 * inc[s])
                    if nz >= 2:
                        pe.e.wait_ge(ez_sb.h, nz - 1)
                    w = wring[:, s, :, :]
                    if n == "v":
                        for q in range(2):
                            tb = 2 * c + q
                            for k in range(KD):
                                mm = nc.tensor.matmul(bank[:, q * 256:(q + 1) * 256], xn[:, k, tb * P:(tb + 1) * P],
                                                      w[:, k, :], start=(k == 0), stop=(k == KD - 1))
                    else:
                        for k in range(KD):
                            if nz == 0:
                                pe.e.wait_ge(xn_ready.h, norms * KD + k + 1)
                            mm = nc.tensor.matmul(bank[:, :], w[:, k, c * P:(c + 1) * P], xn[:, k, :],
                                                  start=(k == 0), stop=(k == KD - 1))
                    mm.then_inc((w_used if c else ez_ps).h, 1)
                    nz += 1
                elif t[0] == "prep":
                    pe.e.wait_ge(par.h, PAR_E)
                    pe.e.wait_ge(s5_in.h, 16 * 7)
                    for q, src in enumerate((e_ere, e_eim, e_cst, e_cst + 1)):
                        for i in range(4):
                            mm = nc.tensor.transpose(pb[2 + q][:, i * P:(i + 1) * P], T(src)[:, i * P:(i + 1) * P], ident)
                        mm.then_inc(bc_ps.h, 1)
                elif t[0] == "bu":
                    j = t[1]
                    if j == 0:
                        pe.e.wait_ge(bt_sb.h, 2)
                        pe.e.wait_ge(cb_sb.h, 4)
                        pe.e.wait_ge(ez_sb.h, 4)
                    if j >= 2:
                        pe.e.wait_ge(s5_rot.h, j - 1)
                    r = slice(32 * (j % 4), 32 * (j % 4) + 32)
                    for q, bt in enumerate((e_btr, e_bti)):
                        mm = nc.tensor.matmul(pb[2 + 2 * (j % 2) + q][:, :], T(bt)[r, (j // 4) * P:(j // 4 + 1) * P],
                                              T(e_u + j // 4)[r, :], start=True, stop=True)
                    mm.then_inc(bu_ps.h, 1)
                else:
                    j = t[1]
                    pe.e.wait_ge(s5_p.h, j + 1)
                    pe.e.wait_ge(s5_q.h, j + 1)
                    if j % 4 == 0 and j >= 8:
                        pe.e.wait_ge(s5_y.h, j // 4 - 1)
                    r = slice(32 * (j % 4), 32 * (j % 4) + 32)
                    a1, p3, p2, p4 = s5_a[j % 3]
                    for q, (cm, a) in enumerate(((e_cre, a1), (e_crn, p2), (e_cin, p3), (e_cin, p4))):
                        mm = nc.tensor.matmul(pb[6 + (j // 4) % 2][r, :], T(cm)[:, j * 32:(j + 1) * 32], a,
                                              start=(q == 0), stop=(q == 3))
                    mm.then_inc(yy_ps.h, 1)
            for i in range(8):
                t = (e_q if i % 2 == 0 else e_k) + i // 2
                if i < 2:
                    pe.e.wait_ge(ez_sb.h, len(E_Z))
                else:
                    pe.e.wait_ge(rot_s.h, i - 1)
                nc.tensor.matmul(pb[i % 2][:, :], C("rot128"), T(t), start=True, stop=True).then_inc(rot_ps.h, 1)
            pe.e.wait_ge(s5_gelu.h, 4)
            for b in range(2):
                s = b % 2
                pe.e.wait_ge(w_in_sem[s].h, 16 * (inc[s] + 1))
                for c in range(2):
                    for k in range(4):
                        mm = nc.tensor.matmul(pb[2 + 2 * b + c][:, :], wring[:, s, k, c * P:(c + 1) * P], T(e_u + k),
                                              start=(k == 0), stop=(k == 3))
                    mm.then_inc((w_used if c else glu_ps).h, 1)
            pe.e.wait_ge(rot_s.h, 8)

        def pe_post(pe, m):
            for k in range(KD):
                pe.e.wait_ge(rsq.h, m * KD + k + 1)
                mm = nc.tensor.matmul(pb[6][:, :], C("mean1024"), T(SQ + k), start=(k == 0), stop=(k == KD - 1))
            mm.then_inc(rn_ps.h, 1)

        def pe_odd(pe):
            inc = list(DMA_ODD)
            st = STAGES["in", "odd"]
            for n in range(2 * KD):
                pe.e.wait_ge(u_lo.h, st.units + n + 1)
                if n >= 4:
                    pe.e.wait_ge(oz_sb.h, n - 3)
                for k in range(KD):
                    if n == 0:
                        pe.e.wait_ge(xn_lo_ready.h, st.splits * KD + k + 1)
                    mm = split_product(pb[n % 4][:, :], n % SLOTS, k, xn_hi[:, k, :], xn_lo[:, k, :], k == 0, k == KD - 1)
                mm.then_inc(unit_ps.h, 1)
            for g in range(2):
                inc[g] += 1
                pe.e.wait_ge(w_in_sem[g].h, 16 * inc[g])
                for m in range(KD):
                    n = g * KD + m
                    if n < 4:
                        pe.e.wait_ge(oz_sb.h, 2 * KD - 3 + n)
                    else:
                        pe.e.wait_ge(og_sb.h, n - 3)
                    b = m // 2
                    pe.e.wait_ge(cv.h, LRU_TAPS * (2 * b + 2))
                    for k in range(2):
                        mm = nc.tensor.matmul(pb[n % 4][:, :], wring[:, g, 2 * b + k, (m % 2) * P:(m % 2 + 1) * P],
                                              T(o_xc + 2 * b + k), start=(k == 0), stop=(k == 1))
                    mm.then_inc((w_used if m == KD - 1 else og_ps).h, 1)
            pe.e.wait_ge(og_sb.h, 2 * KD)

        @block.tensor
        def _(e):
            pe = Eng(e)
            pe.e.wait_ge(consts_in.h, 16)
            pe.e.wait_ge(token_dma.h, 16 * TB)
            for k in range(KD):
                if k >= 2:
                    pe.e.wait_ge(x_ready.h, k - 1)
                for tb in range(TB):
                    mm = nc.tensor.transpose(pb[k % 2][:, tb * P:(tb + 1) * P],
                                             arena[:, 2 * tb + k // 4, (k % 4) * P:(k % 4 + 1) * P], ident)
                mm.then_inc(pro_ps.h, 1)
            pe.e.wait_ge(rows_in.h, 16 * N_ROW_DMAS)
            pe.e.wait_ge(ldt_row.h, 1)
            for i in range(4):
                nc.tensor.transpose(pb[2 + i][:, 0:P], rows[:, i, :], ident).then_inc(pro_ps.h, 1)
            pe.e.wait_ge(relb_in.h, 32)
            pe.e.wait_ge(relb_neg.h, 1)
            half = BIAS_N // 2
            for q in range(2):
                nc.tensor.matmul(pb[6 + q][0:A_HEADS, 0:half], relb[0:33, :], C("onehot")[0:33, q * half:(q + 1) * half],
                                 start=True, stop=True).then_inc(pro_ps.h, 1)
            pe.e.wait_ge(pro_sb.h, 4)
            pe.e.wait_ge(pro_sb.h, 4 + 2)
            pe.e.wait_ge(x_ready.h, KD)
            pe.e.wait_ge(bias_dma.h, 32)
            for h in range(A_HEADS):
                nc.tensor.matmul(pb[h][:, :], C("flip"), arena[:, 8 + h, :], start=True, stop=True).then_inc(pro_ps.h, 1)
            pe.e.wait_ge(pro_sb.h, 4 + 2 + A_HEADS)
            for l in range(DEPTH):
                pe.l = l
                pe_norm(pe, l * 3)
                pe_ffn(pe, STAGES["ffn1", l])
                pe_norm(pe, l * 3 + 1)
                pe_z(pe, STAGES["in", l])
                pe_mixers(pe)
                pe_attention(pe, HYB_UNITS, HYB)
                pe_out(pe, STAGES["out", l], Y_HYB, att_free)
                pe_norm(pe, l * 3 + 2)
                pe_ffn(pe, STAGES["ffn2", l])
            pe.l = DEPTH
            n = 3 * DEPTH
            pe_norm(pe, n)
            pe_even(pe, n)
            pe_attention(pe, E_UNITS, EVEN)
            pe_out(pe, STAGES["out", "even"], Y_EVEN, att_free)
            pe_post(pe, 0)
            pe_norm(pe, n + 1)
            pe_ffn(pe, STAGES["ffn", "even"])
            pe_post(pe, 1)
            pe_norm(pe, n + 2)
            pe_odd(pe)
            pe_out(pe, STAGES["out", "odd"], Y_ODD, lambda pe, m: None)
            pe_post(pe, 2)
            pe_norm(pe, n + 3)
            pe_ffn(pe, STAGES["ffn", "odd"])
            pe_post(pe, 3)
            pe.e.wait_ge(x_ready.h, X1 + 4 * KD)
            for tb in range(TB):
                for q in range(2):
                    n = 2 * tb + q
                    if n >= 2:
                        pe.e.wait_ge(fin_sb.h, n - 1)
                    for k in range(4):
                        mm = nc.tensor.transpose(pb[n % 2][:, k * P:(k + 1) * P], x[:, 4 * q + k, tb * P:(tb + 1) * P], ident)
                    mm.then_inc(fin_ps.h, 1)

        LN_EXP = "natural_log_exp_and_others"

        def act_norm(act, n, st=None):
            nc.scalar.preload_act_table_set(LN_EXP)
            for k in range(KD):
                act.e.wait_ge(x_ready.h, n * KD + (k + 1))
                nc.scalar.activation(T(SQ + k), x[:, k, :], ACT.Square).then_inc(sq_done.h, 1)
            if st:
                for q in range(2):
                    act.e.wait_ge(u_in[q].h, st.loaded(q))
                    split_unit(q)
            act.e.wait_ge(norm_ps.h, n + 1)
            nc.scalar.activation(T(RT), pb[6][:, :], ACT.Ln, bias=C("eps")).then_inc(norm_ln.h, 1)
            act.e.wait_ge(norm_ln.h, n + 1)
            nc.scalar.activation(T(RT), T(RT), ACT.Exp, scale=-0.5).then_inc(norm_r.h, 1)
            if st:
                nc.scalar.preload_act_table(ACT.Silu)
                for k in range(KD):
                    act.e.wait_ge(xn_ready.h, n * KD + k + 1)
                    nc.scalar.activation(chunk_hi(st, k), xn[:, k, :], ACT.Copy).then_inc(xn_hi_ready.h, 1)

        def chunk_hi(st, k):
            return (z_hi if st in Z_STAGES else xn_hi)[:, k, :]

        def split_unit(slot):
            nc.scalar.activation(w_hi[:, slot, :, :].rearrange("p k c -> p (k c)"), wunit[:, slot, :], ACT.Copy).then_inc(u_hi.h, 1)

        def act_ffn(act, st):
            f = st.ffns
            with act.e.Fori(0, NF // 2) as i:
                for c in range(2):
                    n = f * NF + 2 * i + c
                    slots = (2, 3) if c == 0 else (0, 1)
                    act.e.wait_ge(u_in[slots[0]].h, st.loaded(slots[0] + SLOTS * c) + 16 * i)
                    split_unit(slots[0])
                    act.e.wait_ge(unit_ps.h, st.units + SLOTS * i + (2 * c + 1))
                    act.e.wait_ge(h_full.h, h_full.start + n - 1)
                    nc.scalar.activation(sg[:, c, :], pb[c][:, :], ACT.Silu).then_inc(sg_ready.h, 1)
                    act.e.wait_ge(u_in[slots[1]].h, st.loaded(slots[1] + SLOTS * c) + 16 * i)
                    split_unit(slots[1])
                    act.e.wait_ge(h_full.h, h_full.start + n + 1)
                    nc.scalar.activation(h_hi[:, bass.ds(2 * i + c, 1), :].rearrange("p a c -> p (a c)"),
                                         arena[:, bass.ds(2 * i + (H_LO + c), 1), :].rearrange("p a c -> p (a c)"),
                                         ACT.Copy).then_inc(h_hi_ready.h, 1)
            with act.e.Fori(0, NF // SLOTS) as i:
                for q in range(SLOTS):
                    s = (q + 2) % SLOTS
                    act.e.wait_ge(u_in[s].h, st.loaded(2 * NF + 2 + q) + 16 * i)
                    split_unit(s)

        def rstd(act, src, dst, ln, r, k):
            nc.scalar.activation(dst, src, ACT.Ln, bias=C("eps")[0:dst.shape[0], :]).then_inc(ln.h, 1)
            act.e.wait_ge(ln.h, ln.by(act.l, k))
            nc.scalar.activation(dst, dst, ACT.Exp, scale=-0.5).then_inc(r.h, 1)

        def act_z(act, st):
            ni = 0
            dst = dict(iq0=0, iq1=1, ik=2, aq0=3, aq1=4, ak0=5, ak1=6, bq=9, bk=10, br0=13, br1=14, ca0=15, ca1=16, cg0=17,
                       cg1=18, dcq0=19, dcq1=20, dckv=21)
            act_units(act, st, 2, 3)
            for n, t in enumerate(Z_SEQ):
                bank = pb[n % 4]
                if t[0] == "idx":
                    _, tb, h = t
                    N = (tb + 1) * P
                    act.e.wait_ge(idx_ps.h, idx_ps.by(act.l, ni + 1))
                    if ni >= 4:
                        act.e.wait_ge(idx_acc.h, idx_acc.by(act.l, ni - 3))
                    nc.scalar.activation(idx_r[ni % 4][:, 0:N], bank[:, 0:N], ACT.Relu).then_inc(z_sb.h, 1)
                    ni += 1
                elif t[0] == "iw":
                    act.e.wait_ge(z_ps.h, z_ps.by(act.l, 1))
                    nc.scalar.activation(wA, bank[:, 0:32], ACT.Copy,
                                         scale=float((IDX_DIM * IDX_HEADS) ** -0.5)).then_inc(z_sb.h, 1)
                elif t[0] == "z":
                    _, u, label = t
                    act.e.wait_ge(unit_ps.h, st.units + u + 1)
                    if label in ("aq0", "aq1", "ak0", "ak1", "dcq0", "dcq1", "dckv"):
                        q = ("aq0", "aq1", "ak0", "ak1", "dcq0", "dcq1", "dckv").index(label)
                        nc.scalar.activation(T(t_zsq[q]), bank[:, :], ACT.Square).then_inc(zsq.h, 1)
                    if label == "misc":
                        r = slice(32, 32 + IDX_HEADS)
                        nc.scalar.activation(T(t_gl)[0:B_RANK, :], bank[0:B_RANK, :], ACT.Copy)
                        nc.scalar.activation(T(t_iw)[r, :], bank[r, :], ACT.Copy)
                        nc.scalar.activation(T(t_kpe)[64:96, :], bank[64:96, :], ACT.Copy).then_inc(z_sb.h, 1)
                    else:
                        f = {"br": ACT.Silu, "cg": ACT.Sigmoid}.get(label[:2], ACT.Copy)
                        scale = float(B_KEY ** -0.5) if label == "bq" else 1.0
                        nc.scalar.activation(T(dst[label]), bank[:, :], f, scale=scale).then_inc(z_sb.h, 1)
                    act_units(act, st, u + 3, u + 4)
                else:
                    act_units(act, st, NZU - 1, NZU)
                    act.e.wait_ge(unit_ps.h, st.units + NZU)
                    bv, av = [arena[:, v:v + 2, :].rearrange("p t c -> p (t c)").rearrange("p (b c) -> p b c", b=TB)
                              for v in (t_bv, t_av)]
                    for tb in range(TB):
                        nc.scalar.activation(bv[:, tb, :], pb[4 + tb][:, 0:256], ACT.Copy)
                        ins = nc.scalar.activation(av[:, tb, :], pb[4 + tb][:, 256:512], ACT.Copy)
                    ins.then_inc(z_sb.h, 1)

        def act_mixers(act):
            nc.scalar.preload_act_table_set(LN_EXP)
            act.e.wait_ge(idx_acc.h, idx_acc.by(act.l, NIDX))
            act.e.wait_ge(gate_log_ps.h, gate_log_ps.by(act.l, 1))
            act.e.wait_ge(cur_ready.h, cur_ready.by(act.l, 4))
            gb = cur[:, RL["b_gate_bias"]:RL["b_gate_bias"] + 1]
            nc.scalar.activation(W(w_mn), pb[0][:, :], ACT.Identity, bias=gb).then_inc(g_abs.h, 1)
            nc.scalar.activation(T(t_ab), pb[0][:, :], ACT.Abs, bias=gb).then_inc(g_abs.h, 1)
            act.e.wait_ge(g_abs.h, g_abs.by(act.l, 2))
            nc.scalar.activation(T(t_ab), T(t_ab), ACT.Exp, scale=-1.0).then_inc(g_abs.h, 1)
            act.e.wait_ge(g_abs.h, g_abs.by(act.l, 3))
            nc.scalar.activation(T(t_ab), T(t_ab), ACT.Ln, bias=1.0).then_inc(g_abs.h, 1)
            bank = [1, 2, 3, 1, 2, 3]
            for i in range(6):
                act.e.wait_ge(mn_ps.h, mn_ps.by(act.l, i + 1))
                rstd(act, pb[bank[i]][:, :], T(t_zr[i]), mn_ln, mn_r, i + 1)
            g = 1.0 / 16
            act.e.wait_ge(g_b.h, g_b.by(act.l, 6))
            b16 = W(w_mn)
            nc.scalar.activation(T(t_qe), b16, ACT.Exp, scale=g).then_inc(g_exp.h, 1)
            nc.scalar.activation(W(w_e1), W(w_la), ACT.Exp, scale=g).then_inc(g_exp.h, 1)
            nc.scalar.activation(W(w_e1n), W(w_la), ACT.Exp, scale=-g).then_inc(g_exp.h, 1)
            nc.scalar.activation(W(w_e2), T(t_ab), ACT.Exp, scale=g).then_inc(g_exp.h, 1)
            nc.scalar.activation(glast[:, 0:NCH], b16.rearrange("p (c t) -> p c t", c=NCH)[:, :, B_CHUNK - 1],
                                 ACT.Exp, scale=g).then_inc(g_exp.h, 1)
            for ct in range(2):
                act.e.wait_ge(conv.h, conv.by(act.l, 2 * TAPS - 1 + ct))
                nc.scalar.activation(T(t_csq[ct]), T(t_hc[ct]), ACT.Square).then_inc(conv_sq.h, 1)
            for q in range(2):
                act.e.wait_ge(dv_ps.h, dv_ps.by(act.l, q + 1))
                nc.scalar.activation(T(t_dv + q), pb[6 + q][:, :], ACT.Copy).then_inc(dv_sb.h, 1)
            for i in range(8 + 1):
                if i < 8:
                    act.e.wait_ge(dh_ps.h, dh_ps.by(act.l, i + 1))
                    if i >= 2:
                        act.e.wait_ge(dn_x.h, dn_x.by(act.l, i - 1))
                    nc.scalar.activation(T(t_hraw[i % 2])[0:D_QK, :], pb[i % 2][0:D_QK, :], ACT.Copy)
                    nc.scalar.activation(T(t_hsq[i % 2])[0:D_QK, :], pb[i % 2][0:D_QK, :], ACT.Square).then_inc(dh_sq.h, 1)
                if i >= 1:
                    u = i - 1
                    act.e.wait_ge(dn_ps.h, dn_ps.by(act.l, u + 1))
                    if u >= 2:
                        act.e.wait_ge(dh_ready.h, dh_ready.by(act.l, u - 1))
                    rstd(act, pb[2][0:D_QK, :], T(t_hr[u % 2])[0:D_QK, :], dn_ln, dn_r, u + 1)
            act.e.wait_ge(mn_ps.h, mn_ps.by(act.l, 7))
            rstd(act, pb[6][:, :], T(t_cr), mn_ln, mn_r, 7)
            act.e.wait_ge(kt_ps.h, kt_ps.by(act.l, 1))
            nc.scalar.activation(T(t_kdt), pb[7][:, :], ACT.Copy).then_inc(kt_sb.h, 1)
            for pr in range(2):
                act.e.wait_ge(o_ps.h, o_ps.by(act.l, pr + 1))
                nc.scalar.activation(T(t_o[pr]), pb[pr][:, :], ACT.Copy)
                nc.scalar.activation(T(t_osq[pr]), pb[pr][:, :], ACT.Square).then_inc(o_sq.h, 1)
            for pr in range(2):
                act.e.wait_ge(on_ps.h, on_ps.by(act.l, pr + 1))
                rstd(act, pb[2 + pr][:, :], T(t_or[pr]), on_ln, on_r, pr + 1)
            act.e.wait_ge(mn_x.h, mn_x.by(act.l, 9))
            for ct in range(2):
                nc.scalar.activation(y[:, 4 + ct, :], T(t_hc[ct]), ACT.Silu).then_inc(y_conv.h, 1)

        def act_attention(act, units, ytile, st, order, mixed):
            U = len(units)
            for i in range(U + 4):
                if i < U:
                    N = (units[i][2] + 1) * P
                    act.e.wait_ge(att_max.h, att_max.by(act.l, i + 1))
                    if i >= 3:
                        act.e.wait_ge(att_t.h, att_t.by(act.l, i - 2))
                    c = i % 4
                    nc.scalar.activation(p_buf(units, i)[:, 0:N], pb[(0, 1, 4, 5)[i % 4]][:, 0:N], ACT.Exp,
                                         bias=nmax[:, c:c + 1], accum_out=psum_[:, c:c + 1]).then_inc(att_exp.h, 1)
                u = i - 4
                if u >= 0 and u % 8 == 7:
                    act.e.wait_ge(att_o.h, att_o.by(act.l, u + 1))
                    o = pb[6 + (u // 8) % 2][:, :]
                    nc.scalar.activation(xn_hi[:, ytile(u // 8), :], o, ACT.Copy).then_inc(xn_hi_ready.h, 1)
                    nc.scalar.activation(y[:, ytile(u // 8), :], o, ACT.Copy).then_inc(y_att.h, 1)
                if 6 <= i < 10:
                    mixed(act, i - 6)
                    k = order[i - 6]
                    nc.scalar.activation(xn_hi[:, k, :], y[:, k, :], ACT.Copy).then_inc(xn_hi_ready.h, 1)
                if 12 <= i < 12 + SLOTS:
                    act.e.wait_ge(u_in[i - 12].h, st.loaded(i - 12))
                    split_unit(i - 12)
            act_units(act, st, SLOTS, KD)

        def act_units(act, st, a, b):
            for n in range(a, b):
                act.e.wait_ge(u_in[n % SLOTS].h, st.loaded(n))
                split_unit(n % SLOTS)

        def hyb_mixed(act, n):
            if n < 2:
                act.e.wait_ge(y_b.h, y_b.by(act.l, n + 1))
            else:
                act.e.wait_ge(y_conv.h, y_conv.by(act.l, n - 1))

        def even_mixed(act, n):
            act.e.wait_ge(y_ssm.h, n + 1)

        TWO_PI = 6.283185

        def act_even(act):
            act.e.wait_ge(pro_sb.h, 4)
            nc.scalar.activation(c_dt, c_ldt, ACT.Exp).then_inc(par_act.h, 1)
            act.e.wait_ge(par.h, 2)
            nc.scalar.activation(c_r, c_ard, ACT.Exp).then_inc(par_act.h, 1)
            act.e.wait_ge(par.h, 6)
            nc.scalar.activation(c_sin, c_fr, ACT.Sin, scale=TWO_PI).then_inc(par_act.h, 1)
            act.e.wait_ge(par.h, 8)
            nc.scalar.activation(c_cos, c_f2, ACT.Sin, scale=TWO_PI).then_inc(par_act.h, 1)
            nz = j = ny = 0
            nu = 0
            nps = 0

            def trig(j):
                if j >= 3:
                    act.e.wait_ge(s5_p.h, j - 2)
                    act.e.wait_ge(s5_q.h, j - 2)
                act.e.wait_ge(s5_frac.h, j + 1)
                nc.scalar.activation(s5_sin[j % 3], s5_d[j % 2], ACT.Sin, scale=TWO_PI).then_inc(s5_trig.h, 1)
                act.e.wait_ge(s5_quart.h, j + 1)
                nc.scalar.activation(s5_cos[j % 3], s5_d2[j % 2], ACT.Sin, scale=TWO_PI).then_inc(s5_trig.h, 1)
            for t in E_SEQ:
                if t[0] == "z":
                    _, b, c, n, i = t
                    if c:
                        nu += 1
                        act.e.wait_ge(w_used.h, nu)
                    else:
                        nps += 1
                        act.e.wait_ge(ez_ps.h, nps)
                    bank = pb[nz % 2]
                    nz += 1
                    if n == "v":
                        nc.scalar.activation(e_vv[:, 2 * c:2 * c + 2, (b % 2) * 256:(b % 2 + 1) * 256],
                                             bank[:, :].rearrange("p (q c) -> p q c", q=2), ACT.Copy).then_inc(ez_sb.h, 1)
                    else:
                        dst = T(dict(u=e_u, q=e_q, k=e_k)[n] + i)
                        nc.scalar.activation(dst, bank[:, :], ACT.Copy,
                                             scale=float(E_DIM ** -0.5) if n == "q" else 1.0).then_inc(ez_sb.h, 1)
                elif t[0] == "prep":
                    for q, dst in enumerate((e_btr, e_bti)):
                        act.e.wait_ge(bc_ps.h, q + 1)
                        nc.scalar.activation(T(dst), pb[2 + q][:, :], ACT.Copy).then_inc(bt_sb.h, 1)
                    act.e.wait_ge(tab.h, 8)
                    nc.scalar.activation(T(e_sin), T(e_tmp[3]), ACT.Sin).then_inc(tab_sin.h, 1)
                    act.e.wait_ge(tab.h, 16)
                    nc.scalar.activation(T(e_cos), T(e_tmp[3]), ACT.Sin).then_inc(tab_sin.h, 1)
                    trig(0)
                elif t[0] == "bu" and t[1] + 1 < NST:
                    trig(t[1] + 1)
            for i in range(4):
                act.e.wait_ge(s5_y.h, i + 1)
                nc.scalar.activation(T(e_u + i), T(e_u + i), ACT.Gelu_apprx_tanh).then_inc(s5_gelu.h, 1)
            nu += 1
            for c in range(4):
                if c % 2:
                    act.e.wait_ge(w_used.h, nu + c // 2)
                else:
                    act.e.wait_ge(glu_ps.h, c // 2 + 1)
                nc.scalar.activation(T(e_glu + c), pb[2 + c][:, :], ACT.Sigmoid).then_inc(glu_sb.h, 1)

        def act_post(act, m):
            nc.scalar.preload_act_table_set(LN_EXP)
            for k in range(KD):
                act.e.wait_ge(r_ready.h, m * KD + k + 1)
                nc.scalar.activation(T(SQ + k), T(RB + k), ACT.Square).then_inc(rsq.h, 1)
            act.e.wait_ge(rn_ps.h, m + 1)
            nc.scalar.activation(T(RT2), pb[6][:, :], ACT.Ln, bias=C("eps")).then_inc(rn_ln.h, 1)
            act.e.wait_ge(rn_ln.h, m + 1)
            nc.scalar.activation(T(RT2), T(RT2), ACT.Exp, scale=-0.5).then_inc(rn_r.h, 1)

        def act_odd(act):
            act.e.wait_ge(sp_step.h, 2)
            nc.scalar.activation(spc[:, 1, :], spc[:, 0, :], ACT.Exp, scale=-1.0).then_inc(par_act.h, 1)
            act.e.wait_ge(pad_zero.h, 1)
            st = STAGES["in", "odd"]
            act_units(act, st, 2, 3)
            for n in range(2 * KD):
                act.e.wait_ge(unit_ps.h, st.units + n + 1)
                if n < KD:
                    nc.scalar.activation(xpad[:, n, LRU_TAPS - 1:], pb[n % 4][:, :], ACT.Copy).then_inc(oz_sb.h, 1)
                else:
                    nc.scalar.activation(T(o_gel + n - KD), pb[n % 4][:, :], ACT.Gelu_apprx_tanh).then_inc(oz_sb.h, 1)
                act_units(act, st, n + 3, min(n + 4, 2 * KD))
            for n in range(2 * KD):
                g, m = n // KD, n % KD
                if m == KD - 1:
                    act.e.wait_ge(w_used.h, USE_ODD + 1 + g)
                else:
                    act.e.wait_ge(og_ps.h, g * (KD - 1) + m + 1)
                bcol = R2["rg_b_i_2" if g else "rg_b_r_2"] + m
                nc.scalar.activation(T((o_i if g else o_r) + m), pb[n % 4][:, :], ACT.Sigmoid,
                                     bias=col2[:, bcol:bcol + 1]).then_inc(og_sb.h, 1)
            act.e.wait_ge(og_sb.h, KD)
            act.e.wait_ge(sp_step.h, SP_STEPS)
            for k in range(KD):
                nc.scalar.activation(o_fac[:, k, :], T(o_r + k), ACT.Tanh, scale=spc[:, 7, k:k + 1]).then_inc(o_th.h, 1)
            for k in range(KD):
                nc.scalar.activation(T(o_r + k), T(o_r + k), ACT.Exp, scale=spc[:, 7, k:k + 1]).then_inc(o_a.h, 1)
            act_units(act, STAGES["out", "odd"], 0, SLOTS)
            for k in range(KD):
                act.e.wait_ge(o_q.h, k + 1)
                nc.scalar.activation(o_fac[:, k, :], o_fac[:, k, :], ACT.Sqrt, scale=-1.0).then_inc(o_sqrt.h, 1)
            for k in range(KD):
                act.e.wait_ge(y_lru.h, k + 1)
                nc.scalar.activation(xn_hi[:, k, :], y[:, k, :], ACT.Copy).then_inc(xn_hi_ready.h, 1)
            act_units(act, STAGES["out", "odd"], SLOTS, KD)

        @block.scalar
        def _(e):
            act = Eng(e)
            e.sem_inc(sg_ready.h, sg_ready.start)
            act.e.wait_ge(rows_zero.h, 1)
            for i, n in enumerate(R1):
                e.dma_start(rows[R1[n]:R1[n] + 2 * KD, 0, :],
                            I[n].rearrange("l (k p) -> (l k) p", p=P)).then_inc(rows_in.h, 16)
            for l in range(DEPTH):
                for n, c in LAYER_ROWS:
                    r = l * NRL + RL[n]
                    w = I[n].shape[1]
                    if w == 64:
                        for q in range(2):
                            e.dma_start(rows[r:r + 1, 1, q * 64:(q + 1) * 64], I[n][l:l + 1, :]).then_inc(rows_in.h, 16)
                    elif w == D_QK:
                        e.dma_start(rows[r:r + 1, 1, 0:w], I[n][l:l + 1, :]).then_inc(rows_in.h, 16)
                    else:
                        e.dma_start(rows[r:r + c, 1, :], I[n][l].rearrange("(k p) -> k p", p=P)).then_inc(rows_in.h, 16)
            e.dma_start(rows[R2["s5_d_2"]:R2["s5_d_2"] + 4, 1, :],
                        I["s5_d_2"][0].rearrange("(k g) c -> k (g c)", k=4)).then_inc(rows_in.h, 16)
            for n in ("rg_conv_b_2", "rg_b_r_2", "rg_b_i_2", "rg_lam_2"):
                e.dma_start(rows[R2[n]:R2[n] + 8, 1, :], I[n][0].rearrange("(k p) -> k p", p=P)).then_inc(rows_in.h, 16)
            e.dma_start(rows[R2["rg_conv_w_2"]:R2["rg_conv_w_2"] + 32, 1, :],
                        I["rg_conv_w_2"][0].rearrange("j (k p) -> (j k) p", p=P)).then_inc(rows_in.h, 16)
            e.dma_start(rows[0:NR3, 2, :],
                        I["c_dw_w"].rearrange("l j o (t p) -> (l j o t) p", p=P)).then_inc(rows_in.h, 16)
            for i, n in enumerate(("s5_a_re_2", "s5_a_im_2")):
                e.dma_start(rows[i * NST:(i + 1) * NST, 3, :], I[n][0].rearrange("(j q) p -> j (q p)", q=2)).then_inc(rows_in.h, 16)
            e.dma_start(ldt[32:32 + NST, :], I["s5_log_dt_2"][0].rearrange("(j q) -> j q", q=2)).then_inc(ldt_in.h, 16)
            act.e.wait_ge(pro_ps.h, KD + 4)
            for i, (dst, n) in enumerate(((col1, NR1), (col2, NR2), (col3, NR3), (s5col, 3 * NST))):
                dst = dst[:, 0:3, :].rearrange("p a c -> p (a c)") if dst is s5col else dst[:, :]
                nc.scalar.activation(dst, pb[2 + i][:, 0:n], ACT.Copy).then_inc(pro_sb.h, 1)
            half = BIAS_N // 2
            bv4 = arena[0:A_HEADS, 20:22, 0:half]
            act.e.wait_ge(pro_ps.h, KD + 4 + 2)
            for q in range(2):
                nc.scalar.activation(bv4[:, q, :], pb[6 + q][0:A_HEADS, 0:half], ACT.Copy).then_inc(pro_sb.h, 1)
            act.e.wait_ge(pro_sb.h, 4 + 2)
            e.dma_start(bias_dram.ap().rearrange("h (q n) -> h q n", q=2), bv4).then_inc(bias_dma.h, 16)
            act.e.wait_ge(bias_dma.h, 16)
            e.dma_start(arena[:, 8:8 + A_HEADS, :], bass.AP(bias_dram, 0, [[1, P], [BIAS_N, A_HEADS], [1, SEQ]])
                        ).then_inc(bias_dma.h, 16)
            for h in range(A_HEADS):
                act.e.wait_ge(pro_ps.h, KD + 4 + 2 + h + 1)
                nc.scalar.activation(bias[:, h, :], pb[h][:, :], ACT.Copy).then_inc(pro_sb.h, 1)
            for l in range(DEPTH):
                act.l = l
                act_norm(act, l * 3, STAGES["ffn1", l])
                act_ffn(act, STAGES["ffn1", l])
                act_norm(act, l * 3 + 1, STAGES["in", l])
                act_z(act, STAGES["in", l])
                act_mixers(act)
                act_attention(act, HYB_UNITS, lambda p: (6, 7, 0, 1)[p], STAGES["out", l], Y_HYB, hyb_mixed)
                act_norm(act, l * 3 + 2, STAGES["ffn2", l])
                act_ffn(act, STAGES["ffn2", l])
            act.l = DEPTH
            n = 3 * DEPTH
            act_norm(act, n)
            act_even(act)
            act_attention(act, E_UNITS, lambda p: p, STAGES["out", "even"], Y_EVEN, even_mixed)
            act_post(act, 0)
            act_norm(act, n + 1, STAGES["ffn", "even"])
            act_ffn(act, STAGES["ffn", "even"])
            act_post(act, 1)
            act_norm(act, n + 2, STAGES["in", "odd"])
            act_odd(act)
            act_post(act, 2)
            act_norm(act, n + 3, STAGES["ffn", "odd"])
            act_ffn(act, STAGES["ffn", "odd"])
            act_post(act, 3)
            for n in range(2 * TB):
                act.e.wait_ge(fin_ps.h, n + 1)
                nc.scalar.activation(arena[:, n, :], pb[n % 2][:, :], ACT.Copy).then_inc(fin_sb.h, 1)

        def dve_norm(dve, n, g, st=None):
            if st:
                for q in range(2):
                    dve.e.wait_ge(u_hi.h, st.units + q + 1)
                    split_rest(q)
            dve.e.wait_ge(norm_r.h, n + 1)
            for k in range(KD):
                nc.vector.scalar_tensor_tensor(out=xn[:, k, :], in0=x[:, k, :], scalar=g(k), in1=T(RT),
                                               op0=ALU.mult, op1=ALU.mult).then_inc(xn_ready.h, 1)
                if st and k >= 1:
                    split_chunk(dve, st, k - 1, k - 1)
            if st:
                split_chunk(dve, st, KD - 1, KD - 1)

        def split_chunk(dve, st, n, k):
            dve.e.wait_ge(xn_hi_ready.h, st.splits * KD + n + 1)
            nc.vector.tensor_tensor(xn_lo[:, k, :], xn[:, k, :], chunk_hi(st, k).bitcast(F32),
                                    ALU.subtract).then_inc(xn_lo_ready.h, 1)

        def split_rest(slot):
            nc.vector.tensor_tensor(w_lo[:, slot, :, :].rearrange("p k c -> p (k c)"), wunit[:, slot, :],
                                    w_hi[:, slot, :, :].rearrange("p k c -> p (k c)").bitcast(F32),
                                    ALU.subtract).then_inc(u_lo.h, 1)

        def dve_ffn(dve, st, take):
            f = st.ffns
            with dve.e.Fori(0, NF // 2) as i:
                for c in range(2):
                    for q in range(2):
                        dve.e.wait_ge(u_hi.h, st.units + SLOTS * i + (2 * c + q + 3))
                        split_rest((2 * c + q + 2) % SLOTS)
                    dve.e.wait_ge(sg_ready.h, sg_ready.start + f * NF + 2 * i + (c + 1))
                    dve.e.wait_ge(unit_ps.h, st.units + SLOTS * i + (2 * c + 2))
                    h = arena[:, bass.ds(2 * i + (H_LO + c), 1), :].rearrange("p a c -> p (a c)")
                    nc.vector.tensor_tensor(h, pb[2 + c][:, :], sg[:, c, :], ALU.mult).then_inc(h_full.h, 1)
                    dve.e.wait_ge(h_hi_ready.h, f * NF + 2 * i + (c + 1))
                    hi, lo = [t[:, bass.ds(2 * i + c, 1), :].rearrange("p a c -> p (a c)") for t in (h_hi, h_lo)]
                    nc.vector.tensor_tensor(lo, h, hi.bitcast(F32), ALU.subtract).then_inc(h_lo_ready.h, 1)
            with dve.e.Fori(0, NF // SLOTS) as i:
                for q in range(SLOTS):
                    dve.e.wait_ge(u_hi.h, st.units + 2 * NF + SLOTS * i + (q + 3))
                    split_rest((q + 2) % SLOTS)
            dve_take(dve, st, take)

        def dve_take(dve, st, take):
            for m in range(KD):
                if m < KD - 1:
                    dve.e.wait_ge(down_ps.h, st.results * (KD - 1) + m + 1)
                else:
                    dve.e.wait_ge(unit_ps.h, st.units + len(st.loads))
                take(m)

        def dve_units(dve, st, a, b):
            for n in range(a, b):
                dve.e.wait_ge(u_hi.h, st.units + n + 1)
                split_rest(n % SLOTS)

        def add(m):
            nc.vector.tensor_tensor(x[:, m, :], down_bank(m), x[:, m, :], ALU.add).then_inc(x_ready.h, 1)

        def add_half(m):
            nc.vector.scalar_tensor_tensor(out=x[:, m, :], in0=down_bank(m), scalar=0.5, in1=x[:, m, :],
                                           op0=ALU.mult, op1=ALU.add).then_inc(x_ready.h, 1)

        def dve_index(dve):
            ni = nt = 0
            for tb in (3, 2, 1):
                N = (tb + 1) * P
                for h in range(IDX_HEADS):
                    dve.e.wait_ge(z_sb.h, z_sb.by(dve.l, IDX_POS[ni] + 1))
                    w = wA[:, tb * 8 + h:tb * 8 + h + 1]
                    r = idx_r[ni % 4][:, 0:N]
                    if h == 0:
                        ins = nc.vector.tensor_scalar(score(tb), r, w, None, ALU.mult)
                    else:
                        dve.e.wait_ge(idx_acc.h, idx_acc.by(dve.l, ni))
                        ins = nc.vector.scalar_tensor_tensor(out=score(tb), in0=r, scalar=w, in1=score(tb),
                                                             op0=ALU.mult, op1=ALU.add)
                    ins.then_inc(idx_acc.h, 1)
                    ni += 1
                dve.e.wait_ge(idx_acc.h, idx_acc.by(dve.l, ni))
                dg = score(tb)[:, tb * P:]
                nc.vector.tensor_tensor(dg, dg, C("causal"), ALU.add).then_inc(idx_mask.h, 1)
                dve.e.wait_ge(idx_mask.h, idx_mask.by(dve.l, 4 - tb))
                for r in range(TOPK // 8):
                    if r:
                        dve.e.wait_ge(top_rep.h, top_rep.by(dve.l, nt))
                    nc.vector.max(m8, score(tb)).then_inc(top_max.h, 1)
                    nt += 1
                    dve.e.wait_ge(top_max.h, top_max.by(dve.l, nt))
                    nc.vector.match_replace(score(tb), m8, score(tb), SENTINEL).then_inc(top_rep.h, 1)
                dve.e.wait_ge(top_rep.h, top_rep.by(dve.l, nt))
                nc.vector.tensor_scalar(score(tb), score(tb), 0.9 * SENTINEL, NEG, ALU.is_gt, ALU.mult).then_inc(top_done.h, 1)

        def dve_conv(dve):
            dve.e.wait_ge(hp_ready.h, hp_ready.by(dve.l, 2))
            for n in range(2 * TAPS):
                j, ct = n // 2, n % 2
                w = cur_dw[:, n:n + 1]
                src = hpad[:, ct, j:j + SEQ]
                if j == 0:
                    b = RL["c_dw_b"] + ct
                    ins = nc.vector.tensor_scalar(T(t_hc[ct]), src, w, cur[:, b:b + 1], ALU.mult, ALU.add)
                else:
                    dve.e.wait_ge(conv.h, conv.by(dve.l, n - 1))
                    ins = nc.vector.scalar_tensor_tensor(out=T(t_hc[ct]), in0=src, scalar=w, in1=T(t_hc[ct]),
                                                         op0=ALU.mult, op1=ALU.add)
                ins.then_inc(conv.h, 1)

        def dve_mixers(dve):
            dve.e.wait_ge(g_abs.h, g_abs.by(dve.l, 1))
            nc.vector.tensor_scalar(W(w_mn), W(w_mn), 0.0, None, ALU.min).then_inc(g_min.h, 1)
            dve.e.wait_ge(g_min.h, g_min.by(dve.l, 1))
            dve.e.wait_ge(g_abs.h, g_abs.by(dve.l, 4))
            nc.vector.tensor_tensor(W(w_la), W(w_mn), T(t_ab), ALU.subtract).then_inc(g_b.h, 1)
            dve.e.wait_ge(g_b.h, g_b.by(dve.l, 1))
            nc.vector.tensor_tensor_scan(W(w_mn), C("chunkmask"), W(w_la), 0.0, ALU.mult, ALU.add).then_inc(g_b.h, 1)
            dve.e.wait_ge(g_b.h, g_b.by(dve.l, 2))

            def chunks(t):
                return t.rearrange("p (c t) -> p c t", c=NCH)
            b = chunks(W(w_mn))
            mid = b[:, :, B_CHUNK // 2 - 1:B_CHUNK // 2].to_broadcast([P, NCH, B_CHUNK])
            end = b[:, :, B_CHUNK - 1:B_CHUNK].to_broadcast([P, NCH, B_CHUNK])
            nc.vector.tensor_tensor(chunks(T(t_ab)), end, b, ALU.subtract).then_inc(g_b.h, 1)
            nc.vector.tensor_tensor(chunks(W(w_la)), b, mid, ALU.subtract).then_inc(g_b.h, 1)
            dve.e.wait_ge(g_b.h, g_b.by(dve.l, 4))
            lim = 16.0 * 85.0
            nc.vector.tensor_scalar(W(w_la), W(w_la), lim, -lim, ALU.min, ALU.max).then_inc(g_b.h, 1)
            dve.e.wait_ge(g_b.h, g_b.by(dve.l, 5))
            nc.vector.tensor_scalar(T(t_ab), T(t_ab), 0.0, None, ALU.min).then_inc(g_b.h, 1)
            for i, (t, r, gc) in enumerate([(t_aq[0], 0, "a_q_norm"), (t_aq[1], 1, "a_q_norm"), (t_ak[0], 2, "a_k_norm"),
                                            (t_ak[1], 3, "a_k_norm"), (t_dcq[0], 4, "d_qa_norm"),
                                            (t_dcq[1], 4, "d_qa_norm"), (t_dckv, 5, "d_kva_norm")]):
                col = RL[gc] + (1 if i == 5 else 0)
                dve.e.wait_ge(mn_r.h, mn_r.by(dve.l, r + 1))
                nc.vector.scalar_tensor_tensor(out=T(t), in0=T(t), scalar=cur[:, col:col + 1], in1=T(t_zr[r]),
                                               op0=ALU.mult, op1=ALU.mult).then_inc(mn_x.h, 1)
            for n, (e_, t) in enumerate(((T(t_qe), t_bq), (W(w_e1), t_bq), (W(w_e2), t_bk))):
                dve.e.wait_ge(g_exp.h, g_exp.by(dve.l, (1, 2, 4)[n]))
                nc.vector.tensor_tensor(e_, e_, T(t), ALU.mult).then_inc(b_qk.h, 1)
            for i in range(8 + 1):
                if i < 8:
                    col = RL["d_q_norm" if i < 4 else "d_k_norm"]
                    dve.e.wait_ge(dn_r.h, dn_r.by(dve.l, i + 1))
                    if i >= 2:
                        dve.e.wait_ge(dr_c.h, dr_c.by(dve.l, i - 1))
                    nc.vector.scalar_tensor_tensor(out=T(t_hn[i % 2])[0:D_QK, :], in0=T(t_hraw[i % 2])[0:D_QK, :],
                                                   scalar=cur[0:D_QK, col:col + 1], in1=T(t_hr[i % 2])[0:D_QK, :],
                                                   op0=ALU.mult, op1=ALU.mult).then_inc(dn_x.h, 1)
                if i >= 1:
                    u = i - 1
                    dve.e.wait_ge(dr_ps.h, dr_ps.by(dve.l, u + 1))
                    nc.vector.tensor_tensor(T(t_hr[u % 2])[0:D_QK, :], pb[3][0:D_QK, :], C("sin96")[0:D_QK, :],
                                            ALU.mult).then_inc(dr_s.h, 1)
            dve.e.wait_ge(mn_r.h, mn_r.by(dve.l, 7))
            for ct in range(2):
                col = RL["c_norm"] + ct
                nc.vector.scalar_tensor_tensor(out=T(t_hc[ct]), in0=T(t_hc[ct]), scalar=cur[:, col:col + 1], in1=T(t_cr),
                                               op0=ALU.mult, op1=ALU.mult).then_inc(mn_x.h, 1)
            for c in range(NCH - 1):
                dve.e.wait_ge(u_ps.h, u_ps.by(dve.l, c + 1))
                um = Sst(1) if c == 0 else T(t_um)[:, (c % 2) * 256:(c % 2) * 256 + 256]
                nc.vector.tensor_tensor(um, pb[2 + c % 2][:, 0:256], C("headblk"), ALU.mult).then_inc(u_msk.h, 1)
                dve.e.wait_ge(u_msk.h, u_msk.by(dve.l, c + 1))
                if c == 0:
                    dve.e.sem_inc(s_ready.h, 1)
                    continue
                dve.e.wait_ge(s_ready.h, s_ready.by(dve.l, c))
                nc.vector.scalar_tensor_tensor(out=Sst(c + 1), in0=Sst(c), scalar=glast[:, c:c + 1], in1=um,
                                               op0=ALU.mult, op1=ALU.add).then_inc(s_ready.h, 1)
            for tb in range(TB):
                dve.e.wait_ge(at_ps.h, at_ps.by(dve.l, tb + 1))
                for q in range(2):
                    r = slice(64 * q, 64 * q + 64)
                    src = pb[4 + tb % 2][r, :].rearrange("p (h c) -> p h c", h=B_HEADS)[:, :, r]
                    tri = C("tri")[r, :].unsqueeze(1).to_broadcast([64, B_HEADS, B_CHUNK])
                    nc.vector.tensor_tensor(att_diag[r, tb, :, r], src, tri, ALU.mult).then_inc(at_sb.h, 1)
            for pr in range(2):
                col = RL["b_out_norm"]
                dve.e.wait_ge(on_r.h, on_r.by(dve.l, pr + 1))
                nc.vector.scalar_tensor_tensor(out=T(t_o[pr]), in0=T(t_o[pr]), scalar=cur[:, col:col + 1],
                                               in1=T(t_or[pr]), op0=ALU.mult, op1=ALU.mult).then_inc(o_n.h, 1)

        def dve_attention(dve, units, st, order):
            U = len(units)
            for i in range(U + 2):
                if i < U:
                    N = (units[i][2] + 1) * P
                    c = i % 4
                    dve.e.wait_ge(att_s.h, att_s.by(dve.l, i + 1))
                    nc.vector.tensor_reduce(nmax[:, c:c + 1], pb[(0, 1, 4, 5)[i % 4]][:, 0:N], AX.X, ALU.max,
                                            negate=True).then_inc(att_max.h, 1)
                if 1 <= i < U + 1:
                    u = i - 1
                    c = u % 4
                    dve.e.wait_ge(att_exp.h, att_exp.by(dve.l, u + 1))
                    if u >= 4:
                        dve.e.wait_ge(att_p.h, att_p.by(dve.l, u - 3))
                    nc.vector.reciprocal(rsum[:, c:c + 1], psum_[:, c:c + 1]).then_inc(att_rs.h, 1)
                if i >= 2:
                    u = i - 2
                    N = (units[u][2] + 1) * P
                    dve.e.wait_ge(att_t.h, att_t.by(dve.l, u + 1))
                    if u >= 2:
                        dve.e.wait_ge(att_o.h, att_o.by(dve.l, u - 1))
                    nc.vector.tensor_copy(pt_buf(units, u)[:, 0:N], pb[2 + u % 2][:, 0:N]).then_inc(att_pt.h, 1)
                if 8 <= i < 12:
                    split_chunk(dve, st, i - 8, order[i - 8])
                if 15 <= i < 15 + SLOTS:
                    dve_units(dve, st, i - 15, i - 14)
                if i in (13, 21, 29):
                    n = 4 + (i - 13) // 8
                    y_copied(dve, n - 3)
                    split_chunk(dve, st, n, order[n])
            y_copied(dve, 4)
            split_chunk(dve, st, KD - 1, order[KD - 1])
            dve_units(dve, st, SLOTS, KD)

        def y_copied(dve, n):
            dve.e.wait_ge(y_att.h, y_att.by(dve.l, n))

        def to_r(m):
            nc.vector.tensor_copy(T(RB + m), down_bank(m)).then_inc(r_ready.h, 1)

        def dve_post(dve, m, g):
            dve.e.wait_ge(rn_r.h, m + 1)
            for k in range(KD):
                nc.vector.scalar_tensor_tensor(out=T(RB + k), in0=T(RB + k), scalar=g(k), in1=T(RT2),
                                               op0=ALU.mult, op1=ALU.mult).then_inc(r_n.h, 1)
            for k in range(KD):
                dve.e.wait_ge(r_n.h, m * KD + k + 1)
                nc.vector.tensor_tensor(x[:, k, :], x[:, k, :], T(RB + k), ALU.add).then_inc(x_ready.h, 1)

        C1 = 6.28125
        C2 = float(np.float32(np.round((2 * math.pi - C1) * 2 ** 21) / 2 ** 21))
        C3 = float(np.float32(2 * math.pi - C1 - C2))

        def dve_even(dve):
            V = nc.vector
            ts, tt, stt = V.tensor_scalar, V.tensor_tensor, V.scalar_tensor_tensor
            par_n = count(1)
            dve.e.wait_ge(pro_sb.h, 4)
            dve.e.wait_ge(par_act.h, 1)
            tt(c_th, c_aim, c_dt, ALU.mult).then_inc(par.h, 1)
            dve.e.wait_ge(par.h, next(par_n))
            tt(c_ard, c_are, c_dt, ALU.mult).then_inc(par.h, 1)
            dve.e.wait_ge(par.h, next(par_n))
            ts(c_t1, c_th, float(1 / (2 * math.pi)), None, ALU.mult).then_inc(par.h, 1)
            dve.e.wait_ge(par.h, next(par_n))
            ts(c_n, c_t1, MAGIC, None, ALU.add).then_inc(par.h, 1)
            dve.e.wait_ge(par.h, next(par_n))
            ts(c_n, c_n, MAGIC, None, ALU.subtract).then_inc(par.h, 1)
            dve.e.wait_ge(par.h, next(par_n))
            tt(c_fr, c_t1, c_n, ALU.subtract).then_inc(par.h, 1)
            dve.e.wait_ge(par.h, next(par_n))
            ts(c_t2, c_fr, 0.25, None, ALU.is_gt).then_inc(par.h, 1)
            dve.e.wait_ge(par.h, next(par_n))
            stt(c_f2, c_fr, 0.25, c_t2, ALU.add, ALU.subtract).then_inc(par.h, 1)
            dve.e.wait_ge(par.h, next(par_n))
            dve.e.wait_ge(par_act.h, 4)
            tt(c_nre, c_r, c_cos, ALU.mult).then_inc(par.h, 1)
            dve.e.wait_ge(par.h, next(par_n))
            ts(c_nre, c_nre, 1.0, None, ALU.subtract).then_inc(par.h, 1)
            dve.e.wait_ge(par.h, next(par_n))
            tt(c_nim, c_r, c_sin, ALU.mult).then_inc(par.h, 1)
            dve.e.wait_ge(par.h, next(par_n))
            tt(c_den, c_are, c_are, ALU.mult).then_inc(par.h, 1)
            dve.e.wait_ge(par.h, next(par_n))
            tt(c_t1, c_aim, c_aim, ALU.mult).then_inc(par.h, 1)
            dve.e.wait_ge(par.h, next(par_n))
            tt(c_den, c_den, c_t1, ALU.add).then_inc(par.h, 1)
            dve.e.wait_ge(par.h, next(par_n))
            V.reciprocal(c_den, c_den).then_inc(par.h, 1)
            dve.e.wait_ge(par.h, next(par_n))
            tt(c_t1, c_nre, c_are, ALU.mult).then_inc(par.h, 1)
            dve.e.wait_ge(par.h, next(par_n))
            tt(c_t2, c_nim, c_aim, ALU.mult).then_inc(par.h, 1)
            dve.e.wait_ge(par.h, next(par_n))
            tt(c_fre, c_t1, c_t2, ALU.add).then_inc(par.h, 1)
            dve.e.wait_ge(par.h, next(par_n))
            tt(c_fre, c_fre, c_den, ALU.mult).then_inc(par.h, 1)
            dve.e.wait_ge(par.h, next(par_n))
            tt(c_t1, c_nim, c_are, ALU.mult).then_inc(par.h, 1)
            dve.e.wait_ge(par.h, next(par_n))
            tt(c_t2, c_nre, c_aim, ALU.mult).then_inc(par.h, 1)
            dve.e.wait_ge(par.h, next(par_n))
            tt(c_fim, c_t1, c_t2, ALU.subtract).then_inc(par.h, 1)
            dve.e.wait_ge(par.h, next(par_n))
            tt(c_fim, c_fim, c_den, ALU.mult).then_inc(par.h, 1)
            dve.e.wait_ge(par.h, next(par_n))
            dve.e.wait_ge(s5_in.h, 16 * 7)
            bre, bim = [T(e_bst)[:, q * 256:(q + 1) * 256].rearrange("p (j c) -> p j c", c=SSM_C) for q in range(2)]
            sc = [T(e_tmp[1])[:, 0:256], T(e_tmp[1])[:, 256:], T(e_tmp[2])[:, 0:256], T(e_tmp[2])[:, 256:]]
            sc = [t.rearrange("p (j c) -> p j c", c=SSM_C) for t in sc]

            def wide(c):
                return c.unsqueeze(2).to_broadcast([P, NST, SSM_C])
            tt(sc[0], bre, wide(c_fre), ALU.mult).then_inc(par.h, 1)
            dve.e.wait_ge(par.h, next(par_n))
            tt(sc[1], bim, wide(c_fim), ALU.mult).then_inc(par.h, 1)
            dve.e.wait_ge(par.h, next(par_n))
            tt(sc[2], bre, wide(c_fim), ALU.mult).then_inc(par.h, 1)
            dve.e.wait_ge(par.h, next(par_n))
            tt(sc[3], bim, wide(c_fre), ALU.mult).then_inc(par.h, 1)
            dve.e.wait_ge(par.h, next(par_n))
            tt(sc[0], sc[0], sc[1], ALU.subtract).then_inc(par.h, 1)
            dve.e.wait_ge(par.h, next(par_n))
            tt(sc[2], sc[2], sc[3], ALU.add).then_inc(par.h, 1)
            dve.e.wait_ge(par.h, next(par_n))
            half = C("half16").rearrange("p (q c) -> p q c", q=2).unsqueeze(1).to_broadcast([P, NST, 2, SSM_C])
            for src, dst in ((sc[0], e_ere), (sc[2], e_eim)):
                tt(T(dst).rearrange("p (j q c) -> p j q c", j=NST, q=2),
                        src.unsqueeze(2).to_broadcast([P, NST, 2, SSM_C]), half, ALU.mult).then_inc(par.h, 1)
                dve.e.wait_ge(par.h, next(par_n))
            assert next(par_n) == PAR_E + 1
            tab_n = count(1)
            ang, rnd, red = T(e_tmp[1]), T(e_tmp[2]), T(e_tmp[3])
            for q in range(2):
                if q == 0:
                    V.tensor_copy(ang, T(e_pos).bitcast(I32)).then_inc(tab.h, 1)
                    dve.e.wait_ge(tab.h, next(tab_n))
                    ts(ang, ang, C("freq"), None, ALU.mult).then_inc(tab.h, 1)
                    dve.e.wait_ge(tab.h, next(tab_n))
                    ts(rnd, ang, float(1 / (2 * math.pi)), MAGIC, ALU.mult, ALU.add).then_inc(tab.h, 1)
                    dve.e.wait_ge(tab.h, next(tab_n))
                else:
                    ts(rnd, ang, float(1 / (2 * math.pi)), 0.25, ALU.mult, ALU.add).then_inc(tab.h, 1)
                    dve.e.wait_ge(tab.h, next(tab_n))
                    ts(rnd, rnd, MAGIC, None, ALU.add).then_inc(tab.h, 1)
                    dve.e.wait_ge(tab.h, next(tab_n))
                ts(rnd, rnd, MAGIC, None, ALU.subtract).then_inc(tab.h, 1)
                dve.e.wait_ge(tab.h, next(tab_n))
                if q:
                    dve.e.wait_ge(tab_sin.h, 1)
                stt(red, rnd, -C1, ang, ALU.mult, ALU.add).then_inc(tab.h, 1)
                dve.e.wait_ge(tab.h, next(tab_n))
                stt(red, rnd, -C2, red, ALU.mult, ALU.add).then_inc(tab.h, 1)
                dve.e.wait_ge(tab.h, next(tab_n))
                stt(red, rnd, -C3, red, ALU.mult, ALU.add).then_inc(tab.h, 1)
                dve.e.wait_ge(tab.h, next(tab_n))
                if q:
                    ts(red, red, float(np.float32(math.pi / 2)), None, ALU.add).then_inc(tab.h, 1)
                    dve.e.wait_ge(tab.h, next(tab_n))
                lim = float(np.nextafter(np.float32(math.pi), np.float32(0)))
                ts(red, red, lim, -lim, ALU.min, ALU.max).then_inc(tab.h, 1)
                dve.e.wait_ge(tab.h, next(tab_n))
            dve.e.wait_ge(tab_sin.h, 2)
            cw = C("half16").unsqueeze(1).to_broadcast([P, NST, 2 * SSM_C])

            def tiles(t):
                return t.rearrange("p (j c) -> p j c", j=NST)
            dve.e.wait_ge(bc_ps.h, 4)
            dve.e.wait_ge(bt_sb.h, 2)
            tt(tiles(T(e_cre)), tiles(pb[4][:, :]), cw, ALU.mult).then_inc(cb_sb.h, 1)
            tt(tiles(T(e_cin)), tiles(pb[5][:, :]), cw, ALU.mult).then_inc(cb_sb.h, 1)
            dve.e.wait_ge(cb_sb.h, 2)
            ts(T(e_crn), T(e_cre), -1.0, None, ALU.mult).then_inc(cb_sb.h, 1)
            ts(T(e_cin), T(e_cin), -1.0, None, ALU.mult).then_inc(cb_sb.h, 1)

            def angles(j):
                dve.e.wait_ge(s5_rnd.h, 2 * j + 2)
                if j >= 2:
                    dve.e.wait_ge(s5_trig.h, 2 * (j - 2) + 2)
                stt(s5_d[j % 2], C("iota"), c_fr[:, j:j + 1], s5_n[j % 2], ALU.mult, ALU.subtract).then_inc(s5_frac.h, 1)
                dve.e.wait_ge(s5_frac.h, j + 1)
                dve.e.wait_ge(s5_wrap.h, j + 1)
                stt(s5_d2[j % 2], s5_d[j % 2], 0.25, s5_n[j % 2], ALU.add, ALU.subtract).then_inc(s5_quart.h, 1)

            def rotate_in(j):
                a = s5_a[j % 3]
                dve.e.wait_ge(bu_ps.h, j + 1)
                dve.e.wait_ge(s5_trig.h, 2 * j + 2)
                if j >= 3:
                    dve.e.wait_ge(yy_ps.h, j - 2)
                if j == 2:
                    dve.e.wait_ge(tab_sin.h, 2)
                b = [pb[2 + 2 * (j % 2) + q][:, :] for q in range(2)]
                tt(a[0], b[0], s5_cos[j % 3], ALU.mult)
                tt(a[1], b[1], s5_sin[j % 3], ALU.mult)
                tt(a[2], b[1], s5_cos[j % 3], ALU.mult)
                tt(a[3], b[0], s5_sin[j % 3], ALU.mult).then_inc(s5_rot.h, 1)

            def scan(j):
                a = s5_a[j % 3]
                r = c_r[:, j:j + 1].to_broadcast([P, SEQ])
                dve.e.wait_ge(s5_x.h, 2 * j + 2)
                V.tensor_tensor_scan(a[1], r, a[0], 0.0, ALU.mult, ALU.add).then_inc(s5_g.h, 1)
                V.tensor_tensor_scan(a[3], r, a[2], 0.0, ALU.mult, ALU.add).then_inc(s5_g.h, 1)
                dve.e.wait_ge(s5_g.h, 2 * j + 1)
                tt(a[0], a[1], s5_cos[j % 3], ALU.mult)
                tt(a[1], a[1], s5_sin[j % 3], ALU.mult).then_inc(s5_p.h, 1)

            def skip(i):
                dve.e.wait_ge(yy_ps.h, 4 * i + 4)
                dcol = R2["s5_d_2"] + i
                stt(T(e_u + i), T(e_u + i), col2[:, dcol:dcol + 1], pb[6 + i % 2][:, :], ALU.mult, ALU.add).then_inc(s5_y.h, 1)
            angles(0)
            for j in range(NST + 1):
                if j + 1 < NST:
                    angles(j + 1)
                if j < NST:
                    rotate_in(j)
                if j >= 1:
                    scan(j - 1)
                if j >= 6 and (j - 6) % 4 == 0:
                    skip((j - 6) // 4)
            for i in range((NST - 6) // 4 + 1, 4):
                skip(i)
            for i in range(8):
                dve.e.wait_ge(rot_ps.h, i + 1)
                if i >= 2:
                    dve.e.wait_ge(rot_ready.h, i - 1)
                tt(s5_n[i % 2], pb[i % 2][:, :], T(e_sin), ALU.mult).then_inc(rot_s.h, 1)

        def dve_odd(dve):
            V = nc.vector
            ts, tt, stt = V.tensor_scalar, V.tensor_tensor, V.scalar_tensor_tensor
            V.memset(xpad[:, :, 0:LRU_TAPS - 1], 0.0).then_inc(pad_zero.h, 1)
            sp_n = count(1)
            lam = col2[:, R2["rg_lam_2"]:R2["rg_lam_2"] + KD]
            S = [spc[:, i, :] for i in range(8)]
            ts(S[2], lam, -1.0, None, ALU.mult).then_inc(sp_step.h, 1)
            dve.e.wait_ge(sp_step.h, next(sp_n))
            tt(S[0], lam, S[2], ALU.max).then_inc(sp_step.h, 1)
            dve.e.wait_ge(sp_step.h, next(sp_n))
            dve.e.wait_ge(par_act.h, 5)
            ts(S[3], S[1], 2.0, None, ALU.add).then_inc(sp_step.h, 1)
            dve.e.wait_ge(sp_step.h, next(sp_n))
            V.reciprocal(S[3], S[3]).then_inc(sp_step.h, 1)
            dve.e.wait_ge(sp_step.h, next(sp_n))
            tt(S[3], S[1], S[3], ALU.mult).then_inc(sp_step.h, 1)
            dve.e.wait_ge(sp_step.h, next(sp_n))
            tt(S[4], S[3], S[3], ALU.mult).then_inc(sp_step.h, 1)
            dve.e.wait_ge(sp_step.h, next(sp_n))
            ts(S[5], S[4], 1 / 19, None, ALU.mult).then_inc(sp_step.h, 1)
            dve.e.wait_ge(sp_step.h, next(sp_n))
            for o in (17, 15, 13, 11, 9, 7, 5, 3):
                stt(S[5], S[5], 1 / o, S[4], ALU.add, ALU.mult).then_inc(sp_step.h, 1)
                dve.e.wait_ge(sp_step.h, next(sp_n))
            stt(S[5], S[5], 1.0, S[3], ALU.add, ALU.mult).then_inc(sp_step.h, 1)
            dve.e.wait_ge(sp_step.h, next(sp_n))
            ts(S[2], S[2], 0.0, None, ALU.max).then_inc(sp_step.h, 1)
            dve.e.wait_ge(sp_step.h, next(sp_n))
            stt(S[6], S[5], 2.0, S[2], ALU.mult, ALU.add).then_inc(sp_step.h, 1)
            dve.e.wait_ge(sp_step.h, next(sp_n))
            ts(S[7], S[6], -8.0, None, ALU.mult).then_inc(sp_step.h, 1)
            dve.e.wait_ge(sp_step.h, next(sp_n))
            assert next(sp_n) == SP_STEPS + 1
            for k in range(KD):
                dve.e.wait_ge(oz_sb.h, k + 1)
                for j in range(LRU_TAPS):
                    w = R2["rg_conv_w_2"] + j * KD + k
                    w = col2[:, w:w + 1]
                    src = xpad[:, k, j:j + SEQ]
                    if j == 0:
                        b = R2["rg_conv_b_2"] + k
                        ins = ts(T(o_xc + k), src, w, col2[:, b:b + 1], ALU.mult, ALU.add)
                    else:
                        dve.e.wait_ge(cv.h, LRU_TAPS * k + j)
                        ins = stt(T(o_xc + k), src, w, T(o_xc + k), ALU.mult, ALU.add)
                    ins.then_inc(cv.h, 1)
            for k in range(KD):
                dve.e.wait_ge(o_a2.h, k + 1)
                stt(o_fac[:, k, :], xpad[:, k, 0:SEQ], 1.0, o_fac[:, k, :], ALU.add, ALU.mult).then_inc(o_q.h, 1)
            st = STAGES["out", "odd"]
            dve_units(dve, st, 0, SLOTS)
            for k in range(KD):
                dve.e.wait_ge(o_gx.h, k + 1)
                dve.e.wait_ge(o_sqrt.h, k + 1)
                tt(T(o_i + k), T(o_i + k), o_fac[:, k, :], ALU.mult).then_inc(o_b.h, 1)
                dve.e.wait_ge(o_b.h, k + 1)
                V.tensor_tensor_scan(T(o_xc + k), T(o_r + k), T(o_i + k), 0.0, ALU.mult, ALU.add).then_inc(o_h.h, 1)
                if k >= 3:
                    split_chunk(dve, st, k - 3, k - 3)
            for k in range(KD - 3, KD):
                split_chunk(dve, st, k, k)
            dve_units(dve, st, SLOTS, KD)

        @block.vector
        def _(e):
            dve = Eng(e)
            e.sem_inc(h_full.h, h_full.start)
            nc.vector.memset(relb[32:64, :], NEG).then_inc(relb_neg.h, 1)
            dve.e.wait_ge(rows_zero.h, 1)
            dve.e.wait_ge(ldt_in.h, 16)
            nc.vector.tensor_copy(rows[32:32 + NST, 3, :].rearrange("j (q p) -> j q p", q=2),
                                  ldt[32:32 + NST, :].unsqueeze(2).to_broadcast([NST, 2, SSM_P])).then_inc(ldt_row.h, 1)
            for k in range(KD):
                dve.e.wait_ge(pro_ps.h, k + 1)
                nc.vector.tensor_copy(x[:, k, :], pb[k % 2][:, :]).then_inc(x_ready.h, 1)
            dve.e.wait_ge(consts_in.h, 16)
            dve.e.wait_ge(pro_sb.h, 4)
            for l in range(DEPTH):
                dve.l = l
                nc.vector.tensor_copy(cur[:, :], col2[:, bass.ds(l * NRL, NRL)]).then_inc(cur_ready.h, 1)
                nc.vector.tensor_copy(cur_dw[:, :], col3[:, bass.ds(l * TAPS * 2, TAPS * 2)]).then_inc(cur_ready.h, 1)
                dve.e.wait_ge(cur_ready.h, cur_ready.by(dve.l, 1))
                for n, s in (("a_q_norm", A_DIM ** -0.5), ("d_q_norm", D_QK ** -0.5)):
                    c = cur[:, RL[n]:RL[n] + 1]
                    nc.vector.tensor_scalar(c, c, float(s), None, ALU.mult).then_inc(cur_ready.h, 1)

                def gain(name):
                    return lambda k: col1[:, bass.ds(l * KD + (R1[name] + k), 1)]
                dve_norm(dve, l * 3, gain("ffn1_norm"), STAGES["ffn1", l])
                dve_ffn(dve, STAGES["ffn1", l], add_half)
                dve_norm(dve, l * 3 + 1, gain("mix_norm"), STAGES["in", l])
                dve_index(dve)
                dve_conv(dve)
                dve_mixers(dve)
                dve_attention(dve, HYB_UNITS, STAGES["out", l], Y_HYB)
                dve_take(dve, STAGES["out", l], add)
                dve_norm(dve, l * 3 + 2, gain("ffn2_norm"), STAGES["ffn2", l])
                dve_ffn(dve, STAGES["ffn2", l], add_half)
            dve.l = DEPTH
            def gain2(name, i):
                return lambda k: col1[:, R1[name] + i * KD + k:R1[name] + i * KD + k + 1]
            n = 3 * DEPTH
            dve_norm(dve, n, gain2("norm_mix_pre_2", 0))
            dve_even(dve)
            dve_attention(dve, E_UNITS, STAGES["out", "even"], Y_EVEN)
            dve_take(dve, STAGES["out", "even"], to_r)
            dve_post(dve, 0, gain2("norm_mix_post_2", 0))
            dve_norm(dve, n + 1, gain2("norm_ffn_pre_2", 0), STAGES["ffn", "even"])
            dve_ffn(dve, STAGES["ffn", "even"], to_r)
            dve_post(dve, 1, gain2("norm_ffn_post_2", 0))
            dve_norm(dve, n + 2, gain2("norm_mix_pre_2", 1), STAGES["in", "odd"])
            dve_odd(dve)
            dve_take(dve, STAGES["out", "odd"], to_r)
            dve_post(dve, 2, gain2("norm_mix_post_2", 1))
            dve_norm(dve, n + 3, gain2("norm_ffn_pre_2", 1), STAGES["ffn", "odd"])
            dve_ffn(dve, STAGES["ffn", "odd"], to_r)
            dve_post(dve, 3, gain2("norm_ffn_post_2", 1))

        def pool_units(pool, st, a, b):
            for n in range(a, b):
                q = n % SLOTS
                pool.e.wait_ge(u_hi.h, st.units + n + 1)
                nc.gpsimd.tensor_tensor(w_lo[:, q, :, :].rearrange("p k c -> p (k c)"), wunit[:, q, :],
                                        w_hi[:, q, :, :].rearrange("p k c -> p (k c)").bitcast(F32),
                                        ALU.subtract).then_inc(u_lo.h, 1)

        def pool_z(pool, st):
            for n in range(2, NZU):
                pool_units(pool, st, n, n + 1)
                for ct in range(2):
                    if n == Z_LABELS.index(f"ca{ct}") + 3:
                        pool.e.wait_ge(z_sb.h, z_sb.by(pool.l, max(Z_POS[f"ca{ct}"], Z_POS[f"cg{ct}"]) + 1))
                        nc.gpsimd.tensor_tensor(hpad[:, ct, TAPS - 1:], T(t_ca[ct]), T(t_cg[ct]),
                                                ALU.mult).then_inc(hp_ready.h, 1)

        def pool_mixers(pool):
            pool.e.wait_ge(g_exp.h, g_exp.by(pool.l, 3))
            nc.gpsimd.tensor_tensor(W(w_e1n), W(w_e1n), T(t_bk), ALU.mult).then_inc(b_kd.h, 1)
            pool.e.wait_ge(b_kd.h, b_kd.by(pool.l, 1))
            pool.e.wait_ge(g_exp.h, g_exp.by(pool.l, 5))
            for h in range(B_HEADS):
                nc.gpsimd.tensor_scalar(kdm[h], W(w_e1n), C("headcol")[:, h:h + 1], None, ALU.mult).then_inc(b_kd.h, 1)
            for u in range(8):
                dst = T((t_dq + t_dk)[u])[0:D_QK, :]
                pool.e.wait_ge(dn_x.h, dn_x.by(pool.l, u + 1))
                nc.gpsimd.tensor_tensor(dst, T(t_hn[u % 2])[0:D_QK, :], C("cos96")[0:D_QK, :], ALU.mult).then_inc(dr_c.h, 1)
                pool.e.wait_ge(dr_c.h, dr_c.by(pool.l, u + 1))
                pool.e.wait_ge(dr_s.h, dr_s.by(pool.l, u + 1))
                nc.gpsimd.tensor_tensor(dst, dst, T(t_hr[u % 2])[0:D_QK, :], ALU.add).then_inc(dh_ready.h, 1)
            for pr in range(2):
                pool.e.wait_ge(o_n.h, o_n.by(pool.l, pr + 1))
                nc.gpsimd.tensor_tensor(y[:, 2 + pr, :], T(t_o[pr]), T(t_br[pr]), ALU.mult).then_inc(y_b.h, 1)

        def pool_attention(pool, units):
            U = len(units)
            for i in range(U + 1):
                for u in ([0, 1, 2] if i == 0 else [i + 2]):
                    if u in BM and units is HYB_UNITS:
                        _, h, tb = units[u]
                        n = BM.index(u)
                        if n == 0:
                            pool.e.wait_ge(top_done.h, top_done.by(pool.l, 3))
                            pool.e.wait_ge(pro_sb.h, 4 + 2 + A_HEADS)
                        if n >= 3:
                            pool.e.wait_ge(att_s.h, att_s.by(pool.l, BM[n - 3] + 1))
                        nc.gpsimd.tensor_tensor(T(t_bm[n % 3])[:, 0:(tb + 1) * P], bias[:, h, SEQ - (tb + 1) * P:],
                                                score(tb), ALU.add).then_inc(att_bm.h, 1)
                if i >= 1:
                    u = i - 1
                    c = u % 4
                    pool.e.wait_ge(att_rs.h, att_rs.by(pool.l, u + 1))
                    p = p_buf(units, u)[:, 0:(units[u][2] + 1) * P]
                    nc.gpsimd.tensor_scalar(p, p, rsum[:, c:c + 1], None, ALU.mult).then_inc(att_p.h, 1)

        def pool_even(pool):
            G = nc.gpsimd
            ts, tt = G.tensor_scalar, G.tensor_tensor

            def turns(j):
                if j >= 2:
                    pool.e.wait_ge(s5_quart.h, j - 1)
                ts(s5_n[j % 2], C("iota"), c_fr[:, j:j + 1], MAGIC, ALU.mult, ALU.add).then_inc(s5_rnd.h, 1)
                pool.e.wait_ge(s5_rnd.h, 2 * j + 1)
                ts(s5_n[j % 2], s5_n[j % 2], MAGIC, None, ALU.subtract).then_inc(s5_rnd.h, 1)

            def wrap(j):
                pool.e.wait_ge(s5_frac.h, j + 1)
                ts(s5_n[j % 2], s5_d[j % 2], 0.25, None, ALU.is_gt).then_inc(s5_wrap.h, 1)

            def frame(j):
                a = s5_a[j % 3]
                pool.e.wait_ge(s5_rot.h, j + 1)
                tt(a[0], a[0], a[1], ALU.add).then_inc(s5_x.h, 1)
                tt(a[2], a[2], a[3], ALU.subtract).then_inc(s5_x.h, 1)

            def back(j):
                a = s5_a[j % 3]
                pool.e.wait_ge(s5_g.h, 2 * j + 2)
                tt(a[2], a[3], s5_sin[j % 3], ALU.mult)
                tt(a[3], a[3], s5_cos[j % 3], ALU.mult).then_inc(s5_q.h, 1)
            pool.e.wait_ge(par.h, PAR_E)
            turns(0)
            turns(1)
            wrap(0)
            for j in range(NST + 1):
                if j + 1 < NST:
                    wrap(j + 1)
                if j + 2 < NST:
                    turns(j + 2)
                if j < NST:
                    frame(j)
                if j >= 1:
                    back(j - 1)
            for i in range(8):
                t = T((e_q if i % 2 == 0 else e_k) + i // 2)
                pool.e.wait_ge(rot_ps.h, i + 1)
                tt(t, t, T(e_cos), ALU.mult).then_inc(rot_c.h, 1)
                pool.e.wait_ge(rot_c.h, i + 1)
                pool.e.wait_ge(rot_s.h, i + 1)
                tt(t, t, s5_n[i % 2], ALU.add).then_inc(rot_ready.h, 1)
            for c in range(4):
                pool.e.wait_ge(glu_sb.h, c + 1)
                tt(y[:, 4 + c, :], T(e_u + c), T(e_glu + c), ALU.mult).then_inc(y_ssm.h, 1)

        def pool_odd(pool):
            tt = nc.gpsimd.tensor_tensor
            st = STAGES["in", "odd"]
            pool_units(pool, st, 2, 2 * KD)
            for k in range(KD):
                pool.e.wait_ge(og_sb.h, KD + k + 1)
                pool.e.wait_ge(cv.h, LRU_TAPS * (k + 1))
                tt(T(o_i + k), T(o_i + k), T(o_xc + k), ALU.mult).then_inc(o_gx.h, 1)
            for k in range(KD):
                pool.e.wait_ge(o_a.h, k + 1)
                tt(xpad[:, k, 0:SEQ], T(o_r + k), T(o_r + k), ALU.mult).then_inc(o_a2.h, 1)
            for k in range(KD):
                pool.e.wait_ge(o_h.h, k + 1)
                tt(y[:, k, :], T(o_xc + k), T(o_gel + k), ALU.mult).then_inc(y_lru.h, 1)

        @block.gpsimd
        def _(e):
            pool = Eng(e)
            nc.gpsimd.memset(rows[:, :, :], 0.0).then_inc(rows_zero.h, 1)
            pool.e.wait_ge(consts_in.h, 16)
            for l in range(DEPTH):
                pool.l = l
                pool.e.wait_ge(cur_ready.h, cur_ready.by(pool.l, 4))
                pool.e.wait_ge(unit_ps.h, STAGES["ffn1", l].units + 2 * NF)
                nc.gpsimd.memset(hpad[:, :, 0:TAPS - 1], 0.0)
                nc.gpsimd.memset(att_diag[:, :, :, :], 0.0).then_inc(zeros_set.h, 1)
                pool_z(pool, STAGES["in", l])
                pool_mixers(pool)
                pool_attention(pool, HYB_UNITS)
            pool.l = DEPTH
            pool_even(pool)
            pool_attention(pool, E_UNITS)
            pool_odd(pool)


_NAMES = ["x", "ffn1_norm", "ffn1_gate", "ffn1_up", "ffn1_down", "mix_norm", "w_in", "a_q_norm", "a_k_norm", "rel_bias",
          "b_gate_up", "b_gate_bias", "b_out_norm", "c_dw_w", "c_dw_b", "c_norm", "d_qa_norm", "d_uq", "d_kva_norm",
          "d_ukv", "d_q_norm", "d_k_norm", "w_out", "ffn2_norm", "ffn2_gate", "ffn2_up", "ffn2_down", "positions_2",
          "norm_mix_pre_2", "norm_mix_post_2", "norm_ffn_pre_2", "norm_ffn_post_2", "ev_w_in_2", "ev_w_out_2",
          "s5_a_re_2", "s5_a_im_2", "s5_log_dt_2", "s5_b_re_2", "s5_b_im_2", "s5_c_re_2", "s5_c_im_2", "s5_d_2",
          "s5_w_glu_2", "od_w_in_2", "od_w_out_2", "rg_conv_w_2", "rg_conv_b_2", "rg_w_r_2", "rg_b_r_2", "rg_w_i_2",
          "rg_b_i_2", "rg_lam_2", "ffn_w_gate_2", "ffn_w_up_2", "ffn_w_down_2"]


def kernel(**inputs):
    import concourse.bacc as bacc
    from concourse.bass_utils import run_bass_kernel_spmd

    nc = bacc.Bacc("TRN2", target_bir_lowering=False, num_devices=1)
    arrays = {"in_" + n: np.ascontiguousarray(inputs[n]) for n in _NAMES}
    consts = shape_constants()
    arrays["in_consts"] = np.ascontiguousarray(np.concatenate(list(consts.values()), axis=1))
    I = {n[3:]: nc.dram_tensor(n, a.shape, mybir.dt.from_np(a.dtype), kind="ExternalInput").ap()
         for n, a in arrays.items()}
    out = nc.dram_tensor("out_x", (1, SEQ, D), F32, kind="ExternalOutput").ap()
    program(nc, I, out)
    r = run_bass_kernel_spmd(nc, [arrays], core_ids=[0])
    return r.results[0]["out_x"]
```
